# Optimizing a Trainium2 kernel written in Bass

```python
import math
import jax, jax.numpy as jnp
from jax import lax
import numpy as np

D_MODEL = 1024
BATCH = 1
SEQ = 512
DEPTH = 1

RET_HEADS = 4
RET_QK_DIM = 128
RET_V_DIM = 256
RET_CHUNK = 128
RET_QK_WIDTH = RET_HEADS * RET_QK_DIM
RET_V_WIDTH = RET_HEADS * RET_V_DIM
ROPE_BASE = 10000.0
SGU_GROUPS = 4
SGU_GROUP_DIM = 256
SGU_CHUNK = 128
SGU_WIDTH = SGU_GROUPS * SGU_GROUP_DIM
IN_WIDTHS = (RET_QK_WIDTH, RET_QK_WIDTH, RET_V_WIDTH, RET_V_WIDTH, SGU_WIDTH, SGU_WIDTH, D_MODEL, D_MODEL)
IN_WIDTH = 7168
IN_SPLITS = (512, 1024, 2048, 3072, 4096, 5120, 6144)
PEER_HEADS = 8
PEER_N_KEYS = 128
PEER_N_EXPERTS = PEER_N_KEYS * PEER_N_KEYS
PEER_KEY_DIM = 256
PEER_HALF = PEER_KEY_DIM // 2
PEER_TOPK = 16
PEER_TOKEN_BLOCK = 128
N_MOD = 6
EPS = 1e-6


def rms_norm(x, gain):
    xf = x.astype(jnp.float32)
    y = xf * lax.rsqrt(jnp.mean(xf * xf, axis=-1, keepdims=True) + EPS)
    return (y * gain.astype(jnp.float32)).astype(x.dtype)

def modulate(h, shift, scale):
    return h * (1 + scale[:, None, :]) + shift[:, None, :]

def rotary(x, pos):
    d = x.shape[-1]
    half = d // 2
    inv = ROPE_BASE ** (-jnp.arange(half, dtype=jnp.float32) * 2.0 / d)
    ang = pos[:, None] * inv[None, :]
    cos = jnp.cos(ang)[None, :, None, :].astype(x.dtype)
    sin = jnp.sin(ang)[None, :, None, :].astype(x.dtype)
    x1, x2 = x[..., :half], x[..., half:]
    return jnp.concatenate([x1 * cos - x2 * sin, x1 * sin + x2 * cos], axis=-1)

def retention(q, k, v):
    B, S, H, dk = q.shape
    dv = v.shape[-1]
    C = RET_CHUNK
    nc = S // C
    gamma = 1.0 - 2.0 ** (-5.0 - jnp.arange(H, dtype=jnp.float32))
    log_g = jnp.log(gamma)
    idx = jnp.arange(C, dtype=jnp.float32)
    diff = idx[:, None] - idx[None, :]
    decay_in = jnp.where((diff >= 0)[None], jnp.exp(log_g[:, None, None] * jnp.maximum(diff, 0.0)[None]), 0.0).astype(q.dtype)
    decay_q = jnp.exp(log_g[None, :] * (idx[:, None] + 1.0)).astype(q.dtype)[None, :, :, None]
    decay_k = jnp.exp(log_g[None, :] * (C - 1.0 - idx[:, None])).astype(q.dtype)[None, :, :, None]
    decay_chunk = jnp.exp(log_g * C).astype(q.dtype)[None, :, None, None]

    def to_chunks(t):
        return t.reshape(B, nc, C, H, t.shape[-1]).transpose(1, 0, 2, 3, 4)

    def step(state, inp):
        qi, ki, vi = inp
        s = jnp.einsum('bihd,bjhd->bhij', qi, ki) * decay_in
        inner = jnp.einsum('bhij,bjhv->bihv', s, vi)
        cross = jnp.einsum('bihd,bhdv->bihv', qi, state) * decay_q
        new_state = state * decay_chunk + jnp.einsum('bjhd,bjhv->bhdv', ki * decay_k, vi)
        return new_state, inner + cross

    state0 = jnp.zeros((B, H, dk, dv), q.dtype)
    _, y = lax.scan(step, state0, (to_chunks(q), to_chunks(k), to_chunks(v)))
    return y.transpose(1, 0, 2, 3, 4).reshape(B, S, H, dv)

def head_norm(y, gain):
    B, S = y.shape[:2]
    yf = y.astype(jnp.float32)
    mu = jnp.mean(yf, axis=-1, keepdims=True)
    var = jnp.mean(jnp.square(yf - mu), axis=-1, keepdims=True)
    yn = ((yf - mu) * lax.rsqrt(var + EPS)).reshape(B, S, -1)
    return (yn * gain.astype(jnp.float32)).astype(y.dtype)

def spatial_gating(u, sv, ln_g, ln_b, w_s, b_s):
    B, S, _ = u.shape
    vf = sv.astype(jnp.float32)
    mu = jnp.mean(vf, axis=-1, keepdims=True)
    var = jnp.mean(jnp.square(vf - mu), axis=-1, keepdims=True)
    vn = ((vf - mu) * lax.rsqrt(var + EPS) * ln_g.astype(jnp.float32) + ln_b.astype(jnp.float32)).astype(sv.dtype)
    nck = S // SGU_CHUNK
    vn = vn.reshape(B, nck, SGU_CHUNK, SGU_GROUPS, SGU_GROUP_DIM)
    mask = jnp.tril(jnp.ones((SGU_CHUNK, SGU_CHUNK), dtype=bool))
    ws = jnp.where(mask[None], w_s, jnp.zeros_like(w_s))
    mixed = jnp.einsum('gts,bnsgc->bntgc', ws, vn) + b_s.T[None, None, :, :, None]
    return u * mixed.reshape(B, S, SGU_WIDTH)

def peer(h, w_q, sub_keys, expert_u, expert_v):
    B, S, D = h.shape
    blocks = h.reshape(-1, PEER_TOKEN_BLOCK, D)
    K = PEER_TOPK

    def block(hb):
        T = hb.shape[0]
        q = (hb @ w_q).reshape(T, PEER_HEADS, 2, PEER_HALF)
        s = jnp.einsum('thpc,hpnc->thpn', q, sub_keys)
        sub_s, sub_i = lax.top_k(s, K)
        cand = (sub_s[:, :, 0, :, None] + sub_s[:, :, 1, None, :]).reshape(T, PEER_HEADS, K * K)
        top_s, top_i = lax.top_k(cand, K)
        k1 = jnp.take_along_axis(sub_i[:, :, 0], top_i // K, axis=-1)
        k2 = jnp.take_along_axis(sub_i[:, :, 1], top_i % K, axis=-1)
        expert = k1 * PEER_N_KEYS + k2
        g = jax.nn.softmax(top_s.astype(jnp.float32), axis=-1).astype(hb.dtype)
        ue = expert_u[expert]
        act = jax.nn.gelu(jnp.einsum('td,thkd->thk', hb, ue), approximate=False) * g
        ve = expert_v[expert]
        return jnp.einsum('thk,thkd->td', act, ve)

    return lax.map(block, blocks).reshape(B, S, D)

def first_inputs(seed: int = 0) -> dict:
    key = jax.random.key(seed)
    ks = jax.random.split(key, 21)
    L, D = DEPTH, D_MODEL
    f32 = jnp.float32
    nrm = lambda k, shape, s: jax.random.normal(k, shape, f32) * s
    return {
        "x": nrm(ks[0], (BATCH, SEQ, D), 1.0),
        "c": nrm(ks[1], (BATCH, D), 1.0),
        "w_ada": nrm(ks[2], (L, D, N_MOD * D), 0.5 * D ** -0.5),
        "b_ada": nrm(ks[3], (L, N_MOD * D), 0.01),
        "norm1_g": 1.0 + nrm(ks[4], (L, D), 0.02),
        "w_in": nrm(ks[5], (L, D, IN_WIDTH), D ** -0.5),
        "ret_gn_g": 1.0 + nrm(ks[6], (L, RET_V_WIDTH), 0.02),
        "sgu_ln_g": 1.0 + nrm(ks[7], (L, SGU_WIDTH), 0.02),
        "sgu_ln_b": nrm(ks[8], (L, SGU_WIDTH), 0.01),
        "sgu_w": nrm(ks[9], (L, SGU_GROUPS, SGU_CHUNK, SGU_CHUNK), 0.5 * SGU_CHUNK ** -0.5),
        "sgu_b": 1.0 + nrm(ks[10], (L, SGU_GROUPS, SGU_CHUNK), 0.01),
        "w_ret_out": nrm(ks[11], (L, RET_V_WIDTH, D), RET_V_WIDTH ** -0.5),
        "w_sgu_out": nrm(ks[12], (L, SGU_WIDTH, D), SGU_WIDTH ** -0.5),
        "w_out": nrm(ks[13], (L, D, D), D ** -0.5),
        "norm2_g": 1.0 + nrm(ks[14], (L, D), 0.02),
        "peer_w_q": nrm(ks[15], (L, D, PEER_HEADS * PEER_KEY_DIM), D ** -0.5),
        "peer_sub_keys": nrm(ks[16], (L, PEER_HEADS, 2, PEER_N_KEYS, PEER_HALF), PEER_HALF ** -0.5),
        "peer_u": nrm(ks[17], (L, PEER_N_EXPERTS, D), D ** -0.5),
        "peer_v": nrm(ks[18], (L, PEER_N_EXPERTS, D), 1.0),
        "final_g": 1.0 + nrm(ks[19], (D,), 0.02),
    }

def first_block(x, c, w_ada, b_ada, norm1_g, w_in, ret_gn_g, sgu_ln_g, sgu_ln_b, sgu_w, sgu_b, w_ret_out, w_sgu_out, w_out, norm2_g, peer_w_q, peer_sub_keys, peer_u, peer_v, final_g):
    B, S, D = x.shape
    pos = jnp.arange(S, dtype=jnp.float32)
    c_act = jax.nn.silu(c)
    for l in range(DEPTH):
        mod = c_act @ w_ada[l] + b_ada[l]
        shift1, scale1, gate1, shift2, scale2, gate2 = jnp.split(mod, N_MOD, axis=-1)

        h = modulate(rms_norm(x, norm1_g[l]), shift1, scale1)
        proj = h @ w_in[l]
        q, k, v, g_ret, u, sv, gate_a, gate_b = jnp.split(proj, IN_SPLITS, axis=-1)

        q = rotary(q.reshape(B, S, RET_HEADS, RET_QK_DIM), pos)
        k = rotary(k.reshape(B, S, RET_HEADS, RET_QK_DIM), pos) * (RET_QK_DIM ** -0.5)
        v = v.reshape(B, S, RET_HEADS, RET_V_DIM)
        y_ret = head_norm(retention(q, k, v), ret_gn_g[l])
        branch_a = (jax.nn.silu(g_ret) * y_ret) @ w_ret_out[l]

        y_sgu = spatial_gating(jax.nn.gelu(u, approximate=False), jax.nn.gelu(sv, approximate=False),
                               sgu_ln_g[l], sgu_ln_b[l], sgu_w[l], sgu_b[l])
        branch_b = y_sgu @ w_sgu_out[l]

        merged = jax.nn.sigmoid(gate_a) * branch_a + jax.nn.sigmoid(gate_b) * branch_b
        x = x + gate1[:, None, :] * (merged @ w_out[l])

        h2 = modulate(rms_norm(x, norm2_g[l]), shift2, scale2)
        x = x + gate2[:, None, :] * peer(h2, peer_w_q[l], peer_sub_keys[l], peer_u[l], peer_v[l])
    return rms_norm(x, final_g)


_first_inputs = first_inputs


def first_inputs(seed=0):
    import zlib

    import numpy as np

    out = dict(_first_inputs(seed))
    spreads = {}
    factors = {'norm1_g': 4.22,
     'ret_gn_g': 187.671,
     'sgu_ln_g': 200.0,
     'sgu_ln_b': 200.0,
     'sgu_b': 200.0,
     'final_g': 20.429,
     'norm2_g': 64.0}
    for name, (base, spread) in spreads.items():
        noise = np.random.default_rng([zlib.crc32(name.encode()), seed]).standard_normal(out[name].shape)
        drawn = base * np.exp(spread * noise) if base else spread * noise
        out[name] = __import__('jax').numpy.asarray(drawn.astype(out[name].dtype))
    for name, factor in factors.items():
        out[name] = (out[name] * factor).astype(out[name].dtype)
    return out


_narrow_inputs = first_inputs


def first_inputs(seed=0):

    out = dict(_narrow_inputs(seed))
    wider = {'sgu_ln_g': 5.28, 'sgu_ln_b': 11.04, 'sgu_b': 3.48, 'final_g': 3.04}
    for name, times in wider.items():
        mean = out[name].mean()
        out[name] = (mean + times * (out[name] - mean)).astype(out[name].dtype)
    return out


CHUNK = 64
GDN_HEADS = 4
GDN_DK = 128
GDN_DV = 128
CONV_W = 4
GLA_HEADS = 4
GLA_DK = 64
GLA_DV = 128
GLA_RANK = 16
GLA_NORMALIZER = 16.0
HGRN_HEADS = 4
HGRN_EXPAND = 128
HGRN_DV = 128
LB_FLOOR = 1e-30
N_EXPERTS = 16
N_GROUPS = 4
EXPERTS_PER_GROUP = N_EXPERTS // N_GROUPS
TOP_K = 2
D_FF = 256
ALPHA = (2.0 * DEPTH) ** 0.25
BETA = (8.0 * DEPTH) ** -0.25
LN_EPS = 1e-5
RMS_EPS = 1e-6

GDN_QK = GDN_HEADS * GDN_DK
GDN_V = GDN_HEADS * GDN_DV
GLA_QK = GLA_HEADS * GLA_DK
GLA_V = GLA_HEADS * GLA_DV
HGRN_QK = HGRN_HEADS * HGRN_EXPAND
HGRN_V = HGRN_HEADS * HGRN_DV
SPLIT_SIZES = (GDN_QK, GDN_QK, GDN_V, GDN_HEADS, GDN_HEADS, GDN_V,
               GLA_QK, GLA_QK, GLA_V, GLA_RANK, GLA_V,
               HGRN_QK, HGRN_QK, HGRN_V, HGRN_V,
               D_MODEL, D_MODEL, D_MODEL)
SPLIT_POINTS = tuple(int(v) for v in np.cumsum(SPLIT_SIZES)[:-1])
IN_WIDTH_2 = int(sum(SPLIT_SIZES))


def layer_norm(x, g, b):
    xf = x.astype(jnp.float32)
    mu = xf.mean(-1, keepdims=True)
    var = jnp.square(xf - mu).mean(-1, keepdims=True)
    return ((xf - mu) * lax.rsqrt(var + LN_EPS) * g.astype(jnp.float32) + b.astype(jnp.float32)).astype(x.dtype)

def l2_normalize(x):
    return x * lax.rsqrt(jnp.sum(jnp.square(x), -1, keepdims=True) + RMS_EPS)

def to_chunks(x, n_heads):
    b, s, w = x.shape
    return x.reshape(b, s // CHUNK, CHUNK, n_heads, w // n_heads).transpose(0, 3, 1, 2, 4)

def scalar_to_chunks(x):
    b, s, h = x.shape
    return x.reshape(b, s // CHUNK, CHUNK, h).transpose(0, 3, 1, 2)

def from_chunks(o):
    b, h, n, c, d = o.shape
    return o.transpose(0, 2, 3, 1, 4).reshape(b, n * c, h * d)

def masked_exp(diff, mask):
    return jnp.where(mask, jnp.exp(jnp.where(mask, diff, 0.0)), 0.0)

def gated_rms_heads(o, gate, g, n_heads):
    b, s, w = o.shape
    oh = o.astype(jnp.float32).reshape(b, s, n_heads, w // n_heads)
    oh = oh * lax.rsqrt(jnp.mean(jnp.square(oh), -1, keepdims=True) + RMS_EPS) * g.astype(jnp.float32)
    gh = jax.nn.silu(gate.astype(jnp.float32)).reshape(b, s, n_heads, w // n_heads)
    return (oh * gh).reshape(b, s, w).astype(gate.dtype)

def causal_short_conv(x, w):
    s = x.shape[1]
    xp = jnp.pad(x, ((0, 0), (CONV_W - 1, 0), (0, 0)))
    y = xp[:, 0:s] * w[0]
    for k in range(1, CONV_W):
        y = y + xp[:, k:k + s] * w[k]
    return y

def gated_delta_rule(q, k, v, beta, log_decay):
    c = q.shape[-2]
    incl = jnp.tril(jnp.ones((c, c), bool))
    strict = jnp.tril(jnp.ones((c, c), bool), -1)
    cum = jnp.cumsum(log_decay, axis=-1)
    diff = cum[..., :, None] - cum[..., None, :]
    decay_mat = masked_exp(diff, incl)
    kk = jnp.einsum('bhnid,bhnjd->bhnij', k, k)
    a_strict = jnp.where(strict, beta[..., :, None] * kk * decay_mat, 0.0)
    t_mat = a_strict + jnp.eye(c, dtype=q.dtype)
    rhs = jnp.concatenate([v * beta[..., None], k * (beta * jnp.exp(cum))[..., None]], -1)
    sol = lax.linalg.triangular_solve(t_mat, rhs, left_side=True, lower=True, unit_diagonal=True)
    u, w = sol[..., :v.shape[-1]], sol[..., v.shape[-1]:]
    attn = jnp.einsum('bhnid,bhnjd->bhnij', q, k) * decay_mat
    q_inter = q * jnp.exp(cum)[..., None]
    k_state = k * jnp.exp(cum[..., -1:] - cum)[..., None]
    last = jnp.exp(cum[..., -1])

    def step(s, xs):
        qi_c, u_c, w_c, attn_c, ks_c, last_c = xs
        v_new = u_c - jnp.einsum('bhcd,bhde->bhce', w_c, s)
        o = jnp.einsum('bhcd,bhde->bhce', qi_c, s) + jnp.einsum('bhij,bhje->bhie', attn_c, v_new)
        s = s * last_c[..., None, None] + jnp.einsum('bhcd,bhce->bhde', ks_c, v_new)
        return s, o

    b, h = q.shape[0], q.shape[1]
    s0 = jnp.zeros((b, h, q.shape[-1], v.shape[-1]), q.dtype)
    xs = tuple(jnp.moveaxis(a, 2, 0) for a in (q_inter, u, w, attn, k_state, last))
    _, o = lax.scan(step, s0, xs)
    return jnp.moveaxis(o, 0, 2)

def diag_decay_linear_attention(q, k, v, log_a):
    c = q.shape[-2]
    incl = jnp.tril(jnp.ones((c, c), bool))[:, :, None]
    cum = jnp.cumsum(log_a, axis=-2)
    last = cum[..., -1:, :]
    q_inter = q * jnp.exp(cum)
    k_state = k * jnp.exp(last - cum)
    decay_last = jnp.exp(last[..., 0, :])

    def step(s, xs):
        q_c, k_c, v_c, cum_c, qi_c, ks_c, dl_c = xs
        diff = cum_c[..., :, None, :] - cum_c[..., None, :, :]
        rel = masked_exp(diff, incl)
        attn = jnp.einsum('bhid,bhjd,bhijd->bhij', q_c, k_c, rel)
        o = jnp.einsum('bhij,bhje->bhie', attn, v_c) + jnp.einsum('bhid,bhde->bhie', qi_c, s)
        s = s * dl_c[..., :, None] + jnp.einsum('bhjd,bhje->bhde', ks_c, v_c)
        return s, o

    b, h = q.shape[0], q.shape[1]
    s0 = jnp.zeros((b, h, q.shape[-1], v.shape[-1]), q.dtype)
    xs = tuple(jnp.moveaxis(a, 2, 0) for a in (q, k, v, cum, q_inter, k_state, decay_last))
    _, o = lax.scan(step, s0, xs)
    return jnp.moveaxis(o, 0, 2)

def hybrid_mixer(x, lower_bound, w_in, gdn_conv, gdn_a_log, gdn_dt_bias, gdn_norm, gla_w2, gla_b2,
                 gla_norm, hgrn_norm, w_br_a, w_br_b, w_br_c, w_out):
    f32 = jnp.float32
    proj = x @ w_in
    (a_q, a_k, a_v, a_beta, a_dt, a_g, b_q, b_k, b_v, b_lr, b_g,
     c_q, c_f, c_i, c_g, m_a, m_b, m_c) = jnp.split(proj, SPLIT_POINTS, axis=-1)

    qkv = jax.nn.silu(causal_short_conv(jnp.concatenate([a_q, a_k, a_v], -1), gdn_conv)).astype(f32)
    aq, ak, av = jnp.split(qkv, (GDN_QK, 2 * GDN_QK), axis=-1)
    aq = l2_normalize(to_chunks(aq, GDN_HEADS)) * (GDN_DK ** -0.5)
    ak = l2_normalize(to_chunks(ak, GDN_HEADS))
    av = to_chunks(av, GDN_HEADS)
    beta = scalar_to_chunks(jax.nn.sigmoid(a_beta.astype(f32)))
    g_a = -jnp.exp(gdn_a_log.astype(f32)) * jax.nn.softplus(a_dt.astype(f32) + gdn_dt_bias.astype(f32))
    o_a = from_chunks(gated_delta_rule(aq, ak, av, beta, scalar_to_chunks(g_a)))
    o_a = gated_rms_heads(o_a, a_g, gdn_norm, GDN_HEADS)

    bq = to_chunks(b_q.astype(f32), GLA_HEADS) * (GLA_DK ** -0.5)
    bk = to_chunks(b_k.astype(f32), GLA_HEADS)
    bv = to_chunks(b_v.astype(f32), GLA_HEADS)
    log_alpha = jax.nn.log_sigmoid((b_lr @ gla_w2 + gla_b2).astype(f32)) / GLA_NORMALIZER
    o_b = from_chunks(diag_decay_linear_attention(bq, bk, bv, to_chunks(log_alpha, GLA_HEADS)))
    o_b = gated_rms_heads(o_b, b_g, gla_norm, GLA_HEADS)

    cf = c_f.astype(f32)
    lb = lower_bound.astype(f32)
    log_lb = jnp.log(jnp.maximum(lb, LB_FLOOR))
    log_f = jnp.logaddexp(log_lb, jnp.log1p(-lb) + jax.nn.log_sigmoid(cf))
    k_c = (1.0 - lb) * jax.nn.sigmoid(-cf)
    cq = to_chunks(jax.nn.silu(c_q.astype(f32)), HGRN_HEADS) * (HGRN_EXPAND ** -0.5)
    o_c = from_chunks(diag_decay_linear_attention(cq, to_chunks(k_c, HGRN_HEADS),
                                                  to_chunks(c_i.astype(f32), HGRN_HEADS),
                                                  to_chunks(log_f, HGRN_HEADS)))
    o_c = gated_rms_heads(o_c, c_g, hgrn_norm, HGRN_HEADS)

    y = (jax.nn.sigmoid(m_a) * (o_a @ w_br_a) + jax.nn.sigmoid(m_b) * (o_b @ w_br_b)
         + jax.nn.sigmoid(m_c) * (o_c @ w_br_c))
    return y @ w_out

def grouped_moe(x, w_router, router_bias, w_gate, w_up, w_down):
    b, s, d = x.shape
    t = x.reshape(b * s, d)
    scores = jax.nn.sigmoid((t @ w_router).astype(jnp.float32))
    sel = (scores + router_bias.astype(jnp.float32)).reshape(-1, N_GROUPS, EXPERTS_PER_GROUP)
    group_score = lax.top_k(sel, TOP_K)[0].sum(-1)
    g_idx = jnp.argmax(group_score, axis=-1)
    in_group = jnp.take_along_axis(sel, g_idx[:, None, None], axis=1)[:, 0]
    _, e_local = lax.top_k(in_group, TOP_K)
    e_idx = g_idx[:, None] * EXPERTS_PER_GROUP + e_local
    w_sel = jnp.take_along_axis(scores, e_idx, axis=1)
    w_sel = w_sel / jnp.sum(w_sel, -1, keepdims=True)
    combine = jnp.sum(jax.nn.one_hot(e_idx, N_EXPERTS, dtype=jnp.float32) * w_sel[..., None], 1)
    h = jax.nn.silu(jnp.einsum('td,edf->tef', t, w_gate)) * jnp.einsum('td,edf->tef', t, w_up)
    y = jnp.einsum('tef,efd->td', h * combine[..., None].astype(h.dtype), w_down)
    return y.reshape(b, s, d)

def second_inputs(seed: int = 0) -> dict:
    key = jax.random.key(seed)
    ks = jax.random.split(key, 26)
    f32 = jnp.float32

    def nrm(k, shape, scale):
        return jax.random.normal(k, shape, f32) * scale

    dt = jnp.exp(jax.random.uniform(ks[6], (DEPTH, GDN_HEADS), f32, math.log(1e-3), math.log(1e-1)))
    return {
        "x": nrm(ks[0], (BATCH, SEQ, D_MODEL), 1.0),
        "ln0_g": 1.0 + nrm(ks[1], (D_MODEL,), 0.02),
        "ln0_b": nrm(ks[2], (D_MODEL,), 0.02),
        "w_in": nrm(ks[3], (DEPTH, D_MODEL, IN_WIDTH_2), D_MODEL ** -0.5),
        "gdn_conv": nrm(ks[4], (DEPTH, CONV_W, 2 * GDN_QK + GDN_V), CONV_W ** -0.5),
        "gdn_a_log": jnp.log(jax.random.uniform(ks[5], (DEPTH, GDN_HEADS), f32, 1.0, 16.0)),
        "gdn_dt_bias": dt + jnp.log(-jnp.expm1(-dt)),
        "gdn_norm": 1.0 + nrm(ks[7], (DEPTH, GDN_DV), 0.02),
        "gla_w2": nrm(ks[8], (DEPTH, GLA_RANK, GLA_QK), GLA_RANK ** -0.5),
        "gla_b2": nrm(ks[9], (DEPTH, GLA_QK), 0.1),
        "gla_norm": 1.0 + nrm(ks[10], (DEPTH, GLA_DV), 0.02),
        "hgrn_lb_logits": nrm(ks[11], (DEPTH, HGRN_QK), 0.5),
        "hgrn_norm": 1.0 + nrm(ks[12], (DEPTH, HGRN_DV), 0.02),
        "w_br_a": nrm(ks[13], (DEPTH, GDN_V, D_MODEL), BETA * GDN_V ** -0.5),
        "w_br_b": nrm(ks[14], (DEPTH, GLA_V, D_MODEL), BETA * GLA_V ** -0.5),
        "w_br_c": nrm(ks[15], (DEPTH, HGRN_V, D_MODEL), BETA * HGRN_V ** -0.5),
        "w_out": nrm(ks[16], (DEPTH, D_MODEL, D_MODEL), BETA * D_MODEL ** -0.5),
        "ln1_g": 1.0 + nrm(ks[17], (DEPTH, D_MODEL), 0.02),
        "ln1_b": nrm(ks[18], (DEPTH, D_MODEL), 0.02),
        "w_router": nrm(ks[19], (D_MODEL, N_EXPERTS), D_MODEL ** -0.5),
        "router_bias": nrm(ks[20], (N_EXPERTS,), 0.01),
        "w_gate": nrm(ks[21], (DEPTH, N_EXPERTS, D_MODEL, D_FF), BETA * D_MODEL ** -0.5),
        "w_up": nrm(ks[22], (DEPTH, N_EXPERTS, D_MODEL, D_FF), BETA * D_MODEL ** -0.5),
        "w_down": nrm(ks[23], (DEPTH, N_EXPERTS, D_FF, D_MODEL), BETA * D_FF ** -0.5),
        "ln2_g": 1.0 + nrm(ks[24], (DEPTH, D_MODEL), 0.02),
        "ln2_b": nrm(ks[25], (DEPTH, D_MODEL), 0.02),
    }

def second_block(x, ln0_g, ln0_b, w_in, gdn_conv, gdn_a_log, gdn_dt_bias, gdn_norm, gla_w2, gla_b2,
              gla_norm, hgrn_lb_logits, hgrn_norm, w_br_a, w_br_b, w_br_c, w_out, ln1_g, ln1_b,
              w_router, router_bias, w_gate, w_up, w_down, ln2_g, ln2_b):
    p = jax.nn.softmax(hgrn_lb_logits.astype(jnp.float32), axis=0)
    lower_bounds = jnp.clip(jnp.cumsum(p, axis=0) - p[0], 0.0, 1.0)
    h = layer_norm(x, ln0_g, ln0_b)
    for l in range(DEPTH):
        mix = hybrid_mixer(h, lower_bounds[l], w_in[l], gdn_conv[l], gdn_a_log[l], gdn_dt_bias[l],
                           gdn_norm[l], gla_w2[l], gla_b2[l], gla_norm[l], hgrn_norm[l],
                           w_br_a[l], w_br_b[l], w_br_c[l], w_out[l])
        h = layer_norm(ALPHA * h + mix, ln1_g[l], ln1_b[l])
        ffn = grouped_moe(h, w_router, router_bias, w_gate[l], w_up[l], w_down[l])
        h = layer_norm(ALPHA * h + ffn, ln2_g[l], ln2_b[l])
    return h


_first_inputs_2 = second_inputs


def second_inputs(seed=0):
    import zlib

    import numpy as np

    out = dict(_first_inputs_2(seed))
    spreads = {}
    factors = {'gdn_a_log': 7.329,
     'gdn_norm': 8.0,
     'gla_w2': 4.849,
     'gla_b2': 8.0,
     'gla_norm': 8.0,
     'hgrn_norm': 8.0,
     'router_bias': 2.971,
     'ln2_g': 2.858,
     'ln2_b': 2.806}
    for name, (base, spread) in spreads.items():
        noise = np.random.default_rng([zlib.crc32(name.encode()), seed]).standard_normal(out[name].shape)
        drawn = base * np.exp(spread * noise) if base else spread * noise
        out[name] = __import__('jax').numpy.asarray(drawn.astype(out[name].dtype))
    for name, factor in factors.items():
        out[name] = (out[name] * factor).astype(out[name].dtype)
    return out


_narrow_inputs_2 = second_inputs


def second_inputs(seed=0):

    out = dict(_narrow_inputs_2(seed))
    wider = {'gdn_norm': 5.08, 'gla_norm': 4.42, 'hgrn_norm': 5.36, 'ln2_g': 3.21, 'ln2_b': 3.22}
    for name, times in wider.items():
        mean = out[name].mean()
        out[name] = (mean + times * (out[name] - mean)).astype(out[name].dtype)
    return out


M_HEADS = 8
M_DQK = 64
M_DV = 128
M_QK = M_HEADS * M_DQK
M_V = M_HEADS * M_DV
M_CONV = 4
S_HEADDIM = 64
S_INNER = D_MODEL
S_HEADS = S_INNER // S_HEADDIM
S_GROUPS = 4
S_STATE = 128
S_CONV = 4
S_XBC = S_INNER + 2 * S_GROUPS * S_STATE
D_FF_3 = 2752
FFN_CONV = 3
IN_SIZES = (M_QK, M_QK, M_V, M_V, M_HEADS, M_HEADS, S_INNER, S_XBC, S_HEADS, D_MODEL, D_MODEL)
D_IN = sum(IN_SIZES)
ALPHA_3 = (2 * DEPTH) ** 0.25
BETA_3 = (8 * DEPTH) ** -0.25
NEG_BIG = -1e30


def layer_norm_3(x, g, b):
    xf = x.astype(jnp.float32)
    mu = jnp.mean(xf, -1, keepdims=True)
    var = jnp.mean(jnp.square(xf - mu), -1, keepdims=True)
    return ((xf - mu) * lax.rsqrt(var + LN_EPS) * g.astype(jnp.float32) + b.astype(jnp.float32)).astype(x.dtype)

def group_rms_norm(x, g, n_groups):
    shp = x.shape
    xf = x.astype(jnp.float32).reshape(shp[:-1] + (n_groups, shp[-1] // n_groups))
    xf = xf * lax.rsqrt(jnp.mean(xf * xf, -1, keepdims=True) + RMS_EPS)
    return (xf.reshape(shp) * g.astype(jnp.float32)).astype(x.dtype)

def causal_dwconv(x, w, b):
    K, C = w.shape
    y = lax.conv_general_dilated(x, w[:, None, :], window_strides=(1,), padding=[(K - 1, 0)],
                                 dimension_numbers=('NWC', 'WIO', 'NWC'), feature_group_count=C)
    return y + b

def mlstm_chunkwise(q, k, v, i_pre, f_pre):
    f32 = jnp.float32
    Bsz, T = q.shape[0], q.shape[1]
    nc = T // CHUNK

    def chunks(a):
        a = a.reshape((Bsz, nc, CHUNK) + a.shape[2:])
        return jnp.moveaxis(a, 3, 1)

    qc = chunks(q.astype(f32))
    kc = chunks(k.astype(f32)) * (M_DQK ** -0.5)
    vc = chunks(v.astype(f32))
    log_i = chunks(i_pre.astype(f32))
    log_f = jax.nn.log_sigmoid(chunks(f_pre.astype(f32)))
    b = jnp.cumsum(log_f, -1)
    g = b[..., -1]

    a = g[..., None] - b + log_i
    m_loc = jnp.max(a, -1)
    w_s = jnp.exp(a - m_loc[..., None])
    kw = kc * w_s[..., None]
    c_loc = jnp.einsum('bhcsk,bhcsv->bhckv', kw, vc)
    n_loc = jnp.sum(kw, 3)

    def step(carry, inp):
        C, n, m = carry
        g_c, m_l, C_l, n_l = inp
        m_new = jnp.maximum(g_c + m, m_l)
        s_prev = jnp.exp(g_c + m - m_new)
        s_loc = jnp.exp(m_l - m_new)
        C_new = s_prev[..., None, None] * C + s_loc[..., None, None] * C_l
        n_new = s_prev[..., None] * n + s_loc[..., None] * n_l
        return (C_new, n_new, m_new), (C, n, m)

    init = (jnp.zeros((Bsz, M_HEADS, M_DQK, M_DV), f32),
            jnp.zeros((Bsz, M_HEADS, M_DQK), f32),
            jnp.full((Bsz, M_HEADS), NEG_BIG, f32))
    xs = (jnp.moveaxis(g, 2, 0), jnp.moveaxis(m_loc, 2, 0),
          jnp.moveaxis(c_loc, 2, 0), jnp.moveaxis(n_loc, 2, 0))
    _, (C_prev, n_prev, m_prev) = lax.scan(step, init, xs)
    C_prev = jnp.moveaxis(C_prev, 0, 2)
    n_prev = jnp.moveaxis(n_prev, 0, 2)
    m_prev = jnp.moveaxis(m_prev, 0, 2)

    causal = jnp.tril(jnp.ones((CHUNK, CHUNK), bool))
    log_d = jnp.where(causal, b[..., :, None] - b[..., None, :] + log_i[..., None, :], -jnp.inf)
    m_inter = b + m_prev[..., None]
    m_comb = jnp.maximum(m_inter, jnp.max(log_d, -1))
    s_inter = jnp.exp(m_inter - m_comb)
    scores = jnp.einsum('bhctk,bhcsk->bhcts', qc, kc) * jnp.exp(log_d - m_comb[..., None])
    num = (jnp.einsum('bhcts,bhcsv->bhctv', scores, vc)
           + s_inter[..., None] * jnp.einsum('bhctk,bhckv->bhctv', qc, C_prev))
    den = jnp.sum(scores, -1) + s_inter * jnp.einsum('bhctk,bhck->bhct', qc, n_prev)
    h = num / jnp.maximum(jnp.abs(den), jnp.exp(-m_comb))[..., None]
    h = jnp.moveaxis(h, 1, 3).reshape(Bsz, T, M_HEADS, M_DV)
    return h.astype(q.dtype)

def segsum_exp(a):
    cs = jnp.cumsum(a, -1)
    L = a.shape[-1]
    causal = jnp.tril(jnp.ones((L, L), bool))
    return jnp.exp(jnp.where(causal, cs[..., :, None] - cs[..., None, :], -jnp.inf))

def ssd_chunked(x, dt, A, Bm, Cm):
    f32 = jnp.float32
    Bsz, T = x.shape[0], x.shape[1]
    nc = T // CHUNK
    R = S_HEADS // S_GROUPS
    dt = dt.astype(f32)
    xc = (x.astype(f32) * dt[..., None]).reshape(Bsz, nc, CHUNK, S_GROUPS, R, S_HEADDIM)
    a = (dt * A.astype(f32)).reshape(Bsz, nc, CHUNK, S_GROUPS, R)
    a = jnp.transpose(a, (0, 3, 4, 1, 2))
    Bc = Bm.astype(f32).reshape(Bsz, nc, CHUNK, S_GROUPS, S_STATE)
    Cc = Cm.astype(f32).reshape(Bsz, nc, CHUNK, S_GROUPS, S_STATE)
    a_cs = jnp.cumsum(a, -1)

    cb = jnp.einsum('bclgn,bcsgn->bgcls', Cc, Bc)
    mix = cb[:, :, None] * segsum_exp(a)
    y_diag = jnp.einsum('bgrcls,bcsgrp->bclgrp', mix, xc)

    decay_to_end = jnp.transpose(jnp.exp(a_cs[..., -1:] - a_cs), (0, 3, 4, 1, 2))
    states = jnp.einsum('bcsgn,bcsgrp->bcgrpn', Bc, xc * decay_to_end[..., None])

    chunk_decay = jnp.exp(a_cs[..., -1])

    def step(h, inp):
        dec, st = inp
        return dec[..., None, None] * h + st, h

    h0 = jnp.zeros((Bsz, S_GROUPS, R, S_HEADDIM, S_STATE), f32)
    _, h_prev = lax.scan(step, h0, (jnp.moveaxis(chunk_decay, 3, 0), jnp.moveaxis(states, 1, 0)))
    h_prev = jnp.moveaxis(h_prev, 0, 1)

    decay_in = jnp.transpose(jnp.exp(a_cs), (0, 3, 4, 1, 2))
    y_off = jnp.einsum('bclgn,bcgrpn->bclgrp', Cc, h_prev) * decay_in[..., None]
    return (y_diag + y_off).reshape(Bsz, T, S_HEADS, S_HEADDIM)

def mlstm_branch(q, k, v, o_pre, i_pre, f_pre, conv_w, conv_b, i_bias, f_bias, norm_g):
    Bsz, T = q.shape[0], q.shape[1]
    qk = jax.nn.silu(causal_dwconv(jnp.concatenate([q, k], -1), conv_w, conv_b))
    q, k = jnp.split(qk, 2, -1)
    h = mlstm_chunkwise(q.reshape(Bsz, T, M_HEADS, M_DQK), k.reshape(Bsz, T, M_HEADS, M_DQK),
                        v.reshape(Bsz, T, M_HEADS, M_DV), i_pre + i_bias, f_pre + f_bias)
    h = group_rms_norm(h.reshape(Bsz, T, M_V), norm_g, M_HEADS)
    return jax.nn.sigmoid(o_pre) * h

def mamba2_branch(z, xbc, dt_raw, conv_w, conv_b, dt_bias, a_log, d_skip, norm_g):
    Bsz, T = z.shape[0], z.shape[1]
    xbc = jax.nn.silu(causal_dwconv(xbc, conv_w, conv_b))
    xs, Bm, Cm = jnp.split(xbc, [S_INNER, S_INNER + S_GROUPS * S_STATE], -1)
    xs = xs.reshape(Bsz, T, S_HEADS, S_HEADDIM)
    Bm = Bm.reshape(Bsz, T, S_GROUPS, S_STATE)
    Cm = Cm.reshape(Bsz, T, S_GROUPS, S_STATE)
    dt = jax.nn.softplus(dt_raw.astype(jnp.float32) + dt_bias.astype(jnp.float32))
    A = -jnp.exp(a_log.astype(jnp.float32))
    y = ssd_chunked(xs, dt, A, Bm, Cm) + d_skip.astype(jnp.float32)[:, None] * xs.astype(jnp.float32)
    y = y.reshape(Bsz, T, S_INNER).astype(z.dtype)
    return group_rms_norm(y * jax.nn.silu(z), norm_g, S_GROUPS)

def third_inputs(seed: int = 0) -> dict:
    key = jax.random.key(seed)
    ks = jax.random.split(key, 32)
    L = DEPTH
    f32 = jnp.float32

    def nrm(k, shape, scale):
        return scale * jax.random.normal(k, shape, f32)

    dt0 = jnp.exp(jax.random.uniform(ks[12], (L, S_HEADS), f32, math.log(1e-3), math.log(1e-1)))
    return {
        "x": nrm(ks[0], (BATCH, SEQ, D_MODEL), 1.0),
        "in_ln_g": 1.0 + nrm(ks[1], (D_MODEL,), 0.02),
        "in_ln_b": nrm(ks[2], (D_MODEL,), 0.02),
        "w_in": nrm(ks[3], (L, D_MODEL, D_IN), D_MODEL ** -0.5),
        "m_conv_w": nrm(ks[4], (L, M_CONV, 2 * M_QK), M_CONV ** -0.5),
        "m_conv_b": nrm(ks[5], (L, 2 * M_QK), 0.01),
        "m_i_bias": nrm(ks[6], (L, M_HEADS), 0.1),
        "m_f_bias": jnp.linspace(3.0, 6.0, M_HEADS, dtype=f32)[None] + nrm(ks[7], (L, M_HEADS), 0.1),
        "m_norm_g": 1.0 + nrm(ks[8], (L, M_V), 0.02),
        "s_conv_w": nrm(ks[9], (L, S_CONV, S_XBC), S_CONV ** -0.5),
        "s_conv_b": nrm(ks[10], (L, S_XBC), 0.01),
        "s_dt_bias": dt0 + jnp.log(-jnp.expm1(-dt0)),
        "s_a_log": jnp.log(jax.random.uniform(ks[13], (L, S_HEADS), f32, 1.0, 16.0)),
        "s_d": 1.0 + nrm(ks[14], (L, S_HEADS), 0.1),
        "s_norm_g": 1.0 + nrm(ks[15], (L, S_INNER), 0.02),
        "p_a": nrm(ks[16], (L, M_V, D_MODEL), M_V ** -0.5),
        "p_b": nrm(ks[17], (L, S_INNER, D_MODEL), S_INNER ** -0.5),
        "w_out": nrm(ks[18], (L, D_MODEL, D_MODEL), BETA_3 * D_MODEL ** -0.5),
        "ln1_g": 1.0 + nrm(ks[19], (L, D_MODEL), 0.02),
        "ln1_b": nrm(ks[20], (L, D_MODEL), 0.02),
        "w_up": nrm(ks[21], (L, D_MODEL, 2 * D_FF_3), D_MODEL ** -0.5),
        "f_conv_w": nrm(ks[22], (L, FFN_CONV, 2 * D_FF_3), FFN_CONV ** -0.5),
        "f_conv_b": nrm(ks[23], (L, 2 * D_FF_3), 0.01),
        "w_down": nrm(ks[24], (L, D_FF_3, D_MODEL), BETA_3 * D_FF_3 ** -0.5),
        "ln2_g": 1.0 + nrm(ks[25], (L, D_MODEL), 0.02),
        "ln2_b": nrm(ks[26], (L, D_MODEL), 0.02),
    }

def third_block(x, in_ln_g, in_ln_b, w_in, m_conv_w, m_conv_b, m_i_bias, m_f_bias, m_norm_g,
              s_conv_w, s_conv_b, s_dt_bias, s_a_log, s_d, s_norm_g, p_a, p_b, w_out,
              ln1_g, ln1_b, w_up, f_conv_w, f_conv_b, w_down, ln2_g, ln2_b):
    splits = np.cumsum(IN_SIZES)[:-1].tolist()
    x = layer_norm_3(x, in_ln_g, in_ln_b)
    for l in range(DEPTH):
        proj = x @ w_in[l]
        q, k, v, o_pre, i_pre, f_pre, z, xbc, dt_raw, g_a, g_b = jnp.split(proj, splits, -1)
        h_a = mlstm_branch(q, k, v, o_pre, i_pre, f_pre, m_conv_w[l], m_conv_b[l],
                           m_i_bias[l], m_f_bias[l], m_norm_g[l])
        h_b = mamba2_branch(z, xbc, dt_raw, s_conv_w[l], s_conv_b[l], s_dt_bias[l],
                            s_a_log[l], s_d[l], s_norm_g[l])
        merged = jax.nn.sigmoid(g_a) * (h_a @ p_a[l]) + jax.nn.sigmoid(g_b) * (h_b @ p_b[l])
        x = layer_norm_3(ALPHA_3 * x + merged @ w_out[l], ln1_g[l], ln1_b[l])
        u = causal_dwconv(x @ w_up[l], f_conv_w[l], f_conv_b[l])
        u_gate, u_val = jnp.split(u, 2, -1)
        x = layer_norm_3(ALPHA_3 * x + (jax.nn.silu(u_gate) * u_val) @ w_down[l], ln2_g[l], ln2_b[l])
    return x


_first_inputs_3 = third_inputs


def third_inputs(seed=0):
    import zlib

    import numpy as np

    out = dict(_first_inputs_3(seed))
    spreads = {}
    factors = {'m_conv_b': 8.0,
     'm_i_bias': 64.0,
     'm_norm_g': 44.35,
     's_conv_b': 8.0,
     's_norm_g': 23.402,
     'ln1_g': 2.714,
     'ln1_b': 2.806,
     'f_conv_b': 8.0,
     'ln2_g': 7.836,
     'ln2_b': 7.847}
    for name, (base, spread) in spreads.items():
        noise = np.random.default_rng([zlib.crc32(name.encode()), seed]).standard_normal(out[name].shape)
        drawn = base * np.exp(spread * noise) if base else spread * noise
        out[name] = __import__('jax').numpy.asarray(drawn.astype(out[name].dtype))
    for name, factor in factors.items():
        out[name] = (out[name] * factor).astype(out[name].dtype)
    return out


_narrow_inputs_3 = third_inputs


def third_inputs(seed=0):

    out = dict(_narrow_inputs_3(seed))
    wider = {'m_norm_g': 3.86, 's_norm_g': 3.83, 'ln2_g': 3.15, 'ln2_b': 3.15}
    for name, times in wider.items():
        mean = out[name].mean()
        out[name] = (mean + times * (out[name] - mean)).astype(out[name].dtype)
    return out


def setup_inputs(seed=0):
    out = dict(first_inputs(seed))
    for name, value in second_inputs(seed + 1).items():
        if name != "x":
            out[name + "_2"] = value
    for name, value in third_inputs(seed + 2).items():
        if name != "x":
            out[name + "_3"] = value
    return out


def reference(
    x, c, w_ada, b_ada, norm1_g, w_in, ret_gn_g, sgu_ln_g, sgu_ln_b, sgu_w, sgu_b, w_ret_out,
    w_sgu_out, w_out, norm2_g, peer_w_q, peer_sub_keys, peer_u, peer_v, final_g, ln0_g_2,
    ln0_b_2, w_in_2, gdn_conv_2, gdn_a_log_2, gdn_dt_bias_2, gdn_norm_2, gla_w2_2, gla_b2_2,
    gla_norm_2, hgrn_lb_logits_2, hgrn_norm_2, w_br_a_2, w_br_b_2, w_br_c_2, w_out_2, ln1_g_2,
    ln1_b_2, w_router_2, router_bias_2, w_gate_2, w_up_2, w_down_2, ln2_g_2, ln2_b_2, in_ln_g_3,
    in_ln_b_3, w_in_3, m_conv_w_3, m_conv_b_3, m_i_bias_3, m_f_bias_3, m_norm_g_3, s_conv_w_3,
    s_conv_b_3, s_dt_bias_3, s_a_log_3, s_d_3, s_norm_g_3, p_a_3, p_b_3, w_out_3, ln1_g_3,
    ln1_b_3, w_up_3, f_conv_w_3, f_conv_b_3, w_down_3, ln2_g_3, ln2_b_3,
):
    x = first_block(
        x, c, w_ada, b_ada, norm1_g, w_in, ret_gn_g, sgu_ln_g, sgu_ln_b, sgu_w, sgu_b,
        w_ret_out, w_sgu_out, w_out, norm2_g, peer_w_q, peer_sub_keys, peer_u, peer_v, final_g,
    )
    x = second_block(
        x, ln0_g_2, ln0_b_2, w_in_2, gdn_conv_2, gdn_a_log_2, gdn_dt_bias_2, gdn_norm_2,
        gla_w2_2, gla_b2_2, gla_norm_2, hgrn_lb_logits_2, hgrn_norm_2, w_br_a_2, w_br_b_2,
        w_br_c_2, w_out_2, ln1_g_2, ln1_b_2, w_router_2, router_bias_2, w_gate_2, w_up_2,
        w_down_2, ln2_g_2, ln2_b_2,
    )
    return third_block(
        x, in_ln_g_3, in_ln_b_3, w_in_3, m_conv_w_3, m_conv_b_3, m_i_bias_3, m_f_bias_3,
        m_norm_g_3, s_conv_w_3, s_conv_b_3, s_dt_bias_3, s_a_log_3, s_d_3, s_norm_g_3, p_a_3,
        p_b_3, w_out_3, ln1_g_3, ln1_b_3, w_up_3, f_conv_w_3, f_conv_b_3, w_down_3, ln2_g_3,
        ln2_b_3,
    )


_drawn_inputs = setup_inputs


def setup_inputs(seed=0):
    import zlib

    import numpy as np

    out = dict(_drawn_inputs(seed))
    spreads = {}
    factors = {}
    for name, (base, spread) in spreads.items():
        noise = np.random.default_rng([zlib.crc32(name.encode()), seed]).standard_normal(out[name].shape)
        drawn = base * np.exp(spread * noise) if base else spread * noise
        out[name] = __import__('jax').numpy.asarray(drawn.astype(out[name].dtype))
    for name, factor in factors.items():
        out[name] = (out[name] * factor).astype(out[name].dtype)
    return out
```

```python
from contextlib import ExitStack, contextmanager
from itertools import count

import numpy as np
import concourse.bass as bass
from concourse import mybir

F32 = mybir.dt.float32
U32 = mybir.dt.uint32
ACT = mybir.ActivationFunctionType
ALU = mybir.AluOpType
AX = mybir.AxisListType

P = 128
SEQ = 512
NT = SEQ // P
D = 1024
KD = D // P
BANK = 512
QUARTERS = 4
BLOCKS = (1, 2, 3)
NUMBERS = count()
SLOTS = 2
ALPHA = 2.0 ** 0.25


class Core:
    pass


@contextmanager
def stage(nc, name, *signals):
    sems = [nc.alloc_semaphore(f"{name}_{s}") for s in signals]
    with nc.Block() as block:
        yield (block, *sems)
    if sems:
        nc.clear_and_free_semaphores(sems)
        nc.all_engine_barrier()


@contextmanager
def buffers(nc, **shapes):
    with ExitStack() as ctx:
        made = []
        for name, shape in shapes.items():
            shape, dtype = (shape, F32) if isinstance(shape, list) else shape
            made.append(ctx.enter_context(nc.sbuf_tensor(f"{name}_{next(NUMBERS)}", shape, dtype)))
        yield made


def kmajor(w, lo, width):
    return w[:, lo:lo + width].rearrange("(k p) n -> p k n", p=P)


def load_ahead(core, sp, last):
    while core.loaded < min(last + SLOTS, len(core.plan)):
        c = core.loaded
        _, src = core.plan[c]
        k, n = src.shape[1], src.shape[2]
        if c >= SLOTS:
            sp.wait_ge(core.products, QUARTERS * (c - SLOTS + 1))
        dst = core.ring[c % SLOTS][0:src.shape[0], 0:k * n].rearrange("p (k n) -> p k n", k=k)
        sp.dma_start(dst, src).then_inc(core.ring_loaded[c % SLOTS], 16)
        core.loaded += 1


def take(core, name, count):
    first = core.taken
    assert all(core.plan[first + i][0] == name for i in range(count)), (name, core.plan[first][0])
    core.taken += count
    return first


def ring_view(core, slot, k, n):
    return core.ring[slot][:, 0:k * n].rearrange("p (k n) -> p k n", k=k)


def pairs(eng, first, count):
    loops = count // 2 if count >= 4 else 0
    if loops:
        with eng.Fori(0, loops) as i:
            for u in range(2):
                yield 2 * i + u, (first + u) // 2 + i, (first + u) % 2, first + u + 2 * i
    for j in range(2 * loops, count):
        c = first + j
        yield j, c // 2, c % 2, c


def project(nc, core, name, xT, runs, kt=KD, last_rows=P):
    firsts = [take(core, r[0], r[1]) for r in runs]
    base = firsts[0]
    with stage(nc, name, "psum_free") as (block, psum_free):
        @block.sync
        def _(sp):
            load_ahead(core, sp, core.taken)

        @block.tensor
        def _(pe):
            for (_, count, layout, _), first in zip(runs, firsts):
                for _, turn, odd, c in pairs(pe, first, count):
                    pe.wait_ge(core.ring_loaded[odd], 16 * (turn + 1))
                    pe.wait_ge(psum_free, c - base + 1)
                    w = ring_view(core, odd, kt, BANK)
                    for t in range(NT):
                        for k in range(kt):
                            a, b = xT[:, k, t * P:(t + 1) * P], w[:, k, :]
                            if layout == "feature":
                                a, b = w[:, k, t * P:(t + 1) * P], xT[:, k, :]
                            mm = nc.tensor.matmul(core.ps[:, 4 * odd + t, :], a, b, start=k == 0, stop=k == kt - 1)
                        mm.then_inc(core.products, 1)

        def evacuate(eng, mine):
            for (_, count, _, how), first in zip(runs, firsts):
                for j, _, odd, c in pairs(eng, first, count):
                    if (how[0] == "act") != mine:
                        continue
                    for t in range(NT):
                        eng.wait_ge(core.products, QUARTERS * c + t + 1)
                        yield how, core.ps[:, 4 * odd + t, :], t, j

        kinds = {r[3][0] == "act" for r in runs}
        assert len(kinds) == 1

        if kinds == {True}:
            @block.scalar
            def _(act):
                act.sem_inc(psum_free, 2)
                for how, psum, t, j in evacuate(act, True):
                    done = nc.scalar.activation(how[2](t, j), psum, how[1])
                    if t == NT - 1:
                        done.then_inc(psum_free, 1)
        else:
            @block.vector
            def _(dve):
                dve.sem_inc(psum_free, 2)
                for how, psum, t, j in evacuate(dve, False):
                    dest = how[2](t, j)
                    if how[0] == "axpy":
                        done = nc.vector.scalar_tensor_tensor(dest, dest, how[1], psum, ALU.mult, ALU.add)
                    elif how[0] == "mul":
                        done = nc.vector.tensor_tensor(dest, psum, how[1](t, j), ALU.mult)
                    else:
                        done = nc.vector.tensor_tensor(core.tmp[:, t, :], psum, how[1](t, j), ALU.mult)
                    if t == NT - 1:
                        done.then_inc(psum_free, 1)
                    if how[0] == "mad":
                        dve.drain()
                        nc.vector.tensor_tensor(dest, dest, core.tmp[:, t, :], ALU.add)


def columns(buf):
    return lambda t, j: buf[:, t, bass.ds(j * BANK, BANK)]


def feature_tiles(buf):
    return lambda t, j: buf[:, bass.ds(j * 4 + t, 1), :].rearrange("p o n -> p (o n)")


def transpose_tile(nc, core, t, nf, src, transposed):
    halves = nf // 4
    for half in range(halves):
        bank = (halves * t + half) % 8
        for q in range(4):
            f = 4 * half + q
            mm = nc.tensor.transpose(core.ps[:, bank, q * P:(q + 1) * P], src[:, t, f * P:(f + 1) * P], core.ident[:])
        mm.then_inc(transposed, 1)


def untranspose(nc, core, eng, copy, nf, dst, transposed, mine):
    halves = nf // 4
    for n in range(NT * halves):
        if n % 2 != mine:
            continue
        t, half = divmod(n, halves)
        eng.wait_ge(transposed, n + 1)
        copy(dst[:, 4 * half:4 * half + 4, t * P:(t + 1) * P],
             core.ps[:, n % 8, :].rearrange("p (f t) -> p f t", f=4))


def transpose(nc, core, name, src, dst, nf=KD):
    with stage(nc, name, "transposed") as (block, transposed):
        @block.tensor
        def _(pe):
            for t in range(NT):
                transpose_tile(nc, core, t, nf, src, transposed)

        @block.scalar
        def _(act):
            untranspose(nc, core, act, nc.scalar.copy, nf, dst, transposed, 0)

        @block.vector
        def _(dve):
            untranspose(nc, core, dve, nc.vector.tensor_copy, nf, dst, transposed, 1)


def row_stats(nc, core, dve, src, mv, width, groups):
    parts = max(1, width // BANK)
    w = width // parts
    for g in range(groups):
        for q in range(parts):
            nc.vector.bn_stats(core.bn[:, g * parts + q, :], src(g)[:, q * w:(q + 1) * w])
    dve.drain()
    for g in range(groups):
        nc.vector.bn_aggr(mv[:, g, :], core.bn[:, g * parts:(g + 1) * parts, :].rearrange("p q s -> p (q s)"))
    dve.drain()


def mean_square(nc, dve, mv):
    nc.vector.tensor_tensor(mv[:, :, 0:1], mv[:, :, 0:1], mv[:, :, 0:1], ALU.mult)
    dve.drain()
    nc.vector.tensor_tensor(mv[:, :, 1:2], mv[:, :, 1:2], mv[:, :, 0:1], ALU.add)
    dve.drain()


def inverse_root(nc, core, pool, v, eps, ready, done):
    pool.wait_ge(ready, 1)
    nc.gpsimd.tensor_scalar(v, v, eps, None, ALU.add).then_inc(done, 1)
    pool.wait_ge(done, 1)
    nc.gpsimd.tensor_tensor(v, v, core.minus_half[:, 0:v.shape[1], :], ALU.pow).then_inc(done, 1)


def norm(nc, core, name, src, dst, dstT, eps, rms, gain, shift, rows=()):
    with stage(nc, name, "rows_loaded", "var_ready", "root_ready", "normed", "transposed") as (
            block, rows_loaded, var_ready, root_ready, normed, transposed):
        mv = core.mv[:, 0:NT, :]

        @block.gpsimd
        def _(pool):
            inverse_root(nc, core, pool, mv[:, :, 1:2], eps, var_ready, root_ready)

        if rows:
            @block.sync
            def _(sp):
                for buf, vec in rows:
                    sp.dma_start(buf, vec.partition_broadcast(P)).then_inc(rows_loaded, 16)

        @block.vector
        def _(dve):
            row_stats(nc, core, dve, lambda t: src[:, t, :], mv, D, NT)
            if rms:
                mean_square(nc, dve, mv)
            dve.drain().then_inc(var_ready, 1)
            dve.wait_ge(root_ready, 2)
            for t in range(NT):
                if rms:
                    nc.vector.tensor_scalar(dst[:, t, :], src[:, t, :], mv[:, t, 1:2], None, ALU.mult)
                else:
                    nc.vector.tensor_scalar(dst[:, t, :], src[:, t, :], mv[:, t, 0:1], mv[:, t, 1:2], ALU.subtract, ALU.mult)
            dve.drain()
            if rows:
                dve.wait_ge(rows_loaded, 16 * len(rows))
            for t in range(NT):
                done = nc.vector.tensor_tensor(dst[:, t, :], dst[:, t, :], gain, ALU.mult)
                if shift is not None:
                    dve.drain()
                    done = nc.vector.tensor_tensor(dst[:, t, :], dst[:, t, :], shift, ALU.add)
                done.then_inc(normed, 1)
            if dstT is not None:
                untranspose(nc, core, dve, nc.vector.tensor_copy, KD, dstT, transposed, 1)

        if dstT is not None:
            @block.tensor
            def _(pe):
                for t in range(NT):
                    pe.wait_ge(normed, t + 1)
                    transpose_tile(nc, core, t, KD, dst, transposed)

            @block.scalar
            def _(act):
                untranspose(nc, core, act, nc.scalar.copy, KD, dstT, transposed, 0)


RET_HEADS, RET_DV = 4, 256
RET_QK_DIM = 128
SGU_GROUPS, SGU_DIM = 4, 256


def adaptive_rows(nc, core, d, mod, norm1_gain, norm2_gain):
    chunks = 6 * D // BANK
    first = take(core, "ada", chunks)
    with buffers(nc, c_col=[P, KD], c_silu=[P, KD], c_rep=[P, KD, P]) as (c_col, c_silu, c_rep), \
            stage(nc, "ada", "loaded", "silu_done", "c_ready", "evacuated") as (
                block, loaded, silu_done, c_ready, evacuated):
        @block.sync
        def _(sp):
            sp.dma_start(core.x[:], d["x"].rearrange("b (t p) f -> p (b t) f", p=P)).then_inc(loaded, 16)
            sp.dma_start(c_col[:], d["c_col"]).then_inc(loaded, 16)
            sp.dma_start(mod[:].rearrange("p a f -> p (a f)"), d["b_ada"][0, :].partition_broadcast(P)).then_inc(loaded, 16)
            sp.dma_start(norm1_gain, d["norm1_g"][0, :].partition_broadcast(P)).then_inc(loaded, 16)
            sp.dma_start(norm2_gain, d["norm2_g"][0, :].partition_broadcast(P)).then_inc(loaded, 16)
            load_ahead(core, sp, core.taken)

        @block.scalar
        def _(act):
            act.wait_ge(loaded, 80)
            nc.scalar.activation(c_silu[:], c_col[:], ACT.Silu).then_inc(silu_done, 1)

        @block.tensor
        def _(pe):
            pe.wait_ge(c_ready, 1)
            for _, turn, odd, c in pairs(pe, first, chunks):
                pe.wait_ge(core.ring_loaded[odd], 16 * (turn + 1))
                pe.wait_ge(evacuated, c - first + 1)
                w = ring_view(core, odd, KD, BANK)
                for k in range(KD):
                    mm = nc.tensor.matmul(core.ps[:, odd, :], c_rep[:, k, :], w[:, k, :], start=k == 0, stop=k == KD - 1)
                    if k % 2:
                        mm.then_inc(core.products, 1)

        @block.vector
        def _(dve):
            dve.sem_inc(evacuated, 2)
            dve.wait_ge(silu_done, 1)
            nc.vector.tensor_copy(c_rep[:], c_silu[:].unsqueeze(2).to_broadcast([P, KD, P])).then_inc(c_ready, 1)
            dve.wait_ge(loaded, 80)
            rows = mod[:].rearrange("p a f -> p (a f)")
            for j, _, odd, c in pairs(dve, first, chunks):
                dve.wait_ge(core.products, QUARTERS * (c + 1))
                part = rows[:, bass.ds(j * BANK, BANK)]
                nc.vector.tensor_tensor(part, part, core.ps[:, odd, :], ALU.add).then_inc(evacuated, 1)
            dve.drain()
            for which, gain in ((1, norm1_gain), (4, norm2_gain)):
                nc.vector.scalar_tensor_tensor(mod[:, which, :], mod[:, which, :], 1.0, gain, ALU.add, ALU.mult)


def retention(nc, core, d, qkv, rot, qkT, gate, y):
    H = RET_HEADS
    ra, rb, weights = core.row_b[:, 0:512], core.row_b[:, 512:1024], core.tmp
    decay = rot[:, :, 0:SEQ]
    with buffers(nc, cosine=[P, NT, 64], sine=[P, NT, 64]) as (cosine, sine):
        with stage(nc, "rotary", "tables", "rotated", "transposed") as (block, tables, rotated, transposed):
            @block.sync
            def _(sp):
                sp.dma_start(cosine[:], d["const_cos"]).then_inc(tables, 16)
                sp.dma_start(sine[:], d["const_sin"]).then_inc(tables, 16)
                sp.dma_start(core.row_a[:], d["ret_gn_g"][0, :].partition_broadcast(P)).then_inc(tables, 16)

            @block.vector
            def _(dve):
                dve.wait_ge(tables, 48)
                for t in range(NT):
                    heads = qkv[:, t, 0:2 * H * P].rearrange("p (h a f) -> p h a f", a=2, f=64)
                    out = rot[:, t, :].rearrange("p (h a f) -> p h a f", a=2, f=64)
                    cos = cosine[:, t, :].unsqueeze(1).to_broadcast([P, 2 * H, 64])
                    sin = sine[:, t, :].unsqueeze(1).to_broadcast([P, 2 * H, 64])
                    a = ra.rearrange("p (h f) -> p h f", f=64)
                    b = rb.rearrange("p (h f) -> p h f", f=64)
                    nc.vector.tensor_tensor(out[:, :, 0, :], heads[:, :, 0, :], cos, ALU.mult)
                    nc.vector.tensor_tensor(out[:, :, 1, :], heads[:, :, 0, :], sin, ALU.mult)
                    nc.vector.tensor_tensor(a, heads[:, :, 1, :], sin, ALU.mult)
                    nc.vector.tensor_tensor(b, heads[:, :, 1, :], cos, ALU.mult)
                    dve.drain()
                    nc.vector.tensor_tensor(out[:, :, 0, :], out[:, :, 0, :], a, ALU.subtract)
                    nc.vector.tensor_tensor(out[:, :, 1, :], out[:, :, 1, :], b, ALU.add).then_inc(rotated, 1)
                    dve.drain()
                untranspose(nc, core, dve, nc.vector.tensor_copy, KD, qkT, transposed, 1)

            @block.tensor
            def _(pe):
                for t in range(NT):
                    pe.wait_ge(rotated, t + 1)
                    transpose_tile(nc, core, t, KD, rot, transposed)

            @block.scalar
            def _(act):
                untranspose(nc, core, act, nc.scalar.copy, KD, qkT, transposed, 0)

        with stage(nc, "retain", "scores", "weighted", "summed", "copied", "decay_loaded") as (
                block, scores, weighted, summed, copied, decay_loaded):
            @block.sync
            def _(sp):
                sp.dma_start(decay, d["const_ret_decay"]).then_inc(decay_loaded, 16)

            @block.tensor
            def _(pe):
                for h in range(H):
                    if h >= 1:
                        pe.wait_ge(weighted, NT * h)
                    for s in range(NT):
                        nc.tensor.matmul(core.ps[:, s, 0:SEQ - s * P], qkT[:, H + h, s * P:(s + 1) * P],
                                         qkT[:, h, s * P:], start=True, stop=True).then_inc(scores, 1)
                    pe.wait_ge(weighted, NT * (h + 1))
                    if h >= 2:
                        pe.wait_ge(copied, h - 1)
                    for t in range(NT):
                        out = core.ps[:, 4 + 2 * (h % 2) + t // 2, (t % 2) * RET_DV:(t % 2 + 1) * RET_DV]
                        for s in range(t + 1):
                            mm = nc.tensor.matmul(out, weights[:, s, (t - s) * P:(t - s + 1) * P],
                                                  qkv[:, s, 2 * H * P + h * RET_DV:2 * H * P + (h + 1) * RET_DV],
                                                  start=s == 0, stop=s == t)
                    mm.then_inc(summed, 1)

            @block.vector
            def _(dve):
                dve.wait_ge(decay_loaded, 16)
                for h in range(H):
                    if h >= 1:
                        dve.wait_ge(summed, h)
                    for s in range(NT):
                        n = SEQ - s * P
                        dve.wait_ge(scores, NT * h + s + 1)
                        nc.vector.scalar_tensor_tensor(weights[:, s, 0:n], core.ps[:, s, 0:n], RET_QK_DIM ** -0.5,
                                                       decay[:, h, 0:n], ALU.mult, ALU.mult).then_inc(weighted, 1)

            @block.scalar
            def _(act):
                for h in range(H):
                    act.wait_ge(summed, h + 1)
                    for q in range(2):
                        done = nc.scalar.copy(y[:, 2 * q:2 * q + 2, h * RET_DV:(h + 1) * RET_DV],
                                              core.ps[:, 4 + 2 * (h % 2) + q, :].rearrange("p (t f) -> p t f", t=2))
                    done.then_inc(copied, 1)

        with stage(nc, "head_norm", "var_ready", "root_ready") as (block, var_ready, root_ready):
            n = NT * H
            mv = core.mv[:, 0:n, :]

            @block.gpsimd
            def _(pool):
                inverse_root(nc, core, pool, mv[:, :, 1:2], 1e-6, var_ready, root_ready)

            @block.vector
            def _(dve):
                part = lambda g: y[:, g // H, (g % H) * RET_DV:(g % H + 1) * RET_DV]
                row_stats(nc, core, dve, part, mv, RET_DV, n)
                dve.drain().then_inc(var_ready, 1)
                dve.wait_ge(root_ready, 2)
                for g in range(n):
                    nc.vector.tensor_scalar(part(g), part(g), mv[:, g, 0:1], mv[:, g, 1:2], ALU.subtract, ALU.mult)
                dve.drain()
                for t in range(NT):
                    nc.vector.tensor_tensor(y[:, t, :], y[:, t, :], core.row_a[:], ALU.mult)
                dve.drain()
                for t in range(NT):
                    nc.vector.tensor_tensor(y[:, t, :], y[:, t, :], gate[:, t, :], ALU.mult)


def spatial(nc, core, d, usv, y):
    with buffers(nc, mixer=[P, SGU_GROUPS, P], mixer_b=[P, SGU_GROUPS]) as (mixer, mixer_b), \
            stage(nc, "spatial", "loaded", "masked", "var_ready", "root_ready", "normed", "mixed") as (
                block, loaded, masked, var_ready, root_ready, normed, mixed):
        mv = core.mv[:, 0:NT, :]

        @block.sync
        def _(sp):
            sp.dma_start(core.row_a[:], d["sgu_ln_g"][0, :].partition_broadcast(P)).then_inc(loaded, 16)
            sp.dma_start(core.row_b[:], d["sgu_ln_b"][0, :].partition_broadcast(P)).then_inc(loaded, 16)
            sp.dma_start(mixer[:], d["sgu_w_t"]).then_inc(loaded, 16)
            sp.dma_start(mixer_b[:], d["sgu_b_t"]).then_inc(loaded, 16)

        @block.gpsimd
        def _(pool):
            pool.wait_ge(loaded, 64)
            nc.gpsimd.affine_select(out=mixer[:], in_=mixer[:], compare_op=ALU.is_ge, fill=0.0, base=0,
                                    pattern=[[0, SGU_GROUPS], [1, P]], channel_multiplier=-1).then_inc(masked, 1)
            inverse_root(nc, core, pool, mv[:, :, 1:2], 1e-6, var_ready, root_ready)

        @block.vector
        def _(dve):
            sv = lambda t: usv[:, t, D:2 * D]
            row_stats(nc, core, dve, sv, mv, D, NT)
            dve.drain().then_inc(var_ready, 1)
            dve.wait_ge(root_ready, 2)
            dve.wait_ge(loaded, 64)
            for t in range(NT):
                nc.vector.tensor_scalar(sv(t), sv(t), mv[:, t, 0:1], mv[:, t, 1:2], ALU.subtract, ALU.mult)
                dve.drain()
                nc.vector.tensor_tensor(sv(t), sv(t), core.row_a[:], ALU.mult)
                dve.drain()
                nc.vector.tensor_tensor(sv(t), sv(t), core.row_b[:], ALU.add).then_inc(normed, 1)
            for t in range(NT):
                dve.wait_ge(mixed, t + 1)
                for g in range(SGU_GROUPS):
                    nc.vector.scalar_tensor_tensor(
                        y[:, t, g * SGU_DIM:(g + 1) * SGU_DIM],
                        core.ps[:, 2 * t + g // 2, (g % 2) * SGU_DIM:(g % 2 + 1) * SGU_DIM], mixer_b[:, g:g + 1],
                        usv[:, t, g * SGU_DIM:(g + 1) * SGU_DIM], ALU.add, ALU.mult)

        @block.tensor
        def _(pe):
            pe.wait_ge(masked, 1)
            for t in range(NT):
                pe.wait_ge(normed, t + 1)
                for g in range(SGU_GROUPS):
                    mm = nc.tensor.matmul(core.ps[:, 2 * t + g // 2, (g % 2) * SGU_DIM:(g % 2 + 1) * SGU_DIM],
                                          mixer[:, g, :], usv[:, t, D + g * SGU_DIM:D + (g + 1) * SGU_DIM],
                                          start=True, stop=True)
                mm.then_inc(mixed, 1)


def multiply(nc, name, dst, other):
    with stage(nc, name) as (block,):
        @block.vector
        def _(dve):
            for t in range(NT):
                nc.vector.tensor_tensor(dst[:, t, :], dst[:, t, :], other[:, t, :], ALU.mult)


def first_mixer(nc, core, d, mod):
    norm(nc, core, "norm1", core.x, core.h, core.hT, 1e-6, True, mod[:, 1, :], mod[:, 0, :])
    with buffers(nc, wide=[P, NT, 2 * D], gate=[P, NT, D], y=[P, NT, D], yT=[P, KD, SEQ]) as (wide, gate, y, yT):
        project(nc, core, "in_qkvg", core.hT, [("qkv", 4, "token", ("act", ACT.Copy, columns(wide))),
                                               ("g_ret", 2, "token", ("act", ACT.Silu, columns(gate)))])
        retention(nc, core, d, wide, core.h, yT, gate, y)
        transpose(nc, core, "ret_T", y, yT)
        branch = gate
        project(nc, core, "ret_out", yT, [("ret_out", 2, "token", ("act", ACT.Copy, columns(branch)))])
        project(nc, core, "in_usv", core.hT, [("usv", 4, "token", ("act", ACT.Gelu, columns(wide)))])
        spatial(nc, core, d, wide, y)
        transpose(nc, core, "sgu_T", y, yT)
        project(nc, core, "in_gates", core.hT, [("gates", 4, "token", ("act", ACT.Sigmoid, columns(wide)))])
        multiply(nc, "gate_a", branch, wide[:, :, 0:D])
        project(nc, core, "sgu_out", yT, [("sgu_out", 2, "token", ("mad", columns(wide[:, :, D:2 * D]), columns(branch)))])
        transpose(nc, core, "merge_T", branch, yT)
        project(nc, core, "out1", yT, [("out1", 2, "token",
                                        ("mad", lambda t, j: mod[:, 2, bass.ds(j * BANK, BANK)], columns(core.x)))])


PEER_HEADS, PEER_KEYS, TOPK = 8, 128, 16
PICKS = PEER_HEADS * TOPK
PAIRS = 2 * PEER_HEADS
LOWEST = -3.0e38


def top16(nc, dve, n, values, spare, top, index):
    for g in range(n):
        nc.vector.max(top[:, g, 0:8], values(g))
    dve.drain()
    for g in range(n):
        nc.vector.max_index(index[:, g, 0:8], top[:, g, 0:8], values(g))
        nc.vector.match_replace(spare(g), top[:, g, 0:8], values(g), LOWEST)
    dve.drain()
    for g in range(n):
        nc.vector.max(top[:, g, 8:16], spare(g))
    dve.drain()
    for g in range(n):
        nc.vector.max_index(index[:, g, 8:16], top[:, g, 8:16], spare(g))
    dve.drain()


def route_experts(nc, core, d, qT, expert, share):
    H, K = PEER_HEADS, TOPK
    with buffers(nc, keysT=[P, PAIRS, PEER_KEYS], half_scores=[P, 2, PAIRS, PEER_KEYS], half_rest=[P, PAIRS, PEER_KEYS],
                 sub_s=[P, PAIRS, K], sub_i=([P, PAIRS, K], U32), sub_f=[P, PAIRS, K], top_i=([P, H, K], U32),
                 digit=([P, PICKS], U32), digit_f=[P, PICKS], key_f=[P, 2, PICKS], steps=[P, K],
                 total=[P, H], top_s=[P, NT, H, K]) as (
            keysT, half_scores, half_rest, sub_s, sub_i, sub_f, top_i, digit, digit_f, key_f, steps, total, top_s):
        with stage(nc, "route", "keys_loaded", "steps_ready", "scored", "copied", "read", "shifted", "raised") as (
                block, keys_loaded, steps_ready, scored, copied, read, shifted, raised):
            cand = half_rest[:].rearrange("p g n -> p (g n)").rearrange("p (h i j) -> p h i j", h=H, i=K)
            pick = lambda buf: buf.rearrange("p (h k) -> p h k", h=H)

            @block.sync
            def _(sp):
                sp.dma_start(keysT[:], d["sub_keys_t"]).then_inc(keys_loaded, 16)

            @block.gpsimd
            def _(pool):
                nc.gpsimd.iota(steps[:], pattern=[[1, K]], base=0, channel_multiplier=0,
                               allow_small_or_imprecise_dtypes=True).then_inc(steps_ready, 1)

            @block.tensor
            def _(pe):
                pe.wait_ge(keys_loaded, 16)
                for t in range(NT):
                    if t >= 2:
                        pe.wait_ge(copied, 4 * (t - 1))
                    for g in range(PAIRS):
                        mm = nc.tensor.matmul(core.ps[:, 4 * (t % 2) + g // 4, (g % 4) * P:(g % 4 + 1) * P],
                                              qT[:, g, t * P:(t + 1) * P], keysT[:, g, :], start=True, stop=True)
                        if g % 4 == 3:
                            mm.then_inc(scored, 1)

            @block.scalar
            def _(act):
                for t in range(NT):
                    if t >= 2:
                        act.wait_ge(read, t - 1)
                    for q in range(4):
                        act.wait_ge(scored, 4 * t + q + 1)
                        nc.scalar.copy(half_scores[:, t % 2, 4 * q:4 * q + 4, :],
                                       core.ps[:, 4 * (t % 2) + q, :].rearrange("p (g n) -> p g n", g=4)).then_inc(copied, 1)
                for t in range(NT):
                    act.wait_ge(shifted, t + 1)
                    nc.scalar.activation(top_s[:, t], top_s[:, t], ACT.Exp).then_inc(raised, 1)

            @block.vector
            def _(dve):
                dve.wait_ge(steps_ready, 1)
                for t in range(NT):
                    dve.wait_ge(copied, 4 * (t + 1))
                    top16(nc, dve, PAIRS, lambda g: half_scores[:, t % 2, g, :], lambda g: half_rest[:, g, :], sub_s, sub_i)
                    nc.vector.tensor_copy(sub_f[:], sub_i[:])
                    half = sub_s[:].rearrange("p (h a) k -> p h a k", a=2)
                    nc.vector.tensor_tensor(cand, half[:, :, 0, :].unsqueeze(3).to_broadcast([P, H, K, K]),
                                            half[:, :, 1, :].unsqueeze(2).to_broadcast([P, H, K, K]), ALU.add)
                    dve.drain()
                    rest = half_scores[:, t % 2].rearrange("p g n -> p (g n)").rearrange("p (h n) -> p h n", h=H)
                    sums = half_rest[:].rearrange("p g n -> p (g n)").rearrange("p (h n) -> p h n", h=H)
                    top16(nc, dve, H, lambda g: sums[:, g, :], lambda g: rest[:, g, :], top_s[:, t], top_i)
                    dve.drain().then_inc(read, 1)
                    nc.vector.tensor_tensor(top_s[:, t, :, 1:K], top_s[:, t, :, 1:K],
                                            top_s[:, t, :, 0:1].to_broadcast([P, H, K - 1]), ALU.subtract)
                    dve.drain()
                    nc.vector.memset(top_s[:, t, :, 0:1], 0.0).then_inc(shifted, 1)
                    ids = sub_f[:].rearrange("p (h a) k -> p h a k", a=2)
                    for a, (op, by) in enumerate(((ALU.logical_shift_right, 4), (ALU.bitwise_and, K - 1))):
                        nc.vector.tensor_single_scalar(digit[:], top_i[:].rearrange("p h k -> p (h k)"), by, op)
                        dve.drain()
                        nc.vector.tensor_copy(digit_f[:], digit[:])
                        dve.drain()
                        hit = cand.rearrange("p h i j -> p (h i) j")
                        nc.vector.tensor_tensor(hit, steps[:].unsqueeze(1).to_broadcast([P, PICKS, K]),
                                                digit_f[:].unsqueeze(2).to_broadcast([P, PICKS, K]), ALU.is_equal)
                        dve.drain()
                        nc.vector.tensor_tensor(cand, cand, ids[:, :, a, :].unsqueeze(2).to_broadcast([P, H, K, K]), ALU.mult)
                        dve.drain()
                        nc.vector.tensor_reduce(key_f[:, a, :], hit, AX.X, ALU.add)
                        dve.drain()
                    nc.vector.scalar_tensor_tensor(expert[:, t, :], key_f[:, 0, :], float(PEER_KEYS), key_f[:, 1, :],
                                                   ALU.mult, ALU.add)
                for t in range(NT):
                    dve.wait_ge(raised, t + 1)
                    nc.vector.tensor_reduce(total[:], top_s[:, t], AX.X, ALU.add)
                    dve.drain()
                    nc.vector.reciprocal(total[:], total[:])
                    dve.drain()
                    nc.vector.tensor_tensor(pick(share[:, t, :]), top_s[:, t], total[:].unsqueeze(2).to_broadcast([P, H, K]), ALU.mult)
                    dve.drain()


FETCH = 8


def run_experts(nc, core, d, expert, share, gate2):
    groups = PICKS // FETCH
    rows_u, rows_v = d["peer_u"][0], d["peer_v"][0]
    with buffers(nc, got_u=[P, FETCH, D], got_v=[P, FETCH, D], dots=[P, 2, FETCH], score=[P, NT, PICKS],
                 weight=[P, NT, PICKS], diagonal=[P, FETCH, P], zero=[P, P],
                 which_u=([P, 2, FETCH], U32), which_v=([P, 2, FETCH], U32)) as (
            got_u, got_v, dots, score, weight, diagonal, zero, which_u, which_v), \
            stage(nc, "experts", "staged_u", "staged_v", "used_u", "used_v", "scored", "activated", "weighted",
                  "diagonals", "summed", "added", "cleared", "asked", *[f"u_in{b}" for b in range(FETCH)],
                  *[f"v_in{b}" for b in range(FETCH)]) as (
                block, staged_u, staged_v, used_u, used_v, scored, activated, weighted,
                diagonals, summed, added, cleared, asked, *landed):
        u_in, v_in = landed[:FETCH], landed[FETCH:]

        @block.gpsimd
        def _(pool):
            nc.gpsimd.memset(zero[:], 0.0).then_inc(cleared, 1)
            for t in range(NT):
                for rows, got, which, staged, used, arrived in (
                        (rows_u, got_u, which_u, staged_u, used_u, u_in), (rows_v, got_v, which_v, staged_v, used_v, v_in)):
                    with pool.Fori(0, groups // 2) as i:
                        for half in range(2):
                            group = t * groups + 2 * i + half
                            nc.gpsimd.tensor_copy(which[:, half, :],
                                                  expert[:, t, bass.ds((2 * i + half) * FETCH, FETCH)]).then_inc(staged, 1)
                            pool.wait_ge(staged, group + 1)
                            for b in range(FETCH):
                                pool.wait_ge(used, group * FETCH + b + 1)
                                pool.sem_inc(asked, 1)
                                nc.gpsimd.indirect_dma_start(
                                    out=got[:, b, :], out_offset=None, in_=rows,
                                    in_offset=bass.IndirectOffsetOnAxis(ap=which[:, half, b:b + 1], axis=0),
                                ).then_inc(arrived[b], 16)

        @block.vector
        def _(dve):
            dve.sem_inc(used_u, FETCH)

            def add_experts(t):
                dve.wait_ge(summed, t + 1)
                for q in range(2):
                    nc.vector.tensor_tensor(core.tmp[:, q, :], core.ps[:, 2 * (t % 2) + q, :],
                                            gate2[:, q * BANK:(q + 1) * BANK], ALU.mult)
                dve.drain().then_inc(added, 1)
                nc.vector.tensor_tensor(core.x[:, t, :], core.x[:, t, :],
                                        core.tmp[:, 0:2, :].rearrange("p q n -> p (q n)"), ALU.add)
                dve.drain()

            for t in range(NT):
                with dve.Fori(0, groups // 2) as i:
                    for half in range(2):
                        for b in range(FETCH):
                            dve.wait_ge(u_in[b], 16 * (t * groups + 2 * i + half + 1))
                            nc.vector.tensor_tensor_reduce(
                                out=got_u[:, b, :], in0=got_u[:, b, :], in1=core.h[:, t, :], scale=1.0, scalar=0.0,
                                op0=ALU.mult, op1=ALU.add, accum_out=dots[:, half, b:b + 1]).then_inc(used_u, 1)
                        dve.drain()
                        nc.vector.tensor_copy(score[:, t, bass.ds((2 * i + half) * FETCH, FETCH)], dots[:, half, :])
                dve.drain().then_inc(scored, 1)
                dve.wait_ge(activated, t + 1)
                nc.vector.tensor_tensor(weight[:, t, :], score[:, t, :], share[:, t, :], ALU.mult).then_inc(weighted, 1)
                if t >= 1:
                    add_experts(t - 1)
            add_experts(NT - 1)

        @block.scalar
        def _(act):
            for t in range(NT):
                act.wait_ge(scored, t + 1)
                nc.scalar.activation(score[:, t, :], score[:, t, :], ACT.Gelu).then_inc(activated, 1)
                act.wait_ge(weighted, t + 1)
                with act.Fori(0, groups) as i:
                    for b in range(FETCH):
                        act.wait_ge(used_v, (t * groups + i) * FETCH + b + 1)
                        nc.scalar.activation(diagonal[:, b, :], core.ident[:], ACT.Copy,
                                             scale=weight[:, t, bass.ds(i * FETCH + b, 1)]).then_inc(diagonals, 1)

        @block.tensor
        def _(pe):
            pe.sem_inc(used_v, FETCH)
            pe.wait_ge(cleared, 1)
            for t in range(NT):
                if t >= 2:
                    pe.wait_ge(added, t - 1)
                banks = [core.ps[:, 2 * (t % 2) + q, :] for q in range(2)]
                for q in range(2):
                    nc.tensor.matmul(banks[q], zero[:], core.h[:, 0, 0:BANK], start=True, stop=False, skip_group_check=True)
                with pe.Fori(0, groups) as i:
                    for b in range(FETCH):
                        group = t * groups + i
                        pe.wait_ge(diagonals, group * FETCH + b + 1)
                        pe.wait_ge(v_in[b], 16 * (group + 1))
                        for q in range(2):
                            mm = nc.tensor.matmul(banks[q], diagonal[:, b, :], got_v[:, b, q * BANK:(q + 1) * BANK],
                                                  start=False, stop=False, skip_group_check=True)
                        mm.then_inc(used_v, 1)
                pe.drain().then_inc(summed, 1)


def block_one(nc, core, d):
    with buffers(nc, mod=[P, 6, D]) as (mod,):
        adaptive_rows(nc, core, d, mod, core.row_a[:], core.row_b[:])
        first_mixer(nc, core, d, mod)
        norm(nc, core, "norm2", core.x, core.h, core.hT, 1e-6, True, mod[:, 4, :], mod[:, 3, :])
        with buffers(nc, expert=([P, NT, PICKS], U32), share=[P, NT, PICKS]) as (expert, share):
            with buffers(nc, qT=[P, PAIRS, SEQ]) as (qT,):
                project(nc, core, "peer_q", core.hT, [("peer_q", 4, "feature", ("act", ACT.Copy, feature_tiles(qT)))])
                route_experts(nc, core, d, qT, expert, share)
            run_experts(nc, core, d, expert, share, mod[:, 5, :])
    norm(nc, core, "final1", core.x, core.x, None, 1e-6, True, core.row_a[:], None, [(core.row_a[:], d["final_g"])])


def plan_one(d):
    w_in = d["w_in"][0]
    plan = []
    add = lambda name, w, lo, n: plan.extend((name, kmajor(w, lo + i * BANK, BANK)) for i in range(n))
    add("ada", d["w_ada"][0], 0, 12)
    add("qkv", w_in, 0, 4)
    add("g_ret", w_in, 2048, 2)
    add("ret_out", d["w_ret_out"][0], 0, 2)
    add("usv", w_in, 3072, 4)
    add("gates", w_in, 5120, 4)
    add("sgu_out", d["w_sgu_out"][0], 0, 2)
    add("out1", d["w_out"][0], 0, 2)
    add("peer_q", d["peer_w_q"][0], 0, 4)
    return plan


STRIP = [0, 512, 896, 1152]
PACKED = 1280


def strip(buf, s, lo=0, hi=None):
    return buf[:, STRIP[s] + lo:STRIP[s] + (SEQ - s * P if hi is None else hi)]


def row_products(nc, core, name, parts):
    firsts = [take(core, p[0], 1) for p in parts]
    with stage(nc, name) as (block,):
        @block.sync
        def _(sp):
            load_ahead(core, sp, core.taken)

        @block.tensor
        def _(pe):
            bank = 0
            for (_, pieces), c in zip(parts, firsts):
                pe.wait_ge(core.ring_loaded[c % SLOTS], 16 * (c // SLOTS + 1))
                width = core.plan[c][1].shape[2]
                w = ring_view(core, c % SLOTS, KD, width)
                for n, (lo, m, _) in enumerate(pieces):
                    for k in range(KD):
                        mm = nc.tensor.matmul(core.ps[0:m, bank, :], w[:, k, lo:lo + m], core.hT[:, k, :],
                                              start=k == 0, stop=k == KD - 1)
                        if n == len(pieces) - 1 and k % 2:
                            mm.then_inc(core.products, 1)
                    bank += 1

        @block.scalar
        def _(act):
            bank = 0
            for (_, pieces), c in zip(parts, firsts):
                act.wait_ge(core.products, QUARTERS * (c + 1))
                for _, m, dest in pieces:
                    nc.scalar.copy(dest, core.ps[0:m, bank, :])
                    bank += 1


def soft_maximum(nc, name, parts):
    with stage(nc, name, "shifted", "logged") as (block, shifted, logged):
        @block.vector
        def _(dve):
            for x, _, sign, bias, _, _ in parts:
                nc.vector.tensor_scalar(x, x, sign, bias, ALU.mult, ALU.add).then_inc(shifted, 1)
            for n, (x, tmp, _, _, a, _) in enumerate(parts):
                dve.wait_ge(logged, n + 1)
                nc.vector.scalar_tensor_tensor(x, x, a, tmp, ALU.max, ALU.add)

        @block.scalar
        def _(act):
            for n, (x, tmp, _, _, _, minus_a) in enumerate(parts):
                act.wait_ge(shifted, n + 1)
                nc.scalar.activation(tmp, x, ACT.Abs, bias=minus_a)
            act.drain()
            for x, tmp, *_ in parts:
                nc.scalar.activation(tmp, tmp, ACT.Exp, scale=-1.0)
            act.drain()
            for x, tmp, *_ in parts:
                nc.scalar.activation(tmp, tmp, ACT.Ln, bias=1.0).then_inc(logged, 1)


def conv_silu(nc, core, name, raw, dst, taps, bias, tiles, width):
    with stage(nc, name, "convolved") as (block, convolved):
        @block.vector
        def _(dve):
            for f in range(tiles):
                if bias is None:
                    nc.vector.tensor_scalar(dst[:, f, :], raw[:, f, 0:SEQ], taps[:, 0, f:f + 1], None, ALU.mult)
                else:
                    nc.vector.tensor_scalar(dst[:, f, :], raw[:, f, 0:SEQ], taps[:, 0, f:f + 1], bias[:, f:f + 1], ALU.mult, ALU.add)
                dve.drain()
                for k in range(1, width):
                    done = nc.vector.scalar_tensor_tensor(dst[:, f, :], raw[:, f, k:k + SEQ], taps[:, k, f:f + 1],
                                                          dst[:, f, :], ALU.mult, ALU.add)
                    if k < width - 1:
                        dve.drain()
                done.then_inc(convolved, 1)

        @block.scalar
        def _(act):
            for f in range(tiles):
                act.wait_ge(convolved, f + 1)
                nc.scalar.activation(dst[:, f, :], dst[:, f, :], ACT.Silu)


def padded_tiles(raw, pad):
    return lambda t, j: raw[:, bass.ds(j * 4 + t, 1), pad:pad + SEQ].rearrange("p o n -> p (o n)")


def load_rows(nc, name, loads, zeroed=()):
    with stage(nc, name, "loaded") as (block, loaded):
        @block.sync
        def _(sp):
            for dst, src in loads:
                sp.dma_start(dst, src).then_inc(loaded, 16)
            sp.wait_ge(loaded, 16 * len(loads))

        if zeroed:
            @block.gpsimd
            def _(pool):
                for z in zeroed:
                    nc.gpsimd.memset(z, 0.0)


def row_columns(nc, core, name, rows, cols, h):
    with stage(nc, name, "turned") as (block, turned):
        @block.tensor
        def _(pe):
            for n, row in enumerate(rows):
                for t in range(NT):
                    mm = nc.tensor.transpose(core.ps[:, n, t * h:(t + 1) * h], row[:, t * P:(t + 1) * P], core.ident[0:h, 0:h])
                mm.then_inc(turned, 1)

        @block.vector
        def _(dve):
            for n in range(len(rows)):
                dve.wait_ge(turned, n + 1)
                nc.vector.tensor_copy(cols[:, n, :, :].rearrange("p h t -> p t h"),
                                      core.ps[:, n, 0:NT * h].rearrange("p (t h) -> p t h", t=NT))


def gated_heads(nc, core, name, y, gate, gain, width, before=None):
    f = y.shape[2]
    heads = f // width
    n = NT * heads
    with stage(nc, name, "var_ready", "root_ready") as (block, var_ready, root_ready):
        mv = core.mv[:, 0:n, :]

        @block.gpsimd
        def _(pool):
            inverse_root(nc, core, pool, mv[:, :, 1:2], 1e-6, var_ready, root_ready)

        @block.vector
        def _(dve):
            if before is not None:
                for t in range(NT):
                    nc.vector.tensor_tensor(y[:, t, :], y[:, t, :], before[:, t, :], ALU.mult)
                dve.drain()
            part = lambda g: y[:, g // heads, (g % heads) * width:(g % heads + 1) * width]
            row_stats(nc, core, dve, part, mv, width, n)
            mean_square(nc, dve, mv)
            dve.drain().then_inc(var_ready, 1)
            dve.wait_ge(root_ready, 2)
            for g in range(n):
                nc.vector.tensor_scalar(part(g), part(g), mv[:, g, 1:2], None, ALU.mult)
            dve.drain()
            for t in range(NT):
                if gain.shape[1] == f:
                    nc.vector.tensor_tensor(y[:, t, :], y[:, t, :], gain, ALU.mult)
                else:
                    run = y[:, t, :].rearrange("p (h f) -> p h f", h=heads)
                    nc.vector.tensor_tensor(run, run, gain.unsqueeze(1).to_broadcast([P, heads, width]), ALU.mult)
            dve.drain()
            if gate is not None:
                for t in range(NT):
                    nc.vector.tensor_tensor(y[:, t, :], y[:, t, :], gate[:, t, :], ALU.mult)


def decay_strips(nc, core, bank, edge, minus_col, out):
    for s in range(NT):
        nc.scalar.activation(strip(out, s, 0, P), edge[:, s, :], ACT.Exp, bias=minus_col(s))
        if s < NT - 1:
            nc.scalar.activation(strip(out, s, P), core.ps[:, bank, (s + 1) * P:SEQ], ACT.Exp, bias=minus_col(s))


GDN_HEADS, GDN_DK = 4, 128
LEVELS = 7


def unit_rows(nc, core, qkT):
    n = 2 * GDN_HEADS
    with buffers(nc, unit_sq=[P, n, SEQ]) as (sq,), \
            stage(nc, "unit", "squared", "summed", "inverted", "rooted") as (block, squared, summed, inverted, rooted):
        @block.scalar
        def _(act):
            for f in range(n):
                nc.scalar.activation(sq[:, f, :], qkT[:, f, :], ACT.Square).then_inc(squared, 1)
            for f in range(n):
                act.wait_ge(inverted, f + 1)
                nc.scalar.activation(sq[:, f, :], sq[:, f, :], ACT.Sqrt).then_inc(rooted, 1)

        @block.tensor
        def _(pe):
            for f in range(n):
                pe.wait_ge(squared, f + 1)
                nc.tensor.matmul(core.ps[:, f, :], core.ones[:], sq[:, f, :], start=True, stop=True).then_inc(summed, 1)

        @block.vector
        def _(dve):
            for f in range(n):
                dve.wait_ge(summed, f + 1)
                nc.vector.tensor_scalar(sq[:, f, :], core.ps[:, f, :], 1e-6, None, ALU.add)
                dve.drain()
                nc.vector.reciprocal(sq[:, f, :], sq[:, f, :]).then_inc(inverted, 1)
            for f in range(n):
                dve.wait_ge(rooted, f + 1)
                nc.vector.scalar_tensor_tensor(qkT[:, f, :], qkT[:, f, :], GDN_DK ** -0.5 if f < GDN_HEADS else 1.0,
                                               sq[:, f, :], ALU.mult, ALU.mult)


def delta_half(nc, core, half, qkvT, cum_rows, cols, vb, u, o, masks):
    H = GDN_HEADS
    heads = (2 * half, 2 * half + 1)
    kind_beta, kind_cum, kind_minus = 0, 1, 2
    with buffers(nc, keys=[P, 2, PACKED], attn=[P, 2, PACKED], decays=[P, PACKED], edge=[P, NT, P], diag=[P, 8, P],
                 inv=[P, 8, P], invT=[P, 8, P], rhs=[P, 2, P]) as (keys, attn, decays, edge, diag, inv, invT, rhs):
        part, prod = (core.tmp[:, q:q + 2, :].rearrange("p q (n t) -> p (q n) t", t=P) for q in (0, 2))
        with stage(nc, f"delta_scores{half}", "spread", "edged", "decayed", "scored", "applied") as (
                block, spread, edged, decayed, scored, applied):
            @block.tensor
            def _(pe):
                for n, h in enumerate(heads):
                    if n:
                        pe.wait_ge(decayed, n)
                    nc.tensor.matmul(core.ps[:, 0, :], core.onehot[0:H, h, :], cum_rows, start=True, stop=True).then_inc(spread, 1)
                    for m, first in enumerate((H + h, h)):
                        for s in range(NT):
                            if n or m:
                                pe.wait_ge(applied, NT * (2 * n + m - 1) + s + 1)
                            nc.tensor.matmul(core.ps[:, 1 + s, 0:SEQ - s * P], qkvT[:, H + h, s * P:(s + 1) * P],
                                             qkvT[:, first, s * P:], start=True, stop=True).then_inc(scored, 1)

            @block.scalar
            def _(act):
                for n, h in enumerate(heads):
                    act.wait_ge(edged, n + 1)
                    if n:
                        act.wait_ge(applied, 2 * NT * n)
                    decay_strips(nc, core, 0, edge, lambda s: cols[:, kind_minus, h, s:s + 1], decays)
                    act.drain().then_inc(decayed, 1)

            @block.vector
            def _(dve):
                for n, h in enumerate(heads):
                    dve.wait_ge(spread, n + 1)
                    if n:
                        dve.wait_ge(decayed, n)
                    nc.vector.tensor_tensor(edge[:], core.ps[:, 0, :].rearrange("p (s t) -> p s t", s=NT),
                                            core.causal[:].unsqueeze(1).to_broadcast([P, NT, P]), ALU.add).then_inc(edged, 1)
                    dve.wait_ge(decayed, n + 1)
                    for m, dst in enumerate((keys, attn)):
                        for s in range(NT):
                            dve.wait_ge(scored, NT * (2 * n + m) + s + 1)
                            nc.vector.tensor_tensor(strip(dst[:, n, :], s), core.ps[:, 1 + s, 0:SEQ - s * P],
                                                    strip(decays, s), ALU.mult).then_inc(applied, 1)

        with stage(nc, f"delta_inverse{half}", "masked", "first", "scaled", "second", "updated") as (
                block, masked, first, scaled, second, updated):
            banks = lambda b, n: core.ps[:, b + n // 4, (n % 4) * P:(n % 4 + 1) * P]
            flat = lambda b: core.ps[:, b:b + 2, :].rearrange("p b (n t) -> p (b n) t", n=4)
            beta = cols[:, kind_beta, heads[0]:heads[0] + 2, :].rearrange("p h t -> p (h t)")

            @block.vector
            def _(dve):
                for n in range(8):
                    nc.vector.tensor_copy(diag[:, n, :], strip(keys[:, n // 4, :], n % 4, 0, P))
                    nc.vector.tensor_copy(inv[:, n, :], core.ident[:])
                    nc.vector.tensor_copy(invT[:, n, :], core.ident[:])
                dve.drain()
                for level in range(LEVELS):
                    if level:
                        dve.wait_ge(first, level)
                    nc.vector.tensor_tensor(part[:], diag[:], masks[:, level, :].unsqueeze(1).to_broadcast([P, 8, P]),
                                            ALU.mult).then_inc(masked, 1)
                    dve.wait_ge(first, level + 1)
                    nc.vector.tensor_tensor(prod[:], flat(0), beta.unsqueeze(2).to_broadcast([P, 8, P]),
                                            ALU.mult).then_inc(scaled, 1)
                    dve.wait_ge(second, level + 1)
                    nc.vector.tensor_tensor(inv[:], inv[:], flat(2), ALU.subtract)
                    nc.vector.tensor_tensor(invT[:], invT[:], flat(4), ALU.subtract)
                    dve.drain().then_inc(updated, 1)

            @block.tensor
            def _(pe):
                for level in range(LEVELS):
                    pe.wait_ge(masked, level + 1)
                    if level:
                        pe.wait_ge(updated, level)
                    for n in range(8):
                        mm = nc.tensor.matmul(banks(0, n), part[:, n, :], inv[:, n, :], start=True, stop=True)
                    mm.then_inc(first, 1)
                    pe.wait_ge(scaled, level + 1)
                    for n in range(8):
                        nc.tensor.matmul(banks(2, n), invT[:, n, :], prod[:, n, :], start=True, stop=True)
                        mm = nc.tensor.matmul(banks(4, n), prod[:, n, :], invT[:, n, :], start=True, stop=True)
                    mm.then_inc(second, 1)

        with stage(nc, f"delta_solve{half}", "gathered", "sided", "solved", "stored", "output", "copied") as (
                block, gathered, sided, solved, stored, output, copied):
            @block.tensor
            def _(pe):
                for t in range(NT):
                    if t:
                        pe.wait_ge(stored, t)
                        for n, h in enumerate(heads):
                            for s in range(t):
                                mm = nc.tensor.matmul(core.ps[:, 0, n * P:(n + 1) * P], strip(keys[:, n, :], s, (t - s) * P, (t - s + 1) * P),
                                                      u[:, s, h * P:(h + 1) * P], start=s == 0, stop=s == t - 1)
                        mm.then_inc(gathered, 1)
                    pe.wait_ge(sided, t + 1)
                    for n in range(2):
                        mm = nc.tensor.matmul(core.ps[:, 1, n * P:(n + 1) * P], invT[:, 4 * n + t, :], rhs[:, n, :], start=True, stop=True)
                    mm.then_inc(solved, 1)
                pe.wait_ge(stored, NT)
                for n, h in enumerate(heads):
                    for t in range(NT):
                        for s in range(t + 1):
                            mm = nc.tensor.matmul(core.ps[:, 2 + n, t * P:(t + 1) * P], strip(attn[:, n, :], s, (t - s) * P, (t - s + 1) * P),
                                                  u[:, s, h * P:(h + 1) * P], start=s == 0, stop=s == t)
                    mm.then_inc(output, 1)

            @block.vector
            def _(dve):
                for t in range(NT):
                    if t:
                        dve.wait_ge(gathered, t)
                    for n, h in enumerate(heads):
                        v = vb[:, t, h * P:(h + 1) * P]
                        if t:
                            done = nc.vector.scalar_tensor_tensor(rhs[:, n, :], core.ps[:, 0, n * P:(n + 1) * P],
                                                                  cols[:, kind_beta, h, t:t + 1], v, ALU.mult, ALU.subtract)
                        else:
                            done = nc.vector.tensor_scalar(rhs[:, n, :], v, -1.0, None, ALU.mult)
                    done.then_inc(sided, 1)

            @block.scalar
            def _(act):
                for t in range(NT):
                    act.wait_ge(solved, t + 1)
                    nc.scalar.activation(u[:, t, heads[0] * P:(heads[0] + 2) * P], core.ps[:, 1, 0:2 * P], ACT.Copy,
                                         scale=-1.0).then_inc(stored, 1)
                for n, h in enumerate(heads):
                    act.wait_ge(output, n + 1)
                    nc.scalar.copy(o[:, :, h * P:(h + 1) * P], core.ps[:, 2 + n, :].rearrange("p (t f) -> p t f", t=NT))


def delta_branch(nc, core, d, o):
    H = GDN_HEADS
    with buffers(nc, qkvT=[P, 3 * H, SEQ], beta_row=[H, SEQ], g_row=[H, SEQ], g_tmp=[H, SEQ], dt_bias=[H, 1], a_rate=[H, 1],
                 cols=[P, 3, H, NT], masks=[P, LEVELS, P]) as (
            qkvT, beta_row, g_row, g_tmp, dt_bias, a_rate, cols, masks):
        u, vb = core.x[:, :, 0:H * P], core.x[:, :, H * P:2 * H * P]
        with buffers(nc, raw=[P, 3 * H, SEQ + 3], taps=[P, 4, 3 * H]) as (raw, taps):
            load_rows(nc, "delta_loads", [(taps[:], d["gdn_conv_c_2"]), (dt_bias[:], d["gdn_dt_bias_c_2"]),
                                          (a_rate[:], d["gdn_a_log_c_2"]), (masks[:], d["const_levels"])],
                      [raw[:, :, 0:3]])
            project(nc, core, "delta_in", core.hT, [("aqkv", 3, "feature", ("act", ACT.Copy, padded_tiles(raw, 3)))])
            row_products(nc, core, "delta_rows", [("beta_dt", [(0, H, beta_row[:]), (H, H, g_row[:])])])
            conv_silu(nc, core, "delta_conv", raw, qkvT, taps, None, 3 * H, 4)
        unit_rows(nc, core, qkvT)
        soft_maximum(nc, "delta_soft", [(g_row[:], g_tmp[:], 1.0, dt_bias[:], 0.0, 0.0)])
        with stage(nc, "delta_decay", "ready", "scanned") as (block, ready, scanned):
            @block.scalar
            def _(act):
                nc.scalar.activation(a_rate[:], a_rate[:], ACT.Exp).then_inc(ready, 1)
                nc.scalar.activation(beta_row[:], beta_row[:], ACT.Sigmoid)

            @block.vector
            def _(dve):
                dve.wait_ge(ready, 1)
                nc.vector.tensor_scalar(g_tmp[:], g_row[:], a_rate[:], -1.0, ALU.mult, ALU.mult)
                dve.drain()
                nc.vector.tensor_tensor_scan(g_row[:], core.one_row[0:H, :], g_tmp[:], 0.0, ALU.mult, ALU.add)
        row_columns(nc, core, "delta_cols", [beta_row, g_row], cols, H)
        with stage(nc, "delta_values", "turned") as (block, turned):
            @block.tensor
            def _(pe):
                for t in range(NT):
                    for h in range(H):
                        mm = nc.tensor.transpose(core.ps[:, t, h * P:(h + 1) * P], qkvT[:, 2 * H + h, t * P:(t + 1) * P], core.ident[:])
                    mm.then_inc(turned, 1)

            @block.vector
            def _(dve):
                nc.vector.tensor_scalar(cols[:, 2], cols[:, 1], -1.0, None, ALU.mult)
                for t in range(NT):
                    dve.wait_ge(turned, t + 1)
                    nc.vector.tensor_tensor(vb[:, t, :].rearrange("p (h f) -> p h f", h=H),
                                            core.ps[:, t, :].rearrange("p (h f) -> p h f", h=H),
                                            cols[:, 0, :, t:t + 1].to_broadcast([P, H, P]), ALU.mult)
        for half in range(2):
            delta_half(nc, core, half, qkvT, g_row[:], cols, vb, u, o, masks)


SUB = 16
SUBS = P // SUB


def channel_decay_unit(nc, core, name, heads, q, k, cum, last, v, o, sums, own_block):
    TB = SEQ // SUB
    tiles = lambda a: a.rearrange("p (t n) -> p t n", t=NT)
    blocks = lambda a: a.rearrange("p (b i) -> p b i", i=SUB)
    with buffers(nc, q_tile=[P, SEQ], q_block=[P, SEQ], ref=[P, TB], far=[P, 6, P], near=[P, 2, SUBS, P],
                 pair=[P, 4, SEQ], bias=[P, 6], own=[P, SEQ], scores=[P, 2, SEQ], cross=[P, 2, 6, P]) as (
            q_tile, q_block, ref, far, near, pair, bias, own, scores, cross):
        far_pairs = [(s, t) for t in range(NT) for s in range(t)]
        with stage(nc, name, "zeroed", "referred", "shifted", "raised_q", "queries", "biased", "raised_far", "far_ready",
                   "raised_near", "near_ready", "near_used", "differed", "raised", "paired", "pair_used", "far_scored",
                   "near_scored", "own_scored", "crossed", "merged", "output") as (
                block, zeroed, referred, shifted, raised_q, queries, biased, raised_far, far_ready,
                raised_near, near_ready, near_used, differed, raised, paired, pair_used, far_scored,
                near_scored, own_scored, crossed, merged, output):
            @block.gpsimd
            def _(pool):
                nc.gpsimd.memset(near[:], 0.0).then_inc(zeroed, 1)
                for j in range(SUB):
                    if j >= 4:
                        pool.wait_ge(pair_used, j - 3)
                    nc.gpsimd.tensor_tensor(blocks(pair[:, j % 4, :]), blocks(cum),
                                            blocks(cum)[:, :, j:j + 1].to_broadcast([P, TB, SUB]), ALU.subtract).then_inc(differed, 1)

            @block.vector
            def _(dve):
                nc.vector.memset(ref[:], 0.0)
                nc.vector.memset(bias[:], 0.0)
                dve.drain()
                nc.vector.tensor_copy(ref[:].rearrange("p (t b) -> p t b", t=NT)[:, :, 1:SUBS],
                                      tiles(cum).rearrange("p t (b i) -> p t b i", i=SUB)[:, :, 0:SUBS - 1, SUB - 1])
                for n, (s, t) in enumerate(far_pairs):
                    nc.vector.tensor_reduce(bias[:, n:n + 1], last[:, s:t], AX.X, ALU.add)
                dve.drain().then_inc(referred, 1)
                nc.vector.tensor_tensor(blocks(q_block[:]), blocks(cum), ref[:].unsqueeze(2).to_broadcast([P, TB, SUB]),
                                        ALU.subtract).then_inc(shifted, 1)
                dve.wait_ge(raised_q, 2)
                nc.vector.tensor_tensor(q_tile[:], q_tile[:], q, ALU.mult)
                nc.vector.tensor_tensor(q_block[:], q_block[:], q, ALU.mult).then_inc(queries, 1)
                for n, (s, t) in enumerate(far_pairs):
                    dve.wait_ge(raised_far, n + 1)
                    nc.vector.tensor_tensor(far[:, n, :], far[:, n, :], k[:, s * P:(s + 1) * P], ALU.mult).then_inc(far_ready, 1)
                for t in range(NT):
                    dve.wait_ge(raised_near, t + 1)
                    nc.vector.tensor_tensor(near[:, t % 2], near[:, t % 2], k[:, t * P:(t + 1) * P].unsqueeze(1).to_broadcast([P, SUBS, P]),
                                            ALU.mult).then_inc(near_ready, 1)
                for j in range(SUB):
                    dve.wait_ge(raised, j + 1)
                    b = blocks(pair[:, j % 4, :])
                    nc.vector.scalar_tensor_tensor(b, b, 1.0, blocks(k)[:, :, j:j + 1].to_broadcast([P, TB, SUB]), ALU.min, ALU.mult)
                    dve.drain()
                    nc.vector.tensor_tensor(pair[:, j % 4, :], pair[:, j % 4, :], q, ALU.mult).then_inc(paired, 1)
                for n in range(len(heads)):
                    dve.wait_ge(own_scored, n + 1)
                    nc.vector.tensor_tensor(tiles(own[:]), tiles(core.ps[:, 1 + n, :]),
                                            own_block.unsqueeze(1).to_broadcast([P, NT, P]), ALU.mult)
                    dve.drain()
                    dve.wait_ge(near_scored, n + 1)
                    nc.vector.tensor_tensor(scores[:, n, :], own[:], core.ps[:, 3 + n, :], ALU.add).then_inc(merged, 1)
                    dve.drain()

            @block.scalar
            def _(act):
                act.wait_ge(shifted, 1)
                nc.scalar.activation(q_tile[:], cum, ACT.Exp).then_inc(raised_q, 1)
                nc.scalar.activation(q_block[:], q_block[:], ACT.Exp).then_inc(raised_q, 1)
                act.wait_ge(referred, 1)
                for n, (s, t) in enumerate(far_pairs):
                    nc.scalar.activation(far[:, n, :], cum[:, s * P:(s + 1) * P], ACT.Exp, bias=bias[:, n:n + 1],
                                         scale=-1.0).then_inc(raised_far, 1)
                for n in range(len(heads)):
                    act.wait_ge(far_scored, n + 1)
                    nc.scalar.copy(cross[:, n, 0:4, :], core.ps[:, 5, :].rearrange("p (n t) -> p n t", n=4))
                    nc.scalar.copy(cross[:, n, 4:6, :], core.ps[:, 6, 0:2 * P].rearrange("p (n t) -> p n t", n=2)).then_inc(crossed, 1)
                act.wait_ge(zeroed, 1)
                for t in range(NT):
                    if t >= 2:
                        act.wait_ge(near_used, t - 1)
                    for b in range(1, SUBS):
                        done = nc.scalar.activation(near[:, t % 2, b, 0:b * SUB], cum[:, t * P:t * P + b * SUB], ACT.Exp,
                                                    bias=ref[:, t * SUBS + b:t * SUBS + b + 1], scale=-1.0)
                    done.then_inc(raised_near, 1)
                for j in range(SUB):
                    act.wait_ge(differed, j + 1)
                    nc.scalar.activation(pair[:, j % 4, :], pair[:, j % 4, :], ACT.Exp).then_inc(raised, 1)
                for n, (_, _, col) in enumerate(heads):
                    act.wait_ge(output, n + 1)
                    nc.scalar.copy(o[:, :, col:col + P], core.ps[:, (0, 7)[n], :].rearrange("p (t f) -> p t f", t=NT))

            @block.tensor
            def _(pe):
                pe.wait_ge(queries, 1)
                pe.wait_ge(far_ready, len(far_pairs))
                for n, (r, rows, _) in enumerate(heads):
                    if n:
                        pe.wait_ge(crossed, n)
                    for m, (s, t) in enumerate(far_pairs):
                        mm = nc.tensor.matmul(core.ps[:, 5 + m // 4, (m % 4) * P:(m % 4 + 1) * P], far[r:r + rows, m, :],
                                              q_tile[r:r + rows, t * P:(t + 1) * P], start=True, stop=True)
                    mm.then_inc(far_scored, 1)
                for t in range(NT):
                    pe.wait_ge(near_ready, t + 1)
                    for n, (r, rows, _) in enumerate(heads):
                        for b in range(SUBS):
                            at = t * P + b * SUB
                            mm = nc.tensor.matmul(core.ps[:, 3 + n, at:at + SUB], near[r:r + rows, t % 2, b, :],
                                                  q_block[r:r + rows, at:at + SUB], start=True, stop=True)
                        if t == NT - 1:
                            mm.then_inc(near_scored, 1)
                    pe.drain().then_inc(near_used, 1)
                for j in range(SUB):
                    pe.wait_ge(paired, j + 1)
                    for n, (r, rows, _) in enumerate(heads):
                        mm = nc.tensor.matmul(core.ps[:, 1 + n, :], sums[r:r + rows, j, :], pair[r:r + rows, j % 4, :],
                                              start=j == 0, stop=j == SUB - 1)
                    mm.then_inc(pair_used, 1)
                pe.drain().then_inc(own_scored, len(heads))
                for n, (_, _, col) in enumerate(heads):
                    pe.wait_ge(merged, n + 1)
                    pe.wait_ge(crossed, n + 1)
                    for t in range(NT):
                        out = core.ps[:, (0, 7)[n], t * P:(t + 1) * P]
                        for s in range(t):
                            nc.tensor.matmul(out, cross[:, n, far_pairs.index((s, t)), :], v[:, s, col:col + P], start=s == 0, stop=False)
                        mm = nc.tensor.matmul(out, scores[:, n, t * P:(t + 1) * P], v[:, t, col:col + P], start=t == 0, stop=True)
                    mm.then_inc(output, 1)


def tile_sums(nc, core, name, logs, cum, last, units):
    with stage(nc, name) as (block,):
        @block.vector
        def _(dve):
            for u in range(units):
                nc.vector.tensor_tensor_scan(cum[:, u, :], core.tile_row[:], logs[:, u, :], 0.0, ALU.mult, ALU.add)
            dve.drain()
            for u in range(units):
                nc.vector.tensor_copy(last[:, u, :], cum[:, u, :].rearrange("p (t n) -> p t n", t=NT)[:, :, P - 1])


def gla_branch(nc, core, d, o, sums, own_block):
    with buffers(nc, qkT=[P, 4, SEQ], v=[P, NT, SEQ], lr=[16, SEQ], w2=[16, 256], b2=[P, 2], logs=[P, 2, SEQ], cum=[P, 2, SEQ],
                 last=[P, 2, NT]) as (qkT, v, lr, w2, b2, logs, cum, last):
        load_rows(nc, "gla_loads", [(w2[:], d["gla_w2_2"][0]), (b2[:], d["gla_b2_c_2"])])
        project(nc, core, "gla_in", core.hT, [("bqk", 1, "feature", ("act", ACT.Copy, feature_tiles(qkT))),
                                              ("bv", 1, "token", ("act", ACT.Copy, columns(v)))])
        row_products(nc, core, "gla_rows", [("blr", [(0, 16, lr[:])])])
        with stage(nc, "gla_gate", "gated") as (block, gated):
            @block.tensor
            def _(pe):
                for u in range(2):
                    nc.tensor.matmul(core.ps[:, u, :], w2[:, u * P:(u + 1) * P], lr[:], start=True, stop=True).then_inc(gated, 1)

            @block.vector
            def _(dve):
                for u in range(2):
                    dve.wait_ge(gated, u + 1)
                    nc.vector.tensor_scalar(logs[:, u, :], core.ps[:, u, :], b2[:, u:u + 1], None, ALU.add)
                nc.vector.tensor_scalar(qkT[:, 0:2, :], qkT[:, 0:2, :], 64 ** -0.5, None, ALU.mult)
        soft_maximum(nc, "gla_soft", [(logs[:, u, :], cum[:, u, :], -1.0, 0.0, 0.0, 0.0) for u in range(2)])
        with stage(nc, "gla_scale") as (block,):
            @block.vector
            def _(dve):
                nc.vector.tensor_scalar(logs[:], logs[:], -1.0 / 16.0, None, ALU.mult)
        tile_sums(nc, core, "gla_sums", logs, cum, last, 2)
        for u in range(2):
            channel_decay_unit(nc, core, f"gla{u}", [(0, 64, 2 * u * P), (64, 64, (2 * u + 1) * P)], qkT[:, u, :], qkT[:, 2 + u, :],
                               cum[:, u, :], last[:, u, :], v, o, sums, own_block)


def hgrn_branch(nc, core, d, o, sums, own_block):
    H = 4
    with buffers(nc, q=[P, H, SEQ], k=[P, H, SEQ], v=[P, NT, SEQ], logs=[P, H, SEQ], last=[P, H, NT],
                 lb=[P, 7, H]) as (q, k, v, logs, last, lb):
        project(nc, core, "hgrn_q", core.hT, [("cq", 1, "feature", ("act", ACT.Silu, feature_tiles(q)))])
        project(nc, core, "hgrn_fi", core.hT, [("cf", 1, "feature", ("act", ACT.Copy, feature_tiles(logs))),
                                               ("ci", 1, "token", ("act", ACT.Copy, columns(v)))])
        LB, LOG_LB, MINUS_LOG_LB, REST, LOG_REST, EXP, TMP = range(7)
        with stage(nc, "hgrn_bound", "loaded", "differed", "raised", "bounded", "logged", "keyed") as (
                block, loaded, differed, raised, bounded, logged, keyed):
            @block.sync
            def _(sp):
                sp.dma_start(lb[:, TMP, :], d["hgrn_lb_c_2"]).then_inc(loaded, 16)

            @block.vector
            def _(dve):
                dve.wait_ge(loaded, 16)
                nc.vector.tensor_tensor(lb[:, EXP, :], lb[:, TMP, :], lb[:, TMP, :], ALU.subtract).then_inc(differed, 1)
                dve.wait_ge(raised, 1)
                nc.vector.reciprocal(lb[:, TMP, :], lb[:, EXP, :])
                dve.drain()
                nc.vector.tensor_tensor(lb[:, EXP, :], lb[:, EXP, :], lb[:, TMP, :], ALU.mult)
                dve.drain()
                nc.vector.tensor_tensor(lb[:, LB, :], lb[:, EXP, :], lb[:, EXP, :], ALU.subtract)
                dve.drain()
                nc.vector.tensor_scalar(lb[:, LB, :], lb[:, LB, :], 0.0, 1.0, ALU.max, ALU.min)
                dve.drain()
                nc.vector.tensor_scalar(lb[:, REST, :], lb[:, LB, :], -1.0, 1.0, ALU.mult, ALU.add)
                nc.vector.tensor_scalar(lb[:, TMP, :], lb[:, LB, :], 1e-30, 2.0 ** 50, ALU.max, ALU.mult)
                dve.drain().then_inc(bounded, 1)
                dve.wait_ge(logged, 2)
                nc.vector.tensor_scalar(lb[:, LOG_LB, :], lb[:, LOG_LB, :], -50.0 * float(np.log(2.0)), None, ALU.add)
                dve.drain()
                nc.vector.tensor_scalar(lb[:, MINUS_LOG_LB, :], lb[:, LOG_LB, :], -1.0, None, ALU.mult)
                dve.wait_ge(keyed, H)
                for h in range(H):
                    nc.vector.tensor_scalar(k[:, h, :], k[:, h, :], lb[:, REST, h:h + 1], None, ALU.mult)
                nc.vector.tensor_scalar(q[:], q[:], 128 ** -0.5, None, ALU.mult)

            @block.scalar
            def _(act):
                act.wait_ge(differed, 1)
                nc.scalar.activation(lb[:, EXP, :], lb[:, EXP, :], ACT.Exp).then_inc(raised, 1)
                act.wait_ge(bounded, 1)
                nc.scalar.activation(lb[:, LOG_LB, :], lb[:, TMP, :], ACT.Ln).then_inc(logged, 1)
                nc.scalar.activation(lb[:, LOG_REST, :], lb[:, REST, :], ACT.Ln).then_inc(logged, 1)
                for h in range(H):
                    nc.scalar.activation(k[:, h, :], logs[:, h, :], ACT.Sigmoid, scale=-1.0).then_inc(keyed, 1)
        tmp = core.tmp
        soft_maximum(nc, "hgrn_soft", [(logs[:, h, :], tmp[:, h, :], -1.0, 0.0, 0.0, 0.0) for h in range(H)])
        soft_maximum(nc, "hgrn_add", [(logs[:, h, :], tmp[:, h, :], -1.0, lb[:, LOG_REST, h:h + 1], lb[:, LOG_LB, h:h + 1],
                                       lb[:, MINUS_LOG_LB, h:h + 1]) for h in range(H)])
        cum = core.tmp
        tile_sums(nc, core, "hgrn_sums", logs, cum, last, H)
        for h in range(H):
            channel_decay_unit(nc, core, f"hgrn{h}", [(0, P, h * P)], q[:, h, :], k[:, h, :], cum[:, h, :], last[:, h, :],
                               v, o, sums, own_block)


def second_mixer(nc, core, d):
    with buffers(nc, o=[P, NT, SEQ], gain=[P, P]) as (o, gain):
        def close(name, gain_name, gate_plan, share_plan, out_plan, first):
            with buffers(nc, gate=[P, NT, SEQ], oT=[P, 4, SEQ], share=[P, NT, D]) as (gate, oT, share):
                load_rows(nc, f"{name}_gain", [(gain[:], d[gain_name][0, :].partition_broadcast(P))])
                project(nc, core, f"{name}_gate", core.hT, [(gate_plan, 1, "token", ("act", ACT.Silu, columns(gate)))])
                project(nc, core, f"{name}_share", core.hT, [(share_plan, 2, "token", ("act", ACT.Sigmoid, columns(share)))])
                gated_heads(nc, core, f"{name}_heads", o, gate, gain[:], P)
                transpose(nc, core, f"{name}_T", o, oT, 4)
                project(nc, core, f"{name}_out", oT, [(out_plan, 2, "token", ("mul" if first else "mad", columns(share), columns(core.x)))], kt=4)

        delta_branch(nc, core, d, o)
        close("gdn", "gdn_norm_2", "ag", "ma", "br_a", True)
        with buffers(nc, sums=[P, SUB, P], own_block=[P, P]) as (sums, own_block):
            load_rows(nc, "sub_loads", [(sums[:], d["const_sums"]), (own_block[:], d["const_own_block"])])
            gla_branch(nc, core, d, o, sums, own_block[:])
        close("gla", "gla_norm_2", "bg", "mb", "br_b", False)
        with buffers(nc, sums=[P, SUB, P], own_block=[P, P]) as (sums, own_block):
            load_rows(nc, "sub_loads_", [(sums[:], d["const_sums"]), (own_block[:], d["const_own_block"])])
            hgrn_branch(nc, core, d, o, sums, own_block[:])
        close("hgrn", "hgrn_norm_2", "cg", "mc", "br_c", False)
    with buffers(nc, yT=[P, KD, SEQ]) as (yT,):
        transpose(nc, core, "mix_T", core.x, yT)
        project(nc, core, "out2", yT, [("out2", 2, "token", ("axpy", ALPHA, columns(core.h)))])


EXPERTS, GROUPS, MEMBERS, FF = 16, 4, 4, 256


def choose_experts(nc, core, d, combine):
    first = take(core, "router", 1)
    n = NT * GROUPS
    with buffers(nc, score=[P, NT, EXPERTS], sel=[P, NT, EXPERTS], bias=[P, EXPERTS], pair_sums=[P, n, 6], best=[P, n], beats=[P, n, 4, 4],
                 same=[P, n, 4, 4], rank=[P, n, 4], g_rank=[P, n], total=[P, NT], before=[P, 4, 4]) as (
            score, sel, bias, pair_sums, best, beats, same, rank, g_rank, total, before):
        with stage(nc, "choose", "loaded", "scored", "squashed") as (block, loaded, scored, squashed):
            @block.sync
            def _(sp):
                sp.dma_start(bias[:], d["router_bias_2"].partition_broadcast(P)).then_inc(loaded, 16)
                sp.dma_start(before[:], d["const_before"].partition_broadcast(P)).then_inc(loaded, 16)
                load_ahead(core, sp, core.taken)

            @block.tensor
            def _(pe):
                pe.wait_ge(core.ring_loaded[first % SLOTS], 16 * (first // SLOTS + 1))
                w = ring_view(core, first % SLOTS, KD, EXPERTS)
                for t in range(NT):
                    for k in range(KD):
                        mm = nc.tensor.matmul(core.ps[:, 0, t * EXPERTS:(t + 1) * EXPERTS], core.hT[:, k, t * P:(t + 1) * P], w[:, k, :],
                                              start=k == 0, stop=k == KD - 1)
                    mm.then_inc(core.products, 1)

            @block.scalar
            def _(act):
                act.wait_ge(core.products, QUARTERS * (first + 1))
                nc.scalar.activation(score[:].rearrange("p t e -> p (t e)"), core.ps[:, 0, 0:NT * EXPERTS], ACT.Sigmoid).then_inc(squashed, 1)

            def ranks(dve, values, out, count, lists):
                mine = values.unsqueeze(3).to_broadcast([P, lists, count, count])
                other = values.unsqueeze(2).to_broadcast([P, lists, count, count])
                a, b = beats[:, 0:lists], same[:, 0:lists]
                nc.vector.tensor_tensor(a, other, mine, ALU.is_gt)
                nc.vector.tensor_tensor(b, other, mine, ALU.is_equal)
                dve.drain()
                nc.vector.tensor_tensor(b, b, before[:].unsqueeze(1).to_broadcast([P, lists, count, count]), ALU.mult)
                dve.drain()
                nc.vector.tensor_tensor(a, a, b, ALU.add)
                dve.drain()
                nc.vector.tensor_reduce(out, a, AX.X, ALU.add)
                dve.drain()

            @block.vector
            def _(dve):
                dve.wait_ge(loaded, 32)
                dve.wait_ge(squashed, 1)
                nc.vector.tensor_tensor(sel[:], score[:], bias[:].unsqueeze(1).to_broadcast([P, NT, EXPERTS]), ALU.add)
                dve.drain()
                member = sel[:].rearrange("p t (g e) -> p (t g) e", g=GROUPS)
                m = 0
                for i in range(MEMBERS):
                    for j in range(i + 1, MEMBERS):
                        nc.vector.tensor_tensor(pair_sums[:, :, m:m + 1], member[:, :, i:i + 1], member[:, :, j:j + 1], ALU.add)
                        m += 1
                dve.drain()
                nc.vector.tensor_reduce(best[:], pair_sums[:], AX.X, ALU.max)
                ranks(dve, member, rank[:], MEMBERS, n)
                ranks(dve, best[:].rearrange("p (t g) -> p t g", t=NT), g_rank[:].rearrange("p (t g) -> p t g", t=NT), GROUPS, NT)
                nc.vector.tensor_scalar(rank[:], rank[:], 1.5, None, ALU.is_lt)
                nc.vector.tensor_scalar(g_rank[:], g_rank[:], 0.5, None, ALU.is_lt)
                dve.drain()
                nc.vector.tensor_tensor(rank[:], rank[:], g_rank[:].unsqueeze(2).to_broadcast([P, n, MEMBERS]), ALU.mult)
                dve.drain()
                nc.vector.tensor_tensor(score[:], score[:], rank[:].rearrange("p (t g) e -> p t (g e)", t=NT), ALU.mult)
                dve.drain()
                nc.vector.tensor_reduce(total[:], score[:], AX.X, ALU.add)
                dve.drain()
                nc.vector.reciprocal(total[:], total[:])
                dve.drain()
                nc.vector.tensor_tensor(combine[:], score[:], total[:].unsqueeze(2).to_broadcast([P, NT, EXPERTS]), ALU.mult)


def moe(nc, core, d):
    with buffers(nc, combine=[P, NT, EXPERTS], silu_g=[P, 2, SEQ], hidden=[P, 2, SEQ]) as (combine, silu_g, hidden):
        choose_experts(nc, core, d, combine)
        first = take(core, "expert", 2 * EXPERTS)
        in_slot, out_slot = first % 2, 1 - first % 2
        turn = lambda e, second: (first + second) // 2 + e
        with stage(nc, "moe", "added", "activated", "hidden_ready") as (block, added, activated, hidden_ready):
            @block.sync
            def _(sp):
                load_ahead(core, sp, core.taken)

            @block.tensor
            def _(pe):
                w_in = ring_view(core, in_slot, KD, 2 * FF)
                w_out = ring_view(core, out_slot, 2, D)
                with pe.Fori(0, EXPERTS) as e:
                    pe.wait_ge(core.ring_loaded[in_slot], 16 * (turn(e, 0) + 1))
                    pe.wait_ge(hidden_ready, 2 * e + 2)
                    for f in range(2):
                        for part in range(2):
                            col = part * FF + f * P
                            for k in range(KD):
                                mm = nc.tensor.matmul(core.ps[:, 2 * part + f, :], w_in[:, k, col:col + P], core.hT[:, k, :],
                                                      start=k == 0, stop=k == KD - 1)
                            mm.then_inc(core.products, 1)
                    pe.wait_ge(core.ring_loaded[out_slot], 16 * (turn(e, 1) + 1))
                    pe.wait_ge(hidden_ready, 2 * e + 4)
                    for t in range(NT):
                        for half in range(2):
                            pe.wait_ge(added, 8 * e + 2 * t + half + 1)
                            for f in range(2):
                                mm = nc.tensor.matmul(core.ps[:, 4 + (2 * t + half) % 4, :], hidden[:, f, t * P:(t + 1) * P],
                                                      w_out[:, f, half * BANK:(half + 1) * BANK], start=f == 0, stop=f == 1)
                        mm.then_inc(core.products, 1)

            @block.scalar
            def _(act):
                with act.Fori(0, EXPERTS) as e:
                    for f in range(2):
                        act.wait_ge(core.products, QUARTERS * (first + 2 * e) + 2 * f + 1)
                        nc.scalar.activation(silu_g[:, f, :], core.ps[:, f, :], ACT.Silu).then_inc(activated, 1)

            @block.vector
            def _(dve):
                dve.sem_inc(hidden_ready, 2)
                dve.sem_inc(added, 4)
                nc.vector.tensor_scalar(core.x[:], core.x[:], ALPHA, None, ALU.mult)
                with dve.Fori(0, EXPERTS) as e:
                    for f in range(2):
                        dve.wait_ge(activated, 2 * e + f + 1)
                        dve.wait_ge(core.products, QUARTERS * (first + 2 * e) + 2 * f + 2)
                        nc.vector.tensor_tensor(hidden[:, f, :], silu_g[:, f, :], core.ps[:, 2 + f, :], ALU.mult).then_inc(hidden_ready, 1)
                    dve.drain()
                    for t in range(NT):
                        dve.wait_ge(core.products, QUARTERS * (first + 2 * e + 1) + t + 1)
                        for half in range(2):
                            part = core.x[:, t, half * BANK:(half + 1) * BANK]
                            nc.vector.scalar_tensor_tensor(part, core.ps[:, 4 + (2 * t + half) % 4, :], combine[:, t, bass.ds(e, 1)], part,
                                                           ALU.mult, ALU.add).then_inc(added, 1)


def second_block(nc, core, d):
    norm(nc, core, "norm0_2", core.x, core.h, core.hT, 1e-5, False, core.row_a[:], core.row_b[:],
         [(core.row_a[:], d["ln0_g_2"]), (core.row_b[:], d["ln0_b_2"])])
    second_mixer(nc, core, d)
    norm(nc, core, "norm1_2", core.h, core.x, core.hT, 1e-5, False, core.row_a[:], core.row_b[:],
         [(core.row_a[:], d["ln1_g_2"][0]), (core.row_b[:], d["ln1_b_2"][0])])
    moe(nc, core, d)
    norm(nc, core, "norm2_2", core.x, core.x, None, 1e-5, False, core.row_a[:], core.row_b[:],
         [(core.row_a[:], d["ln2_g_2"][0]), (core.row_b[:], d["ln2_b_2"][0])])


def plan_two(d):
    w = d["w_in_2"][0]
    one = lambda name, lo, n=1: [(name, kmajor(w, lo + i * BANK, BANK)) for i in range(n)]
    few = lambda name, lo, n: [(name, kmajor(w, lo, n))]
    wide = lambda name, m, k: [(name, m[:, i * BANK:(i + 1) * BANK].rearrange("(k p) n -> p k n", p=P)) for i in range(2)]
    plan = one("aqkv", 0, 3) + few("beta_dt", 1536, 8)
    plan += one("ag", 1544) + one("ma", 5656, 2) + wide("br_a", d["w_br_a_2"][0], 4)
    plan += one("bqk", 2056) + one("bv", 2568) + few("blr", 3080, 16)
    plan += one("bg", 3096) + one("mb", 6680, 2) + wide("br_b", d["w_br_b_2"][0], 4)
    plan += one("cq", 3608) + one("cf", 4120) + one("ci", 4632)
    plan += one("cg", 5144) + one("mc", 7704, 2) + wide("br_c", d["w_br_c_2"][0], 4)
    plan += wide("out2", d["w_out_2"][0], 8)
    plan += [("router", kmajor(d["w_router_2"], 0, EXPERTS))]
    for e in range(EXPERTS):
        plan += [("expert", kmajor(d["w_gate_up_2"][e], 0, 2 * FF)), ("expert", kmajor(d["w_down_2"][0][e], 0, D))]
    return plan


M_HEADS, M_DQK = 8, 64
S_HEADS, S_HEADDIM, S_GROUPS = 16, 64, 4
D_FF = 2752
FF_TILES = -(-D_FF // P)
FF_CHUNKS = -(-D_FF // 256)


def causal_heads(nc, core, name, heads, rows, bias, keys, queries, share, scale, values, width, dens, finish):
    row_bank = (0, 7)
    with buffers(nc, weights=[P, 2, PACKED], decays=[P, 2, PACKED], edge=[P, 2, NT, P]) as (weights, decays, edge), \
            stage(nc, name, "spread", "edged", "decayed", "scored", "applied", "output", "finished") as (
                block, spread, edged, decayed, scored, applied, output, finished):
        @block.tensor
        def _(pe):
            for h in range(heads + 1):
                if h < heads:
                    if h >= 2:
                        pe.wait_ge(decayed, h - 1)
                    nc.tensor.matmul(core.ps[:, row_bank[h % 2], :], core.onehot[0:heads, h, :], rows, start=True, stop=True).then_inc(spread, 1)
                    if h % share == 0:
                        for s in range(NT):
                            if h:
                                pe.wait_ge(applied, NT * (h - 1) + s + 1)
                            nc.tensor.matmul(core.ps[:, 1 + s, 0:SEQ - s * P], keys(h, s), queries(h, s * P), start=True, stop=True).then_inc(scored, 1)
                if h >= 1:
                    g = h - 1
                    pe.wait_ge(applied, NT * (g + 1))
                    if g:
                        pe.wait_ge(finished, g)
                    for t in range(NT):
                        for s in range(t + 1):
                            w = strip(weights[:, g % 2, :], s, (t - s) * P, (t - s + 1) * P)
                            if dens:
                                nc.tensor.matmul(core.ps[:, 6, t:t + 1], w, core.ones[:, 0:1], start=s == 0, stop=s == t)
                            mm = nc.tensor.matmul(core.ps[:, 5, t * width:(t + 1) * width], w, values(g, s), start=s == 0, stop=s == t)
                    mm.then_inc(output, 1)

        @block.scalar
        def _(act):
            for h in range(heads):
                act.wait_ge(edged, h + 1)
                if h >= 2:
                    act.wait_ge(applied, NT * (h - 1))
                decay_strips(nc, core, row_bank[h % 2], edge[:, h % 2], lambda s: bias(h, s), decays[:, h % 2])
                act.drain().then_inc(decayed, 1)

        @block.vector
        def _(dve):
            for h in range(heads + 2):
                if h < heads:
                    dve.wait_ge(spread, h + 1)
                    if h >= 2:
                        dve.wait_ge(decayed, h - 1)
                    nc.vector.tensor_tensor(edge[:, h % 2], core.ps[:, row_bank[h % 2], :].rearrange("p (s t) -> p s t", s=NT),
                                            core.causal[:].unsqueeze(1).to_broadcast([P, NT, P]), ALU.add).then_inc(edged, 1)
                if 1 <= h <= heads:
                    g = h - 1
                    dve.wait_ge(decayed, g + 1)
                    if g >= 2:
                        dve.wait_ge(output, g - 1)
                    for s in range(NT):
                        dve.wait_ge(scored, NT * (g // share) + s + 1)
                        nc.vector.scalar_tensor_tensor(strip(weights[:, g % 2, :], s), core.ps[:, 1 + s, 0:SEQ - s * P], scale,
                                                       strip(decays[:, g % 2], s), ALU.mult, ALU.mult).then_inc(applied, 1)
                if h >= 2:
                    dve.wait_ge(output, h - 1)
                    finish(dve, h - 2).then_inc(finished, 1)


def mlstm_branch(nc, core, d, y):
    H = M_HEADS
    with buffers(nc, qkT=[P, KD, SEQ], v=[P, NT, D], i_row=[H, SEQ], f_row=[H, SEQ], sum_row=[H, SEQ], top_row=[H, SEQ],
                 i_bias=[H, 1], f_bias=[H, 1], cols=[P, 2, H, NT], den=[P, NT, 1]) as (
            qkT, v, i_row, f_row, sum_row, top_row, i_bias, f_bias, cols, den):
        with buffers(nc, raw=[P, KD, SEQ + 3], taps=[P, 4, KD], conv_bias=[P, KD]) as (raw, taps, conv_bias):
            load_rows(nc, "mlstm_loads", [(taps[:], d["m_conv_c_3"]), (conv_bias[:], d["m_conv_b_c_3"]),
                                          (i_bias[:], d["m_i_bias_c_3"]), (f_bias[:], d["m_f_bias_c_3"])], [raw[:, :, 0:3]])
            project(nc, core, "mlstm_in", core.hT, [("mqk", 2, "feature", ("act", ACT.Copy, padded_tiles(raw, 3))),
                                                    ("mv", 2, "token", ("act", ACT.Copy, columns(v)))])
            row_products(nc, core, "mlstm_rows", [("mif", [(0, H, i_row[:]), (H, H, f_row[:])])])
            conv_silu(nc, core, "mlstm_conv", raw, qkT, taps, conv_bias, KD, 4)
        with stage(nc, "mlstm_bias") as (block,):
            @block.vector
            def _(dve):
                nc.vector.tensor_scalar(f_bias[:], f_bias[:], -1.0, None, ALU.mult)
        soft_maximum(nc, "mlstm_soft", [(f_row[:], sum_row[:], -1.0, f_bias[:], 0.0, 0.0)])
        with stage(nc, "mlstm_gates", "ready") as (block, ready):
            @block.vector
            def _(dve):
                nc.vector.tensor_tensor_scan(sum_row[:], core.one_row[0:H, :], f_row[:], 0.0, ALU.mult, ALU.add)
                dve.drain()
                nc.vector.scalar_tensor_tensor(i_row[:], i_row[:], i_bias[:], sum_row[:], ALU.add, ALU.add)
                dve.drain()
                nc.vector.tensor_tensor_scan(top_row[:], core.one_row[0:H, :], i_row[:], -3e38, ALU.mult, ALU.max)
                dve.drain()
                nc.vector.tensor_scalar(top_row[:], top_row[:], -1.0, None, ALU.mult)
                dve.drain()
                nc.vector.tensor_tensor(sum_row[:], sum_row[:], top_row[:], ALU.add).then_inc(ready, 1)

            @block.scalar
            def _(act):
                act.wait_ge(ready, 1)
                nc.scalar.activation(sum_row[:], sum_row[:], ACT.Exp)
        row_columns(nc, core, "mlstm_cols", [i_row, sum_row], cols, H)
        half = lambda h: slice(h % 2 * M_DQK, (h % 2 + 1) * M_DQK)

        def finish(dve, h):
            nc.vector.scalar_tensor_tensor(den[:, :, 0], core.ps[:, 6, 0:NT], -1.0, cols[:, 1, h, :], ALU.mult, ALU.max)
            dve.drain()
            nc.vector.tensor_tensor(den[:, :, 0], den[:, :, 0], core.ps[:, 6, 0:NT], ALU.max)
            dve.drain()
            nc.vector.reciprocal(den[:], den[:])
            dve.drain()
            return nc.vector.tensor_tensor(y[:, :, h * P:(h + 1) * P], core.ps[:, 5, :].rearrange("p (t f) -> p t f", t=NT),
                                           den[:].to_broadcast([P, NT, P]), ALU.mult)

        causal_heads(nc, core, "mlstm", H, top_row[:], lambda h, s: cols[:, 0, h, s:s + 1],
                     lambda h, s: qkT[half(h), H // 2 + h // 2, s * P:(s + 1) * P], lambda h, lo: qkT[half(h), h // 2, lo:],
                     1, M_DQK ** -0.5, lambda h, s: v[:, s, h * P:(h + 1) * P], P, True, finish)


def mamba_branch(nc, core, d, y):
    H, tiles = S_HEADS, 2 * KD
    with buffers(nc, xbc=[P, tiles, SEQ], dt_row=[H, SEQ], cs_row=[H, SEQ], dt_bias=[H, 1], a_rate=[H, 1], skip=[P, H],
                 cols=[P, 2, H, NT]) as (xbc, dt_row, cs_row, dt_bias, a_rate, skip, cols):
        with buffers(nc, raw=[P, tiles, SEQ + 3], taps=[P, 4, tiles], conv_bias=[P, tiles]) as (raw, taps, conv_bias):
            load_rows(nc, "mamba_loads", [(taps[:], d["s_conv_c_3"]), (conv_bias[:], d["s_conv_b_c_3"]), (dt_bias[:], d["s_dt_bias_c_3"]),
                                          (a_rate[:], d["s_a_log_c_3"]), (skip[:], d["s_d_3"][0, :].partition_broadcast(P))], [raw[:, :, 0:3]])
            project(nc, core, "mamba_in", core.hT, [("xbc", 4, "feature", ("act", ACT.Copy, padded_tiles(raw, 3)))])
            row_products(nc, core, "mamba_rows", [("sdt", [(0, H, dt_row[:])])])
            conv_silu(nc, core, "mamba_conv", raw, xbc, taps, conv_bias, tiles, 4)
        soft_maximum(nc, "mamba_soft", [(dt_row[:], cs_row[:], 1.0, dt_bias[:], 0.0, 0.0)])
        with buffers(nc, xc=[P, NT, D], rates=[H, SEQ]) as (xc, rates):
            with stage(nc, "mamba_decay", "ready") as (block, ready):
                @block.scalar
                def _(act):
                    nc.scalar.activation(a_rate[:], a_rate[:], ACT.Exp).then_inc(ready, 1)

                @block.vector
                def _(dve):
                    dve.wait_ge(ready, 1)
                    nc.vector.tensor_scalar(rates[:], dt_row[:], a_rate[:], -1.0, ALU.mult, ALU.mult)
                    dve.drain()
                    nc.vector.tensor_tensor_scan(cs_row[:], core.one_row[0:H, :], rates[:], 0.0, ALU.mult, ALU.add)
            row_columns(nc, core, "mamba_cols", [dt_row, cs_row], cols, H)
            with stage(nc, "mamba_values", "turned", "copied") as (block, turned, copied):
                @block.tensor
                def _(pe):
                    for t in range(NT):
                        for f in range(KD):
                            mm = nc.tensor.transpose(core.ps[:, 2 * t + f // 4, f % 4 * P:(f % 4 + 1) * P], xbc[:, f, t * P:(t + 1) * P], core.ident[:])
                        mm.then_inc(turned, 1)

                @block.scalar
                def _(act):
                    for t in range(NT):
                        act.wait_ge(turned, t + 1)
                        nc.scalar.copy(y[:, t, :].rearrange("p (b f) -> p b f", b=2), core.ps[:, 2 * t:2 * t + 2, :]).then_inc(copied, 1)

                @block.vector
                def _(dve):
                    nc.vector.tensor_scalar(cols[:, 1], cols[:, 1], -1.0, None, ALU.mult)
                    for t in range(NT):
                        dve.wait_ge(copied, t + 1)
                        nc.vector.tensor_tensor(xc[:, t, :].rearrange("p (h f) -> p h f", h=H),
                                                y[:, t, :].rearrange("p (h f) -> p h f", h=H),
                                                cols[:, 0, :, t:t + 1].to_broadcast([P, H, S_HEADDIM]), ALU.mult)
            share = H // S_GROUPS
            span = lambda h: slice(h * S_HEADDIM, (h + 1) * S_HEADDIM)

            def finish(dve, h):
                return nc.vector.scalar_tensor_tensor(y[:, :, span(h)], y[:, :, span(h)], skip[:, h:h + 1],
                                                      core.ps[:, 5, 0:NT * S_HEADDIM].rearrange("p (t f) -> p t f", t=NT), ALU.mult, ALU.add)

            causal_heads(nc, core, "mamba", H, cs_row[:], lambda h, s: cols[:, 1, h, s:s + 1],
                         lambda h, s: xbc[:, KD + h // share, s * P:(s + 1) * P], lambda h, lo: xbc[:, KD + S_GROUPS + h // share, lo:],
                         share, 1.0, lambda h, s: xc[:, s, span(h)], S_HEADDIM, False, finish)


def third_mixer(nc, core, d):
    with buffers(nc, y=[P, NT, D]) as (y,):
        def close(name, gain_name, gate_plan, share_plan, out_plan, width, first):
            with buffers(nc, gate=[P, NT, D], yT=[P, KD, SEQ], share=[P, NT, D]) as (gate, yT, share):
                load_rows(nc, f"{name}_gain", [(core.row_a[:], d[gain_name][0, :].partition_broadcast(P))])
                project(nc, core, f"{name}_gate", core.hT, [(gate_plan, 2, "token", ("act", ACT.Sigmoid if first else ACT.Silu, columns(gate)))])
                project(nc, core, f"{name}_share", core.hT, [(share_plan, 2, "token", ("act", ACT.Sigmoid, columns(share)))])
                gated_heads(nc, core, f"{name}_heads", y, gate if first else None, core.row_a[:], width, None if first else gate)
                transpose(nc, core, f"{name}_T", y, yT)
                project(nc, core, f"{name}_out", yT, [(out_plan, 2, "token", ("mul" if first else "mad", columns(share), columns(core.x)))])

        mlstm_branch(nc, core, d, y)
        close("mlstm", "m_norm_g_3", "mo", "ga", "pa", P, True)
        mamba_branch(nc, core, d, y)
        close("mamba", "s_norm_g_3", "sz", "gb", "pb", D // S_GROUPS, False)
    with buffers(nc, yT=[P, KD, SEQ]) as (yT,):
        transpose(nc, core, "mix3_T", core.x, yT)
        project(nc, core, "out3", yT, [("out3", 2, "token", ("axpy", ALPHA, columns(core.h)))])


def conv_ffn(nc, core, d):
    first = take(core, "up", FF_CHUNKS)
    down = take(core, "down", 7)
    with buffers(nc, taps=[P, 2, 3, FF_TILES], conv_bias=[P, 2, FF_TILES], hidden=[P, FF_TILES, SEQ], gate=[P, 2, 2, SEQ],
                 value=[P, 2, 2, SEQ]) as (taps, conv_bias, hidden, gate, value):
        load_rows(nc, "ffn_loads", [(taps[:], d["f_conv_c_3"]), (conv_bias[:], d["f_conv_b_c_3"])])

        def chunk_parts(j):
            half = D_FF % 256 if isinstance(j, int) else 256
            return 2 * half, [(part, f, part * half + f * P, min(P, half - f * P)) for part in range(2) for f in range(2)]

        with stage(nc, "ffn_up", "psum_free", "convolved", "activated") as (block, psum_free, convolved, activated):
            @block.sync
            def _(sp):
                load_ahead(core, sp, first + FF_CHUNKS)

            @block.tensor
            def _(pe):
                for j, turn, odd, c in pairs(pe, first, FF_CHUNKS):
                    pe.wait_ge(core.ring_loaded[odd], 16 * (turn + 1))
                    pe.wait_ge(psum_free, c - first + 1)
                    width, parts = chunk_parts(j)
                    w = ring_view(core, odd, KD, width)
                    for part, f, lo, m in parts:
                        for k in range(KD):
                            mm = nc.tensor.matmul(core.ps[0:m, 4 * odd + 2 * part + f, :], w[:, k, lo:lo + m], core.hT[:, k, :],
                                                  start=k == 0, stop=k == KD - 1)
                        mm.then_inc(core.products, 1)

            @block.vector
            def _(dve):
                dve.sem_inc(psum_free, 2)
                for j, _, odd, c in pairs(dve, first, FF_CHUNKS):
                    for part, f, _, m in chunk_parts(j)[1]:
                        dve.wait_ge(core.products, QUARTERS * c + 2 * part + f + 1)
                        u = core.ps[0:m, 4 * odd + 2 * part + f, :]
                        out = (gate, value)[part][0:m, odd, f, :]
                        tap = lambda k: taps[0:m, part, k, bass.ds(2 * j + f, 1)]
                        nc.vector.tensor_scalar(out, u, tap(2), conv_bias[0:m, part, bass.ds(2 * j + f, 1)], ALU.mult, ALU.add)
                        dve.drain()
                        nc.vector.scalar_tensor_tensor(out[:, 1:], u[:, 0:SEQ - 1], tap(1), out[:, 1:], ALU.mult, ALU.add)
                        dve.drain()
                        done = nc.vector.scalar_tensor_tensor(out[:, 2:], u[:, 0:SEQ - 2], tap(0), out[:, 2:], ALU.mult, ALU.add)
                        if part == 0:
                            done.then_inc(convolved, 1)
                    done.then_inc(psum_free, 1)
                    dve.drain()
                    for _, f, _, m in chunk_parts(j)[1][0:2]:
                        dve.wait_ge(activated, 2 * j + f + 1)
                        nc.vector.tensor_tensor(hidden[0:m, bass.ds(2 * j + f, 1), :].rearrange("p o n -> p (o n)"),
                                                gate[0:m, odd, f, :], value[0:m, odd, f, :], ALU.mult)

            @block.scalar
            def _(act):
                for j, _, odd, c in pairs(act, first, FF_CHUNKS):
                    for _, f, _, m in chunk_parts(j)[1][0:2]:
                        act.wait_ge(convolved, 2 * j + f + 1)
                        nc.scalar.activation(gate[0:m, odd, f, :], gate[0:m, odd, f, :], ACT.Silu).then_inc(activated, 1)

        with stage(nc, "ffn_down") as (block,):
            @block.sync
            def _(sp):
                load_ahead(core, sp, core.taken)

            @block.tensor
            def _(pe):
                k0 = 0
                for c in range(down, down + 7):
                    pe.wait_ge(core.ring_loaded[c % SLOTS], 16 * (c // SLOTS + 1))
                    m, kt = core.plan[c][1].shape[0:2]
                    w = ring_view(core, c % SLOTS, kt, D)
                    for t in range(NT):
                        for half in range(2):
                            for k in range(kt):
                                mm = nc.tensor.matmul(core.ps[:, 2 * t + half, :], hidden[0:m, k0 + k, t * P:(t + 1) * P],
                                                      w[0:m, k, half * BANK:(half + 1) * BANK], start=k0 + k == 0, stop=k0 + k == FF_TILES - 1)
                        mm.then_inc(core.products, 1)
                    k0 += kt

            @block.vector
            def _(dve):
                for t in range(NT):
                    dve.wait_ge(core.products, QUARTERS * (down + 6) + t + 1)
                    x = core.x[:, t, :].rearrange("p (b n) -> p b n", b=2)
                    nc.vector.scalar_tensor_tensor(x, x, ALPHA, core.ps[:, 2 * t:2 * t + 2, :], ALU.mult, ALU.add)


def third_block(nc, core, d):
    norm(nc, core, "norm0_3", core.x, core.h, core.hT, 1e-5, False, core.row_a[:], core.row_b[:],
         [(core.row_a[:], d["in_ln_g_3"]), (core.row_b[:], d["in_ln_b_3"])])
    third_mixer(nc, core, d)
    norm(nc, core, "norm1_3", core.h, core.x, core.hT, 1e-5, False, core.row_a[:], core.row_b[:],
         [(core.row_a[:], d["ln1_g_3"][0]), (core.row_b[:], d["ln1_b_3"][0])])
    conv_ffn(nc, core, d)
    norm(nc, core, "norm2_3", core.x, core.x, None, 1e-5, False, core.row_a[:], core.row_b[:],
         [(core.row_a[:], d["ln2_g_3"][0]), (core.row_b[:], d["ln2_b_3"][0])])


def plan_three(d):
    w = d["w_in_3"][0]
    plan = []
    add = lambda name, m, lo, n: plan.extend((name, kmajor(m, lo + i * BANK, BANK)) for i in range(n))
    add("mqk", w, 0, 2)
    add("mv", w, 1024, 2)
    plan.append(("mif", kmajor(w, 3072, 2 * M_HEADS)))
    add("mo", w, 2048, 2)
    add("ga", w, 6176, 2)
    add("pa", d["p_a_3"][0], 0, 2)
    add("xbc", w, 4112, 4)
    plan.append(("sdt", kmajor(w, 6160, S_HEADS)))
    add("sz", w, 3088, 2)
    add("gb", w, 7200, 2)
    add("pb", d["p_b_3"][0], 0, 2)
    add("out3", d["w_out_3"][0], 0, 2)
    plan += [("up", kmajor(d["w_up_pairs_3"], c * BANK, min(BANK, 2 * D_FF - c * BANK))) for c in range(FF_CHUNKS)]
    rows = d["w_down_3"][0]
    plan += [("down", rows[c * 4 * P:(c + 1) * 4 * P, :].rearrange("(k p) n -> p k n", p=P)) for c in range(5)]
    plan += [("down", rows[20 * P:21 * P, :].rearrange("(k p) n -> p k n", p=P)),
             ("down", rows[21 * P:D_FF, :].rearrange("(k p) n -> p k n", p=D_FF % P))]
    return plan


def build(nc, d, out, blocks):
    core = Core()
    core.plan, core.loaded, core.taken = [], 0, 0
    if 1 in blocks:
        core.plan += plan_one(d)
    if 2 in blocks:
        core.plan += plan_two(d)
    if 3 in blocks:
        core.plan += plan_three(d)
    with ExitStack() as ctx:
        sb = lambda n, s, dt=F32: ctx.enter_context(nc.sbuf_tensor(n, s, dt))
        core.x = sb("x_tokens", [P, NT, D])
        core.h = sb("h_tokens", [P, NT, D])
        core.hT = sb("h_features", [P, KD, SEQ])
        core.ring = [sb(f"ring{i}", [P, KD * BANK]) for i in range(SLOTS)]
        core.ident = sb("ident", [P, P])
        core.row_a = sb("row_a", [P, D])
        core.row_b = sb("row_b", [P, D])
        core.tmp = sb("evacuation_tmp", [P, NT, BANK])
        core.bn = sb("bn_parts", [P, 32, 6])
        core.mv = sb("mean_var", [P, 32, 2])
        core.minus_half = sb("minus_half", [P, 32, 1])
        core.ps = ctx.enter_context(nc.psum_tensor("psum", [P, 8, BANK], F32))
        sem = lambda n: ctx.enter_context(nc.semaphore(n))
        core.ring_loaded = [sem(f"ring_loaded{i}") for i in range(SLOTS)]
        core.products = sem("products")
        stored = sem("stored")

        with stage(nc, "start", "zeroed") as (block, zeroed):
            @block.gpsimd
            def _(pool):
                nc.gpsimd.memset(core.minus_half[:], -0.5)
                nc.gpsimd.memset(core.ident[:], 0.0).then_inc(zeroed, 1)
                pool.wait_ge(zeroed, 1)
                nc.gpsimd.affine_select(out=core.ident[:], in_=core.ident[:], compare_op=ALU.not_equal, fill=1.0,
                                        base=0, pattern=[[-1, P]], channel_multiplier=1)

            @block.sync
            def _(sp):
                load_ahead(core, sp, 0)
        if 1 in blocks:
            block_one(nc, core, d)
        else:
            load_rows(nc, "x_load", [(core.x[:], d["x"].rearrange("b (t p) f -> p (b t) f", p=P))])
        core.ones = sb("ones", [P, P])
        core.causal = sb("causal", [P, P])
        core.onehot = sb("onehot", [16, 16, P])
        core.one_row = sb("one_row", [16, SEQ])
        core.tile_row = sb("tile_row", [P, SEQ])
        with stage(nc, "later_start", "zeroed") as (block, zeroed):
            @block.gpsimd
            def _(pool):
                nc.gpsimd.memset(core.ones[:], 1.0)
                nc.gpsimd.memset(core.one_row[:], 1.0)
                nc.gpsimd.memset(core.onehot[:], 0.0)
                nc.gpsimd.memset(core.causal[:], 0.0)
                nc.gpsimd.memset(core.tile_row[:], 1.0).then_inc(zeroed, 1)
                pool.wait_ge(zeroed, 1)
                nc.gpsimd.affine_select(out=core.onehot[:], in_=core.onehot[:], compare_op=ALU.not_equal, fill=1.0,
                                        base=0, pattern=[[-1, 16], [0, P]], channel_multiplier=1)
                nc.gpsimd.affine_select(out=core.causal[:], in_=core.causal[:], compare_op=ALU.is_ge, fill=-1e30,
                                        base=0, pattern=[[1, P]], channel_multiplier=-1)
                nc.gpsimd.memset(core.tile_row[:].rearrange("p (t n) -> p t n", t=NT)[:, :, 0], 0.0)
        if 2 in blocks:
            second_block(nc, core, d)
        if 3 in blocks:
            third_block(nc, core, d)
        with nc.Block() as block:
            @block.sync
            def _(sp):
                sp.dma_start(out.rearrange("b (t p) f -> p (b t) f", p=P), core.x[:]).then_inc(stored, 16)
                sp.wait_ge(stored, 16)


def constants():
    half = RET_QK_DIM // 2
    inv = np.float32(10000.0) ** (-np.arange(half, dtype=np.float32) * np.float32(2.0) / np.float32(RET_QK_DIM))
    ang = np.arange(SEQ, dtype=np.float32)[:, None] * inv[None, :]
    tokens = lambda a: np.ascontiguousarray(a.reshape(NT, P, -1).transpose(1, 0, 2)).astype(np.float32)
    gamma = 1.0 - 2.0 ** (-5.0 - np.arange(RET_HEADS, dtype=np.float64))
    lag = np.arange(SEQ)[None, :] - np.arange(P)[:, None]
    decay = np.where(lag[:, None, :] >= 0, gamma[None, :, None] ** np.maximum(lag, 0)[:, None, :], 0.0)
    row = np.arange(P)
    levels = [(row[:, None] // (2 * b) == row[None, :] // (2 * b)) & (row[:, None] % (2 * b) < b) & (row[None, :] % (2 * b) >= b)
              for b in (2 ** n for n in range(LEVELS))]
    own = (row[:, None] // SUB == row[None, :] // SUB) & (row[None, :] >= row[:, None])
    sums = np.broadcast_to(row[None, None, :] % SUB == np.arange(SUB)[None, :, None], (P, SUB, P))
    order = np.arange(MEMBERS)
    later = {"const_levels": np.stack(levels, 1), "const_own_block": own, "const_sums": sums,
             "const_before": order[None, :] < order[:, None]}
    later = {k: np.ascontiguousarray(v).astype(np.float32) for k, v in later.items()}
    return {**later, "const_cos": tokens(np.cos(ang)), "const_sin": tokens(np.sin(ang)),
            "const_ret_decay": decay.astype(np.float32)}


def column_tiles(v):
    return np.ascontiguousarray(v.reshape(-1, P).T)


def laid_out(inputs):
    a = {k: np.ascontiguousarray(v) for k, v in inputs.items()}
    a["sgu_w_t"] = np.ascontiguousarray(np.transpose(a.pop("sgu_w")[0], (2, 0, 1)))
    a["sgu_b_t"] = np.ascontiguousarray(a.pop("sgu_b")[0].T)
    a["sub_keys_t"] = np.ascontiguousarray(
        np.transpose(a.pop("peer_sub_keys")[0].reshape(PAIRS, PEER_KEYS, P), (2, 0, 1)))
    a["c_col"] = column_tiles(a.pop("c")[0])
    a["gdn_conv_c_2"] = np.stack([column_tiles(tap) for tap in a.pop("gdn_conv_2")[0]], 1)
    a["gdn_dt_bias_c_2"] = a.pop("gdn_dt_bias_2").reshape(-1, 1)
    a["gdn_a_log_c_2"] = a.pop("gdn_a_log_2").reshape(-1, 1)
    a["gla_b2_c_2"] = column_tiles(a.pop("gla_b2_2")[0])
    a["hgrn_lb_c_2"] = column_tiles(a.pop("hgrn_lb_logits_2")[0])
    a["w_gate_up_2"] = np.concatenate([a.pop("w_gate_2")[0], a.pop("w_up_2")[0]], -1)
    taps = lambda w: np.stack([column_tiles(tap) for tap in w], 1)
    for name in ("m_conv", "s_conv"):
        a[f"{name}_c_3"] = taps(a.pop(f"{name}_w_3")[0])
        a[f"{name}_b_c_3"] = column_tiles(a.pop(f"{name}_b_3")[0])
    for name in ("m_i_bias", "m_f_bias", "s_dt_bias", "s_a_log"):
        a[f"{name}_c_3"] = a.pop(f"{name}_3").reshape(-1, 1)
    gate_value = lambda v: (v[..., :D_FF], v[..., D_FF:])
    whole = lambda v: np.pad(v, [(0, 0)] * (v.ndim - 1) + [(0, FF_TILES * P - D_FF)])
    a["f_conv_c_3"] = np.stack([taps(whole(w)) for w in gate_value(a.pop("f_conv_w_3")[0])], 1)
    a["f_conv_b_c_3"] = np.stack([column_tiles(whole(v)) for v in gate_value(a.pop("f_conv_b_3")[0])], 1)
    up = gate_value(a.pop("w_up_3")[0])
    a["w_up_pairs_3"] = np.concatenate([half[:, lo:lo + 256] for lo in range(0, D_FF, 256) for half in up], 1)
    a.update(constants())
    return a


def kernel(**inputs):
    import concourse.bacc as bacc
    from concourse.bass_utils import run_bass_kernel_spmd as run

    nc = bacc.Bacc("TRN2", target_bir_lowering=False, num_devices=1)
    arrays = {f"in_{k}": v for k, v in laid_out(inputs).items()}
    d = {k[3:]: nc.dram_tensor(k, v.shape, mybir.dt.from_np(v.dtype), kind="ExternalInput").ap() for k, v in arrays.items()}
    out = nc.dram_tensor("out_0", (1, SEQ, D), F32, kind="ExternalOutput").ap()
    build(nc, d, out, BLOCKS)
    return run(nc, [arrays], core_ids=[0]).results[0]["out_0"]
```

```python
from contextlib import ExitStack, contextmanager
from itertools import count

import numpy as np
import concourse.bass as bass
from concourse import mybir

F32 = mybir.dt.float32
U32 = mybir.dt.uint32
F32R = mybir.dt.float32r
ACT = mybir.ActivationFunctionType
ALU = mybir.AluOpType
AX = mybir.AxisListType

P = 128
SEQ = 512
NT = SEQ // P
D = 1024
KD = D // P
BANK = 512
QUARTERS = 4
BLOCKS = (1, 2, 3)
PLACES = {}
NUMBERS = count()
PIECE = KD // 2 * BANK
ALPHA = 2.0 ** 0.25


class Core:
    pass


@contextmanager
def stage(nc, name, *signals):
    sems = [nc.alloc_semaphore(f"{name}_{s}") for s in signals]
    with nc.Block() as block:
        yield (block, *sems)
    if sems:
        nc.clear_and_free_semaphores(sems)
        nc.all_engine_barrier()


@contextmanager
def buffers(nc, **shapes):
    with ExitStack() as ctx:
        made = []
        for name, shape in shapes.items():
            shape, dtype = (shape, F32) if isinstance(shape, list) else shape
            made.append(place(nc, ctx, f"{name}_{next(NUMBERS)}", shape, dtype))
        yield made


def place(nc, ctx, name, shape, dtype):
    tensor = ctx.enter_context(nc.sbuf_tensor(name, shape, dtype))
    PLACES[tensor.name] = nc.sbuf_base - 4 * int(np.prod(shape[1:]))
    return tensor


def over(nc, under, name, shape, dtype=F32):
    return nc.alloc_sbuf_tensor_at(f"{name}_{next(NUMBERS)}", shape, dtype, offset=PLACES[under.name])


def kmajor(w, lo, width):
    cut = w[:, lo:lo + width].rearrange("(k p) n -> p k n", p=P)
    half = cut.shape[1] // 2
    return [cut[:, 0:half, :], cut[:, half:, :]]


def load_ahead(core, sp, end):
    while core.loaded < min(end, 2 * len(core.plan)):
        c, half = divmod(core.loaded, 2)
        src = core.plan[c][1][half]
        if c:
            sp.wait_ge(core.split[half], c)
        sp.dma_start(piece(core.raw, half, *src.shape), src).then_inc(core.landed[half], 16)
        core.loaded += 1


def piece(buf, half, p, k, n):
    return buf[0:p, half, 0:k * n].rearrange("p (k n) -> p k n", k=k)


def weights(core, half, p, k, n):
    return [piece(part, half, p, k, n) for part in (core.high, core.low)]


def take(core, name, number):
    first = core.taken
    assert all(core.plan[first + i][0] == name for i in range(number)), (name, core.plan[first][0])
    core.taken += number
    return first


def plan_splits(core, end):
    start, core.splits = core.splits, min(end, 2 * len(core.plan))
    return start


def split(nc, dve, whole, high, low):
    nc.vector.tensor_copy(high, whole)
    dve.drain()
    return nc.vector.tensor_tensor(low, whole, high.bitcast(F32), ALU.subtract)


def split_piece(nc, core, dve, c, half, cols=PIECE):
    if isinstance(c, int):
        if c >= len(core.plan):
            return
        cols = core.plan[c][1][half].shape[1] * core.plan[c][1][half].shape[2]
    dve.wait_ge(core.landed[half], 16 * (c + 1))
    if not isinstance(c, int) or c > 0:
        if half == 0:
            dve.wait_ge(core.used, c)
        else:
            dve.wait_ge(core.products, QUARTERS * c)
    split(nc, dve, core.raw[:, half, 0:cols], core.high[:, half, 0:cols], core.low[:, half, 0:cols]).then_inc(core.split[half], 1)


def split_first(nc, core, dve, start, first):
    for p in range(start, 2 * first + 2):
        split_piece(nc, core, dve, p // 2, p % 2)


def product(nc, out, a, b, start, stop):
    nc.tensor.matmul(out, a[0], b[0], start=start, stop=False)
    nc.tensor.matmul(out, a[0], b[1], start=False, stop=False)
    return nc.tensor.matmul(out, a[1], b[0], start=False, stop=stop)


def two_parts(buf):
    return buf[:, 0], buf[:, 1]


def halves(parts, *index):
    return [part[(slice(None),) + index] for part in parts]


def pairs(eng, first, number):
    loops = number // 2 if number >= 4 else 0
    if loops:
        with eng.Fori(0, loops) as i:
            for u in range(2):
                yield 2 * i + u, (first + u) // 2 + i, (first + u) % 2, first + u + 2 * i
    for j in range(2 * loops, number):
        c = first + j
        yield j, c // 2, c % 2, c


def project(nc, core, name, xT, runs, kt=KD, loads=(), beside=None):
    firsts = [take(core, r[0], r[1]) for r in runs]
    base = firsts[0]
    looped = runs[-1][1] >= 4 and runs[-1][1] % 2 == 0
    start = plan_splits(core, 2 * core.taken + (2 if looped else 1))
    idle = lambda turn, odd: turn - (base + (base % 2 != odd)) // 2 + 1
    bank = lambda odd, t: core.ps[:, 4 * odd + t, :]
    with stage(nc, name, "free0", "free1", "convolved", "loaded", "first_run", "var_ready", "root_ready") as (
            block, free0, free1, convolved, loaded, first_run, var_ready, root_ready):
        free = (free0, free1)

        if beside is not None:
            @block.gpsimd
            def _(pool):
                beside[0](pool, var_ready, root_ready)

        @block.sync
        def _(sp):
            for dst, src in loads:
                sp.dma_start(dst, src).then_inc(loaded, 16)
            load_ahead(core, sp, core.splits + 2)

        @block.tensor
        def _(pe):
            for (_, number, layout, _), first in zip(runs, firsts):
                for _, turn, odd, c in pairs(pe, first, number):
                    pe.wait_ge(free[odd], idle(turn, odd))
                    for half in range(2):
                        pe.wait_ge(core.split[half], c + 1)
                        p, k2, width = core.plan[first][1][half].shape
                        w = weights(core, half, p, k2, width)
                        rows = isinstance(layout, list)
                        count = len(layout) if rows else NT
                        for t in range(count):
                            for k in range(k2):
                                kk = half * k2 + k
                                x = halves(xT, kk, slice(None))
                                if rows:
                                    lo, m = layout[t]
                                    a, b, out = [v[:, k, lo:lo + m] for v in w], x, bank(odd, t)[0:m, :]
                                elif layout == "feature":
                                    a, b, out = [v[:, k, t * P:(t + 1) * P] for v in w], x, bank(odd, t)
                                else:
                                    a, b, out = [v[:, t * P:(t + 1) * P] for v in x], [v[:, k, :] for v in w], bank(odd, t)
                                mm = product(nc, out, a, b, kk == 0, kk == kt - 1)
                            if half == 1:
                                mm.then_inc(core.products, QUARTERS - t if t == count - 1 else 1)
                        if half == 0:
                            mm.then_inc(core.used, 1)

        @block.vector
        def _(dve):
            dve.sem_inc(free[0], 1)
            dve.sem_inc(free[1], 1)
            split_first(nc, core, dve, start, base)
            if loads:
                dve.wait_ge(loaded, 16 * len(loads))
            for n, ((_, number, _, how), first) in enumerate(zip(runs, firsts)):
                if beside is not None and n == 1:
                    dve.wait_ge(first_run, 1)
                    beside[1](dve, var_ready, root_ready)
                for j, _, odd, c in pairs(dve, first, number):
                    split_piece(nc, core, dve, c + 1, 0)
                    if not isinstance(c, int) or c + 1 < core.taken:
                        split_piece(nc, core, dve, c + 1, 1)
                    if how[0] == "act":
                        continue
                    for t in range(NT):
                        psum, dest = bank(odd, t), how[-1](t, j)
                        dve.wait_ge(core.products, QUARTERS * c + t + 1)
                        if how[0] == "conv":
                            done = convolve(nc, dve, psum, how[1], how[2], how[3], 4 * j + t, dest)
                            done.then_inc(convolved, 1)
                            if t == NT - 1:
                                dve.drain().then_inc(free[odd], 1)
                            continue
                        if how[0] == "axpy":
                            done = nc.vector.scalar_tensor_tensor(dest, dest, how[1], psum, ALU.mult, ALU.add)
                        elif how[0] == "mul":
                            done = nc.vector.tensor_tensor(dest, psum, how[1](t, j), ALU.mult)
                        else:
                            done = nc.vector.tensor_tensor(core.tmp[:, t, :], psum, how[1](t, j), ALU.mult)
                        if t == NT - 1:
                            done.then_inc(free[odd], 1)
                        if how[0] == "mad":
                            dve.drain()
                            nc.vector.tensor_tensor(dest, dest, core.tmp[:, t, :], ALU.add)

        @block.scalar
        def _(act):
            convs = 0
            for (_, number, layout, how), first in zip(runs, firsts):
                if how[0] not in ("act", "conv"):
                    continue
                rows = isinstance(layout, list)
                for j, _, odd, c in pairs(act, first, number):
                    count = len(layout) if rows else NT
                    for t in range(count):
                        if how[0] == "conv":
                            act.wait_ge(convolved, convs + NT * j + t + 1)
                            nc.scalar.activation(how[-1](t, j), how[-1](t, j), ACT.Silu)
                            continue
                        act.wait_ge(core.products, QUARTERS * c + (QUARTERS if t == count - 1 else t + 1))
                        psum = bank(odd, t)[0:layout[t][1], :] if rows else bank(odd, t)
                        dest = how[2](t, j)
                        if len(dest.shape) == 3:
                            psum = psum.rearrange("p (h f) -> p h f", h=dest.shape[1])
                        done = nc.scalar.activation(dest, psum, how[1])
                        if t == count - 1:
                            done.then_inc(free[odd], 1)
                if how[0] == "conv":
                    convs += NT * number
                if beside is not None and first == base:
                    act.drain().then_inc(first_run, 1)


def convolve(nc, dve, u, taps, bias, width, f, out):
    m = u.shape[0]
    tap = lambda k: taps[0:m, k, bass.ds(f, 1)]
    if bias is None:
        nc.vector.tensor_scalar(out, u, tap(width - 1), None, ALU.mult)
    else:
        nc.vector.tensor_scalar(out, u, tap(width - 1), bias[0:m, bass.ds(f, 1)], ALU.mult, ALU.add)
    for back in range(1, width):
        dve.drain()
        done = nc.vector.scalar_tensor_tensor(out[:, back:], u[:, 0:SEQ - back], tap(width - 1 - back), out[:, back:], ALU.mult, ALU.add)
    return done


def columns(buf):
    return lambda t, j: buf[:, t, bass.ds(j * BANK, BANK)]


def feature_tiles(buf):
    return lambda t, j: buf[:, bass.ds(j * 4 + t, 1), :].rearrange("p o n -> p (o n)")


def row_buffers(*bufs):
    return lambda t, j: bufs[t][:]


def transpose_tile(nc, core, t, nf, src, transposed):
    groups = nf // 4
    for half in range(groups):
        bank = (groups * t + half) % 8
        for q in range(4):
            f = 4 * half + q
            mm = nc.tensor.transpose(core.ps[:, bank, q * P:(q + 1) * P], src[:, t, f * P:(f + 1) * P], core.ident[:])
        mm.then_inc(transposed, 1)


def transposed_bank(nf, n):
    t, half = divmod(n, nf // 4)
    return (slice(None), slice(4 * half, 4 * half + 4), slice(t * P, (t + 1) * P))


def transposed_view(core, n):
    return core.ps[:, n % 8, :].rearrange("p (f t) -> p f t", f=4)


def copy_transposed(nc, core, act, nf, dst, transposed, copied=None):
    for n in range(NT * nf // 4):
        act.wait_ge(transposed, n + 1)
        done = nc.scalar.copy(dst[transposed_bank(nf, n)], transposed_view(core, n))
        if copied is not None:
            done.then_inc(copied, 1)


def rest_of_transposed(nc, core, dve, nf, parts, copied):
    for n in range(NT * nf // 4):
        at = transposed_bank(nf, n)
        dve.wait_ge(copied, n + 1)
        nc.vector.tensor_tensor(parts[1][at], transposed_view(core, n), parts[0][at].bitcast(F32), ALU.subtract)


def transpose(nc, core, name, src, dst, nf=KD):
    with stage(nc, name, "transposed", "copied") as (block, transposed, copied):
        @block.tensor
        def _(pe):
            for t in range(NT):
                transpose_tile(nc, core, t, nf, src, transposed)

        @block.scalar
        def _(act):
            copy_transposed(nc, core, act, nf, dst[0], transposed, copied)

        @block.vector
        def _(dve):
            rest_of_transposed(nc, core, dve, nf, dst, copied)


def row_stats(nc, core, dve, src, mv, width, groups):
    parts = max(1, width // BANK)
    w = width // parts
    for g in range(groups):
        for q in range(parts):
            nc.vector.bn_stats(core.bn[:, g * parts + q, :], src(g)[:, q * w:(q + 1) * w])
    dve.drain()
    for g in range(groups):
        nc.vector.bn_aggr(mv[:, g, :], core.bn[:, g * parts:(g + 1) * parts, :].rearrange("p q s -> p (q s)"))
    dve.drain()


def mean_square(nc, dve, mv):
    nc.vector.tensor_tensor(mv[:, :, 0:1], mv[:, :, 0:1], mv[:, :, 0:1], ALU.mult)
    dve.drain()
    nc.vector.tensor_tensor(mv[:, :, 1:2], mv[:, :, 1:2], mv[:, :, 0:1], ALU.add)
    dve.drain()


def inverse_root(nc, core, pool, v, eps, ready, done):
    pool.wait_ge(ready, 1)
    nc.gpsimd.tensor_scalar(v, v, eps, None, ALU.add).then_inc(done, 1)
    pool.wait_ge(done, 1)
    nc.gpsimd.tensor_tensor(v, v, core.minus_half[:, 0:v.shape[1], :], ALU.pow).then_inc(done, 1)


def norm(nc, core, name, src, dst, dstT, eps, rms, gain, shift, rows=()):
    with stage(nc, name, "rows_loaded", "var_ready", "root_ready", "scaled_ready", "centred", "gained", "normed", "transposed", "copied") as (
            block, rows_loaded, var_ready, root_ready, scaled_ready, centred, gained, normed, transposed, copied):
        mv = core.mv[:, 0:NT, :]
        last_done = normed if shift is None else gained

        @block.gpsimd
        def _(pool):
            inverse_root(nc, core, pool, mv[:, :, 1:2], eps, var_ready, root_ready)
            if shift is not None:
                for t in range(NT):
                    pool.wait_ge(gained, t + 1)
                    nc.gpsimd.tensor_tensor(dst[:, t, :], dst[:, t, :], shift, ALU.add).then_inc(normed, 1)

        if rows:
            @block.sync
            def _(sp):
                for buf, vec in rows:
                    sp.dma_start(buf, vec.partition_broadcast(P)).then_inc(rows_loaded, 16)

        @block.vector
        def _(dve):
            row_stats(nc, core, dve, lambda t: src[:, t, :], mv, D, NT)
            if rms:
                mean_square(nc, dve, mv)
            dve.drain().then_inc(var_ready, 1)
            dve.wait_ge(root_ready, 2)
            if not rms:
                nc.vector.scalar_tensor_tensor(mv[:, :, 0], mv[:, :, 0], -1.0, mv[:, :, 1], ALU.mult, ALU.mult)
            dve.drain().then_inc(scaled_ready, 1)
            if rows:
                dve.wait_ge(rows_loaded, 16 * len(rows))
            for t in range(NT):
                dve.wait_ge(centred, t + 1)
                nc.vector.tensor_tensor(dst[:, t, :], dst[:, t, :], gain, ALU.mult).then_inc(last_done, 1)
            if dstT is not None:
                rest_of_transposed(nc, core, dve, KD, dstT, copied)

        @block.scalar
        def _(act):
            act.wait_ge(scaled_ready, 1)
            for t in range(NT):
                if rms:
                    nc.scalar.activation(dst[:, t, :], src[:, t, :], ACT.Copy, scale=mv[:, t, 1:2]).then_inc(centred, 1)
                else:
                    nc.scalar.activation(dst[:, t, :], src[:, t, :], ACT.Identity, bias=mv[:, t, 0:1], scale=mv[:, t, 1:2]).then_inc(centred, 1)
            if dstT is not None:
                copy_transposed(nc, core, act, KD, dstT[0], transposed, copied)

        if dstT is not None:
            @block.tensor
            def _(pe):
                for t in range(NT):
                    pe.wait_ge(normed, t + 1)
                    transpose_tile(nc, core, t, KD, dst, transposed)


RET_HEADS, RET_DV = 4, 256
RET_QK_DIM = 128
SGU_GROUPS, SGU_DIM = 4, 256


def adaptive_rows(nc, core, d, mod, norm1_gain, norm2_gain):
    chunks = 6 * D // BANK
    first = take(core, "ada", chunks)
    plan_splits(core, 2 * core.taken)
    with buffers(nc, c_col=[P, KD], c_silu=[P, KD], c_rep=[P, KD, P]) as (c_col, c_silu, c_rep), \
            stage(nc, "ada", "loaded", "silu_done", "c_ready", "evacuated") as (
                block, loaded, silu_done, c_ready, evacuated):
        @block.sync
        def _(sp):
            sp.dma_start(core.x[:], d["x"].rearrange("b (t p) f -> p (b t) f", p=P)).then_inc(loaded, 16)
            sp.dma_start(c_col[:], d["c_col"]).then_inc(loaded, 16)
            sp.dma_start(mod[:].rearrange("p a f -> p (a f)"), d["b_ada"][0, :].partition_broadcast(P)).then_inc(loaded, 16)
            sp.dma_start(norm1_gain, d["norm1_g"][0, :].partition_broadcast(P)).then_inc(loaded, 16)
            sp.dma_start(norm2_gain, d["norm2_g"][0, :].partition_broadcast(P)).then_inc(loaded, 16)
            load_ahead(core, sp, core.splits + 2)

        @block.scalar
        def _(act):
            act.wait_ge(loaded, 80)
            nc.scalar.activation(c_silu[:], c_col[:], ACT.Silu).then_inc(silu_done, 1)

        @block.tensor
        def _(pe):
            pe.wait_ge(c_ready, 1)
            for _, _, odd, c in pairs(pe, first, chunks):
                pe.wait_ge(evacuated, c - first + 1)
                for half in range(2):
                    pe.wait_ge(core.landed[half], 16 * (c + 1))
                    w = piece(core.raw, half, P, KD // 2, BANK)
                    for k in range(KD // 2):
                        kk = half * KD // 2 + k
                        mm = nc.tensor.matmul(core.ps[:, odd, :], c_rep[:, kk, :], w[:, k, :], start=kk == 0, stop=kk == KD - 1)
                    if half == 0:
                        mm.then_inc(core.used, 1)
                    else:
                        mm.then_inc(core.products, QUARTERS)
                    pe.drain().then_inc(core.split[half], 1)

        @block.vector
        def _(dve):
            dve.sem_inc(evacuated, 2)
            dve.wait_ge(silu_done, 1)
            nc.vector.tensor_copy(c_rep[:], c_silu[:].unsqueeze(2).to_broadcast([P, KD, P])).then_inc(c_ready, 1)
            dve.wait_ge(loaded, 80)
            rows = mod[:].rearrange("p a f -> p (a f)")
            for j, _, odd, c in pairs(dve, first, chunks):
                dve.wait_ge(core.products, QUARTERS * (c + 1))
                part = rows[:, bass.ds(j * BANK, BANK)]
                nc.vector.tensor_tensor(part, part, core.ps[:, odd, :], ALU.add).then_inc(evacuated, 1)
            dve.drain()
            for which, gain in ((1, norm1_gain), (4, norm2_gain)):
                nc.vector.scalar_tensor_tensor(mod[:, which, :], mod[:, which, :], 1.0, gain, ALU.add, ALU.mult)


def retention(nc, core, d, qk, v, rot, qkT, y):
    H = RET_HEADS
    ra, rb, weights = core.row_b[:, 0:512], core.row_b[:, 512:1024], core.tmp
    decay = rot[:, :, 0:SEQ]
    with buffers(nc, cosine=[P, NT, 64], sine=[P, NT, 64]) as (cosine, sine):
        with stage(nc, "rotary", "tables", "rotated", "transposed") as (block, tables, rotated, transposed):
            @block.sync
            def _(sp):
                sp.dma_start(cosine[:], d["const_cos"]).then_inc(tables, 16)
                sp.dma_start(sine[:], d["const_sin"]).then_inc(tables, 16)
                sp.dma_start(core.row_a[:], d["ret_gn_g"][0, :].partition_broadcast(P)).then_inc(tables, 16)

            @block.vector
            def _(dve):
                dve.wait_ge(tables, 48)
                for t in range(NT):
                    heads = qk[:, t, :].rearrange("p (h a f) -> p h a f", a=2, f=64)
                    out = rot[:, t, :].rearrange("p (h a f) -> p h a f", a=2, f=64)
                    cos = cosine[:, t, :].unsqueeze(1).to_broadcast([P, 2 * H, 64])
                    sin = sine[:, t, :].unsqueeze(1).to_broadcast([P, 2 * H, 64])
                    a = ra.rearrange("p (h f) -> p h f", f=64)
                    b = rb.rearrange("p (h f) -> p h f", f=64)
                    nc.vector.tensor_tensor(out[:, :, 0, :], heads[:, :, 0, :], cos, ALU.mult)
                    nc.vector.tensor_tensor(out[:, :, 1, :], heads[:, :, 0, :], sin, ALU.mult)
                    nc.vector.tensor_tensor(a, heads[:, :, 1, :], sin, ALU.mult)
                    nc.vector.tensor_tensor(b, heads[:, :, 1, :], cos, ALU.mult)
                    dve.drain()
                    nc.vector.tensor_tensor(out[:, :, 0, :], out[:, :, 0, :], a, ALU.subtract)
                    nc.vector.tensor_tensor(out[:, :, 1, :], out[:, :, 1, :], b, ALU.add).then_inc(rotated, 1)
                    dve.drain()

            @block.tensor
            def _(pe):
                for t in range(NT):
                    pe.wait_ge(rotated, t + 1)
                    transpose_tile(nc, core, t, KD, rot, transposed)

            @block.scalar
            def _(act):
                copy_transposed(nc, core, act, KD, qkT, transposed)

        with stage(nc, "retain", "scores", "weighted", "summed", "copied", "decay_loaded") as (
                block, scores, weighted, summed, copied, decay_loaded):
            @block.sync
            def _(sp):
                sp.dma_start(decay, d["const_ret_decay"]).then_inc(decay_loaded, 16)

            @block.tensor
            def _(pe):
                for h in range(H):
                    if h >= 1:
                        pe.wait_ge(weighted, NT * h)
                    for s in range(NT):
                        nc.tensor.matmul(core.ps[:, s, 0:SEQ - s * P], qkT[:, H + h, s * P:(s + 1) * P],
                                         qkT[:, h, s * P:], start=True, stop=True).then_inc(scores, 1)
                    pe.wait_ge(weighted, NT * (h + 1))
                    if h >= 2:
                        pe.wait_ge(copied, h - 1)
                    for t in range(NT):
                        out = core.ps[:, 4 + 2 * (h % 2) + t // 2, (t % 2) * RET_DV:(t % 2 + 1) * RET_DV]
                        for s in range(t + 1):
                            mm = nc.tensor.matmul(out, weights[:, s, (t - s) * P:(t - s + 1) * P],
                                                  v[:, s, h * RET_DV:(h + 1) * RET_DV],
                                                  start=s == 0, stop=s == t)
                    mm.then_inc(summed, 1)

            @block.vector
            def _(dve):
                dve.wait_ge(decay_loaded, 16)
                for h in range(H):
                    if h >= 1:
                        dve.wait_ge(summed, h)
                    for s in range(NT):
                        n = SEQ - s * P
                        dve.wait_ge(scores, NT * h + s + 1)
                        nc.vector.scalar_tensor_tensor(weights[:, s, 0:n], core.ps[:, s, 0:n], RET_QK_DIM ** -0.5,
                                                       decay[:, h, 0:n], ALU.mult, ALU.mult).then_inc(weighted, 1)

            @block.scalar
            def _(act):
                for h in range(H):
                    act.wait_ge(summed, h + 1)
                    for q in range(2):
                        done = nc.scalar.copy(y[:, 2 * q:2 * q + 2, h * RET_DV:(h + 1) * RET_DV],
                                              core.ps[:, 4 + 2 * (h % 2) + q, :].rearrange("p (t f) -> p t f", t=2))
                    done.then_inc(copied, 1)

        with stage(nc, "head_norm", "var_ready", "root_ready") as (block, var_ready, root_ready):
            n = NT * H
            mv = core.mv[:, 0:n, :]

            @block.gpsimd
            def _(pool):
                inverse_root(nc, core, pool, mv[:, :, 1:2], 1e-6, var_ready, root_ready)

            @block.vector
            def _(dve):
                part = lambda g: y[:, g // H, (g % H) * RET_DV:(g % H + 1) * RET_DV]
                row_stats(nc, core, dve, part, mv, RET_DV, n)
                dve.drain().then_inc(var_ready, 1)
                dve.wait_ge(root_ready, 2)
                for g in range(n):
                    nc.vector.tensor_scalar(part(g), part(g), mv[:, g, 0:1], mv[:, g, 1:2], ALU.subtract, ALU.mult)
                dve.drain()
                for t in range(NT):
                    nc.vector.tensor_tensor(y[:, t, :], y[:, t, :], core.row_a[:], ALU.mult)


def spatial(nc, core, d, u, gates):
    with buffers(nc, mixer=[P, SGU_GROUPS, P], mixer_b=[P, SGU_GROUPS]) as (mixer, mixer_b), \
            stage(nc, "spatial", "loaded", "masked", "var_ready", "root_ready", "normed", "mixed") as (
                block, loaded, masked, var_ready, root_ready, normed, mixed):
        mv = core.mv[:, 0:NT, :]

        @block.sync
        def _(sp):
            sp.dma_start(core.row_a[:], d["sgu_ln_g"][0, :].partition_broadcast(P)).then_inc(loaded, 16)
            sp.dma_start(core.row_b[:], d["sgu_ln_b"][0, :].partition_broadcast(P)).then_inc(loaded, 16)
            sp.dma_start(mixer[:], d["sgu_w_t"]).then_inc(loaded, 16)
            sp.dma_start(mixer_b[:], d["sgu_b_t"]).then_inc(loaded, 16)

        @block.gpsimd
        def _(pool):
            pool.wait_ge(loaded, 64)
            nc.gpsimd.affine_select(out=mixer[:], in_=mixer[:], compare_op=ALU.is_ge, fill=0.0, base=0,
                                    pattern=[[0, SGU_GROUPS], [1, P]], channel_multiplier=-1).then_inc(masked, 1)
            inverse_root(nc, core, pool, mv[:, :, 1:2], 1e-6, var_ready, root_ready)

        @block.vector
        def _(dve):
            sv = lambda t: gates[:, t, :]
            row_stats(nc, core, dve, sv, mv, D, NT)
            dve.drain().then_inc(var_ready, 1)
            dve.wait_ge(root_ready, 2)
            dve.wait_ge(loaded, 64)
            for t in range(NT):
                nc.vector.tensor_scalar(sv(t), sv(t), mv[:, t, 0:1], mv[:, t, 1:2], ALU.subtract, ALU.mult)
                dve.drain()
                nc.vector.tensor_tensor(sv(t), sv(t), core.row_a[:], ALU.mult)
                dve.drain()
                nc.vector.tensor_tensor(sv(t), sv(t), core.row_b[:], ALU.add).then_inc(normed, 1)
            for t in range(NT):
                dve.wait_ge(mixed, t + 1)
                for g in range(SGU_GROUPS):
                    nc.vector.scalar_tensor_tensor(
                        u[:, t, g * SGU_DIM:(g + 1) * SGU_DIM],
                        core.ps[:, 2 * t + g // 2, (g % 2) * SGU_DIM:(g % 2 + 1) * SGU_DIM], mixer_b[:, g:g + 1],
                        u[:, t, g * SGU_DIM:(g + 1) * SGU_DIM], ALU.add, ALU.mult)

        @block.tensor
        def _(pe):
            pe.wait_ge(masked, 1)
            for t in range(NT):
                pe.wait_ge(normed, t + 1)
                for g in range(SGU_GROUPS):
                    mm = nc.tensor.matmul(core.ps[:, 2 * t + g // 2, (g % 2) * SGU_DIM:(g % 2 + 1) * SGU_DIM],
                                          mixer[:, g, :], gates[:, t, g * SGU_DIM:(g + 1) * SGU_DIM],
                                          start=True, stop=True)
                mm.then_inc(mixed, 1)


def gated_sum(nc, name, dst, gate, other, other_gate):
    with stage(nc, name, "scaled") as (block, scaled):
        @block.gpsimd
        def _(pool):
            for t in range(NT):
                nc.gpsimd.tensor_tensor(other[:, t, :], other[:, t, :], other_gate[:, t, :], ALU.mult).then_inc(scaled, 1)

        @block.vector
        def _(dve):
            for t in range(NT):
                nc.vector.tensor_tensor(dst[:, t, :], dst[:, t, :], gate[:, t, :], ALU.mult)
            dve.drain()
            for t in range(NT):
                dve.wait_ge(scaled, t + 1)
                nc.vector.tensor_tensor(dst[:, t, :], dst[:, t, :], other[:, t, :], ALU.add)


def multiply(nc, name, dst, other):
    with stage(nc, name) as (block,):
        @block.vector
        def _(dve):
            for t in range(NT):
                nc.vector.tensor_tensor(dst[:, t, :], dst[:, t, :], other[:, t, :], ALU.mult)


def first_mixer(nc, core, d, mod):
    norm(nc, core, "norm1", core.x, core.h, core.hT, 1e-6, True, mod[:, 1, :], mod[:, 0, :])
    with buffers(nc, a=[P, NT, D], b=[P, NT, D], c=[P, NT, D]) as (a, b, c):
        features = lambda buf: buf[:].rearrange("p t (q n) -> p (t q) n", n=SEQ)
        yT = over(nc, core.h, "yT_high", [P, KD, SEQ], F32R), over(nc, b, "yT_low", [P, KD, SEQ], F32R)
        project(nc, core, "in_qkv", core.hT, [("qk", 2, "token", ("act", ACT.Copy, columns(a))),
                                              ("v", 2, "token", ("act", ACT.Copy, columns(b)))])
        retention(nc, core, d, a, b, core.h, features(c), a)
        project(nc, core, "in_g", core.hT, [("g_ret", 2, "token", ("act", ACT.Silu, columns(c)))])
        multiply(nc, "ret_gate", a, c)
        transpose(nc, core, "ret_T", a, yT)
        project(nc, core, "ret_out", yT, [("ret_out", 2, "token", ("act", ACT.Copy, columns(c)))])
        project(nc, core, "in_usv", core.hT, [("u", 2, "token", ("act", ACT.Gelu, columns(a))),
                                              ("sv", 2, "token", ("act", ACT.Gelu, columns(b)))])
        spatial(nc, core, d, a, b)
        transpose(nc, core, "sgu_T", a, yT)
        project(nc, core, "sgu_out", yT, [("sgu_out", 2, "token", ("act", ACT.Copy, columns(a)))])
        project(nc, core, "in_gates", core.hT, [("gate_a", 2, "token", ("act", ACT.Sigmoid, columns(b))),
                                                ("gate_b", 2, "token", ("act", ACT.Sigmoid, columns(core.h)))])
        gated_sum(nc, "merge", c, b, a, core.h)
        transpose(nc, core, "merge_T", c, yT)
        project(nc, core, "out1", yT, [("out1", 2, "token",
                                        ("mad", lambda t, j: mod[:, 2, bass.ds(j * BANK, BANK)], columns(core.x)))])


PEER_HEADS, PEER_KEYS, TOPK = 8, 128, 16
PICKS = PEER_HEADS * TOPK
PAIRS = 2 * PEER_HEADS
LOWEST = -3.0e38


def top8_first(nc, dve, n, values, spare, top, index):
    for g in range(n):
        nc.vector.max(top[:, g, 0:8], values(g))
    dve.drain()
    for g in range(n):
        nc.vector.max_index(index[:, g, 0:8], top[:, g, 0:8], values(g))
        nc.vector.match_replace(spare(g), top[:, g, 0:8], values(g), LOWEST)
    dve.drain()


def top8_second(nc, dve, n, spare, top, index):
    for g in range(n):
        nc.vector.max(top[:, g, 8:16], spare(g))
    dve.drain()
    for g in range(n):
        nc.vector.max_index(index[:, g, 8:16], top[:, g, 8:16], spare(g))
    dve.drain()


FETCH = 4
GROUPS_OF_PICKS = PICKS // FETCH
ROUTE_PARTS = 8


def peer(nc, core, d, qT, mod):
    H, K, G = PEER_HEADS, TOPK, GROUPS_OF_PICKS
    rows_u, rows_v = d["peer_u"][0], d["peer_v"][0]
    gate2, product_tmp, got_u = mod[:, 5, :], mod[:, 4, :], mod[:, 0:FETCH, :]
    with buffers(nc, expert=([P, NT, PICKS], U32), sub_s=[P, PAIRS, K], sub_i=([P, PAIRS, K], U32), sub_f=[P, PAIRS, K],
                 top_i=([P, H, K], U32), digit=([P, PICKS], U32), digit_f=[P, PICKS], key_f=[P, 2, PICKS], steps=[P, K],
                 total=[P, H], top_s=[P, NT, H, K], dots=[P, 2, FETCH], score=[P, NT, PICKS], diagonal=[P, FETCH, P], zero=[P, P],
                 which_u=([P, 2, FETCH], U32), which_v=([P, 2, FETCH], U32)) as (
            expert, sub_s, sub_i, sub_f, top_i, digit, digit_f, key_f, steps, total, top_s, dots, score, diagonal, zero,
            which_u, which_v), \
            stage(nc, "peer", "keys_loaded", "steps_ready", "key_scored", "copied", "read", "shifted", "raised", "routed",
                  "staged_u", "staged_v", "used_u", "used_v", "scored", "activated", "weighted", "diagonals", "summed", "added",
                  "cleared", "asked", *[f"u_in{b}" for b in range(FETCH)], *[f"v_in{b}" for b in range(FETCH)]) as (
                block, keys_loaded, steps_ready, key_scored, copied, read, shifted, raised, routed, staged_u, staged_v,
                used_u, used_v, scored, activated, weighted, diagonals, summed, added, cleared, asked, *landed):
        u_in, v_in = landed[:FETCH], landed[FETCH:]
        room = over(nc, core.hT_whole, "route_room", [P, 4, PAIRS, PEER_KEYS])
        half_scores, half_rest, keysT = room[:, 0:2], room[:, 2], room[:, 3]
        got_v = over(nc, core.row_a, "got_v", [P, FETCH, D])
        cand = half_rest.rearrange("p g n -> p (g n)").rearrange("p (h i j) -> p h i j", h=H, i=K)

        @block.sync
        def _(sp):
            sp.dma_start(keysT, d["sub_keys_t"]).then_inc(keys_loaded, 16)

        @block.gpsimd
        def _(pool):
            nc.gpsimd.iota(steps[:], pattern=[[1, K]], base=0, channel_multiplier=0,
                           allow_small_or_imprecise_dtypes=True).then_inc(steps_ready, 1)
            nc.gpsimd.memset(zero[:], 0.0).then_inc(cleared, 1)

            def gather(t, i, half, rows, got, which, staged, used, arrived):
                group = t * G + 2 * i + half
                nc.gpsimd.tensor_copy(which[:, half, :], expert[:, t, bass.ds((2 * i + half) * FETCH, FETCH)]).then_inc(staged, 1)
                pool.wait_ge(staged, group + 1)
                for b in range(FETCH):
                    pool.wait_ge(used, group * FETCH + b + 1)
                    pool.sem_inc(asked, 1)
                    nc.gpsimd.indirect_dma_start(
                        out=got[:, b, :], out_offset=None, in_=rows,
                        in_offset=bass.IndirectOffsetOnAxis(ap=which[:, half, b:b + 1], axis=0),
                    ).then_inc(arrived[b], 16)

            for t in range(NT + 1):
                if t < NT:
                    pool.wait_ge(routed, t + 1)
                with pool.Fori(0, G // 2) as i:
                    for half in range(2):
                        if t < NT:
                            gather(t, i, half, rows_u, got_u, which_u, staged_u, used_u, u_in)
                        if t >= 1:
                            gather(t - 1, i, half, rows_v, got_v, which_v, staged_v, used_v, v_in)

        @block.vector
        def _(dve):
            rest_of = lambda t: half_scores[:, t % 2].rearrange("p g n -> p (g n)").rearrange("p (h n) -> p h n", h=H)
            sums = half_rest.rearrange("p g n -> p (g n)").rearrange("p (h n) -> p h n", h=H)
            ids = sub_f[:].rearrange("p (h a) k -> p h a k", a=2)

            def key_digit(a, op, by):
                nc.vector.tensor_single_scalar(digit[:], top_i[:].rearrange("p h k -> p (h k)"), by, op)
                dve.drain()
                nc.vector.tensor_copy(digit_f[:], digit[:])
                dve.drain()
                hit = cand.rearrange("p h i j -> p (h i) j")
                nc.vector.tensor_tensor(hit, steps[:].unsqueeze(1).to_broadcast([P, PICKS, K]),
                                        digit_f[:].unsqueeze(2).to_broadcast([P, PICKS, K]), ALU.is_equal)
                dve.drain()
                nc.vector.tensor_tensor(cand, cand, ids[:, :, a, :].unsqueeze(2).to_broadcast([P, H, K, K]), ALU.mult)
                dve.drain()
                nc.vector.tensor_reduce(key_f[:, a, :], hit, AX.X, ALU.add)
                dve.drain()

            def route(t, part):
                if part == 0:
                    dve.wait_ge(copied, 4 * (t + 1))
                    top8_first(nc, dve, PAIRS, lambda g: half_scores[:, t % 2, g, :], lambda g: half_rest[:, g, :], sub_s, sub_i)
                elif part == 1:
                    top8_second(nc, dve, PAIRS, lambda g: half_rest[:, g, :], sub_s, sub_i)
                elif part == 2:
                    nc.vector.tensor_copy(sub_f[:], sub_i[:])
                    half = sub_s[:].rearrange("p (h a) k -> p h a k", a=2)
                    nc.vector.tensor_tensor(cand, half[:, :, 0, :].unsqueeze(3).to_broadcast([P, H, K, K]),
                                            half[:, :, 1, :].unsqueeze(2).to_broadcast([P, H, K, K]), ALU.add)
                    dve.drain()
                elif part == 3:
                    top8_first(nc, dve, H, lambda g: sums[:, g, :], lambda g: rest_of(t)[:, g, :], top_s[:, t], top_i)
                elif part == 4:
                    top8_second(nc, dve, H, lambda g: rest_of(t)[:, g, :], top_s[:, t], top_i)
                    dve.drain().then_inc(read, 1)
                    nc.vector.tensor_tensor(top_s[:, t, :, 1:K], top_s[:, t, :, 1:K],
                                            top_s[:, t, :, 0:1].to_broadcast([P, H, K - 1]), ALU.subtract)
                    dve.drain()
                    nc.vector.memset(top_s[:, t, :, 0:1], 0.0).then_inc(shifted, 1)
                elif part == 5:
                    key_digit(0, ALU.logical_shift_right, 4)
                elif part == 6:
                    key_digit(1, ALU.bitwise_and, K - 1)
                else:
                    nc.vector.scalar_tensor_tensor(expert[:, t, :], key_f[:, 0, :], float(PEER_KEYS), key_f[:, 1, :],
                                                   ALU.mult, ALU.add).then_inc(routed, 1)

            def weigh(t):
                dve.wait_ge(raised, t + 1)
                nc.vector.tensor_reduce(total[:], top_s[:, t], AX.X, ALU.add)
                dve.drain()
                nc.vector.reciprocal(total[:], total[:])
                dve.drain()
                nc.vector.tensor_tensor(top_s[:, t], top_s[:, t], total[:].unsqueeze(2).to_broadcast([P, H, K]), ALU.mult)
                dve.drain()
                dve.wait_ge(activated, t + 1)
                nc.vector.tensor_tensor(score[:, t, :], score[:, t, :], top_s[:, t].rearrange("p h k -> p (h k)"), ALU.mult).then_inc(weighted, 1)

            def add_experts(t):
                dve.wait_ge(summed, t + 1)
                for q in range(2):
                    nc.vector.tensor_tensor(product_tmp[:, q * BANK:(q + 1) * BANK], core.ps[:, 2 * (t % 2) + q, :],
                                            gate2[:, q * BANK:(q + 1) * BANK], ALU.mult)
                dve.drain().then_inc(added, 1)
                nc.vector.tensor_tensor(core.x[:, t, :], core.x[:, t, :], product_tmp, ALU.add)
                dve.drain()

            dve.sem_inc(used_u, FETCH)
            dve.wait_ge(steps_ready, 1)
            for part in range(ROUTE_PARTS):
                route(0, part)
            for t in range(NT):
                for part in range(ROUTE_PARTS):
                    with dve.Fori(0, G // ROUTE_PARTS // 2) as i:
                        for half in range(2):
                            group = part * (G // ROUTE_PARTS) + 2 * i + half
                            for b in range(FETCH):
                                dve.wait_ge(u_in[b], 16 * (t * G + group + 1))
                                nc.vector.tensor_tensor_reduce(
                                    out=got_u[:, b, :], in0=got_u[:, b, :], in1=core.h[:, t, :], scale=1.0, scalar=0.0,
                                    op0=ALU.mult, op1=ALU.add, accum_out=dots[:, half, b:b + 1]).then_inc(used_u, 1)
                            dve.drain()
                            nc.vector.tensor_copy(score[:, t, bass.ds(group * FETCH, FETCH)], dots[:, half, :])
                    if t + 1 < NT:
                        route(t + 1, part)
                dve.drain().then_inc(scored, 1)
                weigh(t)
                if t >= 1:
                    add_experts(t - 1)
            add_experts(NT - 1)

        @block.scalar
        def _(act):
            def copy_scores(t):
                if t >= 2:
                    act.wait_ge(read, t - 1)
                for q in range(4):
                    act.wait_ge(key_scored, 4 * t + q + 1)
                    nc.scalar.copy(half_scores[:, t % 2, 4 * q:4 * q + 4, :],
                                   core.ps[:, 4 + q, :].rearrange("p (g n) -> p g n", g=4)).then_inc(copied, 1)

            def raise_scores(t):
                act.wait_ge(shifted, t + 1)
                nc.scalar.activation(top_s[:, t], top_s[:, t], ACT.Exp).then_inc(raised, 1)

            copy_scores(0)
            copy_scores(1)
            raise_scores(0)
            for t in range(NT):
                if t + 1 < NT:
                    raise_scores(t + 1)
                if t + 2 < NT:
                    copy_scores(t + 2)
                act.wait_ge(scored, t + 1)
                nc.scalar.activation(score[:, t, :], score[:, t, :], ACT.Gelu).then_inc(activated, 1)
                act.wait_ge(weighted, t + 1)
                with act.Fori(0, G) as i:
                    for b in range(FETCH):
                        act.wait_ge(used_v, (t * G + i) * FETCH + b + 1)
                        nc.scalar.activation(diagonal[:, b, :], core.ident[:], ACT.Copy,
                                             scale=score[:, t, bass.ds(i * FETCH + b, 1)]).then_inc(diagonals, 1)

        @block.tensor
        def _(pe):
            def score_keys(t):
                if t >= 1:
                    pe.wait_ge(copied, 4 * t)
                for g in range(PAIRS):
                    mm = nc.tensor.matmul(core.ps[:, 4 + g // 4, (g % 4) * P:(g % 4 + 1) * P],
                                          qT[:, g, t * P:(t + 1) * P], keysT[:, g, :], start=True, stop=True)
                    if g % 4 == 3:
                        mm.then_inc(key_scored, 1)

            pe.sem_inc(used_v, FETCH)
            pe.wait_ge(keys_loaded, 16)
            score_keys(0)
            score_keys(1)
            pe.wait_ge(cleared, 1)
            for t in range(NT):
                if t + 2 < NT:
                    score_keys(t + 2)
                if t >= 2:
                    pe.wait_ge(added, t - 1)
                banks = [core.ps[:, 2 * (t % 2) + q, :] for q in range(2)]
                for q in range(2):
                    nc.tensor.matmul(banks[q], zero[:], core.h[:, 0, 0:BANK], start=True, stop=False, skip_group_check=True)
                with pe.Fori(0, G) as i:
                    for b in range(FETCH):
                        group = t * G + i
                        pe.wait_ge(diagonals, group * FETCH + b + 1)
                        pe.wait_ge(v_in[b], 16 * (group + 1))
                        for q in range(2):
                            mm = nc.tensor.matmul(banks[q], diagonal[:, b, :], got_v[:, b, q * BANK:(q + 1) * BANK],
                                                  start=False, stop=False, skip_group_check=True)
                        mm.then_inc(used_v, 1)
                pe.drain().then_inc(summed, 1)


def block_one(nc, core, d):
    with buffers(nc, mod=[P, 6, D]) as (mod,):
        adaptive_rows(nc, core, d, mod, core.row_a[:], core.row_b[:])
        first_mixer(nc, core, d, mod)
        norm(nc, core, "norm2", core.x, core.h, core.hT, 1e-6, True, mod[:, 4, :], mod[:, 3, :])
        with buffers(nc, qT=[P, PAIRS, SEQ]) as (qT,):
            project(nc, core, "peer_q", core.hT, [("peer_q", 4, "feature", ("act", ACT.Copy, feature_tiles(qT)))])
            peer(nc, core, d, qT, mod)
    norm(nc, core, "final1", core.x, core.x, None, 1e-6, True, core.row_a[:], None, [(core.row_a[:], d["final_g"])])


def plan_one(d):
    w_in = d["w_in"][0]
    plan = []
    add = lambda name, w, lo, n: plan.extend((name, kmajor(w, lo + i * BANK, BANK)) for i in range(n))
    add("ada", d["w_ada"][0], 0, 12)
    add("qk", w_in, 0, 2)
    add("v", w_in, 1024, 2)
    add("g_ret", w_in, 2048, 2)
    add("ret_out", d["w_ret_out"][0], 0, 2)
    add("u", w_in, 3072, 2)
    add("sv", w_in, 4096, 2)
    add("sgu_out", d["w_sgu_out"][0], 0, 2)
    add("gate_a", w_in, 5120, 2)
    add("gate_b", w_in, 6144, 2)
    add("out1", d["w_out"][0], 0, 2)
    add("peer_q", d["peer_w_q"][0], 0, 4)
    return plan


STRIP = [0, 512, 896, 1152]
PACKED = 1280


def strip(buf, s, lo=0, hi=None):
    return buf[:, STRIP[s] + lo:STRIP[s] + (SEQ - s * P if hi is None else hi)]


def soft_maximum(nc, name, parts):
    with stage(nc, name, "shifted", "logged") as (block, shifted, logged):
        @block.vector
        def _(dve):
            for x, _, sign, bias, _, _ in parts:
                nc.vector.tensor_scalar(x, x, sign, bias, ALU.mult, ALU.add).then_inc(shifted, 1)
            for n, (x, tmp, _, _, a, _) in enumerate(parts):
                dve.wait_ge(logged, n + 1)
                nc.vector.scalar_tensor_tensor(x, x, a, tmp, ALU.max, ALU.add)

        @block.scalar
        def _(act):
            for n, (x, tmp, _, _, _, minus_a) in enumerate(parts):
                act.wait_ge(shifted, n + 1)
                nc.scalar.activation(tmp, x, ACT.Abs, bias=minus_a)
            act.drain()
            for x, tmp, *_ in parts:
                nc.scalar.activation(tmp, tmp, ACT.Exp, scale=-1.0)
            act.drain()
            for x, tmp, *_ in parts:
                nc.scalar.activation(tmp, tmp, ACT.Ln, bias=1.0).then_inc(logged, 1)


def load_rows(nc, name, loads, zeroed=()):
    with stage(nc, name, "loaded") as (block, loaded):
        @block.sync
        def _(sp):
            for dst, src in loads:
                sp.dma_start(dst, src).then_inc(loaded, 16)
            sp.wait_ge(loaded, 16 * len(loads))

        if zeroed:
            @block.gpsimd
            def _(pool):
                for z in zeroed:
                    nc.gpsimd.memset(z, 0.0)


def row_columns(nc, core, name, rows, cols, h):
    with stage(nc, name, "turned") as (block, turned):
        @block.tensor
        def _(pe):
            for n, row in enumerate(rows):
                for t in range(NT):
                    mm = nc.tensor.transpose(core.ps[:, n, t * h:(t + 1) * h], row[:, t * P:(t + 1) * P], core.ident[0:h, 0:h])
                mm.then_inc(turned, 1)

        @block.vector
        def _(dve):
            for n in range(len(rows)):
                dve.wait_ge(turned, n + 1)
                nc.vector.tensor_copy(cols[:, n, :, :].rearrange("p h t -> p t h"),
                                      core.ps[:, n, 0:NT * h].rearrange("p (t h) -> p t h", t=NT))


def gated_heads(nc, core, y, gate, gain, width, before=None):
    f = y.shape[2]
    heads = f // width
    n = NT * heads
    mv = core.mv[:, 0:n, :]

    def pool_part(pool, var_ready, root_ready):
        inverse_root(nc, core, pool, mv[:, :, 1:2], 1e-6, var_ready, root_ready)

    def dve_part(dve, var_ready, root_ready):
        if before is not None:
            for t in range(NT):
                nc.vector.tensor_tensor(y[:, t, :], y[:, t, :], before[:, t, :], ALU.mult)
            dve.drain()
        part = lambda g: y[:, g // heads, (g % heads) * width:(g % heads + 1) * width]
        row_stats(nc, core, dve, part, mv, width, n)
        mean_square(nc, dve, mv)
        dve.drain().then_inc(var_ready, 1)
        dve.wait_ge(root_ready, 2)
        for g in range(n):
            nc.vector.tensor_scalar(part(g), part(g), mv[:, g, 1:2], None, ALU.mult)
        dve.drain()
        for t in range(NT):
            if gain.shape[1] == f:
                nc.vector.tensor_tensor(y[:, t, :], y[:, t, :], gain, ALU.mult)
            else:
                run = y[:, t, :].rearrange("p (h f) -> p h f", h=heads)
                nc.vector.tensor_tensor(run, run, gain.unsqueeze(1).to_broadcast([P, heads, width]), ALU.mult)
        dve.drain()
        if gate is not None:
            for t in range(NT):
                nc.vector.tensor_tensor(y[:, t, :], y[:, t, :], gate[:, t, :], ALU.mult)

    return pool_part, dve_part


def decay_strips(nc, core, bank, edge, minus_col, out):
    for s in range(NT):
        nc.scalar.activation(strip(out, s, 0, P), edge[:, s, :], ACT.Exp, bias=minus_col(s))
        if s < NT - 1:
            nc.scalar.activation(strip(out, s, P), core.ps[:, bank, (s + 1) * P:SEQ], ACT.Exp, bias=minus_col(s))


GDN_HEADS, GDN_DK = 4, 128
LEVELS = 7


def unit_rows(nc, core, qkT):
    n = 2 * GDN_HEADS
    with buffers(nc, squares=[P, n, SEQ], pick=[P, n, n], scale_row=[n, SEQ]) as (squares, pick, scale_row), \
            stage(nc, "unit", "picks", "squared", "summed", "inverted", "rooted", "spread") as (
                block, picks, squared, summed, inverted, rooted, spread):
        @block.gpsimd
        def _(pool):
            nc.gpsimd.memset(pick[:], 0.0)
            pool.drain()
            for f in range(n):
                done = nc.gpsimd.memset(pick[:, f, f:f + 1], 1.0)
            done.then_inc(picks, 1)

        @block.scalar
        def _(act):
            for f in range(n):
                nc.scalar.activation(squares[:, f, :], qkT[:, f, :], ACT.Square).then_inc(squared, 1)
            act.wait_ge(inverted, 1)
            nc.scalar.activation(scale_row[:], scale_row[:], ACT.Sqrt).then_inc(rooted, 1)

        @block.tensor
        def _(pe):
            pe.wait_ge(picks, 1)
            for f in range(n):
                pe.wait_ge(squared, f + 1)
                mm = nc.tensor.matmul(core.ps[0:n, 0, :], pick[:, f, :], squares[:, f, :], start=f == 0, stop=f == n - 1)
            mm.then_inc(summed, 1)
            pe.wait_ge(rooted, 1)
            for f in range(n):
                nc.tensor.matmul(core.ps[:, (f + 1) % 8, :], core.ident[0:n, f:f + 1].to_broadcast([n, P]), scale_row[:],
                                 start=True, stop=True).then_inc(spread, 1)

        @block.vector
        def _(dve):
            dve.wait_ge(summed, 1)
            nc.vector.tensor_scalar(scale_row[:], core.ps[0:n, 0, :], 1e-6, None, ALU.add)
            dve.drain()
            nc.vector.reciprocal(scale_row[:], scale_row[:]).then_inc(inverted, 1)
            for f in range(n):
                dve.wait_ge(spread, f + 1)
                nc.vector.scalar_tensor_tensor(qkT[:, f, :], qkT[:, f, :], GDN_DK ** -0.5 if f < GDN_HEADS else 1.0,
                                               core.ps[:, (f + 1) % 8, :], ALU.mult, ALU.mult)


def delta_half(nc, core, half, qkvT, cum_rows, cols, vb, u, o, masks):
    H = GDN_HEADS
    heads = (2 * half, 2 * half + 1)
    kind_beta, kind_cum, kind_minus = 0, 1, 2
    with buffers(nc, keys=[P, 2, PACKED], attn=[P, 2, PACKED], edge=[P, NT, P], diag=[P, 8, P], rhs=[P, 2, P]) as (
            keys, attn, edge, diag, rhs):
        inv, invT = (qkvT[:, q:q + 2, :].rearrange("p q (n t) -> p (q n) t", t=P) for q in (2 * H, 2 * H + 2))
        part, prod = (core.tmp[:, q:q + 2, :].rearrange("p q (n t) -> p (q n) t", t=P) for q in (0, 2))
        with stage(nc, f"delta_scores{half}", "spread", "edged", "decayed", "scored", "applied") as (
                block, spread, edged, decayed, scored, applied):
            @block.tensor
            def _(pe):
                for n, h in enumerate(heads):
                    if n:
                        pe.wait_ge(decayed, n)
                    nc.tensor.matmul(core.ps[:, 0, :], core.ident[0:H, h:h + 1].to_broadcast([H, P]), cum_rows, start=True, stop=True).then_inc(spread, 1)
                    for m, first in enumerate((H + h, h)):
                        for s in range(NT):
                            if n or m:
                                pe.wait_ge(applied, NT * (2 * n + m - 1) + s + 1)
                            nc.tensor.matmul(core.ps[:, 1 + s, 0:SEQ - s * P], qkvT[:, H + h, s * P:(s + 1) * P],
                                             qkvT[:, first, s * P:], start=True, stop=True).then_inc(scored, 1)

            @block.scalar
            def _(act):
                for n, h in enumerate(heads):
                    act.wait_ge(edged, n + 1)
                    decay_strips(nc, core, 0, edge, lambda s: cols[:, kind_minus, h, s:s + 1], attn[:, n])
                    act.drain().then_inc(decayed, 1)

            @block.vector
            def _(dve):
                for n, h in enumerate(heads):
                    dve.wait_ge(spread, n + 1)
                    if n:
                        dve.wait_ge(decayed, n)
                    nc.vector.tensor_tensor(edge[:], core.ps[:, 0, :].rearrange("p (s t) -> p s t", s=NT),
                                            core.causal[:].unsqueeze(1).to_broadcast([P, NT, P]), ALU.add).then_inc(edged, 1)
                    dve.wait_ge(decayed, n + 1)
                    for m, dst in enumerate((keys, attn)):
                        dve.drain()
                        for s in range(NT):
                            dve.wait_ge(scored, NT * (2 * n + m) + s + 1)
                            nc.vector.tensor_tensor(strip(dst[:, n, :], s), core.ps[:, 1 + s, 0:SEQ - s * P],
                                                    strip(attn[:, n, :], s), ALU.mult).then_inc(applied, 1)

        with stage(nc, f"delta_inverse{half}", "masked", "first", "scaled", "second", "updated") as (
                block, masked, first, scaled, second, updated):
            bank = lambda kind, g: core.ps[:, 2 * kind + g, :].rearrange("p (n t) -> p n t", n=NT)
            of = lambda buf, g: buf[:, NT * g:NT * (g + 1), :]
            beta = lambda g: cols[:, kind_beta, heads[g], :].unsqueeze(2).to_broadcast([P, NT, P])

            @block.vector
            def _(dve):
                def mask(level, g):
                    nc.vector.tensor_tensor(of(part, g), of(diag, g), masks[:, level, :].unsqueeze(1).to_broadcast([P, NT, P]),
                                            ALU.mult).then_inc(masked, 1)

                for n in range(8):
                    nc.vector.tensor_copy(diag[:, n, :], strip(keys[:, n // 4, :], n % 4, 0, P))
                    nc.vector.tensor_copy(inv[:, n, :], core.ident[:])
                    nc.vector.tensor_copy(invT[:, n, :], core.ident[:])
                dve.drain()
                mask(0, 0)
                mask(0, 1)
                for level in range(LEVELS):
                    for g in range(2):
                        dve.wait_ge(first, 2 * level + g + 1)
                        nc.vector.tensor_tensor(of(prod, g), bank(0, g), beta(g), ALU.mult).then_inc(scaled, 1)
                    for g in range(2):
                        if level + 1 < LEVELS:
                            mask(level + 1, g)
                        dve.wait_ge(second, 2 * level + g + 1)
                        nc.vector.tensor_tensor(of(inv, g), of(inv, g), bank(1, g), ALU.subtract)
                        nc.vector.tensor_tensor(of(invT, g), of(invT, g), bank(2, g), ALU.subtract)
                        dve.drain().then_inc(updated, 1)

            @block.tensor
            def _(pe):
                for level in range(LEVELS):
                    for g in range(2):
                        pe.wait_ge(masked, 2 * level + g + 1)
                        if level:
                            pe.wait_ge(updated, 2 * level + g - 1)
                        for n in range(NT):
                            mm = nc.tensor.matmul(bank(0, g)[:, n, :], of(part, g)[:, n, :], of(inv, g)[:, n, :], start=True, stop=True)
                        mm.then_inc(first, 1)
                    for g in range(2):
                        pe.wait_ge(scaled, 2 * level + g + 1)
                        for n in range(NT):
                            nc.tensor.matmul(bank(1, g)[:, n, :], of(invT, g)[:, n, :], of(prod, g)[:, n, :], start=True, stop=True)
                            mm = nc.tensor.matmul(bank(2, g)[:, n, :], of(prod, g)[:, n, :], of(invT, g)[:, n, :], start=True, stop=True)
                        mm.then_inc(second, 1)

        with stage(nc, f"delta_solve{half}", "gathered", "sided", "solved", "stored", "output", "copied") as (
                block, gathered, sided, solved, stored, output, copied):
            @block.tensor
            def _(pe):
                for t in range(NT):
                    if t:
                        pe.wait_ge(stored, t)
                        for n, h in enumerate(heads):
                            for s in range(t):
                                mm = nc.tensor.matmul(core.ps[:, 0, n * P:(n + 1) * P], strip(keys[:, n, :], s, (t - s) * P, (t - s + 1) * P),
                                                      u[:, s, h * P:(h + 1) * P], start=s == 0, stop=s == t - 1)
                        mm.then_inc(gathered, 1)
                    pe.wait_ge(sided, t + 1)
                    for n in range(2):
                        mm = nc.tensor.matmul(core.ps[:, 1, n * P:(n + 1) * P], invT[:, 4 * n + t, :], rhs[:, n, :], start=True, stop=True)
                    mm.then_inc(solved, 1)
                pe.wait_ge(stored, NT)
                for n, h in enumerate(heads):
                    for t in range(NT):
                        for s in range(t + 1):
                            mm = nc.tensor.matmul(core.ps[:, 2 + n, t * P:(t + 1) * P], strip(attn[:, n, :], s, (t - s) * P, (t - s + 1) * P),
                                                  u[:, s, h * P:(h + 1) * P], start=s == 0, stop=s == t)
                    mm.then_inc(output, 1)

            @block.vector
            def _(dve):
                for t in range(NT):
                    if t:
                        dve.wait_ge(gathered, t)
                    for n, h in enumerate(heads):
                        v = vb[:, t, h * P:(h + 1) * P]
                        if t:
                            done = nc.vector.scalar_tensor_tensor(rhs[:, n, :], core.ps[:, 0, n * P:(n + 1) * P],
                                                                  cols[:, kind_beta, h, t:t + 1], v, ALU.mult, ALU.subtract)
                        else:
                            done = nc.vector.tensor_scalar(rhs[:, n, :], v, -1.0, None, ALU.mult)
                    done.then_inc(sided, 1)

            @block.scalar
            def _(act):
                for t in range(NT):
                    act.wait_ge(solved, t + 1)
                    nc.scalar.activation(u[:, t, heads[0] * P:(heads[0] + 2) * P], core.ps[:, 1, 0:2 * P], ACT.Copy,
                                         scale=-1.0).then_inc(stored, 1)
                for n, h in enumerate(heads):
                    act.wait_ge(output, n + 1)
                    nc.scalar.copy(o[:, :, h * P:(h + 1) * P], core.ps[:, 2 + n, :].rearrange("p (t f) -> p t f", t=NT))


def delta_branch(nc, core, d, o):
    H = GDN_HEADS
    with buffers(nc, qkvT=[P, 3 * H, SEQ], beta_row=[H, SEQ], g_row=[H, SEQ], g_tmp=[H, SEQ], dt_bias=[H, 1], a_rate=[H, 1],
                 cols=[P, 3, H, NT], masks=[P, LEVELS, P]) as (
            qkvT, beta_row, g_row, g_tmp, dt_bias, a_rate, cols, masks):
        u, vb = core.x[:, :, 0:H * P], core.x[:, :, H * P:2 * H * P]
        with buffers(nc, taps=[P, 4, 3 * H]) as (taps,):
            project(nc, core, "delta_in", core.hT, [
                ("aqkv", 3, "feature", ("conv", taps, None, 4, feature_tiles(qkvT))),
                ("beta_dt", 1, [(0, H), (H, H)], ("act", ACT.Copy, row_buffers(beta_row, g_row)))],
                    loads=[(taps[:], d["gdn_conv_c_2"]), (dt_bias[:], d["gdn_dt_bias_c_2"]), (a_rate[:], d["gdn_a_log_c_2"]),
                           (masks[:], d["const_levels"])])
        unit_rows(nc, core, qkvT)
        soft_maximum(nc, "delta_soft", [(g_row[:], g_tmp[:], 1.0, dt_bias[:], 0.0, 0.0)])
        with stage(nc, "delta_decay", "ready", "scanned") as (block, ready, scanned):
            @block.scalar
            def _(act):
                nc.scalar.activation(a_rate[:], a_rate[:], ACT.Exp).then_inc(ready, 1)
                nc.scalar.activation(beta_row[:], beta_row[:], ACT.Sigmoid)

            @block.vector
            def _(dve):
                dve.wait_ge(ready, 1)
                nc.vector.tensor_scalar(g_tmp[:], g_row[:], a_rate[:], -1.0, ALU.mult, ALU.mult)
                dve.drain()
                nc.vector.tensor_tensor_scan(g_row[:], core.one_row[0:H, :], g_tmp[:], 0.0, ALU.mult, ALU.add)
        row_columns(nc, core, "delta_cols", [beta_row, g_row], cols, H)
        with stage(nc, "delta_values", "turned") as (block, turned):
            @block.tensor
            def _(pe):
                for t in range(NT):
                    for h in range(H):
                        mm = nc.tensor.transpose(core.ps[:, t, h * P:(h + 1) * P], qkvT[:, 2 * H + h, t * P:(t + 1) * P], core.ident[:])
                    mm.then_inc(turned, 1)

            @block.vector
            def _(dve):
                nc.vector.tensor_scalar(cols[:, 2], cols[:, 1], -1.0, None, ALU.mult)
                for t in range(NT):
                    dve.wait_ge(turned, t + 1)
                    nc.vector.tensor_tensor(vb[:, t, :].rearrange("p (h f) -> p h f", h=H),
                                            core.ps[:, t, :].rearrange("p (h f) -> p h f", h=H),
                                            cols[:, 0, :, t:t + 1].to_broadcast([P, H, P]), ALU.mult)
        for half in range(2):
            delta_half(nc, core, half, qkvT, g_row[:], cols, vb, u, o, masks)


SUB = 16
SUBS = P // SUB


def channel_decay_unit(nc, core, name, heads, q, k, cum, last, v, o, sums, own_block):
    TB = SEQ // SUB
    tiles = lambda a: a.rearrange("p (t n) -> p t n", t=NT)
    blocks = lambda a: a.rearrange("p (b i) -> p b i", i=SUB)
    with buffers(nc, q_tile=[P, SEQ], q_block=[P, SEQ], ref=[P, TB], far=[P, 6, P], near=[P, 2, SUBS, P],
                 pair=[P, 4, SEQ], bias=[P, 6], own=[P, SEQ], scores=[P, len(heads), SEQ], cross=[P, len(heads), 6, P]) as (
            q_tile, q_block, ref, far, near, pair, bias, own, scores, cross):
        far_pairs = [(s, t) for t in range(NT) for s in range(t)]
        with stage(nc, name, "zeroed", "referred", "shifted", "raised_q", "queries", "biased", "raised_far", "far_ready",
                   "raised_near", "near_ready", "near_used", "differed", "raised", "paired", "pair_used", "far_scored",
                   "near_scored", "own_scored", "crossed", "merged", "output") as (
                block, zeroed, referred, shifted, raised_q, queries, biased, raised_far, far_ready,
                raised_near, near_ready, near_used, differed, raised, paired, pair_used, far_scored,
                near_scored, own_scored, crossed, merged, output):
            @block.gpsimd
            def _(pool):
                nc.gpsimd.memset(near[:], 0.0).then_inc(zeroed, 1)
                for j in range(SUB):
                    if j >= 4:
                        pool.wait_ge(pair_used, j - 3)
                    nc.gpsimd.tensor_tensor(blocks(pair[:, j % 4, :]), blocks(cum),
                                            blocks(cum)[:, :, j:j + 1].to_broadcast([P, TB, SUB]), ALU.subtract).then_inc(differed, 1)

            @block.vector
            def _(dve):
                nc.vector.memset(ref[:], 0.0)
                nc.vector.memset(bias[:], 0.0)
                dve.drain()
                nc.vector.tensor_copy(ref[:].rearrange("p (t b) -> p t b", t=NT)[:, :, 1:SUBS],
                                      tiles(cum).rearrange("p t (b i) -> p t b i", i=SUB)[:, :, 0:SUBS - 1, SUB - 1])
                for n, (s, t) in enumerate(far_pairs):
                    nc.vector.tensor_reduce(bias[:, n:n + 1], last[:, s:t], AX.X, ALU.add)
                dve.drain().then_inc(referred, 1)
                nc.vector.tensor_tensor(blocks(q_block[:]), blocks(cum), ref[:].unsqueeze(2).to_broadcast([P, TB, SUB]),
                                        ALU.subtract).then_inc(shifted, 1)
                dve.wait_ge(raised_q, 2)
                nc.vector.tensor_tensor(q_tile[:], q_tile[:], q, ALU.mult)
                nc.vector.tensor_tensor(q_block[:], q_block[:], q, ALU.mult).then_inc(queries, 1)
                for n, (s, t) in enumerate(far_pairs):
                    dve.wait_ge(raised_far, n + 1)
                    nc.vector.tensor_tensor(far[:, n, :], far[:, n, :], k[:, s * P:(s + 1) * P], ALU.mult).then_inc(far_ready, 1)
                for t in range(NT):
                    dve.wait_ge(raised_near, t + 1)
                    nc.vector.tensor_tensor(near[:, t % 2], near[:, t % 2], k[:, t * P:(t + 1) * P].unsqueeze(1).to_broadcast([P, SUBS, P]),
                                            ALU.mult).then_inc(near_ready, 1)
                for j in range(SUB):
                    dve.wait_ge(raised, j + 1)
                    b = blocks(pair[:, j % 4, :])
                    nc.vector.scalar_tensor_tensor(b, b, 1.0, blocks(k)[:, :, j:j + 1].to_broadcast([P, TB, SUB]), ALU.min, ALU.mult)
                    dve.drain()
                    nc.vector.tensor_tensor(pair[:, j % 4, :], pair[:, j % 4, :], q, ALU.mult).then_inc(paired, 1)
                for n in range(len(heads)):
                    dve.wait_ge(own_scored, n + 1)
                    nc.vector.tensor_tensor(tiles(own[:]), tiles(core.ps[:, 1 + n, :]),
                                            own_block.unsqueeze(1).to_broadcast([P, NT, P]), ALU.mult)
                    dve.drain()
                    dve.wait_ge(near_scored, n + 1)
                    nc.vector.tensor_tensor(scores[:, n, :], own[:], core.ps[:, 3 + n, :], ALU.add).then_inc(merged, 1)
                    dve.drain()

            @block.scalar
            def _(act):
                act.wait_ge(shifted, 1)
                nc.scalar.activation(q_tile[:], cum, ACT.Exp).then_inc(raised_q, 1)
                nc.scalar.activation(q_block[:], q_block[:], ACT.Exp).then_inc(raised_q, 1)
                act.wait_ge(referred, 1)
                for n, (s, t) in enumerate(far_pairs):
                    nc.scalar.activation(far[:, n, :], cum[:, s * P:(s + 1) * P], ACT.Exp, bias=bias[:, n:n + 1],
                                         scale=-1.0).then_inc(raised_far, 1)
                for n in range(len(heads)):
                    act.wait_ge(far_scored, n + 1)
                    nc.scalar.copy(cross[:, n, 0:4, :], core.ps[:, 5, :].rearrange("p (n t) -> p n t", n=4))
                    nc.scalar.copy(cross[:, n, 4:6, :], core.ps[:, 6, 0:2 * P].rearrange("p (n t) -> p n t", n=2)).then_inc(crossed, 1)
                act.wait_ge(zeroed, 1)
                for t in range(NT):
                    if t >= 2:
                        act.wait_ge(near_used, t - 1)
                    for b in range(1, SUBS):
                        done = nc.scalar.activation(near[:, t % 2, b, 0:b * SUB], cum[:, t * P:t * P + b * SUB], ACT.Exp,
                                                    bias=ref[:, t * SUBS + b:t * SUBS + b + 1], scale=-1.0)
                    done.then_inc(raised_near, 1)
                for j in range(SUB):
                    act.wait_ge(differed, j + 1)
                    nc.scalar.activation(pair[:, j % 4, :], pair[:, j % 4, :], ACT.Exp).then_inc(raised, 1)
                for n, (_, _, col) in enumerate(heads):
                    act.wait_ge(output, n + 1)
                    nc.scalar.copy(o[:, :, col:col + P], core.ps[:, (0, 7)[n], :].rearrange("p (t f) -> p t f", t=NT))

            @block.tensor
            def _(pe):
                pe.wait_ge(queries, 1)
                pe.wait_ge(far_ready, len(far_pairs))
                for n, (r, rows, _) in enumerate(heads):
                    if n:
                        pe.wait_ge(crossed, n)
                    for m, (s, t) in enumerate(far_pairs):
                        mm = nc.tensor.matmul(core.ps[:, 5 + m // 4, (m % 4) * P:(m % 4 + 1) * P], far[r:r + rows, m, :],
                                              q_tile[r:r + rows, t * P:(t + 1) * P], start=True, stop=True)
                    mm.then_inc(far_scored, 1)
                for t in range(NT):
                    pe.wait_ge(near_ready, t + 1)
                    for n, (r, rows, _) in enumerate(heads):
                        for b in range(SUBS):
                            at = t * P + b * SUB
                            mm = nc.tensor.matmul(core.ps[:, 3 + n, at:at + SUB], near[r:r + rows, t % 2, b, :],
                                                  q_block[r:r + rows, at:at + SUB], start=True, stop=True)
                        if t == NT - 1:
                            mm.then_inc(near_scored, 1)
                    pe.drain().then_inc(near_used, 1)
                for j in range(SUB):
                    pe.wait_ge(paired, j + 1)
                    for n, (r, rows, _) in enumerate(heads):
                        mm = nc.tensor.matmul(core.ps[:, 1 + n, :], sums[r:r + rows, SUB - 1 - j:SUB - 1 - j + P], pair[r:r + rows, j % 4, :],
                                              start=j == 0, stop=j == SUB - 1)
                    mm.then_inc(pair_used, 1)
                pe.drain().then_inc(own_scored, len(heads))
                for n, (_, _, col) in enumerate(heads):
                    pe.wait_ge(merged, n + 1)
                    pe.wait_ge(crossed, n + 1)
                    for t in range(NT):
                        out = core.ps[:, (0, 7)[n], t * P:(t + 1) * P]
                        for s in range(t):
                            nc.tensor.matmul(out, cross[:, n, far_pairs.index((s, t)), :], v[:, s, col:col + P], start=s == 0, stop=False)
                        mm = nc.tensor.matmul(out, scores[:, n, t * P:(t + 1) * P], v[:, t, col:col + P], start=t == 0, stop=True)
                    mm.then_inc(output, 1)


def tile_sums(nc, core, name, logs, cum, last, units):
    with stage(nc, name) as (block,):
        @block.vector
        def _(dve):
            for u in range(units):
                nc.vector.tensor_tensor_scan(cum[:, u, :], core.tile_row[:], logs[:, u, :], 0.0, ALU.mult, ALU.add)
            dve.drain()
            for u in range(units):
                nc.vector.tensor_copy(last[:, u, :], cum[:, u, :].rearrange("p (t n) -> p t n", t=NT)[:, :, P - 1])


def gla_branch(nc, core, d, o, sums, own_block):
    with buffers(nc, qkT=[P, 4, SEQ], v=[P, NT, SEQ], lr=[16, SEQ], w2=[16, 256], b2=[P, 2], logs=[P, 2, SEQ], cum=[P, 2, SEQ],
                 last=[P, 2, NT]) as (qkT, v, lr, w2, b2, logs, cum, last):
        project(nc, core, "gla_in", core.hT, [("bqk", 1, "feature", ("act", ACT.Copy, feature_tiles(qkT))),
                                              ("bv", 1, "token", ("act", ACT.Copy, columns(v))),
                                              ("blr", 1, [(0, 16)], ("act", ACT.Copy, row_buffers(lr)))],
                loads=[(w2[:], d["gla_w2_2"][0]), (b2[:], d["gla_b2_c_2"]), (sums[:], d["const_sums"]), (own_block, d["const_own_block"])])
        with stage(nc, "gla_gate", "gated") as (block, gated):
            @block.tensor
            def _(pe):
                for u in range(2):
                    nc.tensor.matmul(core.ps[:, u, :], w2[:, u * P:(u + 1) * P], lr[:], start=True, stop=True).then_inc(gated, 1)

            @block.vector
            def _(dve):
                for u in range(2):
                    dve.wait_ge(gated, u + 1)
                    nc.vector.tensor_scalar(logs[:, u, :], core.ps[:, u, :], b2[:, u:u + 1], None, ALU.add)
                nc.vector.tensor_scalar(qkT[:, 0:2, :], qkT[:, 0:2, :], 64 ** -0.5, None, ALU.mult)
        soft_maximum(nc, "gla_soft", [(logs[:, u, :], cum[:, u, :], -1.0, 0.0, 0.0, 0.0) for u in range(2)])
        with stage(nc, "gla_scale") as (block,):
            @block.vector
            def _(dve):
                nc.vector.tensor_scalar(logs[:], logs[:], -1.0 / 16.0, None, ALU.mult)
        tile_sums(nc, core, "gla_sums", logs, cum, last, 2)
        for u in range(2):
            channel_decay_unit(nc, core, f"gla{u}", [(0, 64, 2 * u * P), (64, 64, (2 * u + 1) * P)], qkT[:, u, :], qkT[:, 2 + u, :],
                               cum[:, u, :], last[:, u, :], v, o, sums, own_block)


def hgrn_branch(nc, core, d, o, sums, own_block):
    H = 4
    with buffers(nc, q=[P, H, SEQ], k=[P, H, SEQ], v=[P, NT, SEQ], logs=[P, H, SEQ], last=[P, H, NT],
                 lb=[P, 7, H]) as (q, k, v, logs, last, lb):
        project(nc, core, "hgrn_in", core.hT, [("cq", 1, "feature", ("act", ACT.Silu, feature_tiles(q))),
                                               ("cf", 1, "feature", ("act", ACT.Copy, feature_tiles(logs))),
                                               ("ci", 1, "token", ("act", ACT.Copy, columns(v)))],
                loads=[(sums[:], d["const_sums"]), (own_block, d["const_own_block"])])
        LB, LOG_LB, MINUS_LOG_LB, REST, LOG_REST, EXP, TMP = range(7)
        with stage(nc, "hgrn_bound", "loaded", "differed", "raised", "bounded", "logged", "keyed") as (
                block, loaded, differed, raised, bounded, logged, keyed):
            @block.sync
            def _(sp):
                sp.dma_start(lb[:, TMP, :], d["hgrn_lb_c_2"]).then_inc(loaded, 16)

            @block.vector
            def _(dve):
                dve.wait_ge(loaded, 16)
                nc.vector.tensor_tensor(lb[:, EXP, :], lb[:, TMP, :], lb[:, TMP, :], ALU.subtract).then_inc(differed, 1)
                dve.wait_ge(raised, 1)
                nc.vector.reciprocal(lb[:, TMP, :], lb[:, EXP, :])
                dve.drain()
                nc.vector.tensor_tensor(lb[:, EXP, :], lb[:, EXP, :], lb[:, TMP, :], ALU.mult)
                dve.drain()
                nc.vector.tensor_tensor(lb[:, LB, :], lb[:, EXP, :], lb[:, EXP, :], ALU.subtract)
                dve.drain()
                nc.vector.tensor_scalar(lb[:, LB, :], lb[:, LB, :], 0.0, 1.0, ALU.max, ALU.min)
                dve.drain()
                nc.vector.tensor_scalar(lb[:, REST, :], lb[:, LB, :], -1.0, 1.0, ALU.mult, ALU.add)
                nc.vector.tensor_scalar(lb[:, TMP, :], lb[:, LB, :], 1e-30, 2.0 ** 50, ALU.max, ALU.mult)
                dve.drain().then_inc(bounded, 1)
                dve.wait_ge(logged, 2)
                nc.vector.tensor_scalar(lb[:, LOG_LB, :], lb[:, LOG_LB, :], -50.0 * float(np.log(2.0)), None, ALU.add)
                dve.drain()
                nc.vector.tensor_scalar(lb[:, MINUS_LOG_LB, :], lb[:, LOG_LB, :], -1.0, None, ALU.mult)
                dve.wait_ge(keyed, H)
                for h in range(H):
                    nc.vector.tensor_scalar(k[:, h, :], k[:, h, :], lb[:, REST, h:h + 1], None, ALU.mult)
                nc.vector.tensor_scalar(q[:], q[:], 128 ** -0.5, None, ALU.mult)

            @block.scalar
            def _(act):
                act.wait_ge(differed, 1)
                nc.scalar.activation(lb[:, EXP, :], lb[:, EXP, :], ACT.Exp).then_inc(raised, 1)
                act.wait_ge(bounded, 1)
                nc.scalar.activation(lb[:, LOG_LB, :], lb[:, TMP, :], ACT.Ln).then_inc(logged, 1)
                nc.scalar.activation(lb[:, LOG_REST, :], lb[:, REST, :], ACT.Ln).then_inc(logged, 1)
                for h in range(H):
                    nc.scalar.activation(k[:, h, :], logs[:, h, :], ACT.Sigmoid, scale=-1.0).then_inc(keyed, 1)
        tmp = core.tmp
        soft_maximum(nc, "hgrn_soft", [(logs[:, h, :], tmp[:, h, :], -1.0, 0.0, 0.0, 0.0) for h in range(H)])
        soft_maximum(nc, "hgrn_add", [(logs[:, h, :], tmp[:, h, :], -1.0, lb[:, LOG_REST, h:h + 1], lb[:, LOG_LB, h:h + 1],
                                       lb[:, MINUS_LOG_LB, h:h + 1]) for h in range(H)])
        cum = core.tmp
        tile_sums(nc, core, "hgrn_sums", logs, cum, last, H)
        for h in range(H):
            channel_decay_unit(nc, core, f"hgrn{h}", [(0, P, h * P)], q[:, h, :], k[:, h, :], cum[:, h, :], last[:, h, :],
                               v, o, sums, own_block)


def second_mixer(nc, core, d):
    with buffers(nc, o=[P, NT, SEQ], gain=[P, P]) as (o, gain):
        def close(name, gain_name, gate_plan, share_plan, out_plan, first):
            with buffers(nc, gate=[P, NT, SEQ], oT=([P, 2, 4, SEQ], F32R), share=[P, NT, D]) as (gate, oT, share):
                project(nc, core, f"{name}_gates", core.hT, [(gate_plan, 1, "token", ("act", ACT.Silu, columns(gate))),
                                                             (share_plan, 2, "token", ("act", ACT.Sigmoid, columns(share)))],
                        loads=[(gain[:], d[gain_name][0, :].partition_broadcast(P))], beside=gated_heads(nc, core, o, gate, gain[:], P))
                transpose(nc, core, f"{name}_T", o, two_parts(oT), 4)
                project(nc, core, f"{name}_out", two_parts(oT), [(out_plan, 2, "token", ("mul" if first else "mad", columns(share), columns(core.x)))], kt=4)

        delta_branch(nc, core, d, o)
        close("gdn", "gdn_norm_2", "ag", "ma", "br_a", True)
        with buffers(nc, sums=[P, P + SUB], own_block=[P, P]) as (sums, own_block):
            gla_branch(nc, core, d, o, sums, own_block[:])
        close("gla", "gla_norm_2", "bg", "mb", "br_b", False)
        with buffers(nc, sums=[P, P + SUB], own_block=[P, P]) as (sums, own_block):
            hgrn_branch(nc, core, d, o, sums, own_block[:])
        close("hgrn", "hgrn_norm_2", "cg", "mc", "br_c", False)
    with buffers(nc, yT=([P, 2, KD, SEQ], F32R)) as (yT,):
        transpose(nc, core, "mix_T", core.x, two_parts(yT))
        project(nc, core, "out2", two_parts(yT), [("out2", 2, "token", ("axpy", ALPHA, columns(core.h)))])


EXPERTS, GROUPS, MEMBERS, FF = 16, 4, 4, 256


def choose_experts(nc, core, d, combine):
    first = take(core, "router", 1)
    start = plan_splits(core, 2 * core.taken)
    n = NT * GROUPS
    with buffers(nc, score=[P, NT, EXPERTS], sel=[P, NT, EXPERTS], bias=[P, EXPERTS], pair_sums=[P, n, 6], best=[P, n], beats=[P, n, 4, 4],
                 same=[P, n, 4, 4], rank=[P, n, 4], g_rank=[P, n], total=[P, NT], before=[P, 4, 4]) as (
            score, sel, bias, pair_sums, best, beats, same, rank, g_rank, total, before):
        with stage(nc, "choose", "loaded", "scored", "squashed") as (block, loaded, scored, squashed):
            @block.sync
            def _(sp):
                sp.dma_start(bias[:], d["router_bias_2"].partition_broadcast(P)).then_inc(loaded, 16)
                sp.dma_start(before[:], d["const_before"].partition_broadcast(P)).then_inc(loaded, 16)
                load_ahead(core, sp, core.splits + 2)

            @block.tensor
            def _(pe):
                for half in range(2):
                    pe.wait_ge(core.split[half], first + 1)
                w = [weights(core, half, P, KD // 2, EXPERTS) for half in range(2)]
                for t in range(NT):
                    for k in range(KD):
                        mm = product(nc, core.ps[:, 0, t * EXPERTS:(t + 1) * EXPERTS], halves(core.hT, k, slice(t * P, (t + 1) * P)),
                                     [v[:, k % (KD // 2), :] for v in w[k // (KD // 2)]], k == 0, k == KD - 1)
                    mm.then_inc(core.products, 1)
                pe.drain().then_inc(core.used, 1)

            @block.scalar
            def _(act):
                act.wait_ge(core.products, QUARTERS * (first + 1))
                nc.scalar.activation(score[:].rearrange("p t e -> p (t e)"), core.ps[:, 0, 0:NT * EXPERTS], ACT.Sigmoid).then_inc(squashed, 1)

            def ranks(dve, values, out, count, lists):
                mine = values.unsqueeze(3).to_broadcast([P, lists, count, count])
                other = values.unsqueeze(2).to_broadcast([P, lists, count, count])
                a, b = beats[:, 0:lists], same[:, 0:lists]
                nc.vector.tensor_tensor(a, other, mine, ALU.is_gt)
                nc.vector.tensor_tensor(b, other, mine, ALU.is_equal)
                dve.drain()
                nc.vector.tensor_tensor(b, b, before[:].unsqueeze(1).to_broadcast([P, lists, count, count]), ALU.mult)
                dve.drain()
                nc.vector.tensor_tensor(a, a, b, ALU.add)
                dve.drain()
                nc.vector.tensor_reduce(out, a, AX.X, ALU.add)
                dve.drain()

            @block.vector
            def _(dve):
                split_first(nc, core, dve, start, first)
                dve.wait_ge(loaded, 32)
                dve.wait_ge(squashed, 1)
                nc.vector.tensor_tensor(sel[:], score[:], bias[:].unsqueeze(1).to_broadcast([P, NT, EXPERTS]), ALU.add)
                dve.drain()
                member = sel[:].rearrange("p t (g e) -> p (t g) e", g=GROUPS)
                m = 0
                for i in range(MEMBERS):
                    for j in range(i + 1, MEMBERS):
                        nc.vector.tensor_tensor(pair_sums[:, :, m:m + 1], member[:, :, i:i + 1], member[:, :, j:j + 1], ALU.add)
                        m += 1
                dve.drain()
                nc.vector.tensor_reduce(best[:], pair_sums[:], AX.X, ALU.max)
                ranks(dve, member, rank[:], MEMBERS, n)
                ranks(dve, best[:].rearrange("p (t g) -> p t g", t=NT), g_rank[:].rearrange("p (t g) -> p t g", t=NT), GROUPS, NT)
                nc.vector.tensor_scalar(rank[:], rank[:], 1.5, None, ALU.is_lt)
                nc.vector.tensor_scalar(g_rank[:], g_rank[:], 0.5, None, ALU.is_lt)
                dve.drain()
                nc.vector.tensor_tensor(rank[:], rank[:], g_rank[:].unsqueeze(2).to_broadcast([P, n, MEMBERS]), ALU.mult)
                dve.drain()
                nc.vector.tensor_tensor(score[:], score[:], rank[:].rearrange("p (t g) e -> p t (g e)", t=NT), ALU.mult)
                dve.drain()
                nc.vector.tensor_reduce(total[:], score[:], AX.X, ALU.add)
                dve.drain()
                nc.vector.reciprocal(total[:], total[:])
                dve.drain()
                nc.vector.tensor_tensor(combine[:], score[:], total[:].unsqueeze(2).to_broadcast([P, NT, EXPERTS]), ALU.mult)


def moe(nc, core, d):
    with buffers(nc, combine=[P, NT, EXPERTS], silu_g=[P, 2, SEQ], hidden=([P, 2, 2, SEQ], F32R)) as (combine, silu_g, hidden):
        choose_experts(nc, core, d, combine)
        first = take(core, "expert", 2 * EXPERTS)
        start = plan_splits(core, 2 * core.taken + 2)
        with stage(nc, "moe", "added", "activated", "hidden_ready", "outputs") as (block, added, activated, hidden_ready, outputs):
            @block.sync
            def _(sp):
                load_ahead(core, sp, core.splits + 2)

            @block.tensor
            def _(pe):
                with pe.Fori(0, EXPERTS) as e:
                    c_in, c_out = first + 2 * e, first + 2 * e + 1
                    pe.wait_ge(hidden_ready, 2 * e + 2)
                    for half in range(2):
                        pe.wait_ge(core.split[half], c_in + 1)
                        w = weights(core, half, P, KD // 2, 2 * FF)
                        for f in range(2):
                            for part in range(2):
                                col = part * FF + f * P
                                for k in range(KD // 2):
                                    kk = half * KD // 2 + k
                                    mm = product(nc, core.ps[:, 2 * part + f, :], [v[:, k, col:col + P] for v in w],
                                                 halves(core.hT, kk, slice(None)), kk == 0, kk == KD - 1)
                                if half == 1:
                                    mm.then_inc(core.products, 1)
                        if half == 0:
                            mm.then_inc(core.used, 1)
                    pe.wait_ge(hidden_ready, 2 * e + 4)
                    for half in range(2):
                        pe.wait_ge(core.split[half], c_out + 1)
                        w = weights(core, half, P, 2, BANK)
                        for t in range(NT):
                            pe.wait_ge(added, 8 * e + 4 * half + t + 1)
                            for f in range(2):
                                mm = product(nc, core.ps[:, 4 + t, :], halves(two_parts(hidden), f, slice(t * P, (t + 1) * P)),
                                             [v[:, f, :] for v in w], f == 0, f == 1)
                            mm.then_inc(outputs, 1)
                        if half == 0:
                            pe.drain().then_inc(core.used, 1)
                        else:
                            pe.drain().then_inc(core.products, QUARTERS)

            @block.scalar
            def _(act):
                with act.Fori(0, EXPERTS) as e:
                    for f in range(2):
                        act.wait_ge(core.products, QUARTERS * (first + 2 * e) + 2 * f + 1)
                        nc.scalar.activation(silu_g[:, f, :], core.ps[:, f, :], ACT.Silu).then_inc(activated, 1)

            @block.vector
            def _(dve):
                dve.sem_inc(hidden_ready, 2)
                dve.sem_inc(added, 4)
                nc.vector.tensor_scalar(core.x[:], core.x[:], ALPHA, None, ALU.mult)
                split_first(nc, core, dve, start, first)
                with dve.Fori(0, EXPERTS) as e:
                    c_in, c_out = first + 2 * e, first + 2 * e + 1
                    split_piece(nc, core, dve, c_out, 0, 2 * BANK)
                    for f in range(2):
                        dve.wait_ge(activated, 2 * e + f + 1)
                        dve.wait_ge(core.products, QUARTERS * c_in + 2 * f + 2)
                        nc.vector.tensor_tensor(silu_g[:, f, :], silu_g[:, f, :], core.ps[:, 2 + f, :], ALU.mult)
                        dve.drain()
                        split(nc, dve, silu_g[:, f, :], hidden[:, 0, f, :], hidden[:, 1, f, :]).then_inc(hidden_ready, 1)
                    split_piece(nc, core, dve, c_out, 1, 2 * BANK)
                    for half in range(2):
                        for t in range(NT):
                            dve.wait_ge(outputs, 8 * e + 4 * half + t + 1)
                            part = core.x[:, t, half * BANK:(half + 1) * BANK]
                            nc.vector.scalar_tensor_tensor(part, core.ps[:, 4 + t, :], combine[:, t, bass.ds(e, 1)], part,
                                                           ALU.mult, ALU.add).then_inc(added, 1)
                        split_piece(nc, core, dve, c_out + 1, half)


def second_block(nc, core, d):
    norm(nc, core, "norm0_2", core.x, core.h, core.hT, 1e-5, False, core.row_a[:], core.row_b[:],
         [(core.row_a[:], d["ln0_g_2"]), (core.row_b[:], d["ln0_b_2"])])
    second_mixer(nc, core, d)
    norm(nc, core, "norm1_2", core.h, core.x, core.hT, 1e-5, False, core.row_a[:], core.row_b[:],
         [(core.row_a[:], d["ln1_g_2"][0]), (core.row_b[:], d["ln1_b_2"][0])])
    moe(nc, core, d)
    norm(nc, core, "norm2_2", core.x, core.x, None, 1e-5, False, core.row_a[:], core.row_b[:],
         [(core.row_a[:], d["ln2_g_2"][0]), (core.row_b[:], d["ln2_b_2"][0])])


def plan_two(d):
    w = d["w_in_2"][0]
    one = lambda name, lo, n=1: [(name, kmajor(w, lo + i * BANK, BANK)) for i in range(n)]
    few = lambda name, lo, n: [(name, kmajor(w, lo, n))]
    wide = lambda name, m: [(name, kmajor(m, i * BANK, BANK)) for i in range(2)]
    plan = one("aqkv", 0, 3) + few("beta_dt", 1536, 8)
    plan += one("ag", 1544) + one("ma", 5656, 2) + wide("br_a", d["w_br_a_2"][0])
    plan += one("bqk", 2056) + one("bv", 2568) + few("blr", 3080, 16)
    plan += one("bg", 3096) + one("mb", 6680, 2) + wide("br_b", d["w_br_b_2"][0])
    plan += one("cq", 3608) + one("cf", 4120) + one("ci", 4632)
    plan += one("cg", 5144) + one("mc", 7704, 2) + wide("br_c", d["w_br_c_2"][0])
    plan += wide("out2", d["w_out_2"][0])
    plan += [("router", kmajor(d["w_router_2"], 0, EXPERTS))]
    for e in range(EXPERTS):
        plan += [("expert", kmajor(d["w_gate_up_2"][e], 0, 2 * FF)), ("expert", [d["w_down_2"][0][e][:, half * BANK:(half + 1) * BANK].rearrange("(k p) n -> p k n", p=P)
                                                                                            for half in range(2)])]
    return plan


M_HEADS, M_DQK = 8, 64
S_HEADS, S_HEADDIM, S_GROUPS = 16, 64, 4
D_FF = 2752
FF_TILES = -(-D_FF // P)
FF_CHUNKS = -(-D_FF // 256)


def causal_heads(nc, core, name, heads, rows, bias, keys, queries, share, scale, values, outputs, finish):
    row_bank = (0, 7)
    with buffers(nc, weights=[P, 3, PACKED], edge=[P, NT, P]) as (weights, edge), \
            stage(nc, name, "spread", "edged", "decayed", "scored", "applied", "summed", "finished") as (
                block, spread, edged, decayed, scored, applied, summed, finished):
        @block.tensor
        def _(pe):
            for h in range(heads + 2):
                if h < heads:
                    if h >= 2:
                        pe.wait_ge(decayed, h - 1)
                    nc.tensor.matmul(core.ps[:, row_bank[h % 2], :], core.ident[0:heads, h:h + 1].to_broadcast([heads, P]), rows,
                                     start=True, stop=True).then_inc(spread, 1)
                    if h % share == 0:
                        for s in range(NT):
                            if h:
                                pe.wait_ge(applied, NT * (h - 1) + s + 1)
                            nc.tensor.matmul(core.ps[:, 1 + s, 0:SEQ - s * P], keys(h, s), queries(h, s * P), start=True, stop=True).then_inc(scored, 1)
                if h >= 2:
                    g = h - 2
                    pe.wait_ge(applied, NT * (g + 1))
                    if g:
                        pe.wait_ge(finished, g)
                    for t in range(NT):
                        for s in range(t + 1):
                            mm = nc.tensor.matmul(outputs(t), strip(weights[:, g % 3, :], s, (t - s) * P, (t - s + 1) * P), values(g, s),
                                                  start=s == 0, stop=s == t)
                    mm.then_inc(summed, 1)

        @block.scalar
        def _(act):
            for h in range(heads):
                act.wait_ge(edged, h + 1)
                if h >= 3:
                    act.wait_ge(summed, h - 2)
                decay_strips(nc, core, row_bank[h % 2], edge, lambda s: bias(h, s), weights[:, h % 3])
                act.drain().then_inc(decayed, 1)

        @block.vector
        def _(dve):
            for h in range(heads + 3):
                if h >= 3:
                    dve.wait_ge(summed, h - 2)
                    finish(dve, h - 3).then_inc(finished, 1)
                if 1 <= h <= heads:
                    dve.wait_ge(decayed, h)
                if h < heads:
                    dve.wait_ge(spread, h + 1)
                    nc.vector.tensor_tensor(edge[:], core.ps[:, row_bank[h % 2], :].rearrange("p (s t) -> p s t", s=NT),
                                            core.causal[:].unsqueeze(1).to_broadcast([P, NT, P]), ALU.add).then_inc(edged, 1)
                if 1 <= h <= heads:
                    g = h - 1
                    for s in range(NT):
                        dve.wait_ge(scored, NT * (g // share) + s + 1)
                        nc.vector.scalar_tensor_tensor(strip(weights[:, g % 3, :], s), core.ps[:, 1 + s, 0:SEQ - s * P], scale(g, s),
                                                       strip(weights[:, g % 3, :], s), ALU.mult, ALU.mult).then_inc(applied, 1)


def mlstm_branch(nc, core, d, y):
    H = M_HEADS
    with buffers(nc, qkT=[P, KD, SEQ], v=[P, NT, H, P + 1], i_row=[H, SEQ], f_row=[H, SEQ], sum_row=[H, SEQ],
                 i_bias=[H, 1], f_bias=[H, 1], cols=[P, 2, H, NT], den=[P, 2, 2, 1]) as (
            qkT, v, i_row, f_row, sum_row, i_bias, f_bias, cols, den):
        with buffers(nc, taps=[P, 4, KD], conv_bias=[P, KD]) as (taps, conv_bias):
            project(nc, core, "mlstm_in", core.hT, [
                ("mqk", 2, "feature", ("conv", taps, conv_bias, 4, feature_tiles(qkT))),
                ("mv", 2, "token", ("act", ACT.Copy, lambda t, j: v[:, t, 4 * j:4 * j + 4, 0:P])),
                ("mif", 1, [(0, H), (H, H)], ("act", ACT.Copy, row_buffers(i_row, f_row)))],
                    loads=[(taps[:], d["m_conv_c_3"]), (conv_bias[:], d["m_conv_b_c_3"]), (i_bias[:], d["m_i_bias_c_3"]),
                           (f_bias[:], d["m_f_bias_c_3"])])
        with stage(nc, "mlstm_bias") as (block,):
            @block.vector
            def _(dve):
                nc.vector.tensor_scalar(f_bias[:], f_bias[:], -1.0, None, ALU.mult)
                nc.vector.memset(v[:, :, :, P:P + 1], 1.0)
        soft_maximum(nc, "mlstm_soft", [(f_row[:], sum_row[:], -1.0, f_bias[:], 0.0, 0.0)])
        top_row = f_row
        with stage(nc, "mlstm_gates", "ready") as (block, ready):
            @block.vector
            def _(dve):
                nc.vector.tensor_tensor_scan(sum_row[:], core.one_row[0:H, :], f_row[:], 0.0, ALU.mult, ALU.add)
                dve.drain()
                nc.vector.scalar_tensor_tensor(i_row[:], i_row[:], i_bias[:], sum_row[:], ALU.add, ALU.add)
                dve.drain()
                nc.vector.tensor_tensor_scan(top_row[:], core.one_row[0:H, :], i_row[:], -3e38, ALU.mult, ALU.max)
                dve.drain()
                nc.vector.tensor_scalar(top_row[:], top_row[:], -1.0, None, ALU.mult)
                dve.drain()
                nc.vector.tensor_tensor(sum_row[:], sum_row[:], top_row[:], ALU.add).then_inc(ready, 1)

            @block.scalar
            def _(act):
                act.wait_ge(ready, 1)
                nc.scalar.activation(sum_row[:], sum_row[:], ACT.Exp)
        row_columns(nc, core, "mlstm_cols", [i_row, sum_row], cols, H)
        half = lambda h: slice(h % 2 * M_DQK, (h % 2 + 1) * M_DQK)
        out = core.ps[:, 5:7, 0:2 * (P + 1)].rearrange("p b (t f) -> p b t f", t=2)

        def finish(dve, h):
            floor = cols[:, 1, h, :].rearrange("p (b t) -> p b t", b=2)
            nc.vector.scalar_tensor_tensor(den[:, :, :, 0], out[:, :, :, P], -1.0, floor, ALU.mult, ALU.max)
            dve.drain()
            nc.vector.tensor_tensor(den[:, :, :, 0], den[:, :, :, 0], out[:, :, :, P], ALU.max)
            dve.drain()
            nc.vector.reciprocal(den[:], den[:])
            dve.drain()
            return nc.vector.tensor_tensor(y[:, :, h * P:(h + 1) * P].rearrange("p (b t) f -> p b t f", b=2), out[:, :, :, 0:P],
                                           den[:].to_broadcast([P, 2, 2, P]), ALU.mult)

        causal_heads(nc, core, "mlstm", H, top_row[:], lambda h, s: cols[:, 0, h, s:s + 1],
                     lambda h, s: qkT[half(h), H // 2 + h // 2, s * P:(s + 1) * P], lambda h, lo: qkT[half(h), h // 2, lo:],
                     1, lambda h, s: M_DQK ** -0.5, lambda h, s: v[:, s, h, :], lambda t: out[:, t // 2, t % 2, :], finish)


def mamba_branch(nc, core, d, y):
    H, tiles = S_HEADS, 2 * KD
    with buffers(nc, xbc=[P, tiles, SEQ], dt_row=[H, SEQ], cs_row=[H, SEQ], dt_bias=[H, 1], a_rate=[H, 1], skip=[P, H],
                 cols=[P, 2, H, NT]) as (xbc, dt_row, cs_row, dt_bias, a_rate, skip, cols):
        with buffers(nc, taps=[P, 4, tiles], conv_bias=[P, tiles]) as (taps, conv_bias):
            project(nc, core, "mamba_in", core.hT, [
                ("xbc", 4, "feature", ("conv", taps, conv_bias, 4, feature_tiles(xbc))),
                ("sdt", 1, [(0, H)], ("act", ACT.Copy, row_buffers(dt_row)))],
                    loads=[(taps[:], d["s_conv_c_3"]), (conv_bias[:], d["s_conv_b_c_3"]), (dt_bias[:], d["s_dt_bias_c_3"]),
                           (a_rate[:], d["s_a_log_c_3"]), (skip[:], d["s_d_3"][0, :].partition_broadcast(P))])
        soft_maximum(nc, "mamba_soft", [(dt_row[:], cs_row[:], 1.0, dt_bias[:], 0.0, 0.0)])
        with buffers(nc, rates=[H, SEQ]) as (rates,):
            with stage(nc, "mamba_decay", "ready") as (block, ready):
                @block.scalar
                def _(act):
                    nc.scalar.activation(a_rate[:], a_rate[:], ACT.Exp).then_inc(ready, 1)

                @block.vector
                def _(dve):
                    dve.wait_ge(ready, 1)
                    nc.vector.tensor_scalar(rates[:], dt_row[:], a_rate[:], -1.0, ALU.mult, ALU.mult)
                    dve.drain()
                    nc.vector.tensor_tensor_scan(cs_row[:], core.one_row[0:H, :], rates[:], 0.0, ALU.mult, ALU.add)
            row_columns(nc, core, "mamba_cols", [dt_row, cs_row], cols, H)
            with stage(nc, "mamba_values", "turned") as (block, turned):
                @block.tensor
                def _(pe):
                    for t in range(NT):
                        for f in range(KD):
                            mm = nc.tensor.transpose(core.ps[:, 2 * t + f // 4, f % 4 * P:(f % 4 + 1) * P], xbc[:, f, t * P:(t + 1) * P], core.ident[:])
                        mm.then_inc(turned, 1)

                @block.scalar
                def _(act):
                    for t in range(NT):
                        act.wait_ge(turned, t + 1)
                        nc.scalar.copy(y[:, t, :].rearrange("p (b f) -> p b f", b=2), core.ps[:, 2 * t:2 * t + 2, :])

                @block.vector
                def _(dve):
                    nc.vector.tensor_scalar(cols[:, 1], cols[:, 1], -1.0, None, ALU.mult)
            share = H // S_GROUPS
            span = lambda h: slice(h * S_HEADDIM, (h + 1) * S_HEADDIM)

            def finish(dve, h):
                return nc.vector.scalar_tensor_tensor(y[:, :, span(h)], y[:, :, span(h)], skip[:, h:h + 1],
                                                      core.ps[:, 5, 0:NT * S_HEADDIM].rearrange("p (t f) -> p t f", t=NT), ALU.mult, ALU.add)

            causal_heads(nc, core, "mamba", H, cs_row[:], lambda h, s: cols[:, 1, h, s:s + 1],
                         lambda h, s: xbc[:, KD + h // share, s * P:(s + 1) * P], lambda h, lo: xbc[:, KD + S_GROUPS + h // share, lo:],
                         share, lambda h, s: cols[:, 0, h, s:s + 1], lambda h, s: y[:, s, span(h)], lambda t: core.ps[:, 5, t * S_HEADDIM:(t + 1) * S_HEADDIM], finish)


def third_mixer(nc, core, d):
    with buffers(nc, y=[P, NT, D]) as (y,):
        def close(name, gain_name, gate_plan, share_plan, out_plan, width, first):
            with buffers(nc, yT=([P, 2, KD, SEQ], F32R), share=[P, NT, D]) as (yT, share):
                gate = over(nc, yT, "gate", [P, NT, D])
                project(nc, core, f"{name}_gates", core.hT, [(gate_plan, 2, "token", ("act", ACT.Sigmoid if first else ACT.Silu, columns(gate))),
                                                             (share_plan, 2, "token", ("act", ACT.Sigmoid, columns(share)))],
                        loads=[(core.row_a[:], d[gain_name][0, :].partition_broadcast(P))],
                        beside=gated_heads(nc, core, y, gate if first else None, core.row_a[:], width, None if first else gate))
                transpose(nc, core, f"{name}_T", y, two_parts(yT))
                project(nc, core, f"{name}_out", two_parts(yT), [(out_plan, 2, "token", ("mul" if first else "mad", columns(share), columns(core.x)))])

        mlstm_branch(nc, core, d, y)
        close("mlstm", "m_norm_g_3", "mo", "ga", "pa", P, True)
        mamba_branch(nc, core, d, y)
        close("mamba", "s_norm_g_3", "sz", "gb", "pb", D // S_GROUPS, False)
    with buffers(nc, yT=([P, 2, KD, SEQ], F32R)) as (yT,):
        transpose(nc, core, "mix3_T", core.x, two_parts(yT))
        project(nc, core, "out3", two_parts(yT), [("out3", 2, "token", ("axpy", ALPHA, columns(core.h)))])


def conv_ffn(nc, core, d):
    first = take(core, "up", FF_CHUNKS)
    with buffers(nc, taps=[P, 2, 3, FF_TILES], conv_bias=[P, 2, FF_TILES], hidden=[P, FF_TILES, SEQ], gate=[P, 2, 2, SEQ]) as (
            taps, conv_bias, hidden, gate):
        load_rows(nc, "ffn_loads", [(taps[:], d["f_conv_c_3"]), (conv_bias[:], d["f_conv_b_c_3"])])
        value = core.tmp[:].rearrange("p (a f) n -> p a f n", a=2)

        def chunk_parts(j):
            half = D_FF % 256 if isinstance(j, int) else 256
            return 2 * half, [(part, f, part * half + f * P, min(P, half - f * P)) for part in range(2) for f in range(2)]

        start = plan_splits(core, 2 * core.taken + 1)
        idle = lambda turn, odd: turn - (first + (first % 2 != odd)) // 2 + 1
        with stage(nc, "ffn_up", "free0", "free1", "convolved", "activated") as (block, free0, free1, convolved, activated):
            free = (free0, free1)

            @block.sync
            def _(sp):
                load_ahead(core, sp, core.splits + 2)

            @block.tensor
            def _(pe):
                for j, turn, odd, c in pairs(pe, first, FF_CHUNKS):
                    pe.wait_ge(free[odd], idle(turn, odd))
                    width, parts = chunk_parts(j)
                    for half in range(2):
                        pe.wait_ge(core.split[half], c + 1)
                        w = weights(core, half, P, KD // 2, width)
                        for part, f, lo, m in parts:
                            for k in range(KD // 2):
                                kk = half * KD // 2 + k
                                mm = product(nc, core.ps[0:m, 4 * odd + 2 * part + f, :], [v[:, k, lo:lo + m] for v in w],
                                             halves(core.hT, kk, slice(None)), kk == 0, kk == KD - 1)
                            if half == 1:
                                mm.then_inc(core.products, 1)
                        if half == 0:
                            mm.then_inc(core.used, 1)

            @block.vector
            def _(dve):
                dve.sem_inc(free0, 1)
                dve.sem_inc(free1, 1)
                split_first(nc, core, dve, start, first)
                for j, _, odd, c in pairs(dve, first, FF_CHUNKS):
                    split_piece(nc, core, dve, c + 1, 0)
                    if not isinstance(c, int):
                        split_piece(nc, core, dve, c + 1, 1)
                    for part, f, _, m in chunk_parts(j)[1]:
                        dve.wait_ge(core.products, QUARTERS * c + 2 * part + f + 1)
                        done = convolve(nc, dve, core.ps[0:m, 4 * odd + 2 * part + f, :], taps[:, part], conv_bias[:, part], 3,
                                        2 * j + f, (gate, value)[part][0:m, odd, f, :])
                        if part == 0:
                            done.then_inc(convolved, 1)
                    dve.drain().then_inc(free[odd], 1)
                    for _, f, _, m in chunk_parts(j)[1][0:2]:
                        dve.wait_ge(activated, 2 * j + f + 1)
                        nc.vector.tensor_tensor(hidden[0:m, bass.ds(2 * j + f, 1), :].rearrange("p o n -> p (o n)"),
                                                gate[0:m, odd, f, :], value[0:m, odd, f, :], ALU.mult)

            @block.scalar
            def _(act):
                for j, _, odd, c in pairs(act, first, FF_CHUNKS):
                    for _, f, _, m in chunk_parts(j)[1][0:2]:
                        act.wait_ge(convolved, 2 * j + f + 1)
                        nc.scalar.activation(gate[0:m, odd, f, :], gate[0:m, odd, f, :], ACT.Silu).then_inc(activated, 1)

        chunks = -(-FF_TILES // 4)
        down = take(core, "down", chunks)
        start = plan_splits(core, 2 * core.taken)
        high = over(nc, core.h, "hidden_high", [P, 8, SEQ], F32R)
        low = over(nc, core.hT_whole, "hidden_low", [P, 8, SEQ], F32R)
        tile_rows = lambda k: min(P, D_FF - k * P)
        chunk_tiles = lambda j: range(4 * j, min(4 * j + 4, FF_TILES))
        with stage(nc, "ffn_down", "hidden_split") as (block, hidden_split):
            @block.sync
            def _(sp):
                load_ahead(core, sp, core.splits + 2)

            @block.tensor
            def _(pe):
                for j in range(chunks):
                    for half in range(2):
                        pe.wait_ge(core.split[half], down + j + 1)
                        m, k2, _ = core.plan[down + j][1][half].shape
                        w = weights(core, half, m, k2, D)
                        tiles = [4 * j + half * k2 + k for k in range(k2)]
                        pe.wait_ge(hidden_split, tiles[-1] + 1)
                        for t in range(NT):
                            for side in range(2):
                                for k, tile in enumerate(tiles):
                                    mm = product(nc, core.ps[:, 2 * t + side, :], [v[0:m, tile % 8, t * P:(t + 1) * P] for v in (high, low)],
                                                 [v[:, k, side * BANK:(side + 1) * BANK] for v in w], tile == 0, tile == FF_TILES - 1)
                            if half == 1:
                                mm.then_inc(core.products, 1)
                        if half == 0:
                            mm.then_inc(core.used, 1)

            @block.vector
            def _(dve):
                def split_hidden(j):
                    if j >= 2:
                        dve.wait_ge(core.products, QUARTERS * (down + j - 1))
                    for k in chunk_tiles(j):
                        m = tile_rows(k)
                        split(nc, dve, hidden[0:m, k, :], high[0:m, k % 8, :], low[0:m, k % 8, :]).then_inc(hidden_split, 1)

                split_first(nc, core, dve, start, down)
                split_hidden(0)
                for j in range(chunks - 1):
                    split_hidden(j + 1)
                    for half in range(2):
                        split_piece(nc, core, dve, down + j + 1, half)
                for t in range(NT):
                    dve.wait_ge(core.products, QUARTERS * (down + chunks - 1) + t + 1)
                    x = core.x[:, t, :].rearrange("p (b n) -> p b n", b=2)
                    nc.vector.scalar_tensor_tensor(x, x, ALPHA, core.ps[:, 2 * t:2 * t + 2, :], ALU.mult, ALU.add)


def third_block(nc, core, d):
    norm(nc, core, "norm0_3", core.x, core.h, core.hT, 1e-5, False, core.row_a[:], core.row_b[:],
         [(core.row_a[:], d["in_ln_g_3"]), (core.row_b[:], d["in_ln_b_3"])])
    third_mixer(nc, core, d)
    norm(nc, core, "norm1_3", core.h, core.x, core.hT, 1e-5, False, core.row_a[:], core.row_b[:],
         [(core.row_a[:], d["ln1_g_3"][0]), (core.row_b[:], d["ln1_b_3"][0])])
    conv_ffn(nc, core, d)
    norm(nc, core, "norm2_3", core.x, core.x, None, 1e-5, False, core.row_a[:], core.row_b[:],
         [(core.row_a[:], d["ln2_g_3"][0]), (core.row_b[:], d["ln2_b_3"][0])])


def plan_three(d):
    w = d["w_in_3"][0]
    plan = []
    add = lambda name, m, lo, n: plan.extend((name, kmajor(m, lo + i * BANK, BANK)) for i in range(n))
    add("mqk", w, 0, 2)
    add("mv", w, 1024, 2)
    plan.append(("mif", kmajor(w, 3072, 2 * M_HEADS)))
    add("mo", w, 2048, 2)
    add("ga", w, 6176, 2)
    add("pa", d["p_a_3"][0], 0, 2)
    add("xbc", w, 4112, 4)
    plan.append(("sdt", kmajor(w, 6160, S_HEADS)))
    add("sz", w, 3088, 2)
    add("gb", w, 7200, 2)
    add("pb", d["p_b_3"][0], 0, 2)
    add("out3", d["w_out_3"][0], 0, 2)
    plan += [("up", kmajor(d["w_up_pairs_3"], c * BANK, min(BANK, 2 * D_FF - c * BANK))) for c in range(FF_CHUNKS)]
    rows = d["w_down_3"][0]
    tiles = lambda lo, hi: rows[lo * P:hi * P, :].rearrange("(k p) n -> p k n", p=P)
    plan += [("down", [tiles(4 * c, 4 * c + 2), tiles(4 * c + 2, 4 * c + 4)]) for c in range(5)]
    plan += [("down", [tiles(20, 21), rows[21 * P:D_FF, :].rearrange("(k p) n -> p k n", p=D_FF % P)])]
    return plan


def build(nc, d, out, blocks):
    core = Core()
    core.plan, core.loaded, core.taken, core.splits = [], 0, 0, 0
    if 1 in blocks:
        core.plan += plan_one(d)
    if 2 in blocks:
        core.plan += plan_two(d)
    if 3 in blocks:
        core.plan += plan_three(d)
    else:
        core.plan += plan_two(d)[0:1]
    with ExitStack() as ctx:
        sb = lambda n, s, dt=F32: place(nc, ctx, n, s, dt)
        core.x = sb("x_tokens", [P, NT, D])
        core.h = sb("h_tokens", [P, NT, D])
        core.hT_whole = sb("h_features", [P, 2, KD, SEQ], F32R)
        core.hT = two_parts(core.hT_whole)
        core.raw = sb("ring_raw", [P, 2, PIECE])
        core.high = sb("ring_high", [P, 2, PIECE], F32R)
        core.low = sb("ring_low", [P, 2, PIECE], F32R)
        core.ident = sb("ident", [P, P])
        core.row_a = sb("row_a", [P, D])
        core.row_b = sb("row_b", [P, D])
        core.tmp = sb("evacuation_tmp", [P, NT, BANK])
        core.bn = sb("bn_parts", [P, 32, 6])
        core.mv = sb("mean_var", [P, 32, 2])
        core.minus_half = sb("minus_half", [P, 32, 1])
        core.ps = ctx.enter_context(nc.psum_tensor("psum", [P, 8, BANK], F32))
        sem = lambda n: ctx.enter_context(nc.semaphore(n))
        core.landed = [sem(f"piece_landed{h}") for h in range(2)]
        core.split = [sem(f"piece_split{h}") for h in range(2)]
        core.used = sem("half_used")
        core.products = sem("products")
        stored = sem("stored")

        with stage(nc, "start", "zeroed") as (block, zeroed):
            @block.gpsimd
            def _(pool):
                nc.gpsimd.memset(core.minus_half[:], -0.5)
                nc.gpsimd.memset(core.ident[:], 0.0).then_inc(zeroed, 1)
                pool.wait_ge(zeroed, 1)
                nc.gpsimd.affine_select(out=core.ident[:], in_=core.ident[:], compare_op=ALU.not_equal, fill=1.0,
                                        base=0, pattern=[[-1, P]], channel_multiplier=1)

            @block.sync
            def _(sp):
                load_ahead(core, sp, 2)
        if 1 in blocks:
            block_one(nc, core, d)
        else:
            load_rows(nc, "x_load", [(core.x[:], d["x"].rearrange("b (t p) f -> p (b t) f", p=P))])
        core.ones = sb("ones", [P, P])
        core.causal = sb("causal", [P, P])
        core.one_row = sb("one_row", [16, SEQ])
        core.tile_row = sb("tile_row", [P, SEQ])
        with stage(nc, "later_start", "zeroed") as (block, zeroed):
            @block.gpsimd
            def _(pool):
                nc.gpsimd.memset(core.ones[:], 1.0)
                nc.gpsimd.memset(core.one_row[:], 1.0)
                nc.gpsimd.memset(core.causal[:], 0.0)
                nc.gpsimd.memset(core.tile_row[:], 1.0).then_inc(zeroed, 1)
                pool.wait_ge(zeroed, 1)
                nc.gpsimd.affine_select(out=core.causal[:], in_=core.causal[:], compare_op=ALU.is_ge, fill=-1e30,
                                        base=0, pattern=[[1, P]], channel_multiplier=-1)
                nc.gpsimd.memset(core.tile_row[:].rearrange("p (t n) -> p t n", t=NT)[:, :, 0], 0.0)
        if 2 in blocks:
            second_block(nc, core, d)
        if 3 in blocks:
            third_block(nc, core, d)
        with nc.Block() as block:
            @block.sync
            def _(sp):
                sp.dma_start(out.rearrange("b (t p) f -> p (b t) f", p=P), core.x[:]).then_inc(stored, 16)
                sp.wait_ge(stored, 16)


def constants():
    half = RET_QK_DIM // 2
    inv = np.float32(10000.0) ** (-np.arange(half, dtype=np.float32) * np.float32(2.0) / np.float32(RET_QK_DIM))
    ang = np.arange(SEQ, dtype=np.float32)[:, None] * inv[None, :]
    tokens = lambda a: np.ascontiguousarray(a.reshape(NT, P, -1).transpose(1, 0, 2)).astype(np.float32)
    gamma = 1.0 - 2.0 ** (-5.0 - np.arange(RET_HEADS, dtype=np.float64))
    lag = np.arange(SEQ)[None, :] - np.arange(P)[:, None]
    decay = np.where(lag[:, None, :] >= 0, gamma[None, :, None] ** np.maximum(lag, 0)[:, None, :], 0.0)
    row = np.arange(P)
    levels = [(row[:, None] // (2 * b) == row[None, :] // (2 * b)) & (row[:, None] % (2 * b) < b) & (row[None, :] % (2 * b) >= b)
              for b in (2 ** n for n in range(LEVELS))]
    own = (row[:, None] // SUB == row[None, :] // SUB) & (row[None, :] >= row[:, None])
    sums = np.broadcast_to(np.arange(P + SUB)[None, :] % SUB == SUB - 1, (P, P + SUB))
    order = np.arange(MEMBERS)
    later = {"const_levels": np.stack(levels, 1), "const_own_block": own, "const_sums": sums,
             "const_before": order[None, :] < order[:, None]}
    later = {k: np.ascontiguousarray(v).astype(np.float32) for k, v in later.items()}
    return {**later, "const_cos": tokens(np.cos(ang)), "const_sin": tokens(np.sin(ang)),
            "const_ret_decay": decay.astype(np.float32)}


def column_tiles(v):
    return np.ascontiguousarray(v.reshape(-1, P).T)


def laid_out(inputs):
    a = {k: np.ascontiguousarray(v) for k, v in inputs.items()}
    a["sgu_w_t"] = np.ascontiguousarray(np.transpose(a.pop("sgu_w")[0], (2, 0, 1)))
    a["sgu_b_t"] = np.ascontiguousarray(a.pop("sgu_b")[0].T)
    a["sub_keys_t"] = np.ascontiguousarray(
        np.transpose(a.pop("peer_sub_keys")[0].reshape(PAIRS, PEER_KEYS, P), (2, 0, 1)))
    a["c_col"] = column_tiles(a.pop("c")[0])
    a["gdn_conv_c_2"] = np.stack([column_tiles(tap) for tap in a.pop("gdn_conv_2")[0]], 1)
    a["gdn_dt_bias_c_2"] = a.pop("gdn_dt_bias_2").reshape(-1, 1)
    a["gdn_a_log_c_2"] = a.pop("gdn_a_log_2").reshape(-1, 1)
    a["gla_b2_c_2"] = column_tiles(a.pop("gla_b2_2")[0])
    a["hgrn_lb_c_2"] = column_tiles(a.pop("hgrn_lb_logits_2")[0])
    a["w_gate_up_2"] = np.concatenate([a.pop("w_gate_2")[0], a.pop("w_up_2")[0]], -1)
    taps = lambda w: np.stack([column_tiles(tap) for tap in w], 1)
    for name in ("m_conv", "s_conv"):
        a[f"{name}_c_3"] = taps(a.pop(f"{name}_w_3")[0])
        a[f"{name}_b_c_3"] = column_tiles(a.pop(f"{name}_b_3")[0])
    for name in ("m_i_bias", "m_f_bias", "s_dt_bias", "s_a_log"):
        a[f"{name}_c_3"] = a.pop(f"{name}_3").reshape(-1, 1)
    gate_value = lambda v: (v[..., :D_FF], v[..., D_FF:])
    whole = lambda v: np.pad(v, [(0, 0)] * (v.ndim - 1) + [(0, FF_TILES * P - D_FF)])
    a["f_conv_c_3"] = np.stack([taps(whole(w)) for w in gate_value(a.pop("f_conv_w_3")[0])], 1)
    a["f_conv_b_c_3"] = np.stack([column_tiles(whole(v)) for v in gate_value(a.pop("f_conv_b_3")[0])], 1)
    up = gate_value(a.pop("w_up_3")[0])
    a["w_up_pairs_3"] = np.concatenate([half[:, lo:lo + 256] for lo in range(0, D_FF, 256) for half in up], 1)
    a.update(constants())
    return a


def kernel(**inputs):
    import concourse.bacc as bacc
    from concourse.bass_utils import run_bass_kernel_spmd as run

    nc = bacc.Bacc("TRN2", target_bir_lowering=False, num_devices=1)
    arrays = {f"in_{k}": v for k, v in laid_out(inputs).items()}
    d = {k[3:]: nc.dram_tensor(k, v.shape, mybir.dt.from_np(v.dtype), kind="ExternalInput").ap() for k, v in arrays.items()}
    out = nc.dram_tensor("out_0", (1, SEQ, D), F32, kind="ExternalOutput").ap()
    build(nc, d, out, BLOCKS)
    return run(nc, [arrays], core_ids=[0]).results[0]["out_0"]
```

```python
from contextlib import ExitStack, contextmanager
from itertools import count

import numpy as np
import concourse.bass as bass
from concourse import mybir

F32 = mybir.dt.float32
U32 = mybir.dt.uint32
F32R = mybir.dt.float32r
ACT = mybir.ActivationFunctionType
ALU = mybir.AluOpType
AX = mybir.AxisListType

P = 128
SEQ = 512
NT = SEQ // P
D = 1024
KD = D // P
BANK = 512
QUARTERS = 4
PLACES = {}
NUMBERS = count()
PIECE = KD // 2 * BANK
SLOTS = 4
ALPHA = 2.0 ** 0.25


class Core:
    pass


@contextmanager
def stage(nc, name, *signals):
    sems = [nc.alloc_semaphore(f"{name}_{s}") for s in signals]
    with nc.Block() as block:
        yield (block, *sems)
    if sems:
        nc.clear_and_free_semaphores(sems)
        nc.all_engine_barrier()


@contextmanager
def buffers(nc, **shapes):
    with ExitStack() as ctx:
        made = []
        for name, shape in shapes.items():
            shape, dtype = (shape, F32) if isinstance(shape, list) else shape
            made.append(place(nc, ctx, f"{name}_{next(NUMBERS)}", shape, dtype))
        yield made


def place(nc, ctx, name, shape, dtype):
    tensor = ctx.enter_context(nc.sbuf_tensor(name, shape, dtype))
    PLACES[tensor.name] = nc.sbuf_base - 4 * int(np.prod(shape[1:]))
    return tensor


def over(nc, under, name, shape, dtype=F32):
    return nc.alloc_sbuf_tensor_at(f"{name}_{next(NUMBERS)}", shape, dtype, offset=PLACES[under.name])


def kmajor(w, lo, width):
    cut = w[:, lo:lo + width].rearrange("(k p) n -> p k n", p=P)
    half = cut.shape[1] // 2
    return [cut[:, 0:half, :], cut[:, half:, :]]


def load_ahead(core, sp, end):
    while core.loaded < min(end, 2 * len(core.plan)):
        c, half = divmod(core.loaded, 2)
        src = core.plan[c][1][half]
        if c:
            sp.wait_ge(core.split[half], c)
        sp.dma_start(piece(core.raw, half, *src.shape), src).then_inc(core.landed[half], 16)
        core.loaded += 1


def piece(buf, half, p, k, n):
    return buf[0:p, half, 0:k * n].rearrange("p (k n) -> p k n", k=k)


def weights(core, half, p, k, n):
    return [piece(part, half, p, k, n) for part in (core.high, core.low)]


def take(core, name, number):
    first = core.taken
    assert all(core.plan[first + i][0] == name for i in range(number)), (name, core.plan[first][0])
    core.taken += number
    return first


def plan_splits(core, end):
    start, core.splits = core.splits, min(end, 2 * len(core.plan))
    return start


def split(nc, dve, whole, high, low):
    nc.vector.tensor_copy(high, whole)
    dve.drain()
    return nc.vector.tensor_tensor(low, whole, high.bitcast(F32), ALU.subtract)


def split_piece(nc, core, dve, c, half, cols=PIECE):
    if isinstance(c, int):
        if c >= len(core.plan):
            return
        cols = core.plan[c][1][half].shape[1] * core.plan[c][1][half].shape[2]
    dve.wait_ge(core.landed[half], 16 * (c + 1))
    if not isinstance(c, int) or c > 0:
        if half == 0:
            dve.wait_ge(core.used, c)
        else:
            dve.wait_ge(core.products, QUARTERS * c)
    split(nc, dve, core.raw[:, half, 0:cols], core.high[:, half, 0:cols], core.low[:, half, 0:cols]).then_inc(core.split[half], 1)


def split_first(nc, core, dve, start, first):
    for p in range(start, 2 * first + 2):
        split_piece(nc, core, dve, p // 2, p % 2)


def product(nc, out, a, b, start, stop):
    nc.tensor.matmul(out, a[0], b[0], start=start, stop=False)
    nc.tensor.matmul(out, a[0], b[1], start=False, stop=False)
    return nc.tensor.matmul(out, a[1], b[0], start=False, stop=stop)


def two_parts(buf):
    return buf[:, 0], buf[:, 1]


def halves(parts, *index):
    return [part[(slice(None),) + index] for part in parts]


def pairs(eng, first, number):
    loops = number // 2 if number >= 4 else 0
    if loops:
        with eng.Fori(0, loops) as i:
            for u in range(2):
                yield 2 * i + u, (first + u) // 2 + i, (first + u) % 2, first + u + 2 * i
    for j in range(2 * loops, number):
        c = first + j
        yield j, c // 2, c % 2, c


def project(nc, core, name, xT, runs, kt=KD, loads=(), beside=None):
    firsts = [take(core, r[0], r[1]) for r in runs]
    base = firsts[0]
    looped = runs[-1][1] >= 4 and runs[-1][1] % 2 == 0
    start = plan_splits(core, 2 * core.taken + (2 if looped else 1))
    idle = lambda turn, odd: turn - (base + (base % 2 != odd)) // 2 + 1
    bank = lambda odd, t: core.ps[:, 4 * odd + t, :]
    with stage(nc, name, "free0", "free1", "convolved", "loaded", "first_run", "var_ready", "root_ready") as (
            block, free0, free1, convolved, loaded, first_run, var_ready, root_ready):
        free = (free0, free1)

        if beside is not None:
            @block.gpsimd
            def _(pool):
                beside[0](pool, var_ready, root_ready)

        @block.sync
        def _(sp):
            for dst, src in loads:
                sp.dma_start(dst, src).then_inc(loaded, 16)
            load_ahead(core, sp, core.splits + 2)

        @block.tensor
        def _(pe):
            for (_, number, layout, _), first in zip(runs, firsts):
                for _, turn, odd, c in pairs(pe, first, number):
                    pe.wait_ge(free[odd], idle(turn, odd))
                    for half in range(2):
                        pe.wait_ge(core.split[half], c + 1)
                        p, k2, width = core.plan[first][1][half].shape
                        w = weights(core, half, p, k2, width)
                        rows = isinstance(layout, list)
                        count = len(layout) if rows else NT
                        for t in range(count):
                            for k in range(k2):
                                kk = half * k2 + k
                                x = halves(xT, kk, slice(None))
                                if rows:
                                    lo, m = layout[t]
                                    a, b, out = [v[:, k, lo:lo + m] for v in w], x, bank(odd, t)[0:m, :]
                                elif layout == "feature":
                                    a, b, out = [v[:, k, t * P:(t + 1) * P] for v in w], x, bank(odd, t)
                                else:
                                    a, b, out = [v[:, t * P:(t + 1) * P] for v in x], [v[:, k, :] for v in w], bank(odd, t)
                                mm = product(nc, out, a, b, kk == 0, kk == kt - 1)
                            if half == 1:
                                mm.then_inc(core.products, QUARTERS - t if t == count - 1 else 1)
                        if half == 0:
                            mm.then_inc(core.used, 1)

        @block.vector
        def _(dve):
            dve.sem_inc(free[0], 1)
            dve.sem_inc(free[1], 1)
            split_first(nc, core, dve, start, base)
            if loads:
                dve.wait_ge(loaded, 16 * len(loads))
            if beside is not None and len(runs) == 1:
                beside[1](dve, var_ready, root_ready)
            for n, ((_, number, _, how), first) in enumerate(zip(runs, firsts)):
                if beside is not None and n == 1:
                    dve.wait_ge(first_run, 1)
                    beside[1](dve, var_ready, root_ready)
                for j, _, odd, c in pairs(dve, first, number):
                    split_piece(nc, core, dve, c + 1, 0)
                    if not isinstance(c, int) or c + 1 < core.taken:
                        split_piece(nc, core, dve, c + 1, 1)
                    if how[0] == "act":
                        continue
                    for t in range(NT):
                        psum, dest = bank(odd, t), how[-1](t, j)
                        dve.wait_ge(core.products, QUARTERS * c + t + 1)
                        if how[0] == "conv":
                            done = convolve(nc, dve, psum, how[1], how[2], how[3], 4 * j + t, dest)
                            done.then_inc(convolved, 1)
                            if t == NT - 1:
                                dve.drain().then_inc(free[odd], 1)
                            continue
                        if how[0] == "axpy":
                            done = nc.vector.scalar_tensor_tensor(dest, dest, how[1], psum, ALU.mult, ALU.add)
                        elif how[0] == "mul":
                            done = nc.vector.tensor_tensor(dest, psum, how[1](t, j), ALU.mult)
                        else:
                            done = nc.vector.tensor_tensor(core.tmp[:, t, :], psum, how[1](t, j), ALU.mult)
                        if t == NT - 1:
                            done.then_inc(free[odd], 1)
                        if how[0] == "mad":
                            dve.drain()
                            nc.vector.tensor_tensor(dest, dest, core.tmp[:, t, :], ALU.add)

        @block.scalar
        def _(act):
            convs = 0
            for (_, number, layout, how), first in zip(runs, firsts):
                if how[0] not in ("act", "conv"):
                    continue
                rows = isinstance(layout, list)
                for j, _, odd, c in pairs(act, first, number):
                    count = len(layout) if rows else NT
                    for t in range(count):
                        if how[0] == "conv":
                            act.wait_ge(convolved, convs + NT * j + t + 1)
                            nc.scalar.activation(how[-1](t, j), how[-1](t, j), ACT.Silu)
                            continue
                        act.wait_ge(core.products, QUARTERS * c + (QUARTERS if t == count - 1 else t + 1))
                        psum = bank(odd, t)[0:layout[t][1], :] if rows else bank(odd, t)
                        dest = how[2](t, j)
                        if len(dest.shape) == 3:
                            psum = psum.rearrange("p (h f) -> p h f", h=dest.shape[1])
                        done = nc.scalar.activation(dest, psum, how[1])
                        if t == count - 1:
                            done.then_inc(free[odd], 1)
                if how[0] == "conv":
                    convs += NT * number
                if beside is not None and first == base:
                    act.drain().then_inc(first_run, 1)


def convolve(nc, dve, u, taps, bias, width, f, out):
    m = u.shape[0]
    tap = lambda k: taps[0:m, k, bass.ds(f, 1)]
    if bias is None:
        nc.vector.tensor_scalar(out, u, tap(width - 1), None, ALU.mult)
    else:
        nc.vector.tensor_scalar(out, u, tap(width - 1), bias[0:m, bass.ds(f, 1)], ALU.mult, ALU.add)
    for back in range(1, width):
        dve.drain()
        done = nc.vector.scalar_tensor_tensor(out[:, back:], u[:, 0:SEQ - back], tap(width - 1 - back), out[:, back:], ALU.mult, ALU.add)
    return done


def columns(buf):
    return lambda t, j: buf[:, t, bass.ds(j * BANK, BANK)]


def feature_tiles(buf):
    return lambda t, j: buf[:, bass.ds(j * 4 + t, 1), :].rearrange("p o n -> p (o n)")


def row_buffers(*bufs):
    return lambda t, j: bufs[t][:]


def transpose_tile(nc, core, t, nf, src, transposed):
    groups = nf // 4
    for half in range(groups):
        bank = (groups * t + half) % 8
        for q in range(4):
            f = 4 * half + q
            mm = nc.tensor.transpose(core.ps[:, bank, q * P:(q + 1) * P], src[:, t, f * P:(f + 1) * P], core.ident[:])
        mm.then_inc(transposed, 1)


def transposed_bank(nf, n):
    t, half = divmod(n, nf // 4)
    return (slice(None), slice(4 * half, 4 * half + 4), slice(t * P, (t + 1) * P))


def transposed_view(core, n):
    return core.ps[:, n % 8, :].rearrange("p (f t) -> p f t", f=4)


def copy_transposed(nc, core, act, nf, dst, transposed, copied=None):
    for n in range(NT * nf // 4):
        act.wait_ge(transposed, n + 1)
        done = nc.scalar.copy(dst[transposed_bank(nf, n)], transposed_view(core, n))
        if copied is not None:
            done.then_inc(copied, 1)


def rest_of_transposed(nc, core, dve, nf, parts, copied):
    for n in range(NT * nf // 4):
        at = transposed_bank(nf, n)
        dve.wait_ge(copied, n + 1)
        nc.vector.tensor_tensor(parts[1][at], transposed_view(core, n), parts[0][at].bitcast(F32), ALU.subtract)


def transpose(nc, core, name, src, dst, nf=KD):
    with stage(nc, name, "transposed", "copied") as (block, transposed, copied):
        @block.tensor
        def _(pe):
            for t in range(NT):
                transpose_tile(nc, core, t, nf, src, transposed)

        @block.scalar
        def _(act):
            copy_transposed(nc, core, act, nf, dst[0], transposed, copied)

        @block.vector
        def _(dve):
            rest_of_transposed(nc, core, dve, nf, dst, copied)


def row_stats(nc, core, dve, src, mv, width, groups, first=0):
    parts = max(1, width // BANK)
    w = width // parts
    for g in range(groups):
        for q in range(parts):
            nc.vector.bn_stats(core.bn[:, first + g * parts + q, :], src(g)[:, q * w:(q + 1) * w])
    dve.drain()
    for g in range(groups):
        nc.vector.bn_aggr(mv[:, g, :], core.bn[:, first + g * parts:first + (g + 1) * parts, :].rearrange("p q s -> p (q s)"))
    dve.drain()


def mean_square(nc, dve, mv):
    nc.vector.tensor_tensor(mv[:, :, 0:1], mv[:, :, 0:1], mv[:, :, 0:1], ALU.mult)
    dve.drain()
    nc.vector.tensor_tensor(mv[:, :, 1:2], mv[:, :, 1:2], mv[:, :, 0:1], ALU.add)
    dve.drain()


def inverse_root(nc, core, pool, v, eps, ready, done, number=0):
    pool.wait_ge(ready, number + 1)
    nc.gpsimd.tensor_scalar(v, v, eps, None, ALU.add).then_inc(done, 1)
    pool.wait_ge(done, 2 * number + 1)
    nc.gpsimd.tensor_tensor(v, v, core.minus_half[:, 0:v.shape[1], :], ALU.pow).then_inc(done, 1)


def norm(nc, core, name, src, dst, dstT, eps, rms, gain, shift, rows=()):
    with stage(nc, name, "rows_loaded", "var_ready", "root_ready", "scaled_ready", "centred", "gained", "normed", "transposed", "copied") as (
            block, rows_loaded, var_ready, root_ready, scaled_ready, centred, gained, normed, transposed, copied):
        mv = core.mv[:, 0:NT, :]
        last_done = normed if shift is None else gained

        @block.gpsimd
        def _(pool):
            for step in range(NT + 2):
                if step < NT:
                    inverse_root(nc, core, pool, mv[:, step:step + 1, 1:2], eps, var_ready, root_ready, step)
                if step >= 2 and shift is not None:
                    t = step - 2
                    pool.wait_ge(gained, t + 1)
                    nc.gpsimd.tensor_tensor(dst[:, t, :], dst[:, t, :], shift, ALU.add).then_inc(normed, 1)

        if rows:
            @block.sync
            def _(sp):
                for buf, vec in rows:
                    sp.dma_start(buf, vec.partition_broadcast(P)).then_inc(rows_loaded, 16)

        @block.vector
        def _(dve):
            for step in range(NT + 2):
                if step < NT:
                    t = step
                    row_stats(nc, core, dve, lambda g: src[:, t, :], mv[:, t:t + 1, :], D, 1, 2 * t)
                    if rms:
                        mean_square(nc, dve, mv[:, t:t + 1, :])
                    dve.drain().then_inc(var_ready, 1)
                if 1 <= step <= NT:
                    t = step - 1
                    dve.wait_ge(root_ready, 2 * t + 2)
                    if not rms:
                        nc.vector.scalar_tensor_tensor(mv[:, t, 0:1], mv[:, t, 0:1], -1.0, mv[:, t, 1:2], ALU.mult, ALU.mult)
                    dve.drain().then_inc(scaled_ready, 1)
                if step >= 2:
                    t = step - 2
                    if rows and t == 0:
                        dve.wait_ge(rows_loaded, 16 * len(rows))
                    dve.wait_ge(centred, t + 1)
                    nc.vector.tensor_tensor(dst[:, t, :], dst[:, t, :], gain, ALU.mult).then_inc(last_done, 1)
            if dstT is not None:
                rest_of_transposed(nc, core, dve, KD, dstT, copied)

        @block.scalar
        def _(act):
            for t in range(NT):
                act.wait_ge(scaled_ready, t + 1)
                if rms:
                    nc.scalar.activation(dst[:, t, :], src[:, t, :], ACT.Copy, scale=mv[:, t, 1:2]).then_inc(centred, 1)
                else:
                    nc.scalar.activation(dst[:, t, :], src[:, t, :], ACT.Identity, bias=mv[:, t, 0:1], scale=mv[:, t, 1:2]).then_inc(centred, 1)
            if dstT is not None:
                copy_transposed(nc, core, act, KD, dstT[0], transposed, copied)

        if dstT is not None:
            @block.tensor
            def _(pe):
                for t in range(NT):
                    pe.wait_ge(normed, t + 1)
                    transpose_tile(nc, core, t, KD, dst, transposed)


RET_HEADS, RET_DV = 4, 256
RET_QK_DIM = 128
SGU_GROUPS, SGU_DIM = 4, 256


def adaptive_rows(nc, core, d, mod, norm1_gain, norm2_gain):
    chunks = 6 * D // BANK
    pieces = [half for j in range(chunks) for half in kmajor(d["w_ada"][0], j * BANK, BANK)]
    ring = over(nc, core.hT_whole, "ada_ring", [P, SLOTS, PIECE])
    with buffers(nc, c_col=[P, KD], c_silu=[P, KD], c_rep=[P, KD, P]) as (c_col, c_silu, c_rep), \
            stage(nc, "ada", "c_loaded", "bias_loaded", "rest_loaded", "silu_done", "c_ready", "multiplied", "used", "evacuated",
                  *[f"landed{n}" for n in range(SLOTS)]) as (
                block, c_loaded, bias_loaded, rest_loaded, silu_done, c_ready, multiplied, used, evacuated, *landed):
        @block.sync
        def _(sp):
            for n, src in enumerate(pieces):
                if n >= SLOTS:
                    sp.wait_ge(used, n - SLOTS + 1)
                sp.dma_start(ring[:, n % SLOTS, :].rearrange("p (k n) -> p k n", k=KD // 2), src).then_inc(landed[n % SLOTS], 16)
            load_ahead(core, sp, core.splits + 2)

        @block.scalar
        def _(act):
            act.dma_start(c_col[:], d["c_col"]).then_inc(c_loaded, 16)
            act.dma_start(mod[:].rearrange("p a f -> p (a f)"), d["b_ada"][0, :].partition_broadcast(P)).then_inc(bias_loaded, 16)
            act.wait_ge(c_loaded, 16)
            nc.scalar.activation(c_silu[:], c_col[:], ACT.Silu).then_inc(silu_done, 1)
            act.wait_ge(multiplied, 3)
            act.dma_start(norm1_gain, d["norm1_g"][0, :].partition_broadcast(P)).then_inc(rest_loaded, 16)
            act.dma_start(norm2_gain, d["norm2_g"][0, :].partition_broadcast(P)).then_inc(rest_loaded, 16)
            act.wait_ge(multiplied, 6)
            act.dma_start(core.x[:], d["x"].rearrange("b (t p) f -> p (b t) f", p=P)).then_inc(rest_loaded, 16)

        @block.tensor
        def _(pe):
            pe.wait_ge(c_ready, 1)
            for c, turn, odd, _ in pairs(pe, 0, chunks):
                pe.wait_ge(evacuated, c + 1)
                for half in range(2):
                    slot = 2 * odd + half
                    pe.wait_ge(landed[slot], 16 * (turn + 1))
                    w = ring[:, slot, :].rearrange("p (k n) -> p k n", k=KD // 2)
                    for k in range(KD // 2):
                        kk = half * KD // 2 + k
                        mm = nc.tensor.matmul(core.ps[:, odd, :], c_rep[:, kk, :], w[:, k, :], start=kk == 0, stop=kk == KD - 1)
                    mm.then_inc(used, 1)
                    if half == 1:
                        pe.drain().then_inc(multiplied, 1)

        @block.vector
        def _(dve):
            dve.sem_inc(evacuated, 2)
            dve.wait_ge(silu_done, 1)
            nc.vector.tensor_copy(c_rep[:], c_silu[:].unsqueeze(2).to_broadcast([P, KD, P])).then_inc(c_ready, 1)
            dve.wait_ge(bias_loaded, 16)
            rows = mod[:].rearrange("p a f -> p (a f)")
            for j, _, odd, _ in pairs(dve, 0, chunks):
                dve.wait_ge(multiplied, j + 1)
                part = rows[:, bass.ds(j * BANK, BANK)]
                nc.vector.tensor_tensor(part, part, core.ps[:, odd, :], ALU.add).then_inc(evacuated, 1)
            dve.drain()
            dve.wait_ge(rest_loaded, 48)
            for which, gain in ((1, norm1_gain), (4, norm2_gain)):
                nc.vector.scalar_tensor_tensor(mod[:, which, :], mod[:, which, :], 1.0, gain, ALU.add, ALU.mult)


def retention(nc, core, d, qk, v, rot, qkT, y):
    H = RET_HEADS
    ra, rb, weights = core.row_b[:, 0:512], core.row_b[:, 512:1024], core.tmp
    decay = rot[:, :, 0:SEQ]
    with buffers(nc, cosine=[P, NT, 64], sine=[P, NT, 64]) as (cosine, sine):
        with stage(nc, "rotary", "tables", "rotated", "transposed") as (block, tables, rotated, transposed):
            @block.sync
            def _(sp):
                sp.dma_start(cosine[:], d["const_cos"]).then_inc(tables, 16)
                sp.dma_start(sine[:], d["const_sin"]).then_inc(tables, 16)
                sp.dma_start(core.row_a[:], d["ret_gn_g"][0, :].partition_broadcast(P)).then_inc(tables, 16)

            @block.vector
            def _(dve):
                dve.wait_ge(tables, 48)
                for t in range(NT):
                    heads = qk[:, t, :].rearrange("p (h a f) -> p h a f", a=2, f=64)
                    out = rot[:, t, :].rearrange("p (h a f) -> p h a f", a=2, f=64)
                    cos = cosine[:, t, :].unsqueeze(1).to_broadcast([P, 2 * H, 64])
                    sin = sine[:, t, :].unsqueeze(1).to_broadcast([P, 2 * H, 64])
                    a = ra.rearrange("p (h f) -> p h f", f=64)
                    b = rb.rearrange("p (h f) -> p h f", f=64)
                    nc.vector.tensor_tensor(out[:, :, 0, :], heads[:, :, 0, :], cos, ALU.mult)
                    nc.vector.tensor_tensor(out[:, :, 1, :], heads[:, :, 0, :], sin, ALU.mult)
                    nc.vector.tensor_tensor(a, heads[:, :, 1, :], sin, ALU.mult)
                    nc.vector.tensor_tensor(b, heads[:, :, 1, :], cos, ALU.mult)
                    dve.drain()
                    nc.vector.tensor_tensor(out[:, :, 0, :], out[:, :, 0, :], a, ALU.subtract)
                    nc.vector.tensor_tensor(out[:, :, 1, :], out[:, :, 1, :], b, ALU.add).then_inc(rotated, 1)
                    dve.drain()

            @block.tensor
            def _(pe):
                for t in range(NT):
                    pe.wait_ge(rotated, t + 1)
                    transpose_tile(nc, core, t, KD, rot, transposed)

            @block.scalar
            def _(act):
                copy_transposed(nc, core, act, KD, qkT, transposed)

        with stage(nc, "retain", "scores", "weighted", "summed", "copied", "decay_loaded") as (
                block, scores, weighted, summed, copied, decay_loaded):
            @block.sync
            def _(sp):
                sp.dma_start(decay, d["const_ret_decay"]).then_inc(decay_loaded, 16)

            @block.tensor
            def _(pe):
                for h in range(H):
                    if h >= 1:
                        pe.wait_ge(weighted, NT * h)
                    for s in range(NT):
                        nc.tensor.matmul(core.ps[:, s, 0:SEQ - s * P], qkT[:, H + h, s * P:(s + 1) * P],
                                         qkT[:, h, s * P:], start=True, stop=True).then_inc(scores, 1)
                    pe.wait_ge(weighted, NT * (h + 1))
                    if h >= 2:
                        pe.wait_ge(copied, h - 1)
                    for t in range(NT):
                        out = core.ps[:, 4 + 2 * (h % 2) + t // 2, (t % 2) * RET_DV:(t % 2 + 1) * RET_DV]
                        for s in range(t + 1):
                            mm = nc.tensor.matmul(out, weights[:, s, (t - s) * P:(t - s + 1) * P],
                                                  v[:, s, h * RET_DV:(h + 1) * RET_DV],
                                                  start=s == 0, stop=s == t)
                    mm.then_inc(summed, 1)

            @block.vector
            def _(dve):
                dve.wait_ge(decay_loaded, 16)
                for h in range(H):
                    if h >= 1:
                        dve.wait_ge(summed, h)
                    for s in range(NT):
                        n = SEQ - s * P
                        dve.wait_ge(scores, NT * h + s + 1)
                        nc.vector.scalar_tensor_tensor(weights[:, s, 0:n], core.ps[:, s, 0:n], RET_QK_DIM ** -0.5,
                                                       decay[:, h, 0:n], ALU.mult, ALU.mult).then_inc(weighted, 1)

            @block.scalar
            def _(act):
                for h in range(H):
                    act.wait_ge(summed, h + 1)
                    for q in range(2):
                        done = nc.scalar.copy(y[:, 2 * q:2 * q + 2, h * RET_DV:(h + 1) * RET_DV],
                                              core.ps[:, 4 + 2 * (h % 2) + q, :].rearrange("p (t f) -> p t f", t=2))
                    done.then_inc(copied, 1)


def head_norm(nc, core, y):
    n = NT * RET_HEADS
    mv = core.mv[:, 0:n, :]

    def pool_part(pool, var_ready, root_ready):
        inverse_root(nc, core, pool, mv[:, :, 1:2], 1e-6, var_ready, root_ready)

    def dve_part(dve, var_ready, root_ready):
        part = lambda g: y[:, g // RET_HEADS, (g % RET_HEADS) * RET_DV:(g % RET_HEADS + 1) * RET_DV]
        row_stats(nc, core, dve, part, mv, RET_DV, n)
        dve.drain().then_inc(var_ready, 1)
        dve.wait_ge(root_ready, 2)
        for g in range(n):
            nc.vector.tensor_scalar(part(g), part(g), mv[:, g, 0:1], mv[:, g, 1:2], ALU.subtract, ALU.mult)
        dve.drain()
        for t in range(NT):
            nc.vector.tensor_tensor(y[:, t, :], y[:, t, :], core.row_a[:], ALU.mult)
        dve.drain()

    return pool_part, dve_part


def spatial(nc, core, d, u, gates):
    with buffers(nc, mixer=[P, SGU_GROUPS, P], mixer_b=[P, SGU_GROUPS]) as (mixer, mixer_b), \
            stage(nc, "spatial", "loaded", "masked", "var_ready", "root_ready", "normed", "mixed") as (
                block, loaded, masked, var_ready, root_ready, normed, mixed):
        mv = core.mv[:, 0:NT, :]

        @block.sync
        def _(sp):
            sp.dma_start(core.row_a[:], d["sgu_ln_g"][0, :].partition_broadcast(P)).then_inc(loaded, 16)
            sp.dma_start(core.row_b[:], d["sgu_ln_b"][0, :].partition_broadcast(P)).then_inc(loaded, 16)
            sp.dma_start(mixer[:], d["sgu_w_t"]).then_inc(loaded, 16)
            sp.dma_start(mixer_b[:], d["sgu_b_t"]).then_inc(loaded, 16)

        @block.gpsimd
        def _(pool):
            pool.wait_ge(loaded, 64)
            nc.gpsimd.affine_select(out=mixer[:], in_=mixer[:], compare_op=ALU.is_ge, fill=0.0, base=0,
                                    pattern=[[0, SGU_GROUPS], [1, P]], channel_multiplier=-1).then_inc(masked, 1)
            inverse_root(nc, core, pool, mv[:, :, 1:2], 1e-6, var_ready, root_ready)

        @block.vector
        def _(dve):
            sv = lambda t: gates[:, t, :]
            row_stats(nc, core, dve, sv, mv, D, NT)
            dve.drain().then_inc(var_ready, 1)
            dve.wait_ge(root_ready, 2)
            dve.wait_ge(loaded, 64)
            for t in range(NT):
                nc.vector.tensor_scalar(sv(t), sv(t), mv[:, t, 0:1], mv[:, t, 1:2], ALU.subtract, ALU.mult)
                dve.drain()
                nc.vector.tensor_tensor(sv(t), sv(t), core.row_a[:], ALU.mult)
                dve.drain()
                nc.vector.tensor_tensor(sv(t), sv(t), core.row_b[:], ALU.add).then_inc(normed, 1)
            for t in range(NT):
                dve.wait_ge(mixed, t + 1)
                for g in range(SGU_GROUPS):
                    nc.vector.scalar_tensor_tensor(
                        u[:, t, g * SGU_DIM:(g + 1) * SGU_DIM],
                        core.ps[:, 2 * t + g // 2, (g % 2) * SGU_DIM:(g % 2 + 1) * SGU_DIM], mixer_b[:, g:g + 1],
                        u[:, t, g * SGU_DIM:(g + 1) * SGU_DIM], ALU.add, ALU.mult)

        @block.tensor
        def _(pe):
            pe.wait_ge(masked, 1)
            for t in range(NT):
                pe.wait_ge(normed, t + 1)
                for g in range(SGU_GROUPS):
                    mm = nc.tensor.matmul(core.ps[:, 2 * t + g // 2, (g % 2) * SGU_DIM:(g % 2 + 1) * SGU_DIM],
                                          mixer[:, g, :], gates[:, t, g * SGU_DIM:(g + 1) * SGU_DIM],
                                          start=True, stop=True)
                mm.then_inc(mixed, 1)


def gated_sum(nc, name, dst, gate, other, other_gate):
    with stage(nc, name, "scaled") as (block, scaled):
        @block.gpsimd
        def _(pool):
            for t in range(NT):
                nc.gpsimd.tensor_tensor(other[:, t, :], other[:, t, :], other_gate[:, t, :], ALU.mult).then_inc(scaled, 1)

        @block.vector
        def _(dve):
            for t in range(NT):
                nc.vector.tensor_tensor(dst[:, t, :], dst[:, t, :], gate[:, t, :], ALU.mult)
            dve.drain()
            for t in range(NT):
                dve.wait_ge(scaled, t + 1)
                nc.vector.tensor_tensor(dst[:, t, :], dst[:, t, :], other[:, t, :], ALU.add)


def multiply(nc, name, dst, other):
    with stage(nc, name) as (block,):
        @block.vector
        def _(dve):
            for t in range(NT):
                nc.vector.tensor_tensor(dst[:, t, :], dst[:, t, :], other[:, t, :], ALU.mult)


def first_mixer(nc, core, d, mod):
    norm(nc, core, "norm1", core.x, core.h, core.hT, 1e-6, True, mod[:, 1, :], mod[:, 0, :])
    with buffers(nc, a=[P, NT, D], b=[P, NT, D], c=[P, NT, D]) as (a, b, c):
        features = lambda buf: buf[:].rearrange("p t (q n) -> p (t q) n", n=SEQ)
        yT = over(nc, core.h, "yT_high", [P, KD, SEQ], F32R), over(nc, b, "yT_low", [P, KD, SEQ], F32R)
        project(nc, core, "in_qkv", core.hT, [("qk", 2, "token", ("act", ACT.Copy, columns(a))),
                                              ("v", 2, "token", ("act", ACT.Copy, columns(b)))])
        retention(nc, core, d, a, b, core.h, features(c), a)
        project(nc, core, "in_g", core.hT, [("g_ret", 2, "token", ("act", ACT.Silu, columns(c)))], beside=head_norm(nc, core, a))
        multiply(nc, "ret_gate", a, c)
        transpose(nc, core, "ret_T", a, yT)
        project(nc, core, "ret_out", yT, [("ret_out", 2, "token", ("act", ACT.Copy, columns(c)))])
        project(nc, core, "in_usv", core.hT, [("u", 2, "token", ("act", ACT.Gelu, columns(a))),
                                              ("sv", 2, "token", ("act", ACT.Gelu, columns(b)))])
        spatial(nc, core, d, a, b)
        transpose(nc, core, "sgu_T", a, yT)
        project(nc, core, "sgu_out", yT, [("sgu_out", 2, "token", ("act", ACT.Copy, columns(a)))])
        project(nc, core, "in_gates", core.hT, [("gate_a", 2, "token", ("act", ACT.Sigmoid, columns(b))),
                                                ("gate_b", 2, "token", ("act", ACT.Sigmoid, columns(core.h)))])
        gated_sum(nc, "merge", c, b, a, core.h)
        transpose(nc, core, "merge_T", c, yT)
        project(nc, core, "out1", yT, [("out1", 2, "token",
                                        ("mad", lambda t, j: mod[:, 2, bass.ds(j * BANK, BANK)], columns(core.x)))])


PEER_HEADS, PEER_KEYS, TOPK = 8, 128, 16
PICKS = PEER_HEADS * TOPK
PAIRS = 2 * PEER_HEADS
LOWEST = -3.0e38


def top8_first(nc, dve, n, values, spare, top, index):
    for g in range(n):
        nc.vector.max(top[:, g, 0:8], values(g))
    dve.drain()
    for g in range(n):
        nc.vector.max_index(index[:, g, 0:8], top[:, g, 0:8], values(g))
        nc.vector.match_replace(spare(g), top[:, g, 0:8], values(g), LOWEST)
    dve.drain()


def top8_second(nc, dve, n, spare, top, index):
    for g in range(n):
        nc.vector.max(top[:, g, 8:16], spare(g))
    dve.drain()
    for g in range(n):
        nc.vector.max_index(index[:, g, 8:16], top[:, g, 8:16], spare(g))
    dve.drain()


FETCH = 4
UNITS = 4
UNIT_PICKS = PICKS // UNITS
UNIT_GROUPS = UNIT_PICKS // FETCH
ROUTE_PARTS = 8


def peer(nc, core, d, qT, mod):
    H, K, G = PEER_HEADS, TOPK, UNIT_GROUPS
    rows_u, rows_v = d["peer_u"][0], d["peer_v"][0]
    gate2, product_tmp, got_u = mod[:, 5, :], mod[:, 4, :], mod[:, 0:FETCH, :]
    with buffers(nc, expert=([P, NT, PICKS], U32), sub_s=[P, PAIRS, K], sub_i=([P, PAIRS, K], U32), sub_f=[P, PAIRS, K],
                 top_i=([P, H, K], U32), digit=([P, PICKS], U32), digit_f=[P, PICKS], key_f=[P, 2, PICKS], steps=[P, K],
                 total=[P, H], top_s=[P, NT, H, K], dots=[P, 2, FETCH], score=[P, NT, PICKS], diagonal=[P, FETCH, P], zero=[P, P],
                 which_u=([P, 2, FETCH], U32), which_v=([P, 2, FETCH], U32)) as (
            expert, sub_s, sub_i, sub_f, top_i, digit, digit_f, key_f, steps, total, top_s, dots, score, diagonal, zero,
            which_u, which_v), \
            stage(nc, "peer", "keys_loaded", "steps_ready", "key_scored", "copied", "read", "shifted", "raised", "routed",
                  "staged_u", "staged_v", "used_u", "used_v", "scored", "activated", "weighted", "diagonals", "summed", "added",
                  "cleared", "asked", *[f"u_in{b}" for b in range(FETCH)], *[f"v_in{b}" for b in range(FETCH)]) as (
                block, keys_loaded, steps_ready, key_scored, copied, read, shifted, raised, routed, staged_u, staged_v,
                used_u, used_v, scored, activated, weighted, diagonals, summed, added, cleared, asked, *landed):
        u_in, v_in = landed[:FETCH], landed[FETCH:]
        room = over(nc, core.hT_whole, "route_room", [P, 4, PAIRS, PEER_KEYS])
        half_scores, half_rest, keysT = room[:, 0:2], room[:, 2], room[:, 3]
        got_v = over(nc, core.row_a, "got_v", [P, FETCH, D])
        cand = half_rest.rearrange("p g n -> p (g n)").rearrange("p (h i j) -> p h i j", h=H, i=K)

        @block.sync
        def _(sp):
            sp.dma_start(keysT, d["sub_keys_t"]).then_inc(keys_loaded, 16)

        @block.gpsimd
        def _(pool):
            nc.gpsimd.iota(steps[:], pattern=[[1, K]], base=0, channel_multiplier=0,
                           allow_small_or_imprecise_dtypes=True).then_inc(steps_ready, 1)
            nc.gpsimd.memset(zero[:], 0.0).then_inc(cleared, 1)

            def gather(unit, i, half, rows, got, which, staged, used, arrived):
                group = unit * G + 2 * i + half
                first = unit % UNITS * UNIT_PICKS + (2 * i + half) * FETCH
                nc.gpsimd.tensor_copy(which[:, half, :], expert[:, unit // UNITS, bass.ds(first, FETCH)]).then_inc(staged, 1)
                pool.wait_ge(staged, group + 1)
                for b in range(FETCH):
                    pool.wait_ge(used, group * FETCH + b + 1)
                    pool.sem_inc(asked, 1)
                    nc.gpsimd.indirect_dma_start(
                        out=got[:, b, :], out_offset=None, in_=rows,
                        in_offset=bass.IndirectOffsetOnAxis(ap=which[:, half, b:b + 1], axis=0),
                    ).then_inc(arrived[b], 16)

            for unit in range(NT * UNITS + 1):
                if unit < NT * UNITS and unit % UNITS == 0:
                    pool.wait_ge(routed, unit // UNITS + 1)
                with pool.Fori(0, G // 2) as i:
                    for half in range(2):
                        if unit < NT * UNITS:
                            gather(unit, i, half, rows_u, got_u, which_u, staged_u, used_u, u_in)
                        if unit >= 1:
                            gather(unit - 1, i, half, rows_v, got_v, which_v, staged_v, used_v, v_in)

        @block.vector
        def _(dve):
            rest_of = lambda t: half_scores[:, t % 2].rearrange("p g n -> p (g n)").rearrange("p (h n) -> p h n", h=H)
            sums = half_rest.rearrange("p g n -> p (g n)").rearrange("p (h n) -> p h n", h=H)
            ids = sub_f[:].rearrange("p (h a) k -> p h a k", a=2)

            def key_digit(a, op, by):
                nc.vector.tensor_single_scalar(digit[:], top_i[:].rearrange("p h k -> p (h k)"), by, op)
                dve.drain()
                nc.vector.tensor_copy(digit_f[:], digit[:])
                dve.drain()
                hit = cand.rearrange("p h i j -> p (h i) j")
                nc.vector.tensor_tensor(hit, steps[:].unsqueeze(1).to_broadcast([P, PICKS, K]),
                                        digit_f[:].unsqueeze(2).to_broadcast([P, PICKS, K]), ALU.is_equal)
                dve.drain()
                nc.vector.tensor_tensor(cand, cand, ids[:, :, a, :].unsqueeze(2).to_broadcast([P, H, K, K]), ALU.mult)
                dve.drain()
                nc.vector.tensor_reduce(key_f[:, a, :], hit, AX.X, ALU.add)
                dve.drain()

            def route(t, part):
                if part == 0:
                    dve.wait_ge(copied, 4 * (t + 1))
                    top8_first(nc, dve, PAIRS, lambda g: half_scores[:, t % 2, g, :], lambda g: half_rest[:, g, :], sub_s, sub_i)
                elif part == 1:
                    top8_second(nc, dve, PAIRS, lambda g: half_rest[:, g, :], sub_s, sub_i)
                elif part == 2:
                    nc.vector.tensor_copy(sub_f[:], sub_i[:])
                    half = sub_s[:].rearrange("p (h a) k -> p h a k", a=2)
                    nc.vector.tensor_tensor(cand, half[:, :, 0, :].unsqueeze(3).to_broadcast([P, H, K, K]),
                                            half[:, :, 1, :].unsqueeze(2).to_broadcast([P, H, K, K]), ALU.add)
                    dve.drain()
                elif part == 3:
                    top8_first(nc, dve, H, lambda g: sums[:, g, :], lambda g: rest_of(t)[:, g, :], top_s[:, t], top_i)
                elif part == 4:
                    top8_second(nc, dve, H, lambda g: rest_of(t)[:, g, :], top_s[:, t], top_i)
                    dve.drain().then_inc(read, 1)
                    nc.vector.tensor_tensor(top_s[:, t, :, 1:K], top_s[:, t, :, 1:K],
                                            top_s[:, t, :, 0:1].to_broadcast([P, H, K - 1]), ALU.subtract)
                    dve.drain()
                    nc.vector.memset(top_s[:, t, :, 0:1], 0.0).then_inc(shifted, 1)
                elif part == 5:
                    key_digit(0, ALU.logical_shift_right, 4)
                elif part == 6:
                    key_digit(1, ALU.bitwise_and, K - 1)
                else:
                    nc.vector.scalar_tensor_tensor(expert[:, t, :], key_f[:, 0, :], float(PEER_KEYS), key_f[:, 1, :],
                                                   ALU.mult, ALU.add).then_inc(routed, 1)

            def normalise(t):
                dve.wait_ge(raised, t + 1)
                nc.vector.tensor_reduce(total[:], top_s[:, t], AX.X, ALU.add)
                dve.drain()
                nc.vector.reciprocal(total[:], total[:])
                dve.drain()
                nc.vector.tensor_tensor(top_s[:, t], top_s[:, t], total[:].unsqueeze(2).to_broadcast([P, H, K]), ALU.mult)
                dve.drain()

            def add_experts(t):
                dve.wait_ge(summed, t + 1)
                for q in range(2):
                    nc.vector.tensor_tensor(product_tmp[:, q * BANK:(q + 1) * BANK], core.ps[:, 2 * (t % 2) + q, :],
                                            gate2[:, q * BANK:(q + 1) * BANK], ALU.mult)
                dve.drain().then_inc(added, 1)
                nc.vector.tensor_tensor(core.x[:, t, :], core.x[:, t, :], product_tmp, ALU.add)
                dve.drain()

            dve.sem_inc(used_u, FETCH)
            dve.wait_ge(steps_ready, 1)
            for part in range(ROUTE_PARTS):
                route(0, part)
            parts = ROUTE_PARTS // UNITS
            for unit in range(NT * UNITS):
                t, u = divmod(unit, UNITS)
                for part in range(parts):
                    with dve.Fori(0, G // parts // 2) as i:
                        for half in range(2):
                            group = part * (G // parts) + 2 * i + half
                            for b in range(FETCH):
                                dve.wait_ge(u_in[b], 16 * (unit * G + group + 1))
                                nc.vector.tensor_tensor_reduce(
                                    out=got_u[:, b, :], in0=got_u[:, b, :], in1=core.h[:, t, :], scale=1.0, scalar=0.0,
                                    op0=ALU.mult, op1=ALU.add, accum_out=dots[:, half, b:b + 1]).then_inc(used_u, 1)
                            dve.drain()
                            nc.vector.tensor_copy(score[:, t, bass.ds(u * UNIT_PICKS + group * FETCH, FETCH)], dots[:, half, :])
                    if t + 1 < NT:
                        route(t + 1, u * parts + part)
                    if u == 0 and part == 0:
                        normalise(t)
                dve.drain().then_inc(scored, 1)
                span = slice(u * UNIT_PICKS, (u + 1) * UNIT_PICKS)
                dve.wait_ge(activated, unit + 1)
                nc.vector.tensor_tensor(score[:, t, span], score[:, t, span], top_s[:, t].rearrange("p h k -> p (h k)")[:, span],
                                        ALU.mult).then_inc(weighted, 1)
                if t >= 1 and u == 0:
                    add_experts(t - 1)
            add_experts(NT - 1)

        @block.scalar
        def _(act):
            def copy_scores(t):
                if t >= 2:
                    act.wait_ge(read, t - 1)
                for q in range(4):
                    act.wait_ge(key_scored, 4 * t + q + 1)
                    nc.scalar.copy(half_scores[:, t % 2, 4 * q:4 * q + 4, :],
                                   core.ps[:, 4 + q, :].rearrange("p (g n) -> p g n", g=4)).then_inc(copied, 1)

            def raise_scores(t):
                act.wait_ge(shifted, t + 1)
                nc.scalar.activation(top_s[:, t], top_s[:, t], ACT.Exp).then_inc(raised, 1)

            copy_scores(0)
            copy_scores(1)
            raise_scores(0)
            for unit in range(NT * UNITS):
                t, u = divmod(unit, UNITS)
                if u == 0 and t + 2 < NT:
                    copy_scores(t + 2)
                if u == UNITS - 1 and t + 1 < NT:
                    raise_scores(t + 1)
                act.wait_ge(scored, unit + 1)
                span = slice(u * UNIT_PICKS, (u + 1) * UNIT_PICKS)
                nc.scalar.activation(score[:, t, span], score[:, t, span], ACT.Gelu).then_inc(activated, 1)
                act.wait_ge(weighted, unit + 1)
                with act.Fori(0, G) as i:
                    for b in range(FETCH):
                        act.wait_ge(used_v, (unit * G + i) * FETCH + b + 1)
                        nc.scalar.activation(diagonal[:, b, :], core.ident[:], ACT.Copy,
                                             scale=score[:, t, bass.ds(u * UNIT_PICKS + i * FETCH + b, 1)]).then_inc(diagonals, 1)

        @block.tensor
        def _(pe):
            def score_keys(t):
                if t >= 1:
                    pe.wait_ge(copied, 4 * t)
                for g in range(PAIRS):
                    mm = nc.tensor.matmul(core.ps[:, 4 + g // 4, (g % 4) * P:(g % 4 + 1) * P],
                                          qT[:, g, t * P:(t + 1) * P], keysT[:, g, :], start=True, stop=True)
                    if g % 4 == 3:
                        mm.then_inc(key_scored, 1)

            pe.sem_inc(used_v, FETCH)
            pe.wait_ge(keys_loaded, 16)
            score_keys(0)
            score_keys(1)
            pe.wait_ge(cleared, 1)
            for t in range(NT):
                if t + 2 < NT:
                    score_keys(t + 2)
                if t >= 2:
                    pe.wait_ge(added, t - 1)
                banks = [core.ps[:, 2 * (t % 2) + q, :] for q in range(2)]
                for q in range(2):
                    nc.tensor.matmul(banks[q], zero[:], core.h[:, 0, 0:BANK], start=True, stop=False, skip_group_check=True)
                with pe.Fori(0, UNITS * G) as i:
                    for b in range(FETCH):
                        group = t * UNITS * G + i
                        pe.wait_ge(diagonals, group * FETCH + b + 1)
                        pe.wait_ge(v_in[b], 16 * (group + 1))
                        for q in range(2):
                            mm = nc.tensor.matmul(banks[q], diagonal[:, b, :], got_v[:, b, q * BANK:(q + 1) * BANK],
                                                  start=False, stop=False, skip_group_check=True)
                        mm.then_inc(used_v, 1)
                pe.drain().then_inc(summed, 1)


def block_one(nc, core, d):
    with buffers(nc, mod=[P, 6, D]) as (mod,):
        adaptive_rows(nc, core, d, mod, core.row_a[:], core.row_b[:])
        first_mixer(nc, core, d, mod)
        norm(nc, core, "norm2", core.x, core.h, core.hT, 1e-6, True, mod[:, 4, :], mod[:, 3, :])
        with buffers(nc, qT=[P, PAIRS, SEQ]) as (qT,):
            project(nc, core, "peer_q", core.hT, [("peer_q", 4, "feature", ("act", ACT.Copy, feature_tiles(qT)))])
            peer(nc, core, d, qT, mod)
    norm(nc, core, "final1", core.x, core.x, None, 1e-6, True, core.row_a[:], None, [(core.row_a[:], d["final_g"])])


def plan_one(d):
    w_in = d["w_in"][0]
    plan = []
    add = lambda name, w, lo, n: plan.extend((name, kmajor(w, lo + i * BANK, BANK)) for i in range(n))
    add("qk", w_in, 0, 2)
    add("v", w_in, 1024, 2)
    add("g_ret", w_in, 2048, 2)
    add("ret_out", d["w_ret_out"][0], 0, 2)
    add("u", w_in, 3072, 2)
    add("sv", w_in, 4096, 2)
    add("sgu_out", d["w_sgu_out"][0], 0, 2)
    add("gate_a", w_in, 5120, 2)
    add("gate_b", w_in, 6144, 2)
    add("out1", d["w_out"][0], 0, 2)
    add("peer_q", d["peer_w_q"][0], 0, 4)
    return plan


STRIP = [0, 512, 896, 1152]
PACKED = 1280


def strip(buf, s, lo=0, hi=None):
    return buf[:, STRIP[s] + lo:STRIP[s] + (SEQ - s * P if hi is None else hi)]


def soft_maximum(nc, name, parts):
    with stage(nc, name, "shifted", "logged") as (block, shifted, logged):
        @block.vector
        def _(dve):
            for x, _, sign, bias, _, _ in parts:
                nc.vector.tensor_scalar(x, x, sign, bias, ALU.mult, ALU.add).then_inc(shifted, 1)
            for n, (x, tmp, _, _, a, _) in enumerate(parts):
                dve.wait_ge(logged, n + 1)
                nc.vector.scalar_tensor_tensor(x, x, a, tmp, ALU.max, ALU.add)

        @block.scalar
        def _(act):
            for n, (x, tmp, _, _, _, minus_a) in enumerate(parts):
                act.wait_ge(shifted, n + 1)
                nc.scalar.activation(tmp, x, ACT.Abs, bias=minus_a)
            act.drain()
            for x, tmp, *_ in parts:
                nc.scalar.activation(tmp, tmp, ACT.Exp, scale=-1.0)
            act.drain()
            for x, tmp, *_ in parts:
                nc.scalar.activation(tmp, tmp, ACT.Ln, bias=1.0).then_inc(logged, 1)


def load_rows(nc, name, loads, zeroed=()):
    with stage(nc, name, "loaded") as (block, loaded):
        @block.sync
        def _(sp):
            for dst, src in loads:
                sp.dma_start(dst, src).then_inc(loaded, 16)
            sp.wait_ge(loaded, 16 * len(loads))

        if zeroed:
            @block.gpsimd
            def _(pool):
                for z in zeroed:
                    nc.gpsimd.memset(z, 0.0)


def row_columns(nc, core, name, rows, cols, h):
    with stage(nc, name, "turned") as (block, turned):
        @block.tensor
        def _(pe):
            for n, row in enumerate(rows):
                for t in range(NT):
                    mm = nc.tensor.transpose(core.ps[:, n, t * h:(t + 1) * h], row[:, t * P:(t + 1) * P], core.ident[0:h, 0:h])
                mm.then_inc(turned, 1)

        @block.vector
        def _(dve):
            for n in range(len(rows)):
                dve.wait_ge(turned, n + 1)
                nc.vector.tensor_copy(cols[:, n, :, :].rearrange("p h t -> p t h"),
                                      core.ps[:, n, 0:NT * h].rearrange("p (t h) -> p t h", t=NT))


def gated_heads(nc, core, y, gate, gain, width, before=None):
    f = y.shape[2]
    heads = f // width
    n = NT * heads
    mv = core.mv[:, 0:n, :]

    def pool_part(pool, var_ready, root_ready):
        inverse_root(nc, core, pool, mv[:, :, 1:2], 1e-6, var_ready, root_ready)

    def dve_part(dve, var_ready, root_ready):
        if before is not None:
            for t in range(NT):
                nc.vector.tensor_tensor(y[:, t, :], y[:, t, :], before[:, t, :], ALU.mult)
            dve.drain()
        part = lambda g: y[:, g // heads, (g % heads) * width:(g % heads + 1) * width]
        row_stats(nc, core, dve, part, mv, width, n)
        mean_square(nc, dve, mv)
        dve.drain().then_inc(var_ready, 1)
        dve.wait_ge(root_ready, 2)
        for g in range(n):
            nc.vector.tensor_scalar(part(g), part(g), mv[:, g, 1:2], None, ALU.mult)
        dve.drain()
        for t in range(NT):
            if gain.shape[1] == f:
                nc.vector.tensor_tensor(y[:, t, :], y[:, t, :], gain, ALU.mult)
            else:
                run = y[:, t, :].rearrange("p (h f) -> p h f", h=heads)
                nc.vector.tensor_tensor(run, run, gain.unsqueeze(1).to_broadcast([P, heads, width]), ALU.mult)
        dve.drain()
        if gate is not None:
            for t in range(NT):
                nc.vector.tensor_tensor(y[:, t, :], y[:, t, :], gate[:, t, :], ALU.mult)

    return pool_part, dve_part


def decay_strips(nc, core, bank, edge, minus_col, out):
    for s in range(NT):
        nc.scalar.activation(strip(out, s, 0, P), edge[:, s, :], ACT.Exp, bias=minus_col(s))
        if s < NT - 1:
            nc.scalar.activation(strip(out, s, P), core.ps[:, bank, (s + 1) * P:SEQ], ACT.Exp, bias=minus_col(s))


GDN_HEADS, GDN_DK = 4, 128
LEVELS = 7


def unit_rows(nc, core, qkT):
    n = 2 * GDN_HEADS
    with buffers(nc, squares=[P, n, SEQ], pick=[P, n, n], scale_row=[n, SEQ]) as (squares, pick, scale_row), \
            stage(nc, "unit", "picks", "squared", "summed", "inverted", "rooted", "spread") as (
                block, picks, squared, summed, inverted, rooted, spread):
        @block.gpsimd
        def _(pool):
            nc.gpsimd.memset(pick[:], 0.0)
            pool.drain()
            for f in range(n):
                done = nc.gpsimd.memset(pick[:, f, f:f + 1], 1.0)
            done.then_inc(picks, 1)

        @block.scalar
        def _(act):
            for f in range(n):
                nc.scalar.activation(squares[:, f, :], qkT[:, f, :], ACT.Square).then_inc(squared, 1)
            act.wait_ge(inverted, 1)
            nc.scalar.activation(scale_row[:], scale_row[:], ACT.Sqrt).then_inc(rooted, 1)

        @block.tensor
        def _(pe):
            pe.wait_ge(picks, 1)
            for f in range(n):
                pe.wait_ge(squared, f + 1)
                mm = nc.tensor.matmul(core.ps[0:n, 0, :], pick[:, f, :], squares[:, f, :], start=f == 0, stop=f == n - 1)
            mm.then_inc(summed, 1)
            pe.wait_ge(rooted, 1)
            for f in range(n):
                nc.tensor.matmul(core.ps[:, (f + 1) % 8, :], core.ident[0:n, f:f + 1].to_broadcast([n, P]), scale_row[:],
                                 start=True, stop=True).then_inc(spread, 1)

        @block.vector
        def _(dve):
            dve.wait_ge(summed, 1)
            nc.vector.tensor_scalar(scale_row[:], core.ps[0:n, 0, :], 1e-6, None, ALU.add)
            dve.drain()
            nc.vector.reciprocal(scale_row[:], scale_row[:]).then_inc(inverted, 1)
            for f in range(n):
                dve.wait_ge(spread, f + 1)
                nc.vector.scalar_tensor_tensor(qkT[:, f, :], qkT[:, f, :], GDN_DK ** -0.5 if f < GDN_HEADS else 1.0,
                                               core.ps[:, (f + 1) % 8, :], ALU.mult, ALU.mult)


def delta_half(nc, core, half, qkvT, cum_rows, cols, vb, u, o, masks):
    H = GDN_HEADS
    heads = (2 * half, 2 * half + 1)
    kind_beta, kind_cum, kind_minus = 0, 1, 2
    with buffers(nc, keys=[P, 2, PACKED], attn=[P, 2, PACKED], edge=[P, NT, P], diag=[P, 8, P], rhs=[P, 2, P]) as (
            keys, attn, edge, diag, rhs):
        inv, invT = (qkvT[:, q:q + 2, :].rearrange("p q (n t) -> p (q n) t", t=P) for q in (2 * H, 2 * H + 2))
        part, prod = (core.tmp[:, q:q + 2, :].rearrange("p q (n t) -> p (q n) t", t=P) for q in (0, 2))
        with stage(nc, f"delta_scores{half}", "spread", "edged", "decayed", "scored", "applied") as (
                block, spread, edged, decayed, scored, applied):
            @block.tensor
            def _(pe):
                for n, h in enumerate(heads):
                    if n:
                        pe.wait_ge(decayed, n)
                    nc.tensor.matmul(core.ps[:, 0, :], core.ident[0:H, h:h + 1].to_broadcast([H, P]), cum_rows, start=True, stop=True).then_inc(spread, 1)
                    for m, first in enumerate((H + h, h)):
                        for s in range(NT):
                            if n or m:
                                pe.wait_ge(applied, NT * (2 * n + m - 1) + s + 1)
                            nc.tensor.matmul(core.ps[:, 1 + s, 0:SEQ - s * P], qkvT[:, H + h, s * P:(s + 1) * P],
                                             qkvT[:, first, s * P:], start=True, stop=True).then_inc(scored, 1)

            @block.scalar
            def _(act):
                for n, h in enumerate(heads):
                    act.wait_ge(edged, n + 1)
                    decay_strips(nc, core, 0, edge, lambda s: cols[:, kind_minus, h, s:s + 1], attn[:, n])
                    act.drain().then_inc(decayed, 1)

            @block.vector
            def _(dve):
                for n, h in enumerate(heads):
                    dve.wait_ge(spread, n + 1)
                    if n:
                        dve.wait_ge(decayed, n)
                    nc.vector.tensor_tensor(edge[:], core.ps[:, 0, :].rearrange("p (s t) -> p s t", s=NT),
                                            core.causal[:].unsqueeze(1).to_broadcast([P, NT, P]), ALU.add).then_inc(edged, 1)
                    dve.wait_ge(decayed, n + 1)
                    for m, dst in enumerate((keys, attn)):
                        dve.drain()
                        for s in range(NT):
                            dve.wait_ge(scored, NT * (2 * n + m) + s + 1)
                            nc.vector.tensor_tensor(strip(dst[:, n, :], s), core.ps[:, 1 + s, 0:SEQ - s * P],
                                                    strip(attn[:, n, :], s), ALU.mult).then_inc(applied, 1)

        with stage(nc, f"delta_inverse{half}", "masked", "first", "scaled", "second", "updated") as (
                block, masked, first, scaled, second, updated):
            bank = lambda kind, g: core.ps[:, 2 * kind + g, :].rearrange("p (n t) -> p n t", n=NT)
            of = lambda buf, g: buf[:, NT * g:NT * (g + 1), :]
            beta = lambda g: cols[:, kind_beta, heads[g], :].unsqueeze(2).to_broadcast([P, NT, P])

            @block.vector
            def _(dve):
                def mask(level, g):
                    nc.vector.tensor_tensor(of(part, g), of(diag, g), masks[:, level, :].unsqueeze(1).to_broadcast([P, NT, P]),
                                            ALU.mult).then_inc(masked, 1)

                for n in range(8):
                    nc.vector.tensor_copy(diag[:, n, :], strip(keys[:, n // 4, :], n % 4, 0, P))
                    nc.vector.tensor_copy(inv[:, n, :], core.ident[:])
                    nc.vector.tensor_copy(invT[:, n, :], core.ident[:])
                dve.drain()
                mask(0, 0)
                mask(0, 1)
                for level in range(LEVELS):
                    for g in range(2):
                        dve.wait_ge(first, 2 * level + g + 1)
                        nc.vector.tensor_tensor(of(prod, g), bank(0, g), beta(g), ALU.mult).then_inc(scaled, 1)
                    for g in range(2):
                        if level + 1 < LEVELS:
                            mask(level + 1, g)
                        dve.wait_ge(second, 2 * level + g + 1)
                        nc.vector.tensor_tensor(of(inv, g), of(inv, g), bank(1, g), ALU.subtract)
                        nc.vector.tensor_tensor(of(invT, g), of(invT, g), bank(2, g), ALU.subtract)
                        dve.drain().then_inc(updated, 1)

            @block.tensor
            def _(pe):
                for level in range(LEVELS):
                    for g in range(2):
                        pe.wait_ge(masked, 2 * level + g + 1)
                        if level:
                            pe.wait_ge(updated, 2 * level + g - 1)
                        for n in range(NT):
                            mm = nc.tensor.matmul(bank(0, g)[:, n, :], of(part, g)[:, n, :], of(inv, g)[:, n, :], start=True, stop=True)
                        mm.then_inc(first, 1)
                    for g in range(2):
                        pe.wait_ge(scaled, 2 * level + g + 1)
                        for n in range(NT):
                            nc.tensor.matmul(bank(1, g)[:, n, :], of(invT, g)[:, n, :], of(prod, g)[:, n, :], start=True, stop=True)
                            mm = nc.tensor.matmul(bank(2, g)[:, n, :], of(prod, g)[:, n, :], of(invT, g)[:, n, :], start=True, stop=True)
                        mm.then_inc(second, 1)

        with stage(nc, f"delta_solve{half}", "gathered", "sided", "solved", "stored", "output", "copied") as (
                block, gathered, sided, solved, stored, output, copied):
            @block.tensor
            def _(pe):
                for t in range(NT):
                    if t:
                        pe.wait_ge(stored, t)
                        for n, h in enumerate(heads):
                            for s in range(t):
                                mm = nc.tensor.matmul(core.ps[:, 0, n * P:(n + 1) * P], strip(keys[:, n, :], s, (t - s) * P, (t - s + 1) * P),
                                                      u[:, s, h * P:(h + 1) * P], start=s == 0, stop=s == t - 1)
                        mm.then_inc(gathered, 1)
                    pe.wait_ge(sided, t + 1)
                    for n in range(2):
                        mm = nc.tensor.matmul(core.ps[:, 1, n * P:(n + 1) * P], invT[:, 4 * n + t, :], rhs[:, n, :], start=True, stop=True)
                    mm.then_inc(solved, 1)
                pe.wait_ge(stored, NT)
                for n, h in enumerate(heads):
                    for t in range(NT):
                        for s in range(t + 1):
                            mm = nc.tensor.matmul(core.ps[:, 2 + n, t * P:(t + 1) * P], strip(attn[:, n, :], s, (t - s) * P, (t - s + 1) * P),
                                                  u[:, s, h * P:(h + 1) * P], start=s == 0, stop=s == t)
                    mm.then_inc(output, 1)

            @block.vector
            def _(dve):
                for t in range(NT):
                    if t:
                        dve.wait_ge(gathered, t)
                    for n, h in enumerate(heads):
                        v = vb[:, t, h * P:(h + 1) * P]
                        if t:
                            done = nc.vector.scalar_tensor_tensor(rhs[:, n, :], core.ps[:, 0, n * P:(n + 1) * P],
                                                                  cols[:, kind_beta, h, t:t + 1], v, ALU.mult, ALU.subtract)
                        else:
                            done = nc.vector.tensor_scalar(rhs[:, n, :], v, -1.0, None, ALU.mult)
                    done.then_inc(sided, 1)

            @block.scalar
            def _(act):
                for t in range(NT):
                    act.wait_ge(solved, t + 1)
                    nc.scalar.activation(u[:, t, heads[0] * P:(heads[0] + 2) * P], core.ps[:, 1, 0:2 * P], ACT.Copy,
                                         scale=-1.0).then_inc(stored, 1)
                for n, h in enumerate(heads):
                    act.wait_ge(output, n + 1)
                    nc.scalar.copy(o[:, :, h * P:(h + 1) * P], core.ps[:, 2 + n, :].rearrange("p (t f) -> p t f", t=NT))


def delta_branch(nc, core, d, o):
    H = GDN_HEADS
    with buffers(nc, qkvT=[P, 3 * H, SEQ], beta_row=[H, SEQ], g_row=[H, SEQ], g_tmp=[H, SEQ], dt_bias=[H, 1], a_rate=[H, 1],
                 cols=[P, 3, H, NT], masks=[P, LEVELS, P]) as (
            qkvT, beta_row, g_row, g_tmp, dt_bias, a_rate, cols, masks):
        u, vb = core.x[:, :, 0:H * P], core.x[:, :, H * P:2 * H * P]
        with buffers(nc, taps=[P, 4, 3 * H]) as (taps,):
            project(nc, core, "delta_in", core.hT, [
                ("aqkv", 3, "feature", ("conv", taps, None, 4, feature_tiles(qkvT))),
                ("beta_dt", 1, [(0, H), (H, H)], ("act", ACT.Copy, row_buffers(beta_row, g_row)))],
                    loads=[(taps[:], d["gdn_conv_c_2"]), (dt_bias[:], d["gdn_dt_bias_c_2"]), (a_rate[:], d["gdn_a_log_c_2"]),
                           (masks[:], d["const_levels"])])
        unit_rows(nc, core, qkvT)
        soft_maximum(nc, "delta_soft", [(g_row[:], g_tmp[:], 1.0, dt_bias[:], 0.0, 0.0)])
        with stage(nc, "delta_decay", "ready", "scanned") as (block, ready, scanned):
            @block.scalar
            def _(act):
                nc.scalar.activation(a_rate[:], a_rate[:], ACT.Exp).then_inc(ready, 1)
                nc.scalar.activation(beta_row[:], beta_row[:], ACT.Sigmoid)

            @block.vector
            def _(dve):
                dve.wait_ge(ready, 1)
                nc.vector.tensor_scalar(g_tmp[:], g_row[:], a_rate[:], -1.0, ALU.mult, ALU.mult)
                dve.drain()
                nc.vector.tensor_tensor_scan(g_row[:], core.one_row[0:H, :], g_tmp[:], 0.0, ALU.mult, ALU.add)
        row_columns(nc, core, "delta_cols", [beta_row, g_row], cols, H)
        with stage(nc, "delta_values", "turned") as (block, turned):
            @block.tensor
            def _(pe):
                for t in range(NT):
                    for h in range(H):
                        mm = nc.tensor.transpose(core.ps[:, t, h * P:(h + 1) * P], qkvT[:, 2 * H + h, t * P:(t + 1) * P], core.ident[:])
                    mm.then_inc(turned, 1)

            @block.vector
            def _(dve):
                nc.vector.tensor_scalar(cols[:, 2], cols[:, 1], -1.0, None, ALU.mult)
                for t in range(NT):
                    dve.wait_ge(turned, t + 1)
                    nc.vector.tensor_tensor(vb[:, t, :].rearrange("p (h f) -> p h f", h=H),
                                            core.ps[:, t, :].rearrange("p (h f) -> p h f", h=H),
                                            cols[:, 0, :, t:t + 1].to_broadcast([P, H, P]), ALU.mult)
        for half in range(2):
            delta_half(nc, core, half, qkvT, g_row[:], cols, vb, u, o, masks)


SUB = 16
SUBS = P // SUB


def channel_decay(nc, core, name, units, v, o, sums, own_block):
    TB = SEQ // SUB
    H = len(units[0][0])
    STEP = SUB // NT
    tiles = lambda a: a.rearrange("p (t n) -> p t n", t=NT)
    blocks = lambda a: a.rearrange("p (b i) -> p b i", i=SUB)
    far_pairs = [(s, t) for t in range(NT) for s in range(t)]
    FAR = len(far_pairs)
    with buffers(nc, q_tile=[P, H, SEQ], q_block=[P, H, SEQ], ref=[P, TB], far=[P, FAR, P], near=[P, 2, SUBS, P],
                 pair=[P, 4, SEQ], bias=[P, FAR], own=[P, SEQ], scores=[P, H, SEQ], cross=[P, H, FAR, P]) as (
            q_tile, q_block, ref, far, near, pair, bias, own, scores, cross):
        with stage(nc, name, "zeroed", "referred", "shifted", "raised_q", "queries", "raised_far", "far_ready",
                   "raised_near", "near_ready", "near_used", "differed", "raised", "paired", "pair_used", "far_scored",
                   "own_scored", "crossed", "merged", "output", "stored") as (
                block, zeroed, referred, shifted, raised_q, queries, raised_far, far_ready,
                raised_near, near_ready, near_used, differed, raised, paired, pair_used, far_scored,
                own_scored, crossed, merged, output, stored):
            @block.gpsimd
            def _(pool):
                nc.gpsimd.memset(near[:], 0.0).then_inc(zeroed, 1)
                for u, (heads, q, k, cum, last) in enumerate(units):
                    for j in range(SUB):
                        n = u * SUB + j
                        if n >= 4:
                            pool.wait_ge(pair_used, n - 3)
                        nc.gpsimd.tensor_tensor(blocks(pair[:, j % 4, :]), blocks(cum),
                                                blocks(cum)[:, :, j:j + 1].to_broadcast([P, TB, SUB]), ALU.subtract).then_inc(differed, 1)

            @block.vector
            def _(dve):
                def prepare(u):
                    heads, q, k, cum, last = units[u]
                    if u:
                        dve.wait_ge(near_used, NT * u)
                    nc.vector.tensor_copy(ref[:].rearrange("p (t b) -> p t b", t=NT)[:, :, 1:SUBS],
                                          tiles(cum).rearrange("p t (b i) -> p t b i", i=SUB)[:, :, 0:SUBS - 1, SUB - 1])
                    for n, (s, t) in enumerate(far_pairs):
                        if t - s == 1:
                            nc.vector.tensor_copy(bias[:, n:n + 1], last[:, s:t])
                        else:
                            nc.vector.tensor_reduce(bias[:, n:n + 1], last[:, s:t], AX.X, ALU.add)
                    dve.drain().then_inc(referred, 1)
                    for n, (r, rows, _) in enumerate(heads):
                        mine = slice(r, r + rows)
                        nc.vector.tensor_tensor(blocks(q_block[mine, n, :]), blocks(cum[mine]),
                                                ref[mine].unsqueeze(2).to_broadcast([rows, TB, SUB]), ALU.subtract).then_inc(shifted, 1)
                    dve.wait_ge(raised_q, 2 * H * (u + 1))
                    for n, (r, rows, _) in enumerate(heads):
                        mine = slice(r, r + rows)
                        nc.vector.tensor_tensor(q_tile[mine, n, :], q_tile[mine, n, :], q[mine], ALU.mult)
                        nc.vector.tensor_tensor(q_block[mine, n, :], q_block[mine, n, :], q[mine], ALU.mult).then_inc(queries, 1)
                    for n, (s, t) in enumerate(far_pairs):
                        dve.wait_ge(raised_far, FAR * u + n + 1)
                        nc.vector.tensor_tensor(far[:, n, :], far[:, n, :], k[:, s * P:(s + 1) * P], ALU.mult).then_inc(far_ready, 1)

                nc.vector.memset(ref[:], 0.0)
                for n in range(H):
                    for r, rows, _ in units[0][0][:n] + units[0][0][n + 1:]:
                        nc.vector.memset(q_tile[r:r + rows, n, :], 0.0)
                        nc.vector.memset(q_block[r:r + rows, n, :], 0.0)
                dve.drain()
                prepare(0)
                for u, (heads, q, k, cum, last) in enumerate(units):
                    for j in range(SUB):
                        if j % STEP == 0:
                            t = j // STEP
                            dve.wait_ge(raised_near, NT * u + t + 1)
                            nc.vector.tensor_tensor(near[:, t % 2], near[:, t % 2], k[:, t * P:(t + 1) * P].unsqueeze(1).to_broadcast([P, SUBS, P]),
                                                    ALU.mult).then_inc(near_ready, 1)
                        dve.wait_ge(raised, SUB * u + j + 1)
                        b = blocks(pair[:, j % 4, :])
                        nc.vector.scalar_tensor_tensor(b, b, 1.0, blocks(k)[:, :, j:j + 1].to_broadcast([P, TB, SUB]), ALU.min, ALU.mult)
                        dve.drain()
                        nc.vector.tensor_tensor(pair[:, j % 4, :], pair[:, j % 4, :], q, ALU.mult).then_inc(paired, 1)
                    if u + 1 < len(units):
                        prepare(u + 1)
                    dve.wait_ge(own_scored, u + 1)
                    if u:
                        dve.wait_ge(output, H * u)
                    for n in range(H):
                        nc.vector.tensor_tensor(tiles(own[:]), tiles(core.ps[:, 1 + n, :]),
                                                own_block.unsqueeze(1).to_broadcast([P, NT, P]), ALU.mult)
                        dve.drain()
                        nc.vector.tensor_tensor(scores[:, n, :], own[:], core.ps[:, 3 + n, :], ALU.add).then_inc(merged, 1)
                        dve.drain()

            @block.scalar
            def _(act):
                def prepare(u):
                    heads, q, k, cum, last = units[u]
                    for n, (r, rows, _) in enumerate(heads):
                        mine = slice(r, r + rows)
                        act.wait_ge(shifted, H * u + n + 1)
                        nc.scalar.activation(q_tile[mine, n, :], cum[mine], ACT.Exp).then_inc(raised_q, 1)
                        nc.scalar.activation(q_block[mine, n, :], q_block[mine, n, :], ACT.Exp).then_inc(raised_q, 1)
                    act.wait_ge(referred, u + 1)
                    for n, (s, t) in enumerate(far_pairs):
                        nc.scalar.activation(far[:, n, :], cum[:, s * P:(s + 1) * P], ACT.Exp, bias=bias[:, n:n + 1],
                                             scale=-1.0).then_inc(raised_far, 1)

                def finish(u):
                    for n, (_, _, col) in enumerate(units[u][0]):
                        act.wait_ge(output, H * u + n + 1)
                        nc.scalar.copy(o[:, :, col:col + P], core.ps[:, (0, 7)[n], :].rearrange("p (t f) -> p t f", t=NT)).then_inc(stored, 1)
                    if u + 1 < len(units):
                        copy_far(u + 1)

                def copy_far(u):
                    for n in range(H):
                        act.wait_ge(far_scored, H * u + n + 1)
                        nc.scalar.copy(cross[:, n, 0:4, :], core.ps[:, 5, :].rearrange("p (n t) -> p n t", n=4))
                        nc.scalar.copy(cross[:, n, 4:6, :], core.ps[:, 6, 0:2 * P].rearrange("p (n t) -> p n t", n=2)).then_inc(crossed, 1)

                prepare(0)
                act.wait_ge(zeroed, 1)
                for u, (heads, q, k, cum, last) in enumerate(units):
                    for j in range(SUB):
                        if j % STEP == 0:
                            t = j // STEP
                            if NT * u + t >= 2:
                                act.wait_ge(near_used, NT * u + t - 1)
                            for b in range(1, SUBS):
                                done = nc.scalar.activation(near[:, t % 2, b, 0:b * SUB], cum[:, t * P:t * P + b * SUB], ACT.Exp,
                                                            bias=ref[:, t * SUBS + b:t * SUBS + b + 1], scale=-1.0)
                            done.then_inc(raised_near, 1)
                        act.wait_ge(differed, SUB * u + j + 1)
                        nc.scalar.activation(pair[:, j % 4, :], pair[:, j % 4, :], ACT.Exp).then_inc(raised, 1)
                        if j == 1:
                            if u:
                                finish(u - 1)
                            else:
                                copy_far(0)
                    if u + 1 < len(units):
                        prepare(u + 1)
                finish(len(units) - 1)

            @block.tensor
            def _(pe):
                def score_far(u, numbers):
                    pe.wait_ge(queries, H * (u + 1))
                    pe.wait_ge(far_ready, FAR * (u + 1))
                    for n in numbers:
                        if H * u + n:
                            pe.wait_ge(crossed, H * u + n)
                        for m, (s, t) in enumerate(far_pairs):
                            mm = nc.tensor.matmul(core.ps[:, 5 + m // 4, (m % 4) * P:(m % 4 + 1) * P], far[:, m, :],
                                                  q_tile[:, n, t * P:(t + 1) * P], start=True, stop=True)
                        mm.then_inc(far_scored, 1)

                score_far(0, range(H))
                for u, (heads, q, k, cum, last) in enumerate(units):
                    for j in range(SUB):
                        if j % STEP == 0:
                            t = j // STEP
                            pe.wait_ge(near_ready, NT * u + t + 1)
                            for n in range(H):
                                for b in range(SUBS):
                                    at = t * P + b * SUB
                                    nc.tensor.matmul(core.ps[:, 3 + n, at:at + SUB], near[:, t % 2, b, :],
                                                     q_block[:, n, at:at + SUB], start=True, stop=True)
                            pe.drain().then_inc(near_used, 1)
                        pe.wait_ge(paired, SUB * u + j + 1)
                        for n in range(H):
                            mm = nc.tensor.matmul(core.ps[:, 1 + n, :], sums[:, n, SUB - 1 - j:SUB - 1 - j + P], pair[:, j % 4, :],
                                                  start=j == 0, stop=j == SUB - 1)
                        mm.then_inc(pair_used, 1)
                    pe.drain().then_inc(own_scored, 1)
                    if u + 1 < len(units):
                        score_far(u + 1, range(1))
                    if u:
                        pe.wait_ge(stored, H * u)
                    pe.wait_ge(crossed, H * (u + 1))
                    for n, (_, _, col) in enumerate(heads):
                        pe.wait_ge(merged, H * u + n + 1)
                        for t in range(NT):
                            out = core.ps[:, (0, 7)[n], t * P:(t + 1) * P]
                            for s in range(t):
                                nc.tensor.matmul(out, cross[:, n, far_pairs.index((s, t)), :], v[:, s, col:col + P], start=s == 0, stop=False)
                            mm = nc.tensor.matmul(out, scores[:, n, t * P:(t + 1) * P], v[:, t, col:col + P], start=t == 0, stop=True)
                        mm.then_inc(output, 1)
                    if u + 1 < len(units):
                        score_far(u + 1, range(1, H))


def tile_sums(nc, core, name, logs, cum, last, units):
    with stage(nc, name) as (block,):
        @block.vector
        def _(dve):
            for u in range(units):
                nc.vector.tensor_tensor_scan(cum[:, u, :], core.tile_row[:], logs[:, u, :], 0.0, ALU.mult, ALU.add)
            dve.drain()
            for u in range(units):
                nc.vector.tensor_copy(last[:, u, :], cum[:, u, :].rearrange("p (t n) -> p t n", t=NT)[:, :, P - 1])


def gla_branch(nc, core, d, o, sums, own_block):
    with buffers(nc, qkT=[P, 4, SEQ], v=[P, NT, SEQ], lr=[16, SEQ], w2=[16, 256], b2=[P, 2], logs=[P, 2, SEQ],
                 last=[P, 2, NT]) as (qkT, v, lr, w2, b2, logs, last):
        project(nc, core, "gla_in", core.hT, [("bqk", 1, "feature", ("act", ACT.Copy, feature_tiles(qkT))),
                                              ("bv", 1, "token", ("act", ACT.Copy, columns(v))),
                                              ("blr", 1, [(0, 16)], ("act", ACT.Copy, row_buffers(lr)))],
                loads=[(w2[:], d["gla_w2_2"][0]), (b2[:], d["gla_b2_c_2"]), (sums[:], d["const_head_sums"]), (own_block, d["const_own_block"])])
        cum = core.tmp
        with stage(nc, "gla_gate", "gated") as (block, gated):
            @block.tensor
            def _(pe):
                for u in range(2):
                    nc.tensor.matmul(core.ps[:, u, :], w2[:, u * P:(u + 1) * P], lr[:], start=True, stop=True).then_inc(gated, 1)

            @block.vector
            def _(dve):
                for u in range(2):
                    dve.wait_ge(gated, u + 1)
                    nc.vector.tensor_scalar(logs[:, u, :], core.ps[:, u, :], b2[:, u:u + 1], None, ALU.add)
                nc.vector.tensor_scalar(qkT[:, 0:2, :], qkT[:, 0:2, :], 64 ** -0.5, None, ALU.mult)
        soft_maximum(nc, "gla_soft", [(logs[:, u, :], cum[:, u, :], -1.0, 0.0, 0.0, 0.0) for u in range(2)])
        with stage(nc, "gla_scale") as (block,):
            @block.vector
            def _(dve):
                nc.vector.tensor_scalar(logs[:], logs[:], -1.0 / 16.0, None, ALU.mult)
        tile_sums(nc, core, "gla_sums", logs, cum, last, 2)
        units = [([(0, 64, 2 * u * P), (64, 64, (2 * u + 1) * P)], qkT[:, u, :], qkT[:, 2 + u, :], cum[:, u, :], last[:, u, :]) for u in range(2)]
        channel_decay(nc, core, "gla", units, v, o, sums, own_block)


def hgrn_branch(nc, core, d, o, sums, own_block):
    H = 4
    with buffers(nc, q=[P, H, SEQ], k=[P, H, SEQ], v=[P, NT, SEQ], logs=[P, H, SEQ], last=[P, H, NT],
                 lb=[P, 7, H]) as (q, k, v, logs, last, lb):
        project(nc, core, "hgrn_in", core.hT, [("cq", 1, "feature", ("act", ACT.Silu, feature_tiles(q))),
                                               ("cf", 1, "feature", ("act", ACT.Copy, feature_tiles(logs))),
                                               ("ci", 1, "token", ("act", ACT.Copy, columns(v)))],
                loads=[(sums[:, 0, :], d["const_sums"]), (own_block, d["const_own_block"])])
        LB, LOG_LB, MINUS_LOG_LB, REST, LOG_REST, EXP, TMP = range(7)
        with stage(nc, "hgrn_bound", "loaded", "differed", "raised", "bounded", "logged", "keyed") as (
                block, loaded, differed, raised, bounded, logged, keyed):
            @block.sync
            def _(sp):
                sp.dma_start(lb[:, TMP, :], d["hgrn_lb_c_2"]).then_inc(loaded, 16)

            @block.vector
            def _(dve):
                dve.wait_ge(loaded, 16)
                nc.vector.tensor_tensor(lb[:, EXP, :], lb[:, TMP, :], lb[:, TMP, :], ALU.subtract).then_inc(differed, 1)
                dve.wait_ge(raised, 1)
                nc.vector.reciprocal(lb[:, TMP, :], lb[:, EXP, :])
                dve.drain()
                nc.vector.tensor_tensor(lb[:, EXP, :], lb[:, EXP, :], lb[:, TMP, :], ALU.mult)
                dve.drain()
                nc.vector.tensor_tensor(lb[:, LB, :], lb[:, EXP, :], lb[:, EXP, :], ALU.subtract)
                dve.drain()
                nc.vector.tensor_scalar(lb[:, LB, :], lb[:, LB, :], 0.0, 1.0, ALU.max, ALU.min)
                dve.drain()
                nc.vector.tensor_scalar(lb[:, REST, :], lb[:, LB, :], -1.0, 1.0, ALU.mult, ALU.add)
                nc.vector.tensor_scalar(lb[:, TMP, :], lb[:, LB, :], 1e-30, 2.0 ** 50, ALU.max, ALU.mult)
                dve.drain().then_inc(bounded, 1)
                dve.wait_ge(logged, 2)
                nc.vector.tensor_scalar(lb[:, LOG_LB, :], lb[:, LOG_LB, :], -50.0 * float(np.log(2.0)), None, ALU.add)
                dve.drain()
                nc.vector.tensor_scalar(lb[:, MINUS_LOG_LB, :], lb[:, LOG_LB, :], -1.0, None, ALU.mult)
                dve.wait_ge(keyed, H)
                for h in range(H):
                    nc.vector.tensor_scalar(k[:, h, :], k[:, h, :], lb[:, REST, h:h + 1], None, ALU.mult)
                nc.vector.tensor_scalar(q[:], q[:], 128 ** -0.5, None, ALU.mult)

            @block.scalar
            def _(act):
                act.wait_ge(differed, 1)
                nc.scalar.activation(lb[:, EXP, :], lb[:, EXP, :], ACT.Exp).then_inc(raised, 1)
                act.wait_ge(bounded, 1)
                nc.scalar.activation(lb[:, LOG_LB, :], lb[:, TMP, :], ACT.Ln).then_inc(logged, 1)
                nc.scalar.activation(lb[:, LOG_REST, :], lb[:, REST, :], ACT.Ln).then_inc(logged, 1)
                for h in range(H):
                    nc.scalar.activation(k[:, h, :], logs[:, h, :], ACT.Sigmoid, scale=-1.0).then_inc(keyed, 1)
        tmp = core.tmp
        soft_maximum(nc, "hgrn_soft", [(logs[:, h, :], tmp[:, h, :], -1.0, 0.0, 0.0, 0.0) for h in range(H)])
        soft_maximum(nc, "hgrn_add", [(logs[:, h, :], tmp[:, h, :], -1.0, lb[:, LOG_REST, h:h + 1], lb[:, LOG_LB, h:h + 1],
                                       lb[:, MINUS_LOG_LB, h:h + 1]) for h in range(H)])
        cum = core.tmp
        tile_sums(nc, core, "hgrn_sums", logs, cum, last, H)
        units = [([(0, P, h * P)], q[:, h, :], k[:, h, :], cum[:, h, :], last[:, h, :]) for h in range(H)]
        channel_decay(nc, core, "hgrn", units, v, o, sums, own_block)


def second_mixer(nc, core, d):
    with buffers(nc, o=[P, NT, SEQ], gain=[P, P]) as (o, gain):
        def close(name, gain_name, gate_plan, share_plan, out_plan, first):
            with buffers(nc, gate=[P, NT, SEQ], oT=([P, 2, 4, SEQ], F32R), share=[P, NT, D]) as (gate, oT, share):
                project(nc, core, f"{name}_gates", core.hT, [(gate_plan, 1, "token", ("act", ACT.Silu, columns(gate))),
                                                             (share_plan, 2, "token", ("act", ACT.Sigmoid, columns(share)))],
                        loads=[(gain[:], d[gain_name][0, :].partition_broadcast(P))], beside=gated_heads(nc, core, o, gate, gain[:], P))
                transpose(nc, core, f"{name}_T", o, two_parts(oT), 4)
                project(nc, core, f"{name}_out", two_parts(oT), [(out_plan, 2, "token", ("mul" if first else "mad", columns(share), columns(core.x)))], kt=4)

        delta_branch(nc, core, d, o)
        close("gdn", "gdn_norm_2", "ag", "ma", "br_a", True)
        with buffers(nc, sums=[P, 2, P + SUB], own_block=[P, P]) as (sums, own_block):
            gla_branch(nc, core, d, o, sums, own_block[:])
        close("gla", "gla_norm_2", "bg", "mb", "br_b", False)
        with buffers(nc, sums=[P, 1, P + SUB], own_block=[P, P]) as (sums, own_block):
            hgrn_branch(nc, core, d, o, sums, own_block[:])
        close("hgrn", "hgrn_norm_2", "cg", "mc", "br_c", False)
    with buffers(nc, yT=([P, 2, KD, SEQ], F32R)) as (yT,):
        transpose(nc, core, "mix_T", core.x, two_parts(yT))
        project(nc, core, "out2", two_parts(yT), [("out2", 2, "token", ("axpy", ALPHA, columns(core.h)))])


EXPERTS, GROUPS, MEMBERS, FF = 16, 4, 4, 256


def choose_experts(nc, core, d, combine):
    first = take(core, "router", 1)
    start = plan_splits(core, 2 * core.taken)
    n = NT * GROUPS
    with buffers(nc, score_row=[EXPERTS, SEQ], score=[P, NT, EXPERTS], sel=[P, NT, EXPERTS], bias=[P, EXPERTS], pair_sums=[P, n, 6], best=[P, n], beats=[P, n, 4, 4],
                 same=[P, n, 4, 4], rank=[P, n, 4], g_rank=[P, n], total=[P, NT], before=[P, 4, 4]) as (
            score_row, score, sel, bias, pair_sums, best, beats, same, rank, g_rank, total, before):
        with stage(nc, "choose", "loaded", "squashed", "turned") as (block, loaded, squashed, turned):
            @block.sync
            def _(sp):
                sp.dma_start(bias[:], d["router_bias_2"].partition_broadcast(P)).then_inc(loaded, 16)
                sp.dma_start(before[:], d["const_before"].partition_broadcast(P)).then_inc(loaded, 16)
                load_ahead(core, sp, core.splits + 2)

            @block.tensor
            def _(pe):
                for half in range(2):
                    pe.wait_ge(core.split[half], first + 1)
                w = [weights(core, half, P, KD // 2, EXPERTS) for half in range(2)]
                for k in range(KD):
                    product(nc, core.ps[0:EXPERTS, 0, :], [v[:, k % (KD // 2), :] for v in w[k // (KD // 2)]],
                            halves(core.hT, k, slice(None)), k == 0, k == KD - 1)
                pe.drain().then_inc(core.products, QUARTERS)
                pe.sem_inc(core.used, 1)
                pe.wait_ge(squashed, 1)
                for t in range(NT):
                    mm = nc.tensor.transpose(core.ps[:, 1, t * EXPERTS:(t + 1) * EXPERTS], score_row[:, t * P:(t + 1) * P],
                                             core.ident[0:EXPERTS, 0:EXPERTS])
                mm.then_inc(turned, 1)

            @block.scalar
            def _(act):
                act.wait_ge(core.products, QUARTERS * (first + 1))
                nc.scalar.activation(score_row[:], core.ps[0:EXPERTS, 0, :], ACT.Sigmoid).then_inc(squashed, 1)

            def ranks(dve, values, out, count, lists):
                mine = values.unsqueeze(3).to_broadcast([P, lists, count, count])
                other = values.unsqueeze(2).to_broadcast([P, lists, count, count])
                a, b = beats[:, 0:lists], same[:, 0:lists]
                nc.vector.tensor_tensor(a, other, mine, ALU.is_gt)
                nc.vector.tensor_tensor(b, other, mine, ALU.is_equal)
                dve.drain()
                nc.vector.tensor_tensor(b, b, before[:].unsqueeze(1).to_broadcast([P, lists, count, count]), ALU.mult)
                dve.drain()
                nc.vector.tensor_tensor(a, a, b, ALU.add)
                dve.drain()
                nc.vector.tensor_reduce(out, a, AX.X, ALU.add)
                dve.drain()

            @block.vector
            def _(dve):
                split_first(nc, core, dve, start, first)
                dve.wait_ge(loaded, 32)
                dve.wait_ge(turned, 1)
                nc.vector.tensor_copy(score[:].rearrange("p t e -> p (t e)"), core.ps[:, 1, 0:NT * EXPERTS])
                dve.drain()
                nc.vector.tensor_tensor(sel[:], score[:], bias[:].unsqueeze(1).to_broadcast([P, NT, EXPERTS]), ALU.add)
                dve.drain()
                member = sel[:].rearrange("p t (g e) -> p (t g) e", g=GROUPS)
                m = 0
                for i in range(MEMBERS):
                    for j in range(i + 1, MEMBERS):
                        nc.vector.tensor_tensor(pair_sums[:, :, m:m + 1], member[:, :, i:i + 1], member[:, :, j:j + 1], ALU.add)
                        m += 1
                dve.drain()
                nc.vector.tensor_reduce(best[:], pair_sums[:], AX.X, ALU.max)
                ranks(dve, member, rank[:], MEMBERS, n)
                ranks(dve, best[:].rearrange("p (t g) -> p t g", t=NT), g_rank[:].rearrange("p (t g) -> p t g", t=NT), GROUPS, NT)
                nc.vector.tensor_scalar(rank[:], rank[:], 1.5, None, ALU.is_lt)
                nc.vector.tensor_scalar(g_rank[:], g_rank[:], 0.5, None, ALU.is_lt)
                dve.drain()
                nc.vector.tensor_tensor(rank[:], rank[:], g_rank[:].unsqueeze(2).to_broadcast([P, n, MEMBERS]), ALU.mult)
                dve.drain()
                nc.vector.tensor_tensor(score[:], score[:], rank[:].rearrange("p (t g) e -> p t (g e)", t=NT), ALU.mult)
                dve.drain()
                nc.vector.tensor_reduce(total[:], score[:], AX.X, ALU.add)
                dve.drain()
                nc.vector.reciprocal(total[:], total[:])
                dve.drain()
                nc.vector.tensor_tensor(combine[:], score[:], total[:].unsqueeze(2).to_broadcast([P, NT, EXPERTS]), ALU.mult)


def moe(nc, core, d):
    with buffers(nc, combine=[P, NT, EXPERTS], silu_g=[P, 2, SEQ], hidden=([P, 2, 2, SEQ], F32R)) as (combine, silu_g, hidden):
        choose_experts(nc, core, d, combine)
        first = take(core, "expert", 2 * EXPERTS)
        start = plan_splits(core, 2 * core.taken + 1)
        last = EXPERTS - 1
        c_in = lambda n: first + 2 * n - 1
        c_out = lambda n: first + 2 * n + 2
        with stage(nc, "moe", "banks_read", "activated", "hidden_ready", "outputs", "added") as (
                block, banks_read, activated, hidden_ready, outputs, added):
            @block.sync
            def _(sp):
                load_ahead(core, sp, core.splits + 2)

            @block.tensor
            def _(pe):
                def gate_and_up(n, c):
                    pe.wait_ge(banks_read, 2 * n + 2)
                    for half in range(2):
                        pe.wait_ge(core.split[half], c + 1)
                        w = weights(core, half, P, KD // 2, 2 * FF)
                        for f in range(2):
                            for part in range(2):
                                col = part * FF + f * P
                                for k in range(KD // 2):
                                    kk = half * KD // 2 + k
                                    mm = product(nc, core.ps[:, 2 * part + f, :], [v[:, k, col:col + P] for v in w],
                                                 halves(core.hT, kk, slice(None)), kk == 0, kk == KD - 1)
                                if half == 1:
                                    mm.then_inc(core.products, 1)
                        if half == 0:
                            mm.then_inc(core.used, 1)

                def down(n, c):
                    pe.wait_ge(hidden_ready, 2 * n + 2)
                    for half in range(2):
                        pe.wait_ge(core.split[half], c + 1)
                        w = weights(core, half, P, 2, BANK)
                        for t in range(NT):
                            pe.wait_ge(added, 8 * n + 4 * half + t + 1)
                            for f in range(2):
                                mm = product(nc, core.ps[:, 4 + t, :], halves(two_parts(hidden), f, slice(t * P, (t + 1) * P)),
                                             [v[:, f, :] for v in w], f == 0, f == 1)
                            mm.then_inc(outputs, 1)
                        if half == 0:
                            pe.drain().then_inc(core.used, 1)
                        else:
                            pe.drain().then_inc(core.products, QUARTERS)

                gate_and_up(0, first)
                with pe.Fori(0, last) as e:
                    gate_and_up(e + 1, c_in(e + 1))
                    down(e, c_out(e))
                down(last, first + 2 * last + 1)

            @block.scalar
            def _(act):
                def activate(n, c):
                    for f in range(2):
                        act.wait_ge(core.products, QUARTERS * c + 2 * f + 1)
                        nc.scalar.activation(silu_g[:, f, :], core.ps[:, f, :], ACT.Silu).then_inc(activated, 1)

                activate(0, first)
                with act.Fori(0, last) as e:
                    act.wait_ge(hidden_ready, 2 * e + 2)
                    activate(e + 1, c_in(e + 1))

            @block.vector
            def _(dve):
                def gated(n, c):
                    for f in range(2):
                        dve.wait_ge(activated, 2 * n + f + 1)
                        dve.wait_ge(core.products, QUARTERS * c + 2 * f + 2)
                        nc.vector.tensor_tensor(silu_g[:, f, :], silu_g[:, f, :], core.ps[:, 2 + f, :], ALU.mult).then_inc(banks_read, 1)

                def split_hidden():
                    dve.drain()
                    for f in range(2):
                        split(nc, dve, silu_g[:, f, :], hidden[:, 0, f, :], hidden[:, 1, f, :]).then_inc(hidden_ready, 1)

                def add(n, half):
                    for t in range(NT):
                        dve.wait_ge(outputs, 8 * n + 4 * half + t + 1)
                        part = core.x[:, t, half * BANK:(half + 1) * BANK]
                        nc.vector.scalar_tensor_tensor(part, core.ps[:, 4 + t, :], combine[:, t, bass.ds(n, 1)], part,
                                                       ALU.mult, ALU.add).then_inc(added, 1)

                dve.sem_inc(banks_read, 2)
                dve.sem_inc(added, 4)
                nc.vector.tensor_scalar(core.x[:], core.x[:], ALPHA, None, ALU.mult)
                split_first(nc, core, dve, start, first)
                split_piece(nc, core, dve, first + 1, 0)
                gated(0, first)
                split_piece(nc, core, dve, first + 1, 1)
                split_hidden()
                with dve.Fori(0, last) as e:
                    split_piece(nc, core, dve, c_out(e), 0, 2 * BANK)
                    gated(e + 1, c_in(e + 1))
                    split_piece(nc, core, dve, c_out(e), 1, 2 * BANK)
                    add(e, 0)
                    split_piece(nc, core, dve, c_out(e) + 1, 0)
                    add(e, 1)
                    split_piece(nc, core, dve, c_out(e) + 1, 1)
                    split_hidden()
                add(last, 0)
                split_piece(nc, core, dve, first + 2 * EXPERTS, 0)
                add(last, 1)


def second_block(nc, core, d):
    norm(nc, core, "norm0_2", core.x, core.h, core.hT, 1e-5, False, core.row_a[:], core.row_b[:],
         [(core.row_a[:], d["ln0_g_2"]), (core.row_b[:], d["ln0_b_2"])])
    second_mixer(nc, core, d)
    norm(nc, core, "norm1_2", core.h, core.x, core.hT, 1e-5, False, core.row_a[:], core.row_b[:],
         [(core.row_a[:], d["ln1_g_2"][0]), (core.row_b[:], d["ln1_b_2"][0])])
    moe(nc, core, d)
    norm(nc, core, "norm2_2", core.x, core.x, None, 1e-5, False, core.row_a[:], core.row_b[:],
         [(core.row_a[:], d["ln2_g_2"][0]), (core.row_b[:], d["ln2_b_2"][0])])


def plan_two(d):
    w = d["w_in_2"][0]
    one = lambda name, lo, n=1: [(name, kmajor(w, lo + i * BANK, BANK)) for i in range(n)]
    few = lambda name, lo, n: [(name, kmajor(w, lo, n))]
    wide = lambda name, m: [(name, kmajor(m, i * BANK, BANK)) for i in range(2)]
    plan = one("aqkv", 0, 3) + few("beta_dt", 1536, 8)
    plan += one("ag", 1544) + one("ma", 5656, 2) + wide("br_a", d["w_br_a_2"][0])
    plan += one("bqk", 2056) + one("bv", 2568) + few("blr", 3080, 16)
    plan += one("bg", 3096) + one("mb", 6680, 2) + wide("br_b", d["w_br_b_2"][0])
    plan += one("cq", 3608) + one("cf", 4120) + one("ci", 4632)
    plan += one("cg", 5144) + one("mc", 7704, 2) + wide("br_c", d["w_br_c_2"][0])
    plan += wide("out2", d["w_out_2"][0])
    plan += [("router", kmajor(d["w_router_2"], 0, EXPERTS))]
    into = [("expert", kmajor(d["w_gate_up_2"][e], 0, 2 * FF)) for e in range(EXPERTS)]
    down = [("expert", [d["w_down_2"][0][e][:, half * BANK:(half + 1) * BANK].rearrange("(k p) n -> p k n", p=P) for half in range(2)])
            for e in range(EXPERTS)]
    plan += into[0:1]
    for e in range(1, EXPERTS):
        plan += [into[e], down[e - 1]]
    plan += down[-1:]
    return plan


M_HEADS, M_DQK = 8, 64
S_HEADS, S_HEADDIM, S_GROUPS = 16, 64, 4
D_FF = 2752
FF_TILES = -(-D_FF // P)
FF_CHUNKS = -(-D_FF // 256)


def causal_heads(nc, core, name, heads, rows, bias, keys, queries, share, scale, values, outputs, finish):
    row_bank = (0, 7)
    with buffers(nc, weights=[P, 3, PACKED], edge=[P, NT, P]) as (weights, edge), \
            stage(nc, name, "spread", "edged", "decayed", "scored", "applied", "summed", "finished") as (
                block, spread, edged, decayed, scored, applied, summed, finished):
        @block.tensor
        def _(pe):
            for h in range(heads + 2):
                if h < heads:
                    if h >= 2:
                        pe.wait_ge(decayed, h - 1)
                    nc.tensor.matmul(core.ps[:, row_bank[h % 2], :], core.ident[0:heads, h:h + 1].to_broadcast([heads, P]), rows,
                                     start=True, stop=True).then_inc(spread, 1)
                    if h % share == 0:
                        for s in range(NT):
                            if h:
                                pe.wait_ge(applied, NT * (h - 1) + s + 1)
                            nc.tensor.matmul(core.ps[:, 1 + s, 0:SEQ - s * P], keys(h, s), queries(h, s * P), start=True, stop=True).then_inc(scored, 1)
                if h >= 2:
                    g = h - 2
                    pe.wait_ge(applied, NT * (g + 1))
                    if g:
                        pe.wait_ge(finished, g)
                    for t in range(NT):
                        for s in range(t + 1):
                            mm = nc.tensor.matmul(outputs(t), strip(weights[:, g % 3, :], s, (t - s) * P, (t - s + 1) * P), values(g, s),
                                                  start=s == 0, stop=s == t)
                    mm.then_inc(summed, 1)

        @block.scalar
        def _(act):
            for h in range(heads):
                act.wait_ge(edged, h + 1)
                if h >= 3:
                    act.wait_ge(summed, h - 2)
                decay_strips(nc, core, row_bank[h % 2], edge, lambda s: bias(h, s), weights[:, h % 3])
                act.drain().then_inc(decayed, 1)

        @block.vector
        def _(dve):
            for h in range(heads + 3):
                if h >= 3:
                    dve.wait_ge(summed, h - 2)
                    finish(dve, h - 3).then_inc(finished, 1)
                if 1 <= h <= heads:
                    dve.wait_ge(decayed, h)
                if h < heads:
                    dve.wait_ge(spread, h + 1)
                    nc.vector.tensor_tensor(edge[:], core.ps[:, row_bank[h % 2], :].rearrange("p (s t) -> p s t", s=NT),
                                            core.causal[:].unsqueeze(1).to_broadcast([P, NT, P]), ALU.add).then_inc(edged, 1)
                if 1 <= h <= heads:
                    g = h - 1
                    for s in range(NT):
                        dve.wait_ge(scored, NT * (g // share) + s + 1)
                        nc.vector.scalar_tensor_tensor(strip(weights[:, g % 3, :], s), core.ps[:, 1 + s, 0:SEQ - s * P], scale(g, s),
                                                       strip(weights[:, g % 3, :], s), ALU.mult, ALU.mult).then_inc(applied, 1)


def mlstm_branch(nc, core, d, y):
    H = M_HEADS
    with buffers(nc, qkT=[P, KD, SEQ], v=[P, NT, H, P + 1], i_row=[H, SEQ], f_row=[H, SEQ], sum_row=[H, SEQ],
                 i_bias=[H, 1], f_bias=[H, 1], cols=[P, 2, H, NT], den=[P, 2, 2, 1]) as (
            qkT, v, i_row, f_row, sum_row, i_bias, f_bias, cols, den):
        with buffers(nc, taps=[P, 4, KD], conv_bias=[P, KD]) as (taps, conv_bias):
            project(nc, core, "mlstm_in", core.hT, [
                ("mqk", 2, "feature", ("conv", taps, conv_bias, 4, feature_tiles(qkT))),
                ("mv", 2, "token", ("act", ACT.Copy, lambda t, j: v[:, t, 4 * j:4 * j + 4, 0:P])),
                ("mif", 1, [(0, H), (H, H)], ("act", ACT.Copy, row_buffers(i_row, f_row)))],
                    loads=[(taps[:], d["m_conv_c_3"]), (conv_bias[:], d["m_conv_b_c_3"]), (i_bias[:], d["m_i_bias_c_3"]),
                           (f_bias[:], d["m_f_bias_c_3"])])
        with stage(nc, "mlstm_bias") as (block,):
            @block.vector
            def _(dve):
                nc.vector.tensor_scalar(f_bias[:], f_bias[:], -1.0, None, ALU.mult)
                nc.vector.memset(v[:, :, :, P:P + 1], 1.0)
        soft_maximum(nc, "mlstm_soft", [(f_row[:], sum_row[:], -1.0, f_bias[:], 0.0, 0.0)])
        top_row = f_row
        with stage(nc, "mlstm_gates", "ready") as (block, ready):
            @block.vector
            def _(dve):
                nc.vector.tensor_tensor_scan(sum_row[:], core.one_row[0:H, :], f_row[:], 0.0, ALU.mult, ALU.add)
                dve.drain()
                nc.vector.scalar_tensor_tensor(i_row[:], i_row[:], i_bias[:], sum_row[:], ALU.add, ALU.add)
                dve.drain()
                nc.vector.tensor_tensor_scan(top_row[:], core.one_row[0:H, :], i_row[:], -3e38, ALU.mult, ALU.max)
                dve.drain()
                nc.vector.tensor_scalar(top_row[:], top_row[:], -1.0, None, ALU.mult)
                dve.drain()
                nc.vector.tensor_tensor(sum_row[:], sum_row[:], top_row[:], ALU.add).then_inc(ready, 1)

            @block.scalar
            def _(act):
                act.wait_ge(ready, 1)
                nc.scalar.activation(sum_row[:], sum_row[:], ACT.Exp)
        row_columns(nc, core, "mlstm_cols", [i_row, sum_row], cols, H)
        half = lambda h: slice(h % 2 * M_DQK, (h % 2 + 1) * M_DQK)
        out = core.ps[:, 5:7, 0:2 * (P + 1)].rearrange("p b (t f) -> p b t f", t=2)

        def finish(dve, h):
            floor = cols[:, 1, h, :].rearrange("p (b t) -> p b t", b=2)
            nc.vector.scalar_tensor_tensor(den[:, :, :, 0], out[:, :, :, P], -1.0, floor, ALU.mult, ALU.max)
            dve.drain()
            nc.vector.tensor_tensor(den[:, :, :, 0], den[:, :, :, 0], out[:, :, :, P], ALU.max)
            dve.drain()
            nc.vector.reciprocal(den[:], den[:])
            dve.drain()
            return nc.vector.tensor_tensor(y[:, :, h * P:(h + 1) * P].rearrange("p (b t) f -> p b t f", b=2), out[:, :, :, 0:P],
                                           den[:].to_broadcast([P, 2, 2, P]), ALU.mult)

        causal_heads(nc, core, "mlstm", H, top_row[:], lambda h, s: cols[:, 0, h, s:s + 1],
                     lambda h, s: qkT[half(h), H // 2 + h // 2, s * P:(s + 1) * P], lambda h, lo: qkT[half(h), h // 2, lo:],
                     1, lambda h, s: M_DQK ** -0.5, lambda h, s: v[:, s, h, :], lambda t: out[:, t // 2, t % 2, :], finish)


def mamba_branch(nc, core, d, y):
    H, tiles = S_HEADS, 2 * KD
    with buffers(nc, xbc=[P, tiles, SEQ], dt_row=[H, SEQ], cs_row=[H, SEQ], dt_bias=[H, 1], a_rate=[H, 1], skip=[P, H],
                 cols=[P, 2, H, NT]) as (xbc, dt_row, cs_row, dt_bias, a_rate, skip, cols):
        with buffers(nc, taps=[P, 4, tiles], conv_bias=[P, tiles]) as (taps, conv_bias):
            project(nc, core, "mamba_in", core.hT, [
                ("xbc", 4, "feature", ("conv", taps, conv_bias, 4, feature_tiles(xbc))),
                ("sdt", 1, [(0, H)], ("act", ACT.Copy, row_buffers(dt_row)))],
                    loads=[(taps[:], d["s_conv_c_3"]), (conv_bias[:], d["s_conv_b_c_3"]), (dt_bias[:], d["s_dt_bias_c_3"]),
                           (a_rate[:], d["s_a_log_c_3"]), (skip[:], d["s_d_3"][0, :].partition_broadcast(P))])
        soft_maximum(nc, "mamba_soft", [(dt_row[:], cs_row[:], 1.0, dt_bias[:], 0.0, 0.0)])
        with buffers(nc, rates=[H, SEQ]) as (rates,):
            with stage(nc, "mamba_decay", "ready") as (block, ready):
                @block.scalar
                def _(act):
                    nc.scalar.activation(a_rate[:], a_rate[:], ACT.Exp).then_inc(ready, 1)

                @block.vector
                def _(dve):
                    dve.wait_ge(ready, 1)
                    nc.vector.tensor_scalar(rates[:], dt_row[:], a_rate[:], -1.0, ALU.mult, ALU.mult)
                    dve.drain()
                    nc.vector.tensor_tensor_scan(cs_row[:], core.one_row[0:H, :], rates[:], 0.0, ALU.mult, ALU.add)
            row_columns(nc, core, "mamba_cols", [dt_row, cs_row], cols, H)
            with stage(nc, "mamba_values", "turned") as (block, turned):
                @block.tensor
                def _(pe):
                    for t in range(NT):
                        for f in range(KD):
                            mm = nc.tensor.transpose(core.ps[:, 2 * t + f // 4, f % 4 * P:(f % 4 + 1) * P], xbc[:, f, t * P:(t + 1) * P], core.ident[:])
                        mm.then_inc(turned, 1)

                @block.scalar
                def _(act):
                    for t in range(NT):
                        act.wait_ge(turned, t + 1)
                        nc.scalar.copy(y[:, t, :].rearrange("p (b f) -> p b f", b=2), core.ps[:, 2 * t:2 * t + 2, :])

                @block.vector
                def _(dve):
                    nc.vector.tensor_scalar(cols[:, 1], cols[:, 1], -1.0, None, ALU.mult)
            share = H // S_GROUPS
            span = lambda h: slice(h * S_HEADDIM, (h + 1) * S_HEADDIM)

            def finish(dve, h):
                return nc.vector.scalar_tensor_tensor(y[:, :, span(h)], y[:, :, span(h)], skip[:, h:h + 1],
                                                      core.ps[:, 5, 0:NT * S_HEADDIM].rearrange("p (t f) -> p t f", t=NT), ALU.mult, ALU.add)

            causal_heads(nc, core, "mamba", H, cs_row[:], lambda h, s: cols[:, 1, h, s:s + 1],
                         lambda h, s: xbc[:, KD + h // share, s * P:(s + 1) * P], lambda h, lo: xbc[:, KD + S_GROUPS + h // share, lo:],
                         share, lambda h, s: cols[:, 0, h, s:s + 1], lambda h, s: y[:, s, span(h)], lambda t: core.ps[:, 5, t * S_HEADDIM:(t + 1) * S_HEADDIM], finish)


def third_mixer(nc, core, d):
    with buffers(nc, y=[P, NT, D]) as (y,):
        def close(name, gain_name, gate_plan, share_plan, out_plan, width, first):
            with buffers(nc, yT=([P, 2, KD, SEQ], F32R), share=[P, NT, D]) as (yT, share):
                gate = over(nc, yT, "gate", [P, NT, D])
                project(nc, core, f"{name}_gates", core.hT, [(gate_plan, 2, "token", ("act", ACT.Sigmoid if first else ACT.Silu, columns(gate))),
                                                             (share_plan, 2, "token", ("act", ACT.Sigmoid, columns(share)))],
                        loads=[(core.row_a[:], d[gain_name][0, :].partition_broadcast(P))],
                        beside=gated_heads(nc, core, y, gate if first else None, core.row_a[:], width, None if first else gate))
                transpose(nc, core, f"{name}_T", y, two_parts(yT))
                project(nc, core, f"{name}_out", two_parts(yT), [(out_plan, 2, "token", ("mul" if first else "mad", columns(share), columns(core.x)))])

        mlstm_branch(nc, core, d, y)
        close("mlstm", "m_norm_g_3", "mo", "ga", "pa", P, True)
        mamba_branch(nc, core, d, y)
        close("mamba", "s_norm_g_3", "sz", "gb", "pb", D // S_GROUPS, False)
    with buffers(nc, yT=([P, 2, KD, SEQ], F32R)) as (yT,):
        transpose(nc, core, "mix3_T", core.x, two_parts(yT))
        project(nc, core, "out3", two_parts(yT), [("out3", 2, "token", ("axpy", ALPHA, columns(core.h)))])


def conv_ffn(nc, core, d):
    first = take(core, "up", FF_CHUNKS)
    with buffers(nc, taps=[P, 2, 3, FF_TILES], conv_bias=[P, 2, FF_TILES], hidden=[P, FF_TILES, SEQ], gate=[P, 2, 2, SEQ]) as (
            taps, conv_bias, hidden, gate):
        load_rows(nc, "ffn_loads", [(taps[:], d["f_conv_c_3"]), (conv_bias[:], d["f_conv_b_c_3"])])
        value = core.tmp[:].rearrange("p (a f) n -> p a f n", a=2)

        def chunk_parts(j):
            half = D_FF % 256 if isinstance(j, int) else 256
            return 2 * half, [(part, f, part * half + f * P, min(P, half - f * P)) for part in range(2) for f in range(2)]

        start = plan_splits(core, 2 * core.taken + 1)
        idle = lambda turn, odd: turn - (first + (first % 2 != odd)) // 2 + 1
        with stage(nc, "ffn_up", "free0", "free1", "convolved", "activated") as (block, free0, free1, convolved, activated):
            free = (free0, free1)

            @block.sync
            def _(sp):
                load_ahead(core, sp, core.splits + 2)

            @block.tensor
            def _(pe):
                for j, turn, odd, c in pairs(pe, first, FF_CHUNKS):
                    pe.wait_ge(free[odd], idle(turn, odd))
                    width, parts = chunk_parts(j)
                    for half in range(2):
                        pe.wait_ge(core.split[half], c + 1)
                        w = weights(core, half, P, KD // 2, width)
                        for part, f, lo, m in parts:
                            for k in range(KD // 2):
                                kk = half * KD // 2 + k
                                mm = product(nc, core.ps[0:m, 4 * odd + 2 * part + f, :], [v[:, k, lo:lo + m] for v in w],
                                             halves(core.hT, kk, slice(None)), kk == 0, kk == KD - 1)
                            if half == 1:
                                mm.then_inc(core.products, 1)
                        if half == 0:
                            mm.then_inc(core.used, 1)

            @block.vector
            def _(dve):
                dve.sem_inc(free0, 1)
                dve.sem_inc(free1, 1)
                split_first(nc, core, dve, start, first)
                for j, _, odd, c in pairs(dve, first, FF_CHUNKS):
                    split_piece(nc, core, dve, c + 1, 0)
                    if not isinstance(c, int):
                        split_piece(nc, core, dve, c + 1, 1)
                    for part, f, _, m in chunk_parts(j)[1]:
                        dve.wait_ge(core.products, QUARTERS * c + 2 * part + f + 1)
                        done = convolve(nc, dve, core.ps[0:m, 4 * odd + 2 * part + f, :], taps[:, part], conv_bias[:, part], 3,
                                        2 * j + f, (gate, value)[part][0:m, odd, f, :])
                        if part == 0:
                            done.then_inc(convolved, 1)
                    dve.drain().then_inc(free[odd], 1)
                    for _, f, _, m in chunk_parts(j)[1][0:2]:
                        dve.wait_ge(activated, 2 * j + f + 1)
                        nc.vector.tensor_tensor(hidden[0:m, bass.ds(2 * j + f, 1), :].rearrange("p o n -> p (o n)"),
                                                gate[0:m, odd, f, :], value[0:m, odd, f, :], ALU.mult)

            @block.scalar
            def _(act):
                for j, _, odd, c in pairs(act, first, FF_CHUNKS):
                    for _, f, _, m in chunk_parts(j)[1][0:2]:
                        act.wait_ge(convolved, 2 * j + f + 1)
                        nc.scalar.activation(gate[0:m, odd, f, :], gate[0:m, odd, f, :], ACT.Silu).then_inc(activated, 1)

        chunks = -(-FF_TILES // 4)
        down = take(core, "down", chunks)
        start = plan_splits(core, 2 * core.taken)
        high = over(nc, core.h, "hidden_high", [P, 8, SEQ], F32R)
        low = over(nc, core.hT_whole, "hidden_low", [P, 8, SEQ], F32R)
        tile_rows = lambda k: min(P, D_FF - k * P)
        chunk_tiles = lambda j: range(4 * j, min(4 * j + 4, FF_TILES))
        with stage(nc, "ffn_down", "hidden_split") as (block, hidden_split):
            @block.sync
            def _(sp):
                load_ahead(core, sp, core.splits + 2)

            @block.tensor
            def _(pe):
                for j in range(chunks):
                    for half in range(2):
                        pe.wait_ge(core.split[half], down + j + 1)
                        m, k2, _ = core.plan[down + j][1][half].shape
                        w = weights(core, half, m, k2, D)
                        tiles = [4 * j + half * k2 + k for k in range(k2)]
                        pe.wait_ge(hidden_split, tiles[-1] + 1)
                        for t in range(NT):
                            for side in range(2):
                                for k, tile in enumerate(tiles):
                                    mm = product(nc, core.ps[:, 2 * t + side, :], [v[0:m, tile % 8, t * P:(t + 1) * P] for v in (high, low)],
                                                 [v[:, k, side * BANK:(side + 1) * BANK] for v in w], tile == 0, tile == FF_TILES - 1)
                            if half == 1:
                                mm.then_inc(core.products, 1)
                        if half == 0:
                            mm.then_inc(core.used, 1)

            @block.vector
            def _(dve):
                def split_hidden(j):
                    if j >= 2:
                        dve.wait_ge(core.products, QUARTERS * (down + j - 1))
                    for k in chunk_tiles(j):
                        m = tile_rows(k)
                        split(nc, dve, hidden[0:m, k, :], high[0:m, k % 8, :], low[0:m, k % 8, :]).then_inc(hidden_split, 1)

                split_first(nc, core, dve, start, down)
                split_hidden(0)
                for j in range(chunks - 1):
                    split_hidden(j + 1)
                    for half in range(2):
                        split_piece(nc, core, dve, down + j + 1, half)
                for t in range(NT):
                    dve.wait_ge(core.products, QUARTERS * (down + chunks - 1) + t + 1)
                    x = core.x[:, t, :].rearrange("p (b n) -> p b n", b=2)
                    nc.vector.scalar_tensor_tensor(x, x, ALPHA, core.ps[:, 2 * t:2 * t + 2, :], ALU.mult, ALU.add)


def third_block(nc, core, d):
    norm(nc, core, "norm0_3", core.x, core.h, core.hT, 1e-5, False, core.row_a[:], core.row_b[:],
         [(core.row_a[:], d["in_ln_g_3"]), (core.row_b[:], d["in_ln_b_3"])])
    third_mixer(nc, core, d)
    norm(nc, core, "norm1_3", core.h, core.x, core.hT, 1e-5, False, core.row_a[:], core.row_b[:],
         [(core.row_a[:], d["ln1_g_3"][0]), (core.row_b[:], d["ln1_b_3"][0])])
    conv_ffn(nc, core, d)
    norm(nc, core, "norm2_3", core.x, core.x, None, 1e-5, False, core.row_a[:], core.row_b[:],
         [(core.row_a[:], d["ln2_g_3"][0]), (core.row_b[:], d["ln2_b_3"][0])])


def plan_three(d):
    w = d["w_in_3"][0]
    plan = []
    add = lambda name, m, lo, n: plan.extend((name, kmajor(m, lo + i * BANK, BANK)) for i in range(n))
    add("mqk", w, 0, 2)
    add("mv", w, 1024, 2)
    plan.append(("mif", kmajor(w, 3072, 2 * M_HEADS)))
    add("mo", w, 2048, 2)
    add("ga", w, 6176, 2)
    add("pa", d["p_a_3"][0], 0, 2)
    add("xbc", w, 4112, 4)
    plan.append(("sdt", kmajor(w, 6160, S_HEADS)))
    add("sz", w, 3088, 2)
    add("gb", w, 7200, 2)
    add("pb", d["p_b_3"][0], 0, 2)
    add("out3", d["w_out_3"][0], 0, 2)
    plan += [("up", kmajor(d["w_up_pairs_3"], c * BANK, min(BANK, 2 * D_FF - c * BANK))) for c in range(FF_CHUNKS)]
    rows = d["w_down_3"][0]
    tiles = lambda lo, hi: rows[lo * P:hi * P, :].rearrange("(k p) n -> p k n", p=P)
    plan += [("down", [tiles(4 * c, 4 * c + 2), tiles(4 * c + 2, 4 * c + 4)]) for c in range(5)]
    plan += [("down", [tiles(20, 21), rows[21 * P:D_FF, :].rearrange("(k p) n -> p k n", p=D_FF % P)])]
    return plan


def build(nc, d, out):
    core = Core()
    core.plan, core.loaded, core.taken, core.splits = plan_one(d) + plan_two(d) + plan_three(d), 0, 0, 0
    with ExitStack() as ctx:
        sb = lambda n, s, dt=F32: place(nc, ctx, n, s, dt)
        core.x = sb("x_tokens", [P, NT, D])
        core.h = sb("h_tokens", [P, NT, D])
        core.hT_whole = sb("h_features", [P, 2, KD, SEQ], F32R)
        core.hT = two_parts(core.hT_whole)
        core.raw = sb("ring_raw", [P, 2, PIECE])
        core.high = sb("ring_high", [P, 2, PIECE], F32R)
        core.low = sb("ring_low", [P, 2, PIECE], F32R)
        core.ident = sb("ident", [P, P])
        core.row_a = sb("row_a", [P, D])
        core.row_b = sb("row_b", [P, D])
        core.tmp = sb("evacuation_tmp", [P, NT, BANK])
        core.bn = sb("bn_parts", [P, 32, 6])
        core.mv = sb("mean_var", [P, 32, 2])
        core.minus_half = sb("minus_half", [P, 32, 1])
        core.ps = ctx.enter_context(nc.psum_tensor("psum", [P, 8, BANK], F32))
        sem = lambda n: ctx.enter_context(nc.semaphore(n))
        core.landed = [sem(f"piece_landed{h}") for h in range(2)]
        core.split = [sem(f"piece_split{h}") for h in range(2)]
        core.used = sem("half_used")
        core.products = sem("products")
        stored = sem("stored")

        with stage(nc, "start", "zeroed") as (block, zeroed):
            @block.gpsimd
            def _(pool):
                nc.gpsimd.memset(core.minus_half[:], -0.5)
                nc.gpsimd.memset(core.ident[:], 0.0).then_inc(zeroed, 1)
                pool.wait_ge(zeroed, 1)
                nc.gpsimd.affine_select(out=core.ident[:], in_=core.ident[:], compare_op=ALU.not_equal, fill=1.0,
                                        base=0, pattern=[[-1, P]], channel_multiplier=1)
        block_one(nc, core, d)
        core.ones = sb("ones", [P, P])
        core.causal = sb("causal", [P, P])
        core.one_row = sb("one_row", [16, SEQ])
        core.tile_row = sb("tile_row", [P, SEQ])
        with stage(nc, "later_start", "zeroed") as (block, zeroed):
            @block.gpsimd
            def _(pool):
                nc.gpsimd.memset(core.ones[:], 1.0)
                nc.gpsimd.memset(core.one_row[:], 1.0)
                nc.gpsimd.memset(core.causal[:], 0.0)
                nc.gpsimd.memset(core.tile_row[:], 1.0).then_inc(zeroed, 1)
                pool.wait_ge(zeroed, 1)
                nc.gpsimd.affine_select(out=core.causal[:], in_=core.causal[:], compare_op=ALU.is_ge, fill=-1e30,
                                        base=0, pattern=[[1, P]], channel_multiplier=-1)
                nc.gpsimd.memset(core.tile_row[:].rearrange("p (t n) -> p t n", t=NT)[:, :, 0], 0.0)
        second_block(nc, core, d)
        third_block(nc, core, d)
        with nc.Block() as block:
            @block.sync
            def _(sp):
                sp.dma_start(out.rearrange("b (t p) f -> p (b t) f", p=P), core.x[:]).then_inc(stored, 16)
                sp.wait_ge(stored, 16)


def constants():
    half = RET_QK_DIM // 2
    inv = np.float32(10000.0) ** (-np.arange(half, dtype=np.float32) * np.float32(2.0) / np.float32(RET_QK_DIM))
    ang = np.arange(SEQ, dtype=np.float32)[:, None] * inv[None, :]
    tokens = lambda a: np.ascontiguousarray(a.reshape(NT, P, -1).transpose(1, 0, 2)).astype(np.float32)
    gamma = 1.0 - 2.0 ** (-5.0 - np.arange(RET_HEADS, dtype=np.float64))
    lag = np.arange(SEQ)[None, :] - np.arange(P)[:, None]
    decay = np.where(lag[:, None, :] >= 0, gamma[None, :, None] ** np.maximum(lag, 0)[:, None, :], 0.0)
    row = np.arange(P)
    levels = [(row[:, None] // (2 * b) == row[None, :] // (2 * b)) & (row[:, None] % (2 * b) < b) & (row[None, :] % (2 * b) >= b)
              for b in (2 ** n for n in range(LEVELS))]
    own = (row[:, None] // SUB == row[None, :] // SUB) & (row[None, :] >= row[:, None])
    sums = np.broadcast_to(np.arange(P + SUB)[None, :] % SUB == SUB - 1, (P, P + SUB))
    order = np.arange(MEMBERS)
    later = {"const_levels": np.stack(levels, 1), "const_own_block": own, "const_sums": sums,
             "const_head_sums": np.stack([sums * (row[:, None] // 64 == h) for h in range(2)], 1),
             "const_before": order[None, :] < order[:, None]}
    later = {k: np.ascontiguousarray(v).astype(np.float32) for k, v in later.items()}
    return {**later, "const_cos": tokens(np.cos(ang)), "const_sin": tokens(np.sin(ang)),
            "const_ret_decay": decay.astype(np.float32)}


def column_tiles(v):
    return np.ascontiguousarray(v.reshape(-1, P).T)


def laid_out(inputs):
    a = {k: np.ascontiguousarray(v) for k, v in inputs.items()}
    a["sgu_w_t"] = np.ascontiguousarray(np.transpose(a.pop("sgu_w")[0], (2, 0, 1)))
    a["sgu_b_t"] = np.ascontiguousarray(a.pop("sgu_b")[0].T)
    a["sub_keys_t"] = np.ascontiguousarray(
        np.transpose(a.pop("peer_sub_keys")[0].reshape(PAIRS, PEER_KEYS, P), (2, 0, 1)))
    a["c_col"] = column_tiles(a.pop("c")[0])
    a["gdn_conv_c_2"] = np.stack([column_tiles(tap) for tap in a.pop("gdn_conv_2")[0]], 1)
    a["gdn_dt_bias_c_2"] = a.pop("gdn_dt_bias_2").reshape(-1, 1)
    a["gdn_a_log_c_2"] = a.pop("gdn_a_log_2").reshape(-1, 1)
    a["gla_b2_c_2"] = column_tiles(a.pop("gla_b2_2")[0])
    a["hgrn_lb_c_2"] = column_tiles(a.pop("hgrn_lb_logits_2")[0])
    a["w_gate_up_2"] = np.concatenate([a.pop("w_gate_2")[0], a.pop("w_up_2")[0]], -1)
    taps = lambda w: np.stack([column_tiles(tap) for tap in w], 1)
    for name in ("m_conv", "s_conv"):
        a[f"{name}_c_3"] = taps(a.pop(f"{name}_w_3")[0])
        a[f"{name}_b_c_3"] = column_tiles(a.pop(f"{name}_b_3")[0])
    for name in ("m_i_bias", "m_f_bias", "s_dt_bias", "s_a_log"):
        a[f"{name}_c_3"] = a.pop(f"{name}_3").reshape(-1, 1)
    gate_value = lambda v: (v[..., :D_FF], v[..., D_FF:])
    whole = lambda v: np.pad(v, [(0, 0)] * (v.ndim - 1) + [(0, FF_TILES * P - D_FF)])
    a["f_conv_c_3"] = np.stack([taps(whole(w)) for w in gate_value(a.pop("f_conv_w_3")[0])], 1)
    a["f_conv_b_c_3"] = np.stack([column_tiles(whole(v)) for v in gate_value(a.pop("f_conv_b_3")[0])], 1)
    up = gate_value(a.pop("w_up_3")[0])
    a["w_up_pairs_3"] = np.concatenate([half[:, lo:lo + 256] for lo in range(0, D_FF, 256) for half in up], 1)
    a.update(constants())
    return a


def kernel(**inputs):
    import concourse.bacc as bacc
    from concourse.bass_utils import run_bass_kernel_spmd as run

    nc = bacc.Bacc("TRN2", target_bir_lowering=False, num_devices=1)
    arrays = {f"in_{k}": v for k, v in laid_out(inputs).items()}
    d = {k[3:]: nc.dram_tensor(k, v.shape, mybir.dt.from_np(v.dtype), kind="ExternalInput").ap() for k, v in arrays.items()}
    out = nc.dram_tensor("out_0", (1, SEQ, D), F32, kind="ExternalOutput").ap()
    build(nc, d, out)
    return run(nc, [arrays], core_ids=[0]).results[0]["out_0"]
```
